# Optimizing a Trainium2 kernel written in Bass

```python
import jax
import jax.numpy as jnp
from jax import lax
import numpy as np
import jax, jax.numpy as jnp

D_MODEL = 1024
BATCH = 1
SEQ = 256
DEPTH = 1

CTX_LEN = 256
GRID_W = 64
CHUNK = 64
EPS = 1e-6
HG_DK = 128
HG_HEADS = D_MODEL // HG_DK
HG_DV = D_MODEL // HG_HEADS
HG_FDIM = HG_HEADS * HG_DK
HG_VDIM = HG_HEADS * HG_DV
ML_HEADS = 4
ML_DV = D_MODEL // ML_HEADS
ML_DK = ML_DV // 2
ML_QKDIM = ML_HEADS * ML_DK
ML_VDIM = ML_HEADS * ML_DV
CONV_W = 5
N_GROUPS = 4
EXPERTS_PER_GROUP = 8
N_EXPERTS = N_GROUPS * EXPERTS_PER_GROUP
TOP_K = 2
D_EXPERT = 512
SEG_SIZES = (HG_FDIM, HG_FDIM, HG_FDIM, HG_VDIM, HG_VDIM,
             ML_QKDIM, ML_QKDIM, ML_VDIM, 2 * ML_HEADS, 2 * ML_HEADS, ML_VDIM,
             D_MODEL, D_MODEL)
SEG_OFFSETS = tuple(int(o) for o in np.cumsum(SEG_SIZES))
D_IN = SEG_OFFSETS[-1]
ML_F_OFFSET = SEG_OFFSETS[8]


def rms_norm(x, g):
    xf = x.astype(jnp.float32)
    y = xf * lax.rsqrt(jnp.mean(xf * xf, axis=-1, keepdims=True) + EPS)
    return (y * g.astype(jnp.float32)).astype(x.dtype)

def head_rms_norm(y, g, n_heads):
    b, t, ch = y.shape
    yf = y.astype(jnp.float32).reshape(b, t, n_heads, ch // n_heads)
    yf = yf * lax.rsqrt(jnp.mean(yf * yf, axis=-1, keepdims=True) + EPS)
    return (yf.reshape(b, t, ch) * g.astype(jnp.float32)).astype(y.dtype)

def modulation(cvec, w_ada, b_ada):
    m = jax.nn.silu(cvec) @ w_ada + b_ada
    return jnp.split(m, 6, axis=-1)

def to_heads(a, n_heads):
    b, t, ch = a.shape
    return a.reshape(b, t, n_heads, ch // n_heads).transpose(0, 2, 1, 3)

def from_heads(a):
    b, h, t, d = a.shape
    return a.transpose(0, 2, 1, 3).reshape(b, t, h * d)

def to_colmajor(a):
    b, t, ch = a.shape
    rows = t // GRID_W
    return a.reshape(b, rows, GRID_W, ch).transpose(0, 2, 1, 3).reshape(b, t, ch)

def from_colmajor(a):
    b, t, ch = a.shape
    rows = t // GRID_W
    return a.reshape(b, GRID_W, rows, ch).transpose(0, 2, 1, 3).reshape(b, t, ch)

def flip_t(a):
    return jnp.flip(a, axis=2)

def chunked(a):
    nc = a.shape[2] // CHUNK
    a = a.reshape(a.shape[:2] + (nc, CHUNK) + a.shape[3:])
    return jnp.moveaxis(a, 2, 0)

def unchunk(a):
    a = jnp.moveaxis(a, 0, 2)
    return a.reshape(a.shape[:2] + (a.shape[2] * a.shape[3],) + a.shape[4:])

def short_conv(a, w, b):
    ch = a.shape[-1]
    pad = CONV_W // 2
    y = lax.conv_general_dilated(a, w[:, None, :].astype(a.dtype), window_strides=(1,),
                                 padding=[(pad, pad)], dimension_numbers=('NWC', 'WIO', 'NWC'),
                                 feature_group_count=ch)
    return y + b

def gla_scan(q, k, v, logf, s0):
    mask = jnp.tril(jnp.ones((CHUNK, CHUNK), dtype=bool))

    def step(s, inp):
        qc, kc, vc, lc = inp
        b = jnp.cumsum(lc, axis=2)
        diff = b[:, :, :, None, :] - b[:, :, None, :, :]
        w = jnp.exp(jnp.where(mask[:, :, None], diff, -jnp.inf))
        a = jnp.einsum('bhtk,bhtsk,bhsk->bhts', qc, w, kc)
        o = a @ vc + jnp.einsum('bhtk,bhkv->bhtv', qc * jnp.exp(b), s)
        bl = b[:, :, -1]
        s = jnp.exp(bl)[..., None] * s + jnp.einsum('bhsk,bhsv->bhkv', kc * jnp.exp(bl[:, :, None] - b), vc)
        return s, o

    s, o = lax.scan(step, s0, (chunked(q), chunked(k), chunked(v), chunked(logf)))
    return unchunk(o), s

def mlstm_scan(q, k, v, li, lf, state):
    mask = jnp.tril(jnp.ones((CHUNK, CHUNK), dtype=bool))

    def step(carry, inp):
        c_st, n_st, m_st = carry
        qc, kc, vc, ic, fc = inp
        b = jnp.cumsum(fc, axis=-1)
        d = jnp.where(mask, b[..., :, None] - b[..., None, :] + ic[..., None, :], -jnp.inf)
        g = b + m_st[..., None]
        m_t = jnp.maximum(jnp.max(d, axis=-1), g)
        p = jnp.exp(d - m_t[..., None]) * jnp.einsum('bhtk,bhsk->bhts', qc, kc)
        inter = jnp.exp(g - m_t)
        num = p @ vc + inter[..., None] * jnp.einsum('bhtk,bhkv->bhtv', qc, c_st)
        den = jnp.sum(p, axis=-1) + inter * jnp.einsum('bhtk,bhk->bht', qc, n_st)
        h = num / jnp.maximum(jnp.abs(den), jnp.exp(-m_t))[..., None]
        bl = b[..., -1]
        lw = bl[..., None] - b + ic
        m_new = jnp.maximum(bl + m_st, jnp.max(lw, axis=-1))
        decay = jnp.exp(bl + m_st - m_new)
        wk = jnp.exp(lw - m_new[..., None])[..., None] * kc
        c_st = decay[..., None, None] * c_st + jnp.einsum('bhsk,bhsv->bhkv', wk, vc)
        n_st = decay[..., None] * n_st + jnp.sum(wk, axis=2)
        return (c_st, n_st, m_new), h

    state, h = lax.scan(step, state, (chunked(q), chunked(k), chunked(v), chunked(li), chunked(lf)))
    return unchunk(h), state

def hgrn_core(hq, hff, hfb, hi, lb, s_f, s_b):
    f32 = jnp.float32
    q = to_heads(jax.nn.silu(hq.astype(f32)), HG_HEADS)
    v = to_heads(hi.astype(f32), HG_HEADS)

    def gates(hf, lbd):
        z = hf.astype(f32)
        f = lbd + (1.0 - lbd) * jax.nn.sigmoid(z)
        k = (1.0 - lbd) * jax.nn.sigmoid(-z)
        return to_heads(k, HG_HEADS), to_heads(jnp.log(f), HG_HEADS)

    kf, lff = gates(hff, lb[0])
    kb, lfb = gates(hfb, lb[1])
    o_f, s_f = gla_scan(q, kf, v, lff, s_f)
    o_b, s_b = gla_scan(flip_t(q), flip_t(kb), flip_t(v), flip_t(lfb), s_b)
    o = from_heads(o_f + flip_t(o_b))
    return o.astype(hq.dtype), s_f, s_b

def mlstm_core(hq, hk, hv, hi, hf, conv_w, conv_b, st_f, st_b, grid):
    f32 = jnp.float32
    if grid:
        hq, hk, hv, hi, hf = [to_colmajor(a) for a in (hq, hk, hv, hi, hf)]
    qk = jax.nn.silu(short_conv(jnp.concatenate([hq, hk], axis=-1), conv_w, conv_b))
    q = to_heads(qk[..., :ML_QKDIM].astype(f32), ML_HEADS) * (ML_DK ** -0.5)
    k = to_heads(qk[..., ML_QKDIM:].astype(f32), ML_HEADS)
    v = to_heads(hv.astype(f32), ML_HEADS)
    li = hi.astype(f32).transpose(0, 2, 1)
    lf = jax.nn.log_sigmoid(hf.astype(f32)).transpose(0, 2, 1)
    h_f, st_f = mlstm_scan(q, k, v, li[:, :ML_HEADS], lf[:, :ML_HEADS], st_f)
    h_b, st_b = mlstm_scan(flip_t(q), flip_t(k), flip_t(v), flip_t(li[:, ML_HEADS:]),
                           flip_t(lf[:, ML_HEADS:]), st_b)
    h = from_heads(h_f + flip_t(h_b))
    if grid:
        h = from_colmajor(h)
    return h.astype(hq.dtype), st_f, st_b

def token_mixer(h_lat, h_ctx, w_in, b_in, lb, conv_w, conv_b, hg_norm_g, ml_norm_g,
                w_pa, w_pb, w_out, need_ctx):
    f32 = jnp.float32
    p_lat = jnp.split(h_lat @ w_in + b_in, SEG_OFFSETS[:-1], axis=-1)
    p_ctx = jnp.split(h_ctx @ w_in + b_in, SEG_OFFSETS[:-1], axis=-1)
    bsz = h_lat.shape[0]
    s0 = jnp.zeros((bsz, HG_HEADS, HG_DK, HG_DV), f32)
    m0 = (jnp.zeros((bsz, ML_HEADS, ML_DK, ML_DV), f32),
          jnp.zeros((bsz, ML_HEADS, ML_DK), f32),
          jnp.zeros((bsz, ML_HEADS), f32))
    o_ctx, hs_f, hs_b = hgrn_core(p_ctx[0], p_ctx[1], p_ctx[2], p_ctx[3], lb, s0, s0)
    o_lat, _, _ = hgrn_core(p_lat[0], p_lat[1], p_lat[2], p_lat[3], lb, hs_f, hs_b)
    r_ctx, ms_f, ms_b = mlstm_core(p_ctx[5], p_ctx[6], p_ctx[7], p_ctx[8], p_ctx[9],
                                   conv_w, conv_b, m0, m0, False)
    r_lat, _, _ = mlstm_core(p_lat[5], p_lat[6], p_lat[7], p_lat[8], p_lat[9],
                             conv_w, conv_b, ms_f, ms_b, True)

    def merge(parts, o, r):
        y_a = head_rms_norm(o, hg_norm_g, HG_HEADS) * jax.nn.silu(parts[4])
        y_b = head_rms_norm(r, ml_norm_g, ML_HEADS) * jax.nn.sigmoid(parts[10])
        y = jax.nn.sigmoid(parts[11]) * (y_a @ w_pa) + jax.nn.sigmoid(parts[12]) * (y_b @ w_pb)
        return y @ w_out

    out_lat = merge(p_lat, o_lat, r_lat)
    out_ctx = merge(p_ctx, o_ctx, r_ctx) if need_ctx else None
    return out_lat, out_ctx

def hier_moe(h, w_group, b_group, w_router, b_router, w_gate, w_up, w_down):
    bsz, t, d = h.shape
    tok = h.reshape(bsz * t, d)
    n_tok = tok.shape[0]
    g_logits = (tok @ w_group + b_group).astype(jnp.float32)
    g_idx = jnp.argmax(g_logits, axis=-1)
    g_w = jnp.max(jax.nn.softmax(g_logits, axis=-1), axis=-1, keepdims=True)
    e_logits = (tok @ w_router + b_router).astype(jnp.float32).reshape(n_tok, N_GROUPS, EXPERTS_PER_GROUP)
    e_logits = e_logits[jnp.arange(n_tok), g_idx]
    top_v, top_i = lax.top_k(e_logits, TOP_K)
    top_w = jax.nn.softmax(top_v, axis=-1) * g_w
    expert_id = g_idx[:, None] * EXPERTS_PER_GROUP + top_i
    combine = jnp.sum(jax.nn.one_hot(expert_id, N_EXPERTS, dtype=jnp.float32) * top_w[..., None],
                      axis=1).astype(h.dtype)
    out = jnp.zeros_like(tok)
    for e in range(N_EXPERTS):
        a = jax.nn.silu(tok @ w_gate[e]) * (tok @ w_up[e])
        out = out + combine[:, e:e + 1] * (a @ w_down[e])
    return out.reshape(bsz, t, d)

def first_inputs(seed: int = 0) -> dict:
    key = jax.random.key(seed)
    ks = jax.random.split(key, 32)
    nrm = jax.random.normal
    f32 = jnp.float32
    b_in = 0.02 * nrm(ks[9], (DEPTH, D_IN), f32)
    forget_bias = jnp.tile(jnp.linspace(3.0, 6.0, ML_HEADS), 2)
    b_in = b_in.at[:, ML_F_OFFSET:ML_F_OFFSET + 2 * ML_HEADS].add(forget_bias)
    return {
        'x': nrm(ks[0], (BATCH, SEQ, D_MODEL), f32),
        'c': nrm(ks[1], (BATCH, D_MODEL), f32),
        'ctx': nrm(ks[2], (BATCH, CTX_LEN, D_MODEL), f32),
        'c_ctx': nrm(ks[3], (D_MODEL,), f32),
        'w_ada': 0.5 * D_MODEL ** -0.5 * nrm(ks[4], (DEPTH, D_MODEL, 6 * D_MODEL), f32),
        'b_ada': 0.02 * nrm(ks[5], (DEPTH, 6 * D_MODEL), f32),
        'norm1_g': 1.0 + 0.02 * nrm(ks[6], (DEPTH, D_MODEL), f32),
        'norm2_g': 1.0 + 0.02 * nrm(ks[7], (DEPTH, D_MODEL), f32),
        'w_in': D_MODEL ** -0.5 * nrm(ks[8], (DEPTH, D_MODEL, D_IN), f32),
        'b_in': b_in,
        'hg_lb_logits': 0.5 * nrm(ks[10], (2, DEPTH + 1, HG_FDIM), f32),
        'hg_norm_g': 1.0 + 0.02 * nrm(ks[11], (DEPTH, HG_VDIM), f32),
        'ml_conv_w': CONV_W ** -0.5 * nrm(ks[12], (DEPTH, CONV_W, 2 * ML_QKDIM), f32),
        'ml_conv_b': 0.02 * nrm(ks[13], (DEPTH, 2 * ML_QKDIM), f32),
        'ml_norm_g': 1.0 + 0.02 * nrm(ks[14], (DEPTH, ML_VDIM), f32),
        'w_branch_a': HG_VDIM ** -0.5 * nrm(ks[15], (DEPTH, HG_VDIM, D_MODEL), f32),
        'w_branch_b': ML_VDIM ** -0.5 * nrm(ks[16], (DEPTH, ML_VDIM, D_MODEL), f32),
        'w_out': D_MODEL ** -0.5 * nrm(ks[17], (DEPTH, D_MODEL, D_MODEL), f32),
        'w_group': D_MODEL ** -0.5 * nrm(ks[18], (DEPTH, D_MODEL, N_GROUPS), f32),
        'b_group': 0.01 * nrm(ks[19], (DEPTH, N_GROUPS), f32),
        'w_router': D_MODEL ** -0.5 * nrm(ks[20], (DEPTH, D_MODEL, N_EXPERTS), f32),
        'b_router': 0.01 * nrm(ks[21], (DEPTH, N_EXPERTS), f32),
        'w_gate': D_MODEL ** -0.5 * nrm(ks[22], (DEPTH, N_EXPERTS, D_MODEL, D_EXPERT), f32),
        'w_up': D_MODEL ** -0.5 * nrm(ks[23], (DEPTH, N_EXPERTS, D_MODEL, D_EXPERT), f32),
        'w_down': D_EXPERT ** -0.5 * nrm(ks[24], (DEPTH, N_EXPERTS, D_EXPERT, D_MODEL), f32),
        'final_norm_g': 1.0 + 0.02 * nrm(ks[25], (D_MODEL,), f32),
    }

def first_block(x, c, ctx, c_ctx, w_ada, b_ada, norm1_g, norm2_g, w_in, b_in, hg_lb_logits,
              hg_norm_g, ml_conv_w, ml_conv_b, ml_norm_g, w_branch_a, w_branch_b, w_out,
              w_group, b_group, w_router, b_router, w_gate, w_up, w_down, final_norm_g):
    lb_all = jnp.cumsum(jax.nn.softmax(hg_lb_logits.astype(jnp.float32), axis=1), axis=1)
    for l in range(DEPTH):
        need_ctx = l < DEPTH - 1
        sh1, sc1, g1, sh2, sc2, g2 = [m[:, None, :] for m in modulation(c, w_ada[l], b_ada[l])]
        csh1, csc1, cg1, csh2, csc2, cg2 = modulation(c_ctx, w_ada[l], b_ada[l])
        h_lat = rms_norm(x, norm1_g[l]) * (1.0 + sc1) + sh1
        h_ctx = rms_norm(ctx, norm1_g[l]) * (1.0 + csc1) + csh1
        mix_lat, mix_ctx = token_mixer(h_lat, h_ctx, w_in[l], b_in[l], lb_all[:, l], ml_conv_w[l],
                                       ml_conv_b[l], hg_norm_g[l], ml_norm_g[l], w_branch_a[l],
                                       w_branch_b[l], w_out[l], need_ctx)
        x = x + g1 * mix_lat
        h2 = rms_norm(x, norm2_g[l]) * (1.0 + sc2) + sh2
        x = x + g2 * hier_moe(h2, w_group[l], b_group[l], w_router[l], b_router[l],
                              w_gate[l], w_up[l], w_down[l])
        if need_ctx:
            ctx = ctx + cg1 * mix_ctx
            hc2 = rms_norm(ctx, norm2_g[l]) * (1.0 + csc2) + csh2
            ctx = ctx + cg2 * hier_moe(hc2, w_group[l], b_group[l], w_router[l], b_router[l],
                                       w_gate[l], w_up[l], w_down[l])
    return rms_norm(x, final_norm_g)


F_GROUP_W = 128
F_WIDTH = D_MODEL // 2
F_GROUPS = F_WIDTH // F_GROUP_W

D_INNER = (3 * D_MODEL) // 2
SSD_HEAD_DIM = 64
SSD_HEADS = D_INNER // SSD_HEAD_DIM
SSD_GROUPS = 4
D_STATE = 128
CONV_W_2 = 3
CHUNK_2 = 128
CONV_CH = D_INNER + 2 * SSD_GROUPS * D_STATE

N_BRANCH = 2
P_IN = F_WIDTH + D_INNER + CONV_CH + 2 * SSD_HEADS + N_BRANCH * D_MODEL

N_EXPERTS_2 = 16
EC_FACTOR = 2
EXPERT_FF = D_MODEL

N_MOD = 6
RMS_EPS = 1e-6


def rms_norm_2(x, w):
    xf = x.astype(jnp.float32)
    y = xf * lax.rsqrt(jnp.mean(xf * xf, axis=-1, keepdims=True) + RMS_EPS)
    return (y * w.astype(jnp.float32)).astype(x.dtype)

def modulate(x, gain, shift, scale):
    return rms_norm_2(x, gain) * (1 + scale) + shift

def centred_dwconv(u, w, b, n_rows):
    bn, length, ch = u.shape
    row_len = length // n_rows
    r = u.reshape(bn, n_rows, row_len, ch)
    pad = CONV_W_2 // 2
    rp = jnp.pad(r, ((0, 0), (0, 0), (pad, pad), (0, 0)))
    out = sum(rp[:, :, k:k + row_len] * w[k] for k in range(CONV_W_2)) + b
    return out.reshape(bn, length, ch)

def ssd_chunked(xh, dt, a, bm, cm, h0):
    bn, length, nh, hp = xh.shape
    g, n = bm.shape[2], bm.shape[3]
    hg = nh // g
    nc = length // CHUNK_2
    x = xh.reshape(bn, nc, CHUNK_2, g, hg, hp)
    dtc = dt.reshape(bn, nc, CHUNK_2, g, hg)
    bc = bm.reshape(bn, nc, CHUNK_2, g, n)
    cc = cm.reshape(bn, nc, CHUNK_2, g, n)
    acum = jnp.cumsum(dtc * a.reshape(g, hg), axis=2)
    xdt = x * dtc[..., None]
    seg = acum[:, :, :, None] - acum[:, :, None, :]
    lower = jnp.tril(jnp.ones((CHUNK_2, CHUNK_2), dtype=bool))[:, :, None, None]
    decay = jnp.where(lower, jnp.exp(jnp.where(lower, seg, 0.0)), 0.0)
    cb = jnp.einsum('bctgn,bcsgn->bctsg', cc, bc)
    y_diag = jnp.einsum('bctsg,bctsgh,bcsghp->bctghp', cb, decay, xdt)
    decay_end = jnp.exp(acum[:, :, -1:] - acum)
    states = jnp.einsum('bcsgn,bcsgh,bcsghp->bcghpn', bc, decay_end, xdt)
    chunk_decay = jnp.exp(acum[:, :, -1])

    def step(h, inp):
        dec, st = inp
        return dec[..., None, None] * h + st, h

    h_final, h_prev = lax.scan(step, h0, (jnp.moveaxis(chunk_decay, 1, 0), jnp.moveaxis(states, 1, 0)))
    h_prev = jnp.moveaxis(h_prev, 0, 1)
    y_off = jnp.einsum('bctgn,bctgh,bcghpn->bctghp', cc, jnp.exp(acum), h_prev)
    y = (y_diag + y_off).reshape(bn, length, nh, hp)
    return y, h_final

def bidir_ssd(xh, dt_raw, bm, cm, dt_bias, a_log, h0_f, h0_b):
    dt_f = jax.nn.softplus(dt_raw[:, :, 0] + dt_bias[0])
    dt_b = jax.nn.softplus(dt_raw[:, :, 1] + dt_bias[1])
    a_f = -jnp.exp(a_log[0].astype(jnp.float32))
    a_b = -jnp.exp(a_log[1].astype(jnp.float32))
    y_f, h_f = ssd_chunked(xh, dt_f, a_f, bm, cm, h0_f)
    flip = lambda t: jnp.flip(t, axis=1)
    y_b, h_b = ssd_chunked(flip(xh), flip(dt_b), a_b, flip(bm), flip(cm), h0_b)
    return y_f + flip(y_b), h_f, h_b

def token_mixer_2(h, n_rows, h0_f, h0_b, w_in, conv_w, conv_b, dt_bias, a_log, d_skip, ssd_norm,
                w_fourier, w_ssd_out, b_gate, w_out):
    bn, length, _ = h.shape
    proj = h @ w_in
    i1 = F_WIDTH
    i2 = i1 + D_INNER
    i3 = i2 + CONV_CH
    i4 = i3 + 2 * SSD_HEADS
    u_f, z, xbc, dt_raw, gate_logits = jnp.split(proj, [i1, i2, i3, i4], axis=-1)
    uf = u_f.reshape(bn, length, F_GROUPS, F_GROUP_W).astype(jnp.float32)
    f = jnp.fft.fft2(uf, axes=(1, 3), norm='ortho').real.astype(h.dtype).reshape(bn, length, F_WIDTH)
    f_branch = f @ w_fourier
    xbc = jax.nn.silu(centred_dwconv(xbc, conv_w, conv_b, n_rows))
    xs, bm, cm = jnp.split(xbc, [D_INNER, D_INNER + SSD_GROUPS * D_STATE], axis=-1)
    xh = xs.reshape(bn, length, SSD_HEADS, SSD_HEAD_DIM).astype(jnp.float32)
    bm = bm.reshape(bn, length, SSD_GROUPS, D_STATE).astype(jnp.float32)
    cm = cm.reshape(bn, length, SSD_GROUPS, D_STATE).astype(jnp.float32)
    dt_raw = dt_raw.reshape(bn, length, 2, SSD_HEADS).astype(jnp.float32)
    y, h_f, h_b = bidir_ssd(xh, dt_raw, bm, cm, dt_bias, a_log, h0_f, h0_b)
    y = y + d_skip[:, None].astype(jnp.float32) * xh
    y = y.reshape(bn, length, D_INNER).astype(h.dtype)
    y = rms_norm_2(y * jax.nn.silu(z), ssd_norm)
    s_branch = y @ w_ssd_out
    g = jax.nn.sigmoid(gate_logits.reshape(bn, length, N_BRANCH, D_MODEL) + b_gate)
    merged = g[:, :, 0] * f_branch + g[:, :, 1] * s_branch
    return merged @ w_out, h_f, h_b

def expert_choice_ffn(h, w_router, w_e_gate, w_e_up, w_e_down):
    bn, length, d = h.shape
    cap = EC_FACTOR * length // N_EXPERTS_2
    aff = jax.nn.softmax((h @ w_router).astype(jnp.float32), axis=-1)
    top_aff, top_idx = lax.top_k(jnp.swapaxes(aff, 1, 2), cap)
    xe = jax.vmap(lambda hb, ib: hb[ib])(h, top_idx)
    hid = jax.nn.silu(jnp.einsum('becd,edf->becf', xe, w_e_gate)) * jnp.einsum('becd,edf->becf', xe, w_e_up)
    ye = jnp.einsum('becf,efd->becd', hid, w_e_down) * top_aff[..., None].astype(h.dtype)
    return jax.vmap(lambda ib, yb: jnp.zeros((length, d), yb.dtype).at[ib.reshape(-1)].add(yb.reshape(-1, d)))(top_idx, ye)

def second_inputs(seed: int = 0) -> dict:
    key = jax.random.key(seed)
    ks = jax.random.split(key, 32)
    nrm = lambda k, shape, s: jax.random.normal(k, shape, jnp.float32) * s
    L = DEPTH
    dt0 = jnp.exp(jax.random.uniform(ks[12], (L, 2, SSD_HEADS), jnp.float32, np.log(1e-3), np.log(1e-1)))
    return {
        'x': nrm(ks[0], (BATCH, SEQ, D_MODEL), 1.0),
        'c': nrm(ks[1], (BATCH, D_MODEL), 1.0),
        'ctx': nrm(ks[2], (BATCH, CTX_LEN, D_MODEL), 1.0),
        'c_ctx': nrm(ks[3], (D_MODEL,), 1.0),
        'w_mod': nrm(ks[4], (L, D_MODEL, N_MOD * D_MODEL), 0.5 * D_MODEL ** -0.5),
        'b_mod': nrm(ks[5], (L, N_MOD * D_MODEL), 0.02),
        'norm_mix_pre': 1.0 + nrm(ks[6], (L, D_MODEL), 0.05),
        'norm_mix_post': 1.0 + nrm(ks[7], (L, D_MODEL), 0.05),
        'norm_ffn_pre': 1.0 + nrm(ks[8], (L, D_MODEL), 0.05),
        'norm_ffn_post': 1.0 + nrm(ks[9], (L, D_MODEL), 0.05),
        'w_in': nrm(ks[10], (L, D_MODEL, P_IN), D_MODEL ** -0.5),
        'conv_w': nrm(ks[11], (L, CONV_W_2, CONV_CH), CONV_W_2 ** -0.5),
        'conv_b': nrm(ks[13], (L, CONV_CH), 0.02),
        'dt_bias': dt0 + jnp.log(-jnp.expm1(-dt0)),
        'a_log': jnp.log(jax.random.uniform(ks[14], (L, 2, SSD_HEADS), jnp.float32, 1.0, 16.0)),
        'd_skip': 1.0 + nrm(ks[15], (L, SSD_HEADS), 0.1),
        'ssd_norm': 1.0 + nrm(ks[16], (L, D_INNER), 0.05),
        'w_fourier': nrm(ks[17], (L, F_WIDTH, D_MODEL), F_WIDTH ** -0.5),
        'w_ssd_out': nrm(ks[18], (L, D_INNER, D_MODEL), D_INNER ** -0.5),
        'b_gate': nrm(ks[19], (L, N_BRANCH, D_MODEL), 0.1),
        'w_out': nrm(ks[20], (L, D_MODEL, D_MODEL), D_MODEL ** -0.5),
        'w_router': nrm(ks[21], (L, D_MODEL, N_EXPERTS_2), D_MODEL ** -0.5),
        'w_e_gate': nrm(ks[22], (L, N_EXPERTS_2, D_MODEL, EXPERT_FF), D_MODEL ** -0.5),
        'w_e_up': nrm(ks[23], (L, N_EXPERTS_2, D_MODEL, EXPERT_FF), D_MODEL ** -0.5),
        'w_e_down': nrm(ks[24], (L, N_EXPERTS_2, EXPERT_FF, D_MODEL), EXPERT_FF ** -0.5),
    }

def second_block(x, c, ctx, c_ctx, w_mod, b_mod, norm_mix_pre, norm_mix_post, norm_ffn_pre, norm_ffn_post,
              w_in, conv_w, conv_b, dt_bias, a_log, d_skip, ssd_norm, w_fourier, w_ssd_out, b_gate, w_out,
              w_router, w_e_gate, w_e_up, w_e_down):
    bn, length, d = x.shape
    rows = length // GRID_W
    hx, hc = x, ctx
    for l in range(DEPTH):
        mod_x = (jax.nn.silu(c) @ w_mod[l] + b_mod[l]).reshape(bn, N_MOD, 1, d)
        mod_c = (jax.nn.silu(c_ctx) @ w_mod[l] + b_mod[l]).reshape(N_MOD, d)
        sh1, sc1, g1, sh2, sc2, g2 = [mod_x[:, i] for i in range(N_MOD)]
        csh1, csc1, cg1, csh2, csc2, cg2 = [mod_c[i] for i in range(N_MOD)]
        mix_w = (w_in[l], conv_w[l], conv_b[l], dt_bias[l], a_log[l], d_skip[l], ssd_norm[l],
                 w_fourier[l], w_ssd_out[l], b_gate[l], w_out[l])
        h0 = jnp.zeros((bn, SSD_GROUPS, SSD_HEADS // SSD_GROUPS, SSD_HEAD_DIM, D_STATE), jnp.float32)
        mix_c, hf_c, hb_c = token_mixer_2(modulate(hc, norm_mix_pre[l], csh1, csc1), 1, h0, h0, *mix_w)
        mix_x, _, _ = token_mixer_2(modulate(hx, norm_mix_pre[l], sh1, sc1), rows, hf_c, hb_c, *mix_w)
        hx = hx + g1 * rms_norm_2(mix_x, norm_mix_post[l])
        ffn_x = expert_choice_ffn(modulate(hx, norm_ffn_pre[l], sh2, sc2), w_router[l], w_e_gate[l], w_e_up[l], w_e_down[l])
        hx = hx + g2 * rms_norm_2(ffn_x, norm_ffn_post[l])
        if l + 1 < DEPTH:
            hc = hc + cg1 * rms_norm_2(mix_c, norm_mix_post[l])
            ffn_c = expert_choice_ffn(modulate(hc, norm_ffn_pre[l], csh2, csc2), w_router[l], w_e_gate[l], w_e_up[l], w_e_down[l])
            hc = hc + cg2 * rms_norm_2(ffn_c, norm_ffn_post[l])
    return hx


def setup_inputs(seed=0):
    out = dict(first_inputs(seed))
    for name, value in second_inputs(seed + 1).items():
        if name != "x":
            out[name + "_2"] = value
    return out


def reference(
    x, c, ctx, c_ctx, w_ada, b_ada, norm1_g, norm2_g, w_in, b_in, hg_lb_logits, hg_norm_g,
    ml_conv_w, ml_conv_b, ml_norm_g, w_branch_a, w_branch_b, w_out, w_group, b_group, w_router,
    b_router, w_gate, w_up, w_down, final_norm_g, c_2, ctx_2, c_ctx_2, w_mod_2, b_mod_2,
    norm_mix_pre_2, norm_mix_post_2, norm_ffn_pre_2, norm_ffn_post_2, w_in_2, conv_w_2,
    conv_b_2, dt_bias_2, a_log_2, d_skip_2, ssd_norm_2, w_fourier_2, w_ssd_out_2, b_gate_2,
    w_out_2, w_router_2, w_e_gate_2, w_e_up_2, w_e_down_2,
):
    x = first_block(
        x, c, ctx, c_ctx, w_ada, b_ada, norm1_g, norm2_g, w_in, b_in, hg_lb_logits, hg_norm_g,
        ml_conv_w, ml_conv_b, ml_norm_g, w_branch_a, w_branch_b, w_out, w_group, b_group,
        w_router, b_router, w_gate, w_up, w_down, final_norm_g,
    )
    return second_block(
        x, c_2, ctx_2, c_ctx_2, w_mod_2, b_mod_2, norm_mix_pre_2, norm_mix_post_2,
        norm_ffn_pre_2, norm_ffn_post_2, w_in_2, conv_w_2, conv_b_2, dt_bias_2, a_log_2,
        d_skip_2, ssd_norm_2, w_fourier_2, w_ssd_out_2, b_gate_2, w_out_2, w_router_2,
        w_e_gate_2, w_e_up_2, w_e_down_2,
    )


_drawn_inputs = setup_inputs


def setup_inputs(seed=0):
    import zlib

    import numpy as np

    out = dict(_drawn_inputs(seed))
    spreads = {}
    factors = {'norm1_g': 3.444,
     'norm2_g': 4.703,
     'hg_lb_logits': 3.125,
     'hg_norm_g': 3.387,
     'ml_conv_b': 6.155,
     'ml_norm_g': 8.0,
     'b_group': 3.417,
     'b_router': 4.895,
     'norm_ffn_post_2': 4.01}
    for name, (base, spread) in spreads.items():
        noise = np.random.default_rng([zlib.crc32(name.encode()), seed]).standard_normal(out[name].shape)
        drawn = base * np.exp(spread * noise) if base else spread * noise
        out[name] = jnp.asarray(drawn.astype(out[name].dtype))
    for name, factor in factors.items():
        out[name] = (out[name] * factor).astype(out[name].dtype)
    return out
```

```python
import numpy as np
import concourse.bass as bass
from concourse import mybir
from concourse.alu_op_type import AluOpType as ALU
from contextlib import ExitStack

F32 = mybir.dt.float32
ACT = mybir.ActivationFunctionType
AX = mybir.AxisListType

P = 128
D = 1024
KT = D // P
SEQ = 256
CTX = 256
TOK = CTX + SEQ
NC = TOK // P
LAT = CTX // P
GRID = 64
ROWS = SEQ // GRID
EPS = 1e-6
HG_H = 8
ML_H, ML_DV = 4, 256
LEVELS = 7
N_EXP, D_EXP = 32, 512
N_GRP, PER_GRP = 4, 8
D_SSD, SSD_H, HP, SSD_G = 1536, 24, 64, 4
CONV2 = D_SSD + 2 * SSD_G * P
N_EXP2, CAP = 16, 32
BIG = 1e30
FIRST_STAGE_SEM = 150

O_HQ, O_HFF, O_HFB, O_HI, O_GA, O_MQ, O_MK, O_MV = 0, 1024, 2048, 3072, 4096, 5120, 5632, 6144
O_MI, O_GB, O_G1, O_G2 = 7168, 7184, 8208, 9232
O_UF, O_Z, O_XBC, O_DT, O_GL = 0, 512, 2048, 4608, 4656
ORDER = ((0, 1, 2, 3), (1, 0, 3, 2))

PARAMS = [
    ("b_ada", "b_ada", 0, 48), ("b_mod", "b_mod_2", 0, 48),
    ("b_hq", "b_in", O_HQ, 8), ("b_hff", "b_in", O_HFF, 8), ("b_hfb", "b_in", O_HFB, 8),
    ("norm1", "norm1_g", 0, 8),
    ("b_ga", "b_in", O_GA, 8), ("b_mq", "b_in", O_MQ, 4), ("b_mk", "b_in", O_MK, 4),
    ("b_gb", "b_in", O_GB, 8), ("b_g1", "b_in", O_G1, 8), ("b_g2", "b_in", O_G2, 8),
    ("norm2", "norm2_g", 0, 8), ("final", "final_norm_g", 0, 8),
    ("lb", "hg_lb_logits", 0, 32), ("hg_g", "hg_norm_g", 0, 8), ("ml_g", "ml_norm_g", 0, 8),
    ("cb1", "ml_conv_b", 0, 8),
    ("cw1", "ml_conv_w", 0, 40), ("cw2", "conv_w_2", 0, 60), ("cb2", "conv_b_2", 0, 20),
    ("mix_pre", "norm_mix_pre_2", 0, 8),
    ("mix_post", "norm_mix_post_2", 0, 8), ("ffn_pre", "norm_ffn_pre_2", 0, 8),
    ("ffn_post", "norm_ffn_post_2", 0, 8), ("ssd_g", "ssd_norm_2", 0, 12), ("b_gate", "b_gate_2", 0, 16),
    ("c", "c", 0, 8), ("c_ctx", "c_ctx", 0, 8), ("c2", "c_2", 0, 8), ("c_ctx2", "c_ctx_2", 0, 8),
]
N_PAR = sum(n for *_, n in PARAMS)
PAR_TILES = -(-N_PAR // P)


def param_columns():
    at, out = 0, {}
    for name, _, _, n in PARAMS:
        out[name] = (at, n)
        at += n
    return out


def constants():
    t = np.arange(P)
    sel, masks = [], []
    for flip in (False, True):
        cols, ms = [], []
        for lev in range(LEVELS):
            m = P >> (lev + 1)
            mid = (t // (2 * m)) * 2 * m + m
            second = t % (2 * m) >= m
            s, tt = t[:, None], t[None, :]
            c = np.where(second[None, :], (s >= mid[None, :]) & (s <= tt), (s > tt) & (s < mid[None, :]))
            cols.append(c)
            same = (t[:, None] // (2 * m)) == (t[None, :] // (2 * m))
            ms.append(same & ~second[:, None] & second[None, :])
        cols.append(t[:, None] <= t[None, :])
        cols.append(t[:, None] > t[None, :])
        ms.append(np.eye(P, dtype=bool))
        if flip:
            cols = [c[::-1, ::-1] for c in cols]
            ms = [c[::-1, ::-1] for c in ms]
        sel.append(np.concatenate(cols, 1))
        masks.append(np.concatenate(ms, 1))
    w = np.arange(P)[:, None] * np.arange(P)[None, :] % P * (2 * np.pi / P)
    l = np.arange(SEQ)[:, None] * np.arange(SEQ)[None, :] % SEQ * (2 * np.pi / SEQ)
    scale = 1.0 / np.sqrt(SEQ * P)
    f = np.float32
    rows = np.zeros((N_GRP, N_GRP * P))
    for h in range(N_GRP):
        rows[h, h * P:(h + 1) * P] = 1
    rows32 = np.zeros((N_EXP, N_EXP * P))
    for h in range(N_EXP):
        rows32[h, h * P:(h + 1) * P] = 1
    return {
        "k_sel": np.concatenate(sel, 1).astype(f), "k_mask": np.concatenate(masks, 1).astype(f),
        "k_dftw": np.concatenate([np.cos(w), np.sin(w)], 1).astype(f),
        "k_dftl": np.concatenate([np.cos(l) * scale, -np.sin(l) * scale], 1).astype(f),
        "k_ident": np.eye(P).astype(f), "k_rows4": rows.astype(f), "k_rows32": rows32.astype(f),
        "k_iota": np.tile(np.arange(SEQ), (P, 1)).astype(f),
    }


def bcast(ap, shape):
    return ap.broadcast_to(shape)


class Arena:

    def __init__(self, tensor, at, end):
        self.tensor, self.at, self.end = tensor, at, end

    def take(self, *dims, parts=P):
        n = 1
        for d in dims:
            n *= d
        assert self.at + n <= self.end, (self.at, n, self.end)
        v = self.tensor[0:parts, self.at:self.at + n]
        self.at += n
        if len(dims) == 2:
            v = v.rearrange("p (a b) -> p a b", b=dims[1])
        if len(dims) == 3:
            v = v.rearrange("p (a b c) -> p a b c", b=dims[1], c=dims[2])
        return v


class Steps:

    def __init__(self, sem):
        self.sem, self.n = sem, 0

    def do(self, eng, ins):
        ins.then_inc(self.sem, 1)
        self.n += 1
        eng.wait_ge(self.sem, self.n)


class Ring:

    def __init__(self, slots, loaded, used):
        self.slots, self.loaded, self.used = slots, loaded, used
        self.queue, self.sent, self.taken = [], 0, 0

    def plan(self, blocks):
        self.queue += blocks
        return len(self.queue)

    def send(self, sp, until):
        n = len(self.slots)
        while self.sent < min(until, len(self.queue)):
            src, i = self.queue[self.sent], self.sent
            if i >= n:
                sp.wait_ge(self.used[i % n], i // n)
            dst = self.slots[i % n][:, 0:src.shape[1] * src.shape[2]].rearrange("p (k c) -> p k c", c=src.shape[2])
            sp.dma_start(dst, src).then_inc(self.loaded[i % n], 16)
            self.sent += 1

    def take(self, pe):
        n, i = len(self.slots), self.taken
        pe.wait_ge(self.loaded[i % n], 16 * (i // n + 1))
        src = self.queue[i]
        self.taken += 1
        return (self.slots[i % n][:, 0:src.shape[1] * src.shape[2]].rearrange("p (k c) -> p k c", c=src.shape[2]),
                self.used[i % n])


def col_blocks(w, first, n, kt=KT, width=512):
    v = w.rearrange("(k p) n -> p k n", p=P)
    return [v[:, :, c:min(c + width, first + n)] for c in range(first, first + n, width)]


def row_blocks(w, kt=4):
    v = w.rearrange("(k p) n -> p k n", p=P)
    return [v[:, k:k + kt, :] for k in range(0, w.shape[0] // P, kt)]


def shaped(d):
    out = {}
    for name, ap in d.items():
        if name.startswith("k_"):
            out[name] = ap
        elif len(ap.shape) >= 3 and ap.shape[0] == 1 and name not in ("x", "ctx", "ctx_2"):
            out[name] = ap[0]
        else:
            out[name] = ap
    return out


class Net:

    def __init__(self, nc, d, out, last=99):
        self.nc, self.d, self.out, self.last = nc, d, out, last

    def sem(self, name):
        self.stage_sems += 1
        return self.stage.enter_context(self.nc.semaphore(name, num=FIRST_STAGE_SEM + self.stage_sems - 1))

    def lasting_sem(self, name):
        return self.ctx.enter_context(self.nc.semaphore(name))

    def build(self):
        with ExitStack() as self.ctx:
            nc, d = self.nc, self.d
            words = 53000
            self.arena_t = self.ctx.enter_context(nc.sbuf_tensor("arena", [P, words], F32))
            self.ps = self.ctx.enter_context(nc.psum_tensor("ps", [P, 8, 512], F32))
            A = self.A = Arena(self.arena_t, 0, words)
            self.ident = A.take(P)
            self.ones = A.take(P)
            self.par = A.take(PAR_TILES * P)
            self.cp = param_columns()
            self.k_sel = A.take(2 * (LEVELS + 2) * P)
            self.xT = A.take(KT, SEQ)
            self.hT = A.take(KT, TOK)
            self.mod1 = A.take(48, 2)
            self.mod2 = A.take(48, 2)
            self.lbs = A.take(2, 16)
            self.silu_c = A.take(2, 8, 2)
            self.gain1 = A.take(8, 2)
            self.gain2 = A.take(8, 2)
            slots = [A.take(4096) for _ in range(3)]
            self.ring = Ring(slots, [self.lasting_sem(f"ring_loaded{i}") for i in range(3)],
                             [self.lasting_sem(f"ring_used{i}") for i in range(3)])
            self.vs = Steps(self.lasting_sem("vector_step"))
            self.ss = Steps(self.lasting_sem("scalar_step"))
            self.gs = Steps(self.lasting_sem("pool_step"))
            self.work = A.at
            R = self.ring
            w1, w2 = d["w_in"], d["w_in_2"]
            self.ends = {}
            self.ends["mod1"] = R.plan(col_blocks(d["w_ada"], 0, 6 * D))
            self.ends["mod2"] = R.plan(col_blocks(d["w_mod_2"], 0, 6 * D))
            for half in range(2):
                c = 512 * half
                self.ends[f"hgrn{half}"] = R.plan([b for o in (O_HFF, O_HFB, O_HI, O_HQ)
                                                   for b in col_blocks(w1, o + c, 512)])
            self.ends["mlstm"] = R.plan(col_blocks(w1, O_MQ, 2048))
            self.ends["gates1"] = R.plan(col_blocks(w1, O_GA, 1024) + col_blocks(w1, O_GB, 3072)
                                         + col_blocks(d["w_branch_a"], 0, D) + col_blocks(d["w_branch_b"], 0, D)
                                         + col_blocks(d["w_out"], 0, D))
            self.ends["xbc"] = R.plan(col_blocks(w2, O_XBC, CONV2))
            self.ends["rest2"] = R.plan(col_blocks(w2, O_UF, 512) + col_blocks(w2, O_Z, D_SSD) + col_blocks(w2, O_GL, 2 * D))
            self.ends["merge2"] = R.plan(row_blocks(d["w_fourier_2"]) + col_blocks(d["w_ssd_out_2"], 0, D, width=256)
                                         + col_blocks(d["w_out_2"], 0, D))
            self.stages()

    def P_(self, name):
        a, n = self.cp[name]
        return self.par[:, a:a + n]

    def stages(self):
        todo = [lambda: self.setup(), lambda: self.modulation(), lambda: self.gla(0), lambda: self.gla(1),
                lambda: self.mlstm_in(), lambda: self.mlstm(), lambda: self.merge1(), lambda: self.router1(),
                lambda: self.moe1(), lambda: self.ssd_in(), lambda: self.ssd(), lambda: self.ssd_out(),
                lambda: self.merge2(), lambda: self.route2(), lambda: self.moe2(), lambda: self.finish()]
        for stage in todo[:self.last + 1]:
            self.stage_sems = 0
            with ExitStack() as self.stage:
                stage()
                self.nc.all_engine_barrier(sems_to_clear=range(FIRST_STAGE_SEM, FIRST_STAGE_SEM + self.stage_sems))
        with self.nc.Block() as block:
            @block.sync
            def _(sp):
                for i in range(3):
                    n = -(-(self.ring.sent - i) // 3)
                    if n > 0:
                        sp.wait_ge(self.ring.loaded[i], 16 * n)

    def setup(self):
        nc, d, ring, ps = self.nc, self.d, self.ring, self.ps
        A = Arena(self.arena_t, self.work, self.A.end)
        rows = A.take(PAR_TILES, P)
        xin = A.take(4, D)
        raw = A.take(KT, TOK)
        sq = A.take(TOK)
        rstd = A.take(TOK)
        self.rawctx = raw
        sig = A.take(2, 8, 2)
        consts, pars, xl = self.sem("consts_loaded"), self.sem("params_loaded"), self.sem("x_loaded")
        zeroed, par_t, par_c = self.sem("zeroed"), self.sem("params_turned"), self.sem("params_kept")
        x_t, x_c = self.sem("x_turned"), self.sem("x_kept")
        vs, ss = self.vs, self.ss
        n_par_dma = [0]
        pieces = []
        at = 0
        for name, src, first, n in PARAMS:
            flat = d[src].rearrange(" ".join("abcdef"[:len(d[src].shape)]) + " -> (" + " ".join("abcdef"[:len(d[src].shape)]) + ")")
            v = flat[first:first + n * P].rearrange("(r c) -> r c", c=P)
            done = 0
            while done < n:
                tile, row = divmod(at, P)
                m = min(n - done, P - row)
                pieces.append((tile, row, m, v[done:done + m, :]))
                at += m
                done += m
        last_rows = at - (PAR_TILES - 1) * P

        with nc.Block() as block:
            @block.sync
            def _(sp):
                sp.dma_start(self.ident, d["k_ident"]).then_inc(consts, 16)
                sp.dma_start(self.k_sel, d["k_sel"]).then_inc(consts, 16)
                for i in range(2):
                    sp.dma_start(xin[:, i, :], d["ctx"][0, i * P:(i + 1) * P, :]).then_inc(xl, 16)
                for i in range(2):
                    sp.dma_start(xin[:, 2 + i, :], d["x"][0, i * P:(i + 1) * P, :]).then_inc(xl, 16)
                ring.send(sp, 3)

            @block.scalar
            def _(act):
                act.wait_ge(zeroed, 2)
                for tile, row, m, v in pieces:
                    act.dma_start(rows[row:row + m, tile, :], v).then_inc(pars, 16)

            @block.vector
            def _(dve):
                dve.memset(self.ones, 1.0).then_inc(zeroed, 1)
                dve.memset(rows[:, PAR_TILES - 1, :], 0.0).then_inc(zeroed, 1)
                for i in range(PAR_TILES):
                    dve.wait_ge(par_t, i + 1)
                    dve.tensor_copy(self.par[:, i * P:(i + 1) * P], ps[:, i % 2, 0:P]).then_inc(par_c, 1)
                for k in range(KT):
                    dve.wait_ge(x_t, k + 1)
                    dve.tensor_copy(raw[:, k, :], ps[:, 2 + k % 4, :]).then_inc(x_c, 1)

            @block.tensor
            def _(pe):
                pe.wait_ge(consts, 32)
                pe.wait_ge(pars, 16 * len(pieces))
                for i in range(PAR_TILES):
                    if i >= 2:
                        pe.wait_ge(par_c, i - 1)
                    pe.transpose(ps[:, i % 2, 0:P], rows[:, i, :], self.ident).then_inc(par_t, 1)
                pe.wait_ge(xl, 64)
                for k in range(KT):
                    if k >= 4:
                        pe.wait_ge(x_c, k - 3)
                    for i in range(4):
                        ins = pe.transpose(ps[:, 2 + k % 4, i * P:(i + 1) * P], xin[:, i, k * P:(k + 1) * P], self.ident)
                    ins.then_inc(x_t, 1)
        self.raw = raw
        names = [("c", "c_ctx"), ("c2", "c_ctx2")]
        logits = self.P_("lb").rearrange("p (d l h) -> p d l h", d=2, l=2)
        lb, one_lb = self.lbs[:, 0, :], self.lbs[:, 1, :]
        inputs_set, sigmoids = self.sem("silu_inputs"), self.sem("silu_sigmoids")
        with nc.Block() as block:
            @block.vector
            def _(dve):
                for b in range(2):
                    for v in range(2):
                        dve.tensor_copy(self.silu_c[:, b, :, v], self.P_(names[b][v])).then_inc(inputs_set, 1)
                dve.tensor_tensor(one_lb.rearrange("p (d h) -> p d h", d=2), logits[:, :, 0, :], logits[:, :, 1, :],
                                  ALU.subtract).then_inc(inputs_set, 1)
                dve.wait_ge(sigmoids, 2)
                dve.tensor_tensor(self.silu_c, self.silu_c, sig, ALU.mult)
                dve.tensor_scalar(one_lb, lb, -1.0, 1.0, ALU.mult, ALU.add)
                dve.tensor_copy(self.xT, raw[:, :, CTX:TOK])

            @block.scalar
            def _(act):
                act.wait_ge(inputs_set, 5)
                act.activation(lb, one_lb, ACT.Sigmoid).then_inc(sigmoids, 1)
                act.activation(sig, self.silu_c, ACT.Sigmoid).then_inc(sigmoids, 1)
        self.rms("norm1", raw, KT, TOK, rstd, self.hT)
        with nc.Block() as block:
            @block.vector
            def _(dve):
                dve.tensor_tensor(self.hT, raw, bcast(rstd.unsqueeze(1), [P, KT, TOK]), ALU.mult)

    def rms(self, name, src, kt, n, out, square):
        ps = self.ps
        squared, summed = self.sem(f"{name}_squared"), self.sem(f"{name}_summed")
        meaned, rooted = self.sem(f"{name}_meaned"), self.sem(f"{name}_rooted")
        with self.nc.Block() as block:
            @block.scalar
            def _(act):
                act.activation(square, src, ACT.Square).then_inc(squared, 1)
                act.wait_ge(meaned, 1)
                act.activation(out, out, ACT.Sqrt).then_inc(rooted, 1)

            @block.tensor
            def _(pe):
                pe.wait_ge(squared, 1)
                for k in range(kt):
                    ins = pe.matmul(ps[:, 0, 0:n], self.ones, square[:, k, :], start=k == 0, stop=k == kt - 1)
                ins.then_inc(summed, 1)

            @block.vector
            def _(dve):
                dve.wait_ge(summed, 1)
                dve.tensor_scalar(out, ps[:, 0, 0:n], 1.0 / (kt * P), EPS, ALU.mult, ALU.add).then_inc(meaned, 1)
                dve.wait_ge(rooted, 1)
                dve.reciprocal(out, out)

    def modulation(self):
        nc, ring, ps = self.nc, self.ring, self.ps
        done, kept = self.sem("mod_products"), self.sem("mod_kept")
        with nc.Block() as block:
            @block.sync
            def _(sp):
                ring.send(sp, self.ends["mod2"] + 3)

            @block.tensor
            def _(pe):
                for b in range(2):
                    for blk in range(12):
                        w, used = ring.take(pe)
                        for j in range(4):
                            t = blk * 4 + j
                            for k in range(KT):
                                ins = pe.matmul(ps[:, b, 2 * t:2 * t + 2], w[:, k, j * P:(j + 1) * P],
                                                self.silu_c[:, b, k, :], start=k == 0, stop=k == KT - 1)
                        ins.then_inc(used, 1)
                    pe.drain().then_inc(done, 1)

            @block.vector
            def _(dve):
                for b, (mod, bias) in enumerate(((self.mod1, "b_ada"), (self.mod2, "b_mod"))):
                    dve.wait_ge(done, b + 1)
                    dve.tensor_tensor(mod, ps[:, b, 0:96].rearrange("p (t v) -> p t v", v=2),
                                      bcast(self.P_(bias).unsqueeze(2), [P, 48, 2]), ALU.add).then_inc(kept, 1)
                dve.wait_ge(kept, 2)
                for gain, mod, g in ((self.gain1, self.mod1, "norm1"), (self.gain2, self.mod2, "mix_pre")):
                    dve.scalar_tensor_tensor(gain, mod[:, 8:16, :], 1.0, bcast(self.P_(g).unsqueeze(2), [P, 8, 2]),
                                             ALU.add, ALU.mult).then_inc(kept, 1)
                dve.wait_ge(kept, 4)
                self.modulate(dve, self.hT, self.gain1, self.mod1)

    def modulate(self, dve, h, gain, mod):
        for k in range(KT):
            for v, (a, b) in enumerate(((CTX, TOK), (0, CTX))):
                dve.tensor_scalar(h[:, k, a:b], h[:, k, a:b], gain[:, k, v:v + 1], mod[:, k, v:v + 1],
                                  ALU.mult, ALU.add)

    def products(self, pe, blocks, made, freed, first=0):
        n = first
        for tiles in blocks:
            w, used = self.ring.take(pe)
            for lhsT, rhs, cols, kt in tiles:
                if n >= 8:
                    pe.wait_ge(freed, n - 7)
                for k in range(kt):
                    ins = pe.matmul(self.ps[:, n % 8, 0:cols], lhsT(w, k), rhs(w, k), start=k == 0, stop=k == kt - 1)
                ins.then_inc(made, 1)
                n += 1
            pe.drain().then_inc(used, 1)
        return n

    def feature_tiles(self, h, a, b, n=4):
        return [(lambda w, k, j=j: w[:, k, j * P:(j + 1) * P], lambda w, k: h[:, k, a:b], b - a, KT) for j in range(n)]

    def token_tiles(self, token_columns, width=512):
        return [(lambda w, k, t=t: t(k), lambda w, k: w[:, k, 0:width], width, KT) for t in token_columns]

    def gla(self, half):
        nc, d, ring, ps, hT = self.nc, self.d, self.ring, self.ps, self.hT
        A = Arena(self.arena_t, self.work, self.A.end)
        self.o_all = A.take(2, D)
        kk = A.take(8, TOK)
        zz = A.take(8, TOK)
        LT = A.take(8, NC, P)
        q = A.take(4, SEQ)
        v = A.take(NC, 512)
        st = A.take(8, 2, P)
        dec = A.take(8)
        mask = A.take(2, (LEVELS + 1) * P)
        brow = A.take(512)
        G = [A.take(LEVELS + 1, P) for _ in range(2)]
        X = [A.take(LEVELS, P) for _ in range(2)]
        AA = [A.take(LEVELS + 1, P) for _ in range(4)]
        QD = [A.take(P) for _ in range(4)]
        Es = [a.rearrange("p a b -> p (a b)")[:, 0:512] for a in AA[0:2]]
        KP = zz
        n = f"hgrn{half}_"
        S = lambda name: self.sem(n + name)
        lb = self.lbs.rearrange("p two (d h) -> p two d h", d=2)[:, :, :, 4 * half:4 * half + 4]

        made, freed, rows_in = S("made"), S("freed"), S("rows_loaded")
        with nc.Block() as block:
            @block.sync
            def _(sp):
                sp.dma_start(brow, d["b_in"][0:1, O_HI + 512 * half:O_HI + 512 * half + 512]
                             .partition_broadcast(P)).then_inc(rows_in, 16)
                sp.dma_start(mask, d["k_mask"].rearrange("p (d n) -> p d n", d=2)).then_inc(rows_in, 16)
                ring.send(sp, self.ends[f"hgrn{half}"] + 3)

            @block.tensor
            def _(pe):
                self.products(pe, [self.feature_tiles(hT, 0, TOK), self.feature_tiles(hT, 0, TOK),
                                   self.token_tiles([lambda k, c=c: hT[:, k, c * P:(c + 1) * P] for c in range(NC)]),
                                   self.feature_tiles(hT, CTX, TOK)], made, freed)

            @block.vector
            def _(dve):
                dve.wait_ge(rows_in, 32)
                for t in range(16):
                    dve.wait_ge(made, t + 1)
                    bank = ps[:, t % 8, :]
                    if t < 8:
                        b = self.P_("b_hff" if t < 4 else "b_hfb")[:, 4 * half + t % 4:4 * half + t % 4 + 1]
                        ins = dve.tensor_scalar(zz[:, t, :], bank, b, None, ALU.add)
                    elif t < 12:
                        ins = dve.tensor_tensor(v[:, t - 8, :], bank, brow, ALU.add)
                    else:
                        b = self.P_("b_hq")[:, 4 * half + t - 12:4 * half + t - 11]
                        ins = dve.tensor_scalar(q[:, t - 12, :], bank[:, 0:SEQ], b, None, ALU.add)
                    ins.then_inc(freed, 1)

        sig, f_made, ksig = S("sigmoids"), S("forget_made"), S("k_sigmoid")
        lbu = [lb[:, i, :, :] for i in range(2)]
        fourd = lambda a: a.rearrange("p (d h) t -> p d h t", d=2)
        with nc.Block() as block:
            @block.scalar
            def _(act):
                for dr in range(2):
                    u = slice(4 * dr, 4 * dr + 4)
                    act.activation(kk[:, u, :], zz[:, u, :], ACT.Sigmoid, scale=-1.0).then_inc(ksig, 1)
                    act.wait_ge(ksig, dr + 1)
                    act.activation(zz[:, u, :], zz[:, u, :], ACT.Sigmoid).then_inc(sig, 1)
                act.activation(q, q, ACT.Silu)
                for dr in range(2):
                    u = slice(4 * dr, 4 * dr + 4)
                    act.wait_ge(f_made, 4 * dr + 4)
                    act.activation(zz[:, u, :], zz[:, u, :], ACT.Ln)

            @block.vector
            def _(dve):
                for dr in range(2):
                    dve.wait_ge(sig, dr + 1)
                    for h in range(4):
                        dve.tensor_scalar(zz[:, 4 * dr + h, :], zz[:, 4 * dr + h, :], lbu[1][:, dr, h:h + 1],
                                          lbu[0][:, dr, h:h + 1], ALU.mult, ALU.add).then_inc(f_made, 1)
                for dr in range(2):
                    for h in range(4):
                        dve.tensor_scalar(kk[:, 4 * dr + h, :], kk[:, 4 * dr + h, :], lbu[1][:, dr, h:h + 1], None,
                                          ALU.mult)

        turned, kept = S("logf_turned"), S("logf_kept")
        with nc.Block() as block:
            @block.tensor
            def _(pe):
                for u in range(8):
                    for c in range(NC):
                        ins = pe.transpose(ps[:, u, c * P:(c + 1) * P], zz[:, u, c * P:(c + 1) * P], self.ident)
                    ins.then_inc(turned, 1)

            @block.vector
            def _(dve):
                for u in range(8):
                    dve.wait_ge(turned, u + 1)
                    dve.tensor_copy(LT[:, u, :, :].rearrange("p c f -> p (c f)"), ps[:, u, :])

        sums, exped, weighted = S("decay_sums"), S("decay_exp"), S("keys_weighted")
        kturned, kback, kmade, kdone = S("keys_turned"), S("keys_back"), S("states_made"), S("states_kept")
        sel = self.k_sel.rearrange("p (d n) -> p d n", d=2)
        rest = [sel[:, dr, (LEVELS + 1) * P:(LEVELS + 2) * P] for dr in range(2)]
        with nc.Block() as block:
            @block.tensor
            def _(pe):
                def decays(u):
                    dr, (o0, o1, o2, _) = u // 4, ORDER[u // 4]
                    if u >= 2:
                        pe.wait_ge(exped, u - 1)
                    bank = ps[:, u % 2, :]
                    pe.matmul(bank[:, o0 * P:(o0 + 1) * P], LT[:, u, o0, :], rest[dr], start=True, stop=False)
                    pe.matmul(bank[:, o0 * P:(o0 + 1) * P], LT[:, u, o1, :], self.ones, start=False, stop=True)
                    pe.matmul(bank[:, o1 * P:(o1 + 1) * P], LT[:, u, o1, :], rest[dr], start=True, stop=True)
                    pe.matmul(bank[:, 256:384], LT[:, u, o2, :], rest[dr], start=True, stop=True)
                    pe.matmul(bank[:, 384:512], LT[:, u, o2, :], self.ones, start=True, stop=True).then_inc(sums, 1)

                def turn(u):
                    pe.wait_ge(weighted, 2 * u + 2)
                    if u >= 2:
                        pe.wait_ge(kback, u - 1)
                    for c in range(3):
                        ins = pe.transpose(ps[:, 2 + u % 2, c * P:(c + 1) * P], KP[:, u, c * P:(c + 1) * P], self.ident)
                    ins.then_inc(kturned, 1)

                def state(u):
                    h, o2 = u % 4, ORDER[u // 4][2]
                    pe.wait_ge(kback, u + 1)
                    if u >= 2:
                        pe.wait_ge(kdone, 2 * u - 2)
                    bank, hv = ps[:, 4 + u % 2, :], slice(h * P, (h + 1) * P)
                    pe.matmul(bank[:, 0:P], KP[:, u, 0:P], v[:, 0, hv], start=True, stop=False)
                    pe.matmul(bank[:, 0:P], KP[:, u, P:2 * P], v[:, 1, hv], start=False, stop=True)
                    pe.matmul(bank[:, P:2 * P], KP[:, u, 2 * P:3 * P], v[:, o2, hv], start=True, stop=True).then_inc(kmade, 1)

                for step in range(10):
                    if step < 8:
                        decays(step)
                    if 1 <= step < 9:
                        turn(step - 1)
                    if step >= 2:
                        state(step - 2)

            @block.scalar
            def _(act):
                def back(u):
                    act.wait_ge(kturned, u + 1)
                    act.activation(KP[:, u, 0:384], ps[:, 2 + u % 2, 0:384], ACT.Copy).then_inc(kback, 1)
                for u in range(8):
                    act.wait_ge(sums, u + 1)
                    if u >= 2:
                        act.wait_ge(weighted, 2 * u - 2)
                    act.activation(Es[u % 2], ps[:, u % 2, :], ACT.Exp).then_inc(exped, 1)
                    if u >= 1:
                        back(u - 1)
                back(7)

            @block.vector
            def _(dve):
                def keep(u):
                    dve.wait_ge(kmade, u + 1)
                    bank = ps[:, 4 + u % 2, :]
                    dve.tensor_copy(st[:, u, 0, :], bank[:, 0:P]).then_inc(kdone, 1)
                    dve.wait_ge(kdone, 2 * u + 1)
                    dve.scalar_tensor_tensor(st[:, u, 1, :], st[:, u, 0, :], dec[:, u:u + 1], bank[:, P:2 * P],
                                             ALU.mult, ALU.add).then_inc(kdone, 1)
                for u in range(8):
                    o2 = ORDER[u // 4][2]
                    dve.wait_ge(exped, u + 1)
                    dve.tensor_copy(dec[:, u:u + 1], Es[u % 2][:, 384:385])
                    dve.tensor_tensor(KP[:, u, 0:256], Es[u % 2][:, 0:256], kk[:, u, 0:256], ALU.mult).then_inc(weighted, 1)
                    dve.tensor_tensor(KP[:, u, 256:384], Es[u % 2][:, 256:384], kk[:, u, o2 * P:(o2 + 1) * P],
                                      ALU.mult).then_inc(weighted, 1)
                    if u >= 2:
                        keep(u - 2)
                keep(6)
                keep(7)

        works = [(h, c, dr) for h in range(4) for c in (2, 3) for dr in range(2)]
        gsum, gexp, xq, xk = S("level_sums"), S("level_exp"), S("queries_weighted"), S("level_keys_weighted")
        smade, amade, omade, okept = S("scores_made"), S("scores_masked"), S("o_made"), S("o_kept")
        with nc.Block() as block:
            @block.tensor
            def _(pe):
                def level_sums(i):
                    h, c, dr = works[i]
                    if i >= 1:
                        pe.wait_ge(gexp, i)
                    for b in range(2):
                        ins = pe.matmul(ps[:, b, :], LT[:, dr * 4 + h, c, :], sel[:, dr, b * 512:(b + 1) * 512],
                                        start=True, stop=True)
                    ins.then_inc(gsum, 1)

                def scores(i):
                    h, c, dr = works[i]
                    pe.wait_ge(xk, i + 1)
                    pe.wait_ge(xq, i + 1)
                    if i >= 1:
                        pe.wait_ge(amade, i)
                    for lev in range(LEVELS + 1):
                        out = ps[:, 2 + lev // 4, lev % 4 * P:(lev % 4 + 1) * P]
                        if lev < LEVELS:
                            ins = pe.matmul(out, X[i % 2][:, lev, :], X[i % 2][:, lev, :], start=True, stop=True)
                        else:
                            ins = pe.matmul(out, kk[:, dr * 4 + h, c * P:(c + 1) * P], q[:, h, (c - 2) * P:(c - 1) * P],
                                            start=True, stop=True)
                    ins.then_inc(smade, 1)

                def outputs(i):
                    h, c, _ = works[i]
                    pe.wait_ge(amade, i + 1)
                    m = i // 2
                    if m >= 2:
                        pe.wait_ge(okept, m - 1)
                    out = ps[:, 4 + m % 2, 0:P]
                    for j in (i - 1, i):
                        dr = works[j][2]
                        for lev in range(LEVELS + 1):
                            pe.matmul(out, AA[j % 4][:, lev, :], v[:, c, h * P:(h + 1) * P],
                                      start=j == i - 1 and lev == 0, stop=False)
                        ins = pe.matmul(out, QD[j % 4], st[:, dr * 4 + h, int(c == ORDER[dr][3]), :],
                                        start=False, stop=j == i)
                    ins.then_inc(omade, 1)

                for i in range(len(works) + 2):
                    if i < len(works):
                        level_sums(i)
                    if 1 <= i <= len(works):
                        scores(i - 1)
                    if i >= 2 and i % 2 == 1:
                        outputs(i - 2)

            @block.scalar
            def _(act):
                def keep(m):
                    h, c, _ = works[2 * m]
                    act.wait_ge(omade, m + 1)
                    col = (4 * half + h) * P
                    act.activation(self.o_all[:, c - 2, col:col + P], ps[:, 4 + m % 2, 0:P], ACT.Copy).then_inc(okept, 1)
                for i in range(len(works)):
                    act.wait_ge(gsum, i + 1)
                    if i >= 2:
                        act.wait_ge(xk, i - 1)
                        act.wait_ge(xq, i - 1)
                    act.activation(G[i % 2], ps[:, 0:2, :].rearrange("p b (l t) -> p (b l) t", l=4), ACT.Exp).then_inc(gexp, 1)
                    if i >= 4 and i % 2 == 0:
                        keep(i // 2 - 2)
                keep(6)
                keep(7)

            def halves(eng, i, keys, done):
                h, c, dr = works[i]
                src = kk[:, dr * 4 + h, c * P:(c + 1) * P] if keys else q[:, h, (c - 2) * P:(c - 1) * P]
                side = (0 if keys else 1) ^ dr
                for lev in range(LEVELS):
                    m = P >> (lev + 1)
                    w = lambda a: a.rearrange("p (n two m) -> p n two m", two=2, m=m)[:, :, side, :]
                    ins = eng.tensor_tensor(w(X[i % 2][:, lev, :]), w(G[i % 2][:, lev, :]), w(src), ALU.mult)
                if not keys:
                    ins = eng.tensor_tensor(QD[i % 4], G[i % 2][:, LEVELS, :], src, ALU.mult)
                ins.then_inc(done, 1)

            @block.gpsimd
            def _(pool):
                for i in range(len(works)):
                    pool.wait_ge(gexp, i + 1)
                    if i >= 2:
                        pool.wait_ge(smade, i - 1)
                    halves(pool, i, True, xk)

            @block.vector
            def _(dve):
                def masked(i):
                    dr = works[i][2]
                    dve.wait_ge(smade, i + 1)
                    if i >= 4:
                        dve.wait_ge(omade, (i - 4) // 2 + 1)
                    dve.tensor_tensor(AA[i % 4].rearrange("p l t -> p (l t)"),
                                      ps[:, 2:4, :].rearrange("p b t -> p (b t)"), mask[:, dr, :], ALU.mult).then_inc(amade, 1)
                for i in range(len(works)):
                    dve.wait_ge(gexp, i + 1)
                    if i >= 2:
                        dve.wait_ge(smade, i - 1)
                    if i >= 4:
                        dve.wait_ge(omade, (i - 4) // 2 + 1)
                    halves(dve, i, False, xq)
                    if i >= 1:
                        masked(i - 1)
                masked(len(works) - 1)

    def mlstm_in(self):
        nc, d, ring, ps, hT = self.nc, self.d, self.ring, self.ps, self.hT
        A = Arena(self.arena_t, self.work + 2 * D, self.A.end)
        self.r_all = A.take(2, D)
        self.ml_v = V = A.take(NC, ML_H, ML_DV + 1)
        self.ml_qk = A.take(8, SEQ)
        self.ml_kc = A.take(4, CTX)
        self.ml_area = A.at
        raw = A.take(8, SEQ + 4)
        rawc = A.take(4, CTX + 4)
        wif = A.take(KT, 16)
        brow = A.take(1024)
        bif = A.take(1)
        mif = A.take(TOK)
        hp = A.take(KT, SEQ)
        S = lambda name: self.sem("mlstm_" + name)
        made, freed, small, permuted = S("made"), S("freed"), S("small_loaded"), S("permuted")
        imade = S("gate_rows_made")
        grid = lambda a: a.rearrange("p (r c) -> p c r", c=GRID)
        cols = lambda a: a.rearrange("p (c r) -> p c r", r=ROWS)
        token_cols = [lambda k, c=c: hT[:, k, c * P:(c + 1) * P] for c in range(2)] + \
                     [lambda k, c=c: hp[:, k, c * P:(c + 1) * P] for c in range(2)]
        with nc.Block() as block:
            @block.sync
            def _(sp):
                sp.dma_start(brow, d["b_in"][0:1, O_MV:O_MV + D].partition_broadcast(P)).then_inc(small, 16)
                sp.dma_start(wif, d["w_in"].rearrange("(k p) n -> p k n", p=P)[:, :, O_MI:O_MI + 16]).then_inc(small, 16)
                sp.dma_start(bif[0:16, :], d["b_in"][0:1, O_MI:O_MI + 16].rearrange("a b -> b a")).then_inc(small, 16)
                ring.send(sp, self.ends["mlstm"] + 3)

            @block.gpsimd
            def _(pool):
                pool.memset(raw, 0.0)
                pool.memset(rawc, 0.0)
                pool.memset(V[:, :, :, ML_DV:ML_DV + 1], 1.0).then_inc(permuted, 1)
                for k in range(KT):
                    pool.tensor_copy(cols(hp[:, k, :]), grid(hT[:, k, CTX:TOK])).then_inc(permuted, 1)

            @block.tensor
            def _(pe):
                def first():
                    pe.wait_ge(permuted, 1 + KT)
                self.products(pe, [self.feature_tiles(hT, CTX, TOK), self.feature_tiles(hT, 0, TOK)], made, freed)
                first()
                self.products(pe, [self.token_tiles(token_cols), self.token_tiles(token_cols)], made, freed, first=8)
                pe.wait_ge(small, 48)
                pe.wait_ge(freed, 9)
                for k in range(KT):
                    ins = pe.matmul(ps[0:16, 0, :], wif[:, k, :], hT[:, k, :], start=k == 0, stop=k == KT - 1)
                ins.then_inc(imade, 1)

            @block.vector
            def _(dve):
                dve.wait_ge(permuted, 1 + KT)
                dve.wait_ge(small, 48)
                for t in range(16):
                    dve.wait_ge(made, t + 1)
                    bank = ps[:, t % 8, :]
                    if t < 4:
                        ins = dve.tensor_scalar(cols(raw[:, t, 2:2 + SEQ]), grid(bank[:, 0:SEQ]),
                                                self.P_("b_mq")[:, t:t + 1], None, ALU.add)
                    elif t < 8:
                        b = self.P_("b_mk")[:, t - 4:t - 3]
                        dve.tensor_scalar(rawc[:, t - 4, 2:2 + CTX], bank[:, 0:CTX], b, None, ALU.add)
                        ins = dve.tensor_scalar(cols(raw[:, t, 2:2 + SEQ]), grid(bank[:, CTX:TOK]), b, None, ALU.add)
                    else:
                        blk, c = divmod(t - 8, 4)
                        ins = dve.tensor_tensor(V[:, c, 2 * blk:2 * blk + 2, 0:ML_DV],
                                                bank.rearrange("p (h v) -> p h v", v=ML_DV),
                                                brow[:, 512 * blk:512 * blk + 512].rearrange("p (h v) -> p h v", v=ML_DV), ALU.add)
                    ins.then_inc(freed, 1)
                dve.wait_ge(imade, 1)
                dve.tensor_scalar(mif[0:16, 0:CTX], ps[0:16, 0, 0:CTX], bif[0:16, :], None, ALU.add)
                dve.tensor_scalar(cols(mif[0:16, CTX:TOK]), grid(ps[0:16, 0, CTX:TOK]), bif[0:16, :], None, ALU.add)

        conv = [S(f"conv{i}") for i in range(3)]
        row_made, rows = S("rows_split"), S("rows")
        self.ml_rows = [A.take(2, TOK) for _ in range(6)]
        with nc.Block() as block:
            @block.tensor
            def _(pe):
                for g in range(4):
                    ins = pe.matmul(ps[0:4, g, :], self.ident[0:16, 4 * g:4 * g + 4], mif[0:16, :], start=True, stop=True)
                ins.then_inc(row_made, 1)

            @block.vector
            def _(dve):
                dve.wait_ge(row_made, 1)
                for which, g in ((0, 0), (1, 2)):
                    dst = self.ml_rows[which]
                    dve.tensor_copy(dst[0:4, 0, :], ps[0:4, g, :])
                    for a in (0, CTX):
                        dve.tensor_copy(dst[0:4, 1, a:a + SEQ], ps[0:4, g + 1, a:a + SEQ][:, ::-1])
                w, b = self.P_("cw1"), self.P_("cb1")
                todo = [(self.ml_qk[:, t, :], raw[:, t, :], t) for t in range(8)] + \
                       [(self.ml_kc[:, t, :], rawc[:, t, :], t + 4) for t in range(4)]
                for tap in range(5):
                    for dst, src, t in todo:
                        if tap == 0:
                            ins = dve.tensor_scalar(dst, src[:, 0:SEQ], w[:, t:t + 1], b[:, t:t + 1], ALU.mult, ALU.add)
                        else:
                            ins = dve.scalar_tensor_tensor(dst, src[:, tap:tap + SEQ], w[:, 8 * tap + t:8 * tap + t + 1], dst,
                                                           ALU.mult, ALU.add)
                    ins.then_inc(conv[0], 1)
                    dve.wait_ge(conv[0], tap + 1)
                dve.wait_ge(conv[1], 1)
                dve.tensor_scalar(self.ml_qk[:, 0:4, :], self.ml_qk[:, 0:4, :], float(P) ** -0.5, None, ALU.mult)

            @block.scalar
            def _(act):
                act.wait_ge(conv[0], 5)
                act.activation(self.ml_qk, self.ml_qk, ACT.Silu).then_inc(conv[1], 1)
                act.activation(self.ml_kc, self.ml_kc, ACT.Silu)

    def mlstm(self):
        nc, d, ps = self.nc, self.d, self.ps
        I, F, B, M, T1, T2 = [r[0:4] for r in self.ml_rows]
        A = Arena(self.arena_t, self.ml_area, self.A.end)
        arg = [A.take(4, SEQ) for _ in range(2)]
        Pm = [A.take(4, SEQ) for _ in range(2)]
        A.at = max(A.at, self.ml_area + 12 * (SEQ + 4) + 16 * KT + 1025 + TOK + KT * SEQ + 12 * TOK)
        cols = A.take(48)
        rows4 = A.take(ML_H, P)
        nat = A.take(2, TOK)
        natmu = A.take(2, SEQ)
        natem = A.take(2, SEQ)
        mask = A.take(2, 2, SEQ)
        small = A.take(4)
        S = lambda name: self.sem("ml_" + name)
        sv, sa = S("vector_rows"), S("scalar_rows")
        rowsin, turned, mset = S("rows4_loaded"), S("turned"), S("masks_set")
        incl = [self.k_sel[:, dr * (LEVELS + 2) * P + LEVELS * P:dr * (LEVELS + 2) * P + (LEVELS + 1) * P] for dr in range(2)]
        with nc.Block() as block:
            @block.sync
            def _(sp):
                sp.dma_start(rows4[0:4], d["k_rows4"].rearrange("p (a b) -> p a b", b=P)).then_inc(rowsin, 16)
                sp.wait_ge(rowsin, 16)

            @block.gpsimd
            def _(pool):
                pool.memset(mask[:, 0, 0, P:SEQ], 1.0)
                pool.memset(mask[:, 0, 1, 0:P], 0.0)
                pool.memset(mask[:, 1, 0, P:SEQ], 0.0)
                pool.memset(mask[:, 1, 1, 0:P], 1.0)
                for dr in range(2):
                    for c in range(2):
                        pool.tensor_copy(mask[:, dr, c, c * P:(c + 1) * P], incl[dr])

            @block.scalar
            def _(act):
                act.wait_ge(sv, 1)
                act.activation(T1, T1, ACT.Exp, scale=-1.0).then_inc(sa, 1)
                act.wait_ge(sa, 1)
                act.activation(T1, T1, ACT.Ln, bias=1.0).then_inc(sa, 1)
                act.wait_ge(sv, 6)
                act.activation(T2, T2, ACT.Exp, scale=-1.0).then_inc(sa, 1)

            @block.vector
            def _(dve):
                n = [0]
                def step(ins):
                    n[0] += 1
                    ins.then_inc(sv, 1)
                    dve.wait_ge(sv, n[0])
                step(dve.scalar_tensor_tensor(T1, F, -1.0, F, ALU.mult, ALU.max))
                dve.wait_ge(sa, 2)
                step(dve.scalar_tensor_tensor(F, F, 0.0, T1, ALU.min, ALU.subtract))
                dve.memset(T2, 1.0)
                dve.drain()
                for dr in range(2):
                    ins = dve.tensor_tensor_scan(B[:, dr, :], T2[:, dr, :], F[:, dr, :], 0.0, ALU.mult, ALU.add)
                step(ins)
                step(dve.tensor_tensor(I, I, B, ALU.subtract))
                for dr in range(2):
                    ins = dve.tensor_tensor_scan(M[:, dr, :], T2[:, dr, :], I[:, dr, :], 0.0, ALU.mult, ALU.max)
                step(ins)
                step(dve.tensor_tensor(T2, B, M, ALU.add))
                dve.tensor_copy(nat[0:4, 0, :], I[:, 0, :])
                for a in (0, CTX):
                    dve.tensor_copy(nat[0:4, 1, a:a + SEQ], I[:, 1, a:a + SEQ][:, ::-1])
                dve.tensor_scalar(natmu[0:4, 0, :], M[:, 0, CTX:TOK], -1.0, None, ALU.mult)
                dve.tensor_scalar(natmu[0:4, 1, :], M[:, 1, CTX:TOK][:, ::-1], -1.0, None, ALU.mult)
                dve.wait_ge(sa, 3)
                dve.tensor_copy(natem[0:4, 0, :], T2[:, 0, CTX:TOK])
                dve.tensor_copy(natem[0:4, 1, :], T2[:, 1, CTX:TOK][:, ::-1])
        with nc.Block() as block:
            @block.tensor
            def _(pe):
                for dr in range(2):
                    for c in range(NC):
                        i = dr * NC + c
                        pe.transpose(ps[:, 0, 4 * i:4 * i + 4], nat[0:4, dr, c * P:(c + 1) * P], self.ident[0:4, 0:4])
                    for c in range(2):
                        i = 8 + dr * 2 + c
                        ins = pe.transpose(ps[:, 0, 4 * i:4 * i + 4], natem[0:4, dr, c * P:(c + 1) * P], self.ident[0:4, 0:4])
                ins.then_inc(turned, 1)

            @block.vector
            def _(dve):
                dve.wait_ge(turned, 1)
                dve.tensor_copy(cols, ps[:, 0, 0:48])

        q, k, kc, V = self.ml_qk[:, 0:4, :], self.ml_qk[:, 4:8, :], self.ml_kc, self.ml_v
        units = [(h, dr) for h in range(ML_H) for dr in range(2)]
        bmade, smade, argd, exped = S("mu_rows_made"), S("scores_made"), S("arguments"), S("exped")
        pmade, pmask, nmade, nkept = S("weights_made"), S("weights_masked"), S("numerators_made"), S("outputs_kept")
        vd = S("denominators")
        tiles = {(0, 0): (0, 1, 2), (0, 1): (0, 1, 2, 3), (1, 0): (0, 1, 2, 3), (1, 1): (0, 1, 3)}
        with nc.Block() as block:
            @block.tensor
            def _(pe):
                def arguments(u):
                    h, dr = units[u]
                    if u >= 2:
                        pe.wait_ge(argd, u - 1)
                    pe.matmul(ps[:, u % 2, 0:SEQ], rows4[0:4, h, :], natmu[0:4, dr, :], start=True, stop=True).then_inc(bmade, 1)
                    if dr == 0:
                        if h >= 2:
                            pe.wait_ge(pmade, 2 * h - 2)
                        for c in range(NC):
                            lhsT = kc[:, h, c * P:(c + 1) * P] if c < LAT else k[:, h, (c - 2) * P:(c - 1) * P]
                            ins = pe.matmul(ps[:, 2 + 2 * (h % 2) + c // 2, c % 2 * SEQ:(c % 2 + 1) * SEQ], lhsT,
                                            q[:, h, :], start=True, stop=True)
                        ins.then_inc(smade, 1)

                def numerators(u):
                    h, dr = units[u]
                    pe.wait_ge(pmask, u + 1)
                    for c in range(2):
                        if u >= 1:
                            pe.wait_ge(nkept, 2 * u - 1 + c)
                        use = tiles[dr, c]
                        for i in use:
                            ins = pe.matmul(ps[:, 6 + c, 0:ML_DV + 1], Pm[u % 2][:, i, c * P:(c + 1) * P], V[:, i, h, :],
                                            start=i == use[0], stop=i == use[-1])
                        ins.then_inc(nmade, 1)
                for u in range(9):
                    if u < 8:
                        arguments(u)
                    if u >= 1:
                        numerators(u - 1)

            @block.scalar
            def _(act):
                for u in range(8):
                    act.wait_ge(argd, u + 1)
                    act.activation(arg[u % 2], arg[u % 2], ACT.Exp).then_inc(exped, 1)

            @block.gpsimd
            def _(pool):
                for u in range(8):
                    pool.wait_ge(pmade, u + 1)
                    pool.tensor_tensor(Pm[u % 2][:, 2:4, :], Pm[u % 2][:, 2:4, :], mask[:, units[u][1]], ALU.mult).then_inc(pmask, 1)

            @block.vector
            def _(dve):
                def outputs(u):
                    h, dr = units[u]
                    for c in range(2):
                        dve.wait_ge(nmade, 2 * u + c + 1)
                        num, n = ps[:, 6 + c, :], 3 * (2 * u + c)
                        em = cols[:, 32 + (dr * 2 + c) * 4 + h:33 + (dr * 2 + c) * 4 + h]
                        den, s = num[:, ML_DV:ML_DV + 1], small[:, c:c + 1]
                        dve.scalar_tensor_tensor(s, den, -1.0, em, ALU.mult, ALU.max).then_inc(vd, 1)
                        dve.wait_ge(vd, n + 1)
                        dve.tensor_tensor(s, s, den, ALU.max).then_inc(vd, 1)
                        dve.wait_ge(vd, n + 2)
                        dve.reciprocal(s, s).then_inc(vd, 1)
                        dve.wait_ge(vd, n + 3)
                        r = self.r_all[:, c, h * ML_DV:(h + 1) * ML_DV]
                        if dr == 0:
                            ins = dve.tensor_scalar(r, num[:, 0:ML_DV], small[:, c:c + 1], None, ALU.mult)
                        else:
                            ins = dve.scalar_tensor_tensor(r, num[:, 0:ML_DV], small[:, c:c + 1], r, ALU.mult, ALU.add)
                        ins.then_inc(nkept, 1)
                for u in range(8):
                    h, dr = units[u]
                    dve.wait_ge(bmade, u + 1)
                    if u >= 2:
                        dve.wait_ge(pmade, u - 1)
                    for c in range(NC):
                        i = (dr * NC + c) * 4 + h
                        ins = dve.tensor_scalar(arg[u % 2][:, c, :], ps[:, u % 2, 0:SEQ], cols[:, i:i + 1], 0.0, ALU.add, ALU.min)
                    ins.then_inc(argd, 1)
                    dve.wait_ge(exped, u + 1)
                    dve.wait_ge(smade, h + 1)
                    if u >= 2:
                        dve.wait_ge(nmade, 2 * (u - 2) + 2)
                    dve.tensor_tensor(Pm[u % 2].rearrange("p a t -> p (a t)"), arg[u % 2].rearrange("p a t -> p (a t)"),
                                      ps[:, 2 + 2 * (h % 2):4 + 2 * (h % 2), :].rearrange("p b t -> p (b t)"), ALU.mult).then_inc(pmade, 1)
                    if u >= 1:
                        outputs(u - 1)
                outputs(7)

    def merge1(self):
        nc, d, ring, ps, hT = self.nc, self.d, self.ring, self.ps, self.hT
        A = Arena(self.arena_t, self.work + 4 * D, self.A.end)
        o, r = self.o_all, self.r_all
        gates = [A.take(KT, SEQ) for _ in range(4)]
        sq = A.take(2, D)
        ss = [A.take(2, HG_H), A.take(2, ML_H)]
        S = lambda name: self.sem("merge1_" + name)
        made, freed = S("gates_made"), S("gates_kept")
        squared, summed, rooted, meaned, normed = S("squared"), S("summed"), S("rooted"), S("meaned"), S("normed")
        srcs = [(o, HG_H), (r, ML_H)]
        with nc.Block() as block:
            @block.sync
            def _(sp):
                ring.send(sp, self.ends["gates1"] - 6 + 3)

            @block.tensor
            def _(pe):
                self.products(pe, [self.feature_tiles(hT, CTX, TOK)] * 8, made, freed)

            @block.scalar
            def _(act):
                for i, (src, _) in enumerate(srcs):
                    if i == 1:
                        act.wait_ge(summed, 1)
                    act.activation(sq, src, ACT.Square).then_inc(squared, 1)
                for i in range(2):
                    act.wait_ge(meaned, i + 1)
                    act.activation(ss[i], ss[i], ACT.Sqrt).then_inc(rooted, 1)
                for t in range(32):
                    act.wait_ge(made, t + 1)
                    g, k = divmod(t, 8)
                    bias = self.P_(("b_ga", "b_gb", "b_g1", "b_g2")[g])[:, k:k + 1]
                    act.activation(gates[g][:, k, :], ps[:, t % 8, 0:SEQ], ACT.Silu if g == 0 else ACT.Sigmoid,
                                   bias=bias).then_inc(freed, 1)

            @block.vector
            def _(dve):
                for i, (src, h) in enumerate(srcs):
                    dve.wait_ge(squared, i + 1)
                    dve.reduce_sum(ss[i], sq.rearrange("p c (h v) -> p c h v", h=h), axis=AX.X).then_inc(summed, 1)
                    dve.wait_ge(summed, i + 1)
                    dve.tensor_scalar(ss[i], ss[i], float(h) / D, EPS, ALU.mult, ALU.add).then_inc(meaned, 1)
                for i, (src, h) in enumerate(srcs):
                    dve.wait_ge(rooted, i + 1)
                    dve.reciprocal(ss[i], ss[i]).then_inc(normed, 1)
                    dve.wait_ge(normed, i + 1)
                    for c in range(2):
                        v = src[:, c, :].rearrange("p (h v) -> p h v", h=h)
                        dve.tensor_tensor(v, v, bcast(ss[i][:, c, :].unsqueeze(2), [P, h, D // h]), ALU.mult)
        yT = [A.take(KT, SEQ) for _ in range(2)]
        turned, kept = S("turned"), S("turned_kept")
        grid = lambda a: a.rearrange("p (r c) -> p c r", c=GRID)
        cols = lambda a: a.rearrange("p (c r) -> p c r", r=ROWS)
        with nc.Block() as block:
            @block.tensor
            def _(pe):
                for t in range(16):
                    if t >= 8:
                        pe.wait_ge(kept, t - 7)
                    src, k = srcs[t // 8][0], t % 8
                    for c in range(2):
                        ins = pe.transpose(ps[:, t % 8, c * P:(c + 1) * P], src[:, c, k * P:(k + 1) * P], self.ident)
                    ins.then_inc(turned, 1)

            @block.vector
            def _(dve):
                for t in range(16):
                    dve.wait_ge(turned, t + 1)
                    b, k = divmod(t, 8)
                    if b == 0:
                        ins = dve.scalar_tensor_tensor(yT[0][:, k, :], ps[:, t % 8, 0:SEQ], self.P_("hg_g")[:, k:k + 1],
                                                       gates[0][:, k, :], ALU.mult, ALU.mult)
                    else:
                        ins = dve.scalar_tensor_tensor(grid(yT[1][:, k, :]), cols(ps[:, t % 8, 0:SEQ]),
                                                       self.P_("ml_g")[:, k:k + 1], grid(gates[1][:, k, :]), ALU.mult, ALU.mult)
                    ins.then_inc(kept, 1)
        y = A.take(KT, SEQ)
        t2 = [A.take(SEQ) for _ in range(2)]
        tiles = [(lambda w, k, j=j: w[:, k, j * P:(j + 1) * P], lambda w, k, b=b: yT[b][:, k, :], SEQ, KT) for b in range(2) for j in range(4)]
        self.merge_out("merge1b", [tiles[0:4]] * 2 + [tiles[4:8]] * 2, gates[2:4], y, t2, self.ends["gates1"],
                       gain=self.mod1[:, 16:24, 0])

    def merge_out(self, name, branch_tiles, gates, y, t2, end, gain=None, store=None):
        nc, ring, ps = self.nc, self.ring, self.ps
        S = lambda n: self.sem(name + "_" + n)
        made, freed, ydone, part = S("made"), S("kept"), S("y_done"), S("gated")
        with nc.Block() as block:
            @block.sync
            def _(sp):
                ring.send(sp, end)

            @block.tensor
            def _(pe):
                tiles = lambda src: [(lambda w, k, j=j: w[:, k, j * P:(j + 1) * P], lambda w, k: src[:, k, :], SEQ, KT)
                                     for j in range(4)]
                n = self.products(pe, branch_tiles, made, freed)
                pe.wait_ge(ydone, KT)
                self.products(pe, [tiles(y)] * 2, made, freed, first=n)

            @block.vector
            def _(dve):
                for t in range(24):
                    dve.wait_ge(made, t + 1)
                    b, k = divmod(t, 8)
                    bank = ps[:, t % 8, 0:SEQ]
                    if b == 0:
                        ins = dve.tensor_tensor(y[:, k, :], bank, gates[0][:, k, :], ALU.mult)
                    elif b == 1:
                        ins = dve.tensor_tensor(t2[k % 2], bank, gates[1][:, k, :], ALU.mult)
                    elif store is None:
                        ins = dve.scalar_tensor_tensor(self.xT[:, k, :], bank, gain[:, k:k + 1], self.xT[:, k, :], ALU.mult, ALU.add)
                    else:
                        ins = dve.tensor_copy(store[:, k, :], bank)
                    ins.then_inc(freed, 1)
                    if b == 1:
                        dve.wait_ge(freed, t + 1)
                        dve.tensor_tensor(y[:, k, :], y[:, k, :], t2[k % 2], ALU.add).then_inc(ydone, 1)

    def norm_modulate(self, name, src, dst, gain_col, scale, shift, A):
        rstd, sq, g = A.take(SEQ), A.take(KT, SEQ), A.take(KT)
        self.rms(name, src, KT, SEQ, rstd, sq)
        s = self.sem(name + "_scaled")
        with self.nc.Block() as block:
            @block.vector
            def _(dve):
                if scale is not None:
                    dve.scalar_tensor_tensor(g, scale, 1.0, gain_col, ALU.add, ALU.mult)
                else:
                    dve.tensor_copy(g, gain_col)
                dve.tensor_tensor(dst, src, bcast(rstd.unsqueeze(1), [P, KT, SEQ]), ALU.mult).then_inc(s, 1)
                dve.wait_ge(s, 1)
                for k in range(KT):
                    dve.tensor_scalar(dst[:, k, :], dst[:, k, :], g[:, k:k + 1], shift[:, k:k + 1] if shift is not None else None,
                                      ALU.mult, ALU.add if shift is not None else ALU.bypass)

    def router1(self):
        nc, d, ps = self.nc, self.d, self.ps
        A = Arena(self.arena_t, self.work, self.A.end)
        self.h2 = self.hT[:, :, 0:SEQ]
        self.comb = A.take(N_EXP, SEQ)
        self.moe_area = A.at
        wr = A.take(KT, N_GRP + N_EXP)
        br = A.take(N_GRP + N_EXP)
        iota = A.take(SEQ)
        rows32 = A.take(N_EXP * P)
        self.norm_modulate("norm2", self.xT, self.h2, self.P_("norm2"), self.mod1[:, 32:40, 0], self.mod1[:, 24:32, 0], A)
        S = lambda n: self.sem("router1_" + n)
        loaded, made, st, sa = S("loaded"), S("logits_made"), S("step"), S("exped")
        n = N_GRP + N_EXP
        lg, e, e2, pri = A.take(2, n), A.take(2, N_EXP), A.take(2, N_EXP), A.take(2, N_EXP)
        oh1, oh2, comb = A.take(2, N_EXP), A.take(2, N_EXP), A.take(2, N_EXP)
        gh, gex = A.take(2, N_GRP), A.take(2, N_GRP)
        desc = A.take(N_EXP)
        v = A.take(8, 2)
        combT = A.take(SEQ)
        with nc.Block() as block:
            @block.sync
            def _(sp):
                sp.dma_start(wr[:, :, 0:N_GRP], d["w_group"].rearrange("(k p) n -> p k n", p=P)).then_inc(loaded, 16)
                sp.dma_start(wr[:, :, N_GRP:n], d["w_router"].rearrange("(k p) n -> p k n", p=P)).then_inc(loaded, 16)
                sp.dma_start(br[:, 0:N_GRP], d["b_group"].partition_broadcast(P)).then_inc(loaded, 16)
                sp.dma_start(br[:, N_GRP:n], d["b_router"].partition_broadcast(P)).then_inc(loaded, 16)
                sp.dma_start(iota, d["k_iota"]).then_inc(loaded, 16)
                sp.dma_start(rows32[0:N_EXP], d["k_rows32"]).then_inc(loaded, 16)
                sp.wait_ge(loaded, 96)

            @block.tensor
            def _(pe):
                pe.wait_ge(loaded, 96)
                for c in range(2):
                    for k in range(KT):
                        ins = pe.matmul(ps[:, c, 0:n], self.h2[:, k, c * P:(c + 1) * P], wr[:, k, :], start=k == 0, stop=k == KT - 1)
                ins.then_inc(made, 1)

            @block.scalar
            def _(act):
                act.wait_ge(st, 3)
                act.activation(gex, gex, ACT.Exp).then_inc(sa, 1)
                act.wait_ge(st, 4)
                act.activation(v[:, 4, :], v[:, 4, :], ACT.Exp).then_inc(sa, 1)

            @block.vector
            def _(dve):
                vs = self.vs
                do = lambda ins: vs.do(dve, ins)
                bc = lambda a, m: bcast(a.unsqueeze(2), [P, 2, m])
                dve.wait_ge(made, 1)
                dve.wait_ge(loaded, 96)
                do(dve.tensor_tensor(lg, ps[:, 0:2, 0:n], bcast(br.unsqueeze(1), [P, 2, n]), ALU.add))
                do(dve.tensor_scalar(desc, iota[:, 0:N_EXP], -1.0, float(N_EXP), ALU.mult, ALU.add))

                def first_max(src, m, top, hot, tmp):
                    do(dve.reduce_max(top, src, axis=AX.X))
                    do(dve.tensor_tensor(tmp, src, bc(top, m), ALU.is_equal))
                    do(dve.tensor_tensor(tmp, tmp, bcast(desc[:, 0:m].unsqueeze(1), [P, 2, m]), ALU.mult))
                    do(dve.reduce_max(v[:, 7, :], tmp, axis=AX.X))
                    do(dve.tensor_tensor(hot, tmp, bc(v[:, 7, :], m), ALU.is_equal))
                g = lg[:, :, 0:N_GRP]
                first_max(g, N_GRP, v[:, 0, :], gh, pri[:, :, 0:N_GRP])
                dve.tensor_tensor(gex, g, bc(v[:, 0, :], N_GRP), ALU.subtract).then_inc(st, 3)
                do(dve.tensor_scalar(gh, gh, BIG, -BIG, ALU.mult, ALU.add))
                do(dve.tensor_tensor(e.rearrange("p c (g e) -> p c g e", g=N_GRP),
                                     lg[:, :, N_GRP:n].rearrange("p c (g e) -> p c g e", g=N_GRP),
                                     bcast(gh.unsqueeze(3), [P, 2, N_GRP, PER_GRP]), ALU.add))
                first_max(e, N_EXP, v[:, 1, :], oh1, pri)
                do(dve.scalar_tensor_tensor(e2, oh1, -3 * BIG, e, ALU.mult, ALU.add))
                first_max(e2, N_EXP, v[:, 2, :], oh2, pri)
                dve.tensor_tensor(v[:, 4, :], v[:, 2, :], v[:, 1, :], ALU.subtract).then_inc(st, 1)
                dve.wait_ge(sa, 2)
                do(dve.reduce_sum(v[:, 3, :], gex, axis=AX.X))
                do(dve.tensor_scalar(v[:, 5, :], v[:, 4, :], 1.0, None, ALU.add))
                do(dve.tensor_tensor(v[:, 5, :], v[:, 5, :], v[:, 3, :], ALU.mult))
                do(dve.reciprocal(v[:, 5, :], v[:, 5, :]))
                do(dve.tensor_tensor(v[:, 6, :], v[:, 5, :], v[:, 4, :], ALU.mult))
                do(dve.tensor_tensor(oh1, oh1, bc(v[:, 5, :], N_EXP), ALU.mult))
                do(dve.tensor_tensor(oh2, oh2, bc(v[:, 6, :], N_EXP), ALU.mult))
                do(dve.tensor_tensor(comb, oh1, oh2, ALU.add))
        turned, kept, made2, kept2 = S("turned"), S("turned_kept"), S("rows_made"), S("rows_kept")
        with nc.Block() as block:
            @block.tensor
            def _(pe):
                for c in range(2):
                    ins = pe.transpose(ps[0:N_EXP, 0, c * P:(c + 1) * P], comb[:, c, :], self.ident)
                ins.then_inc(turned, 1)
                pe.wait_ge(kept, 1)
                for i in range(N_EXP // 2):
                    if i >= 4:
                        pe.wait_ge(kept2, i - 3)
                    for j in range(2):
                        e = 2 * i + j
                        ins = pe.matmul(ps[:, 1 + i % 4, j * SEQ:(j + 1) * SEQ], rows32[0:N_EXP, e * P:(e + 1) * P], combT[0:N_EXP, :],
                                        start=True, stop=True)
                    ins.then_inc(made2, 1)

            @block.vector
            def _(dve):
                dve.wait_ge(turned, 1)
                dve.tensor_copy(combT[0:N_EXP, :], ps[0:N_EXP, 0, 0:SEQ]).then_inc(kept, 1)

            @block.scalar
            def _(act):
                for i in range(N_EXP // 2):
                    act.wait_ge(made2, i + 1)
                    act.activation(self.comb[:, 2 * i:2 * i + 2, :], ps[:, 1 + i % 4, :].rearrange("p (a t) -> p a t", a=2),
                                   ACT.Copy).then_inc(kept2, 1)

    def moe1(self):
        nc, d, ps, h2 = self.nc, self.d, self.ps, self.h2
        A = Arena(self.arena_t, self.moe_area, self.A.end)
        slots = self.ring.slots + [A.take(4096) for _ in range(3)]
        act_g = [A.take(SEQ) for _ in range(4)]
        a = [[A.take(SEQ) for _ in range(4)] for _ in range(2)]
        zero = A.take(512)
        S = lambda n: self.sem("moe1_" + n)
        loaded, used = [S(f"loaded{i}") for i in range(6)], [S(f"used{i}") for i in range(6)]
        up_made, silud, gated, ready, zeroed = S("up_made"), S("silu_made"), S("gated"), S("weighted"), S("zeroed")
        src = [d["w_gate"].rearrange("e (k p) f -> e p k f", p=P), d["w_up"].rearrange("e (k p) f -> e p k f", p=P),
               d["w_down"].rearrange("e (k p) n -> e p k n", p=P)]
        mat = [s.rearrange("p (k c) -> p k c", c=1024 if i % 3 == 2 else 512) for i, s in enumerate(slots)]
        acc = lambda o: ps[:, 4 + o // 2, o % 2 * SEQ:(o % 2 + 1) * SEQ]
        with nc.Block() as block:
            @block.sync
            def _(sp):
                for i in range(6):
                    sp.dma_start(mat[i], src[i % 3][i // 3]).then_inc(loaded[i], 16)
                with sp.Fori(1, N_EXP // 2) as it:
                    for i in range(6):
                        sp.wait_ge(used[i], it)
                        sp.dma_start(mat[i], src[i % 3][bass.ds(it * 2 + i // 3, 1)].rearrange("o p k f -> p (o k) f")
                                     ).then_inc(loaded[i], 16)

            @block.tensor
            def _(pe):
                pe.wait_ge(zeroed, 1)
                for b in range(4):
                    pe.matmul(ps[:, 4 + b, :], zero[:, 0:P], zero, start=True, stop=False, skip_group_check=True)

                def gate_up(j, it):
                    for which in range(2):
                        pe.wait_ge(loaded[3 * j + which], it * 16 + 16)
                    for f in range(4):
                        pe.wait_ge(ready, it * 8 + (4 * j + f + 1))
                        for which in range(2):
                            w = mat[3 * j + which]
                            for k in range(KT):
                                ins = pe.matmul(ps[:, f, which * SEQ:(which + 1) * SEQ], w[:, k, f * P:(f + 1) * P],
                                                h2[:, k, :], start=k == 0, stop=k == KT - 1)
                        ins.then_inc(up_made, 1)
                    pe.drain().then_inc(used[3 * j], 1)
                    pe.drain().then_inc(used[3 * j + 1], 1)

                def down(j, it):
                    w = mat[3 * j + 2]
                    pe.wait_ge(loaded[3 * j + 2], it * 16 + 16)
                    for f in range(4):
                        pe.wait_ge(ready, it * 8 + (4 * j + f + 5))
                        for o in range(KT):
                            ins = pe.matmul(acc(o), w[:, f, o * P:(o + 1) * P], a[j][f], start=False, stop=False,
                                            skip_group_check=True)
                    ins.then_inc(used[3 * j + 2], 1)
                gate_up(0, 0)
                with pe.Fori(0, N_EXP // 2 - 1) as it:
                    gate_up(1, it)
                    down(0, it)
                    gate_up(0, it + 1)
                    down(1, it)
                last = N_EXP // 2 - 1
                gate_up(1, last)
                down(0, last)
                down(1, last)
                for b in range(4):
                    pe.matmul(ps[:, 4 + b, :], zero[:, 0:P], zero, start=False, stop=True, skip_group_check=True)

            @block.scalar
            def _(act):
                with act.Fori(0, N_EXP // 2) as it:
                    for u in range(8):
                        act.wait_ge(up_made, it * 8 + (u + 1))
                        act.activation(act_g[u % 4], ps[:, u % 4, 0:SEQ], ACT.Silu).then_inc(silud, 1)

            @block.vector
            def _(dve):
                dve.memset(zero, 0.0).then_inc(zeroed, 1)
                dve.wait_ge(zeroed, 1)
                dve.sem_inc(ready, 4)
                with dve.Fori(0, N_EXP // 2) as it:
                    for u in range(8):
                        j, f = divmod(u, 4)
                        dve.wait_ge(silud, it * 8 + (u + 1))
                        dve.tensor_tensor(a[j][f], act_g[f], ps[:, f, SEQ:2 * SEQ], ALU.mult).then_inc(gated, 1)
                        dve.wait_ge(gated, it * 8 + (u + 1))
                        dve.tensor_tensor(a[j][f], a[j][f], self.comb[:, bass.ds(it * 2 + j, 1), :].rearrange("p o t -> p (o t)"),
                                          ALU.mult).then_inc(ready, 1)
        with nc.Block() as block:
            @block.sync
            def _(sp):
                self.ring.send(sp, self.ends["gates1"] + 3)

            @block.vector
            def _(dve):
                for o in range(KT):
                    dve.scalar_tensor_tensor(self.xT[:, o, :], acc(o), self.mod1[:, 40 + o, 0:1], self.xT[:, o, :], ALU.mult, ALU.add)
        A = Arena(self.arena_t, self.work, self.A.end)
        self.norm_modulate("final", self.xT, self.xT, self.P_("final"), None, None, A)

    def ssd_in(self):
        nc, d, ring, ps, hT = self.nc, self.d, self.ring, self.ps, self.hT
        A = Arena(self.arena_t, self.work, self.A.end)
        xin, raw, rstd, sq = A.take(2, D), A.take(KT, TOK), A.take(TOK), A.take(KT, TOK)
        S = lambda n: self.sem("ssd_in_" + n)
        xl, turned, kept, scaled = S("ctx_loaded"), S("ctx_turned"), S("ctx_kept"), S("scaled")
        with nc.Block() as block:
            @block.sync
            def _(sp):
                for i in range(2):
                    sp.dma_start(xin[:, i, :], d["ctx_2"][0, i * P:(i + 1) * P, :]).then_inc(xl, 16)

            @block.tensor
            def _(pe):
                pe.wait_ge(xl, 32)
                for k in range(KT):
                    for i in range(2):
                        ins = pe.transpose(ps[:, k, i * P:(i + 1) * P], xin[:, i, k * P:(k + 1) * P], self.ident)
                    ins.then_inc(turned, 1)

            @block.vector
            def _(dve):
                dve.tensor_copy(raw[:, :, CTX:TOK], self.xT)
                for k in range(KT):
                    dve.wait_ge(turned, k + 1)
                    dve.tensor_copy(raw[:, k, 0:CTX], ps[:, k, 0:CTX])
        self.rms("mix_pre", raw, KT, TOK, rstd, sq)
        with nc.Block() as block:
            @block.vector
            def _(dve):
                dve.tensor_tensor(hT, raw, bcast(rstd.unsqueeze(1), [P, KT, TOK]), ALU.mult).then_inc(scaled, 1)
                dve.wait_ge(scaled, 1)
                self.modulate(dve, hT, self.gain2, self.mod2)

        A = Arena(self.arena_t, self.work, self.A.end)
        self.s_lat = lat = A.take(20, SEQ)
        self.s_y = A.take(2, D_SSD)
        at = A.at
        rawc, rawl = A.take(16, CTX + 2), A.take(20, ROWS, GRID + 2)
        end = A.at
        A.at = at
        self.s_x, self.s_B = A.take(NC, D_SSD), A.take(NC, SSD_G * P)
        A.at = end
        self.s_ctx = ctx = A.take(16, CTX)
        self.s_H = A.take(2, 2, D_SSD)
        self.s_dt, self.s_dtA = A.take(NC, 2 * SSD_H), A.take(NC, 2 * SSD_H)
        self.s_area = A.at
        wdt, bdt, al, tmp = A.take(KT, 48), A.take(48), A.take(48), A.take(NC, 48)
        made, freed, small, zeroed, dmade = S("made"), S("freed"), S("small_loaded"), S("zeroed"), S("dt_made")
        rows = lambda a: a.rearrange("p (r c) -> p r c", c=GRID)
        with nc.Block() as block:
            @block.sync
            def _(sp):
                sp.dma_start(wdt, d["w_in_2"].rearrange("(k p) n -> p k n", p=P)[:, :, O_DT:O_DT + 48]).then_inc(small, 16)
                sp.dma_start(bdt, d["dt_bias_2"].rearrange("a b -> (a b)").partition_broadcast(P)).then_inc(small, 16)
                sp.dma_start(al, d["a_log_2"].rearrange("a b -> (a b)").partition_broadcast(P)).then_inc(small, 16)
                ring.send(sp, self.ends["xbc"] + 3)

            @block.gpsimd
            def _(pool):
                pool.memset(rawc, 0.0)
                pool.memset(rawl, 0.0).then_inc(zeroed, 1)

            @block.tensor
            def _(pe):
                self.products(pe, [self.feature_tiles(hT, 0, TOK)] * 4 + [self.feature_tiles(hT, CTX, TOK)], made, freed)
                pe.wait_ge(small, 48)
                pe.wait_ge(freed, 13)
                for c in range(NC):
                    for k in range(KT):
                        ins = pe.matmul(ps[:, 4, c * 48:(c + 1) * 48], hT[:, k, c * P:(c + 1) * P], wdt[:, k, :],
                                        start=k == 0, stop=k == KT - 1)
                ins.then_inc(dmade, 1)

            @block.vector
            def _(dve):
                dve.wait_ge(zeroed, 1)
                for t in range(20):
                    dve.wait_ge(made, t + 1)
                    bank = ps[:, t % 8, :]
                    if t < 16:
                        dve.tensor_copy(rawc[:, t, 1:1 + CTX], bank[:, 0:CTX])
                    ins = dve.tensor_copy(rawl[:, t, :, 1:1 + GRID], rows(bank[:, CTX:TOK] if t < 16 else bank[:, 0:SEQ]))
                    ins.then_inc(freed, 1)
                dve.wait_ge(dmade, 1)
                dve.tensor_tensor(self.s_dt, ps[:, 4, 0:NC * 48].rearrange("p (c n) -> p c n", n=48),
                                  bcast(bdt.unsqueeze(1), [P, NC, 48]), ALU.add)
        tap_done, silud, sv, sa = S("tap_done"), S("silu_done"), S("dt_steps"), S("dt_functions")
        with nc.Block() as block:
            @block.vector
            def _(dve):
                dt, dtA = self.s_dt, self.s_dtA
                dve.scalar_tensor_tensor(tmp, dt, -1.0, dt, ALU.mult, ALU.max).then_inc(sv, 1)
                w, b = self.P_("cw2"), self.P_("cb2")
                todo = [(rows(lat[:, t, :]), lambda tap, t=t: rawl[:, t, :, tap:tap + GRID], t) for t in range(20)] + \
                       [(ctx[:, t, :], lambda tap, t=t: rawc[:, t, tap:tap + CTX], t) for t in range(16)]
                for tap in range(3):
                    for dst, src, t in todo:
                        if tap == 0:
                            ins = dve.tensor_scalar(dst, src(tap), w[:, t:t + 1], b[:, t:t + 1], ALU.mult, ALU.add)
                        else:
                            ins = dve.scalar_tensor_tensor(dst, src(tap), w[:, 20 * tap + t:20 * tap + t + 1], dst, ALU.mult, ALU.add)
                    ins.then_inc(tap_done, 1)
                    dve.wait_ge(tap_done, tap + 1)
                dve.wait_ge(sa, 3)
                dve.scalar_tensor_tensor(dt, dt, 0.0, tmp, ALU.max, ALU.add).then_inc(sv, 1)
                dve.wait_ge(sv, 2)
                dve.scalar_tensor_tensor(dtA, dt, -1.0, bcast(al.unsqueeze(1), [P, NC, 48]), ALU.mult, ALU.mult)

            @block.scalar
            def _(act):
                act.activation(al, al, ACT.Exp).then_inc(sa, 1)
                act.wait_ge(sv, 1)
                act.activation(tmp, tmp, ACT.Exp, scale=-1.0).then_inc(sa, 1)
                act.wait_ge(sa, 2)
                act.activation(tmp, tmp, ACT.Ln, bias=1.0).then_inc(sa, 1)
                act.wait_ge(tap_done, 3)
                act.activation(lat, lat, ACT.Silu)
                act.activation(ctx, ctx, ACT.Silu)
        t2, k2 = S("x_turned"), S("x_kept")
        with nc.Block() as block:
            @block.tensor
            def _(pe):
                for t in range(16):
                    if t >= 8:
                        pe.wait_ge(k2, t - 7)
                    for c in range(NC):
                        src = ctx[:, t, c * P:(c + 1) * P] if c < 2 else lat[:, t, (c - 2) * P:(c - 1) * P]
                        ins = pe.transpose(ps[:, t % 8, c * P:(c + 1) * P], src, self.ident)
                    ins.then_inc(t2, 1)

            @block.vector
            def _(dve):
                for t in range(16):
                    dve.wait_ge(t2, t + 1)
                    dst = self.s_x[:, :, t * P:(t + 1) * P] if t < 12 else self.s_B[:, :, (t - 12) * P:(t - 11) * P]
                    dve.tensor_copy(dst, ps[:, t % 8, :].rearrange("p (c f) -> p c f", c=NC)).then_inc(k2, 1)

    def ssd(self):
        nc, ps = self.nc, self.ps
        lat, y, x, Bt, H, dt, dtA = self.s_lat, self.s_y, self.s_x, self.s_B, self.s_H, self.s_dt, self.s_dtA
        free = self.s_ctx.rearrange("p t c -> p (t c)")
        xw = [free[:, i * D_SSD:(i + 1) * D_SSD] for i in range(2)]
        xdt = xw
        CB = free[:, 2 * D_SSD:2 * D_SSD + 1024].rearrange("p (d g t) -> p d g t", d=2, g=4)
        A = Arena(self.arena_t, self.s_area, self.A.end)
        ex, wt = A.take(2, 6, SSD_H), A.take(2, 3, SSD_H)
        R = [A.take(3, P) for _ in range(2)]
        E = [A.take(3, P) for _ in range(2)]
        Pm = [A.take(3, P) for _ in range(2)]
        S = lambda n: self.sem("ssd_" + n)
        sel = self.k_sel.rearrange("p (d n) -> p d n", d=2)
        rest = [sel[:, dr, (LEVELS + 1) * P:(LEVELS + 2) * P] for dr in range(2)]
        incl = [sel[:, dr, LEVELS * P:(LEVELS + 1) * P] for dr in range(2)]
        hd = lambda a, h: a.rearrange("p (h v) -> p h v", h=h)
        dsum, dexp, wts = S("decay_sums"), S("decays"), S("weights")
        with nc.Block() as block:
            @block.tensor
            def _(pe):
                for dr in range(2):
                    o0, o1, o2, o3 = ORDER[dr]
                    da = lambda c: dtA[:, c, dr * SSD_H:(dr + 1) * SSD_H]
                    out = lambda i: ps[:, 0, (dr * 6 + i) * SSD_H:(dr * 6 + i + 1) * SSD_H]
                    pe.matmul(out(0), rest[dr], da(o0), start=True, stop=False)
                    pe.matmul(out(0), self.ones, da(o1), start=False, stop=True)
                    pe.matmul(out(1), rest[dr], da(o1), start=True, stop=True)
                    pe.matmul(out(2), rest[dr], da(o2), start=True, stop=True)
                    pe.matmul(out(3), self.ones, da(o2), start=True, stop=True)
                    for c in range(2):
                        ins = pe.matmul(out(4 + c), incl[dr], da(2 + c), start=True, stop=True)
                ins.then_inc(dsum, 1)

            @block.scalar
            def _(act):
                act.wait_ge(dsum, 1)
                act.activation(ex.rearrange("p a b c -> p (a b c)"),
                               ps[:, 0, 0:12 * SSD_H], ACT.Exp).then_inc(dexp, 1)

            @block.vector
            def _(dve):
                dve.wait_ge(dexp, 1)
                for dr in range(2):
                    for i in range(3):
                        dve.tensor_tensor(wt[:, dr, i, :], ex[:, dr, i, :], dt[:, ORDER[dr][i], dr * SSD_H:(dr + 1) * SSD_H], ALU.mult)
        xmade, smade, skept = S("x_weighted"), S("states_made"), S("states_kept")
        jobs = [(dr, i) for dr in range(2) for i in range(3)]
        with nc.Block() as block:
            @block.tensor
            def _(pe):
                for n, (dr, i) in enumerate(jobs):
                    c = ORDER[dr][i]
                    pe.wait_ge(xmade, n + 1)
                    if dr == 1 and i == 0:
                        pe.wait_ge(skept, 1)
                    if dr == 1 and i == 2:
                        pe.wait_ge(skept, 2)
                    for g in range(SSD_G):
                        ins = pe.matmul(ps[:, (4 if i == 2 else 0) + g, 0:384], Bt[:, c, g * P:(g + 1) * P],
                                        xw[n % 2][:, g * 384:(g + 1) * 384], start=i != 1, stop=i != 0)
                    ins.then_inc(smade, 1)

            @block.vector
            def _(dve):
                def weigh(n):
                    dr, i = jobs[n]
                    if n >= 2:
                        dve.wait_ge(smade, n - 1)
                    dve.tensor_tensor(hd(xw[n % 2], SSD_H), hd(x[:, ORDER[dr][i], :], SSD_H),
                                      bcast(wt[:, dr, i, :].unsqueeze(2), [P, SSD_H, HP]), ALU.mult).then_inc(xmade, 1)

                def keep(dr):
                    four = lambda a: a.rearrange("p (g n) -> p g n", g=4)
                    dve.wait_ge(smade, 3 * dr + 2)
                    dve.tensor_copy(four(H[:, dr, 0, :]), ps[:, 0:4, 0:384]).then_inc(skept, 1)
                    dve.wait_ge(skept, 2 * dr + 1)
                    dve.tensor_tensor(hd(H[:, dr, 1, :], SSD_H), hd(H[:, dr, 0, :], SSD_H),
                                      bcast(ex[:, dr, 3, :].unsqueeze(2), [P, SSD_H, HP]), ALU.mult).then_inc(wts, 1)
                    dve.wait_ge(wts, dr + 1)
                    dve.wait_ge(smade, 3 * dr + 3)
                    dve.tensor_tensor(four(H[:, dr, 1, :]), four(H[:, dr, 1, :]), ps[:, 4:8, 0:384], ALU.add).then_inc(skept, 1)
                for n in range(6):
                    weigh(n)
                    if n == 3:
                        keep(0)
                keep(1)

        cbm, cbk, xd = S("cb_made"), S("cb_kept"), S("x_scaled")
        rmade, dmade, emade, pmade, ymade = S("selectors"), S("exponents"), S("exped"), S("weighted"), S("diagonal_made")
        omade, okept, oscaled, yk = S("offsets_made"), S("offsets_kept"), S("offsets_scaled"), S("y_kept")
        tmp = [self.hT[:, 0:6, HP * i:HP * (i + 1)] for i in range(2)]
        units = [(c, hb, dr) for c in range(2) for hb in range(8) for dr in range(2)]
        with nc.Block() as block:
            @block.tensor
            def _(pe):
                def exponents(i):
                    pe.wait_ge(rmade, i + 1)
                    if i >= 2:
                        pe.wait_ge(emade, i - 1)
                    pe.matmul(ps[:, 3 + i % 2, 0:384], rest[units[i][2]], R[i % 2].rearrange("p h t -> p (h t)"),
                              start=True, stop=True).then_inc(dmade, 1)

                def diagonal(i):
                    c, hb, _ = units[i]
                    pe.wait_ge(pmade, i + 1)
                    for h in range(3):
                        for dr in range(2):
                            col = (hb * 3 + h) * HP
                            ins = pe.matmul(ps[:, col // 512, col % 512:col % 512 + HP], Pm[dr][:, h, :],
                                            xdt[dr][:, col:col + HP], start=dr == 0, stop=dr == 1)
                    ins.then_inc(ymade, 1)
                for c in range(2):
                    for dr in range(2):
                        n = 2 * c + dr
                        if n >= 1:
                            pe.wait_ge(cbk, n)
                        for g in range(4):
                            ins = pe.matmul(ps[:, 5, g * P:(g + 1) * P], lat[:, 12 + g, c * P:(c + 1) * P],
                                            lat[:, 16 + g, c * P:(c + 1) * P], start=True, stop=True)
                        ins.then_inc(cbm, 1)
                    for n in range(8):
                        dr, g = divmod(n, 4)
                        m = 8 * c + n
                        if m >= 2:
                            pe.wait_ge(oscaled, m - 1)
                        which = int(2 + c == ORDER[dr][3])
                        pe.matmul(ps[:, 6 + m % 2, 0:384], lat[:, 16 + g, c * P:(c + 1) * P],
                                  H[:, dr, which, g * 384:(g + 1) * 384], start=True, stop=True).then_inc(omade, 1)
                    if c == 1:
                        pe.wait_ge(yk, 1)
                    for i in range(16 * c, 16 * c + 17):
                        if i < 16 * c + 16:
                            exponents(i)
                        if i > 16 * c and (i - 1) % 2 == 1:
                            diagonal(i - 1)

            @block.gpsimd
            def _(pool):
                for i, (c, hb, dr) in enumerate(units):
                    if i >= 2:
                        pool.wait_ge(dmade, i - 1)
                    h = dr * SSD_H + hb * 3
                    pool.tensor_tensor(R[i % 2], bcast(incl[dr].unsqueeze(1), [P, 3, P]),
                                       bcast(dtA[:, 2 + c, h:h + 3].unsqueeze(2), [P, 3, P]), ALU.mult).then_inc(rmade, 1)

            @block.scalar
            def _(act):
                for i in range(len(units)):
                    act.wait_ge(dmade, i + 1)
                    if i >= 2:
                        act.wait_ge(pmade, i - 1)
                    act.activation(E[i % 2].rearrange("p h t -> p (h t)"), ps[:, 3 + i % 2, 0:384], ACT.Exp).then_inc(emade, 1)

            @block.vector
            def _(dve):
                for c in range(2):
                    for dr in range(2):
                        dve.wait_ge(cbm, 2 * c + dr + 1)
                        if c == 1:
                            dve.wait_ge(ymade, 8)
                        dve.tensor_tensor(CB[:, dr], ps[:, 5, :].rearrange("p (g t) -> p g t", g=4),
                                          bcast(incl[dr].unsqueeze(1), [P, 4, P]), ALU.mult).then_inc(cbk, 1)
                        dve.tensor_tensor(hd(xdt[dr], SSD_H), hd(x[:, 2 + c, :], SSD_H),
                                          bcast(dt[:, 2 + c, dr * SSD_H:(dr + 1) * SSD_H].unsqueeze(2), [P, SSD_H, HP]), ALU.mult)
                    for n in range(8):
                        dr, g = divmod(n, 4)
                        m = 8 * c + n
                        dve.wait_ge(omade, m + 1)
                        ysl = y[:, c, g * 384:(g + 1) * 384]
                        dst = hd(ysl, 6) if dr == 0 else tmp[m % 2]
                        dve.tensor_tensor(dst, hd(ps[:, 6 + m % 2, 0:384], 6),
                                          bcast(ex[:, dr, 4 + c, g * 6:(g + 1) * 6].unsqueeze(2), [P, 6, HP]), ALU.mult).then_inc(oscaled, 1)
                        if dr == 1:
                            dve.wait_ge(oscaled, m + 1)
                            dve.tensor_tensor(hd(ysl, 6), hd(ysl, 6), tmp[m % 2], ALU.add).then_inc(okept, 1)
                    dve.wait_ge(cbk, 2 * c + 2)
                    for i in range(16 * c, 16 * c + 16):
                        _, hb, dr = units[i]
                        dve.wait_ge(emade, i + 1)
                        if i >= 2:
                            dve.wait_ge(ymade, i // 2)
                        dve.tensor_tensor(Pm[dr], E[i % 2], bcast(CB[:, dr, hb // 2, :].unsqueeze(1), [P, 3, P]), ALU.mult).then_inc(pmade, 1)
                    dve.wait_ge(ymade, 8 * c + 8)
                    dve.wait_ge(okept, 4 * c + 4)
                    dve.tensor_tensor(y[:, c, :], y[:, c, :], ps[:, 0:3, :].rearrange("p b n -> p (b n)"), ALU.add).then_inc(yk, 1)

    def ssd_out(self):
        nc, d, ring, ps, hT = self.nc, self.d, self.ring, self.ps, self.hT
        lat, y = self.s_lat, self.s_y
        A = Arena(self.arena_t, self.work + 20 * SEQ + 2 * D_SSD, self.A.end)
        self.m_f, self.m_y, self.m_g = A.take(4, SEQ), A.take(12, SEQ), A.take(16, SEQ)
        self.merge_area = A.at
        uT, zT, sq, rstd = A.take(4, SEQ), A.take(12, SEQ), A.take(12, SEQ), A.take(SEQ)
        F1 = A.take(2, 4, SEQ)
        dftw, dftl, dsk, skips = A.take(2 * P), A.take(2, 2 * SEQ), A.take(12), A.take(SSD_H)
        spread = self.sem("skips_spread")
        S = lambda n: self.sem("ssd_out_" + n)
        made, freed, small = S("made"), S("freed"), S("tables_loaded")
        turned, kept, f1, f1k, f2 = S("y_turned"), S("y_kept"), S("width_made"), S("width_kept"), S("length_made")
        with nc.Block() as block:
            @block.sync
            def _(sp):
                sp.dma_start(dftw, d["k_dftw"]).then_inc(small, 16)
                sp.dma_start(dftl, d["k_dftl"].rearrange("(c p) n -> p c n", p=P)).then_inc(small, 16)
                sp.dma_start(skips, d["d_skip_2"].partition_broadcast(P)).then_inc(small, 16)
                ring.send(sp, self.ends["rest2"] + 3)

            @block.tensor
            def _(pe):
                self.products(pe, [self.feature_tiles(hT, CTX, TOK)] * 8, made, freed)
                pe.wait_ge(freed, 32)
                for t in range(12):
                    if t >= 8:
                        pe.wait_ge(kept, t - 7)
                    for c in range(2):
                        ins = pe.transpose(ps[:, t % 8, c * P:(c + 1) * P], y[:, c, t * P:(t + 1) * P], self.ident)
                    ins.then_inc(turned, 1)

            @block.scalar
            def _(act):
                for t in range(32):
                    act.wait_ge(made, t + 1)
                    bank = ps[:, t % 8, 0:SEQ]
                    if t < 4:
                        ins = act.activation(uT[:, t, :], bank, ACT.Copy)
                    elif t < 16:
                        ins = act.activation(zT[:, t - 4, :], bank, ACT.Silu)
                    else:
                        ins = act.activation(self.m_g[:, t - 16, :], bank, ACT.Sigmoid, bias=self.P_("b_gate")[:, t - 16:t - 15])
                    ins.then_inc(freed, 1)

            @block.vector
            def _(dve):
                dve.wait_ge(small, 48)
                for two in range(2):
                    half = slice(two * HP, (two + 1) * HP)
                    dve.tensor_copy(dsk[half, :], skips[half, :].rearrange("p (i two) -> p i two", two=2)[:, :, two]).then_inc(spread, 1)
                dve.wait_ge(spread, 2)
                dve.wait_ge(freed, 32)
                for t in range(12):
                    dve.wait_ge(turned, t + 1)
                    dve.scalar_tensor_tensor(self.m_y[:, t, :], lat[:, t, :], dsk[:, t:t + 1], ps[:, t % 8, 0:SEQ],
                                             ALU.mult, ALU.add).then_inc(kept, 1)
                dve.wait_ge(kept, 12)
                dve.tensor_tensor(self.m_y, self.m_y, zT, ALU.mult)
        self.rms("ssd_norm", self.m_y, 12, SEQ, rstd, sq)
        scaled = S("y_scaled")
        with nc.Block() as block:
            @block.vector
            def _(dve):
                dve.tensor_tensor(self.m_y, self.m_y, bcast(rstd.unsqueeze(1), [P, 12, SEQ]), ALU.mult).then_inc(scaled, 1)
                dve.wait_ge(scaled, 1)
                for t in range(12):
                    dve.tensor_scalar(self.m_y[:, t, :], self.m_y[:, t, :], self.P_("ssd_g")[:, t:t + 1], None, ALU.mult)
                for g in range(4):
                    dve.wait_ge(f2, g + 1)
                    dve.tensor_copy(self.m_f[:, g, :], ps[:, 4 + g, 0:SEQ])

            @block.tensor
            def _(pe):
                for c in range(2):
                    for g in range(4):
                        ins = pe.matmul(ps[:, c * 2 + g // 2, g % 2 * SEQ:(g % 2 + 1) * SEQ], uT[:, g, c * P:(c + 1) * P], dftw,
                                        start=True, stop=True)
                    ins.then_inc(f1, 1)
                pe.wait_ge(f1k, 2)
                for g in range(4):
                    for n in range(4):
                        c, part = divmod(n, 2)
                        ins = pe.matmul(ps[:, 4 + g, 0:SEQ], F1[:, c, g, part * P:(part + 1) * P], dftl[:, c, part * SEQ:(part + 1) * SEQ],
                                        start=n == 0, stop=n == 3)
                    ins.then_inc(f2, 1)

            @block.scalar
            def _(act):
                for c in range(2):
                    act.wait_ge(f1, c + 1)
                    act.activation(F1[:, c].rearrange("p g n -> p (g n)"), ps[:, 2 * c:2 * c + 2, :].rearrange("p b n -> p (b n)"),
                                   ACT.Copy).then_inc(f1k, 1)

    def merge2(self):
        A = Arena(self.arena_t, self.merge_area, self.A.end)
        y, mix, t2 = A.take(KT, SEQ), A.take(KT, SEQ), [A.take(SEQ) for _ in range(2)]
        first = [(lambda w, k, j=j: w[:, k, j * P:(j + 1) * P], lambda w, k: self.m_f[:, k, :], SEQ, 4) for j in range(8)]
        second = [(lambda w, k, j=j: w[:, k, j * P:(j + 1) * P], lambda w, k: self.m_y[:, k, :], SEQ, 12) for j in range(2)]
        self.merge_out("merge2", [first] + [second] * 4, [self.m_g[:, 0:8, :], self.m_g[:, 8:16, :]], y, t2,
                       self.ends["merge2"], store=mix)
        self.add_normed("mix_post", mix, self.P_("mix_post"), self.mod2[:, 16:24, 0], A)

    def add_normed(self, name, src, gain, gate, A):
        rstd, sq, g = A.take(SEQ), A.take(KT, SEQ), A.take(KT)
        self.rms(name, src, KT, SEQ, rstd, sq)
        s = self.sem(name + "_scaled")
        with self.nc.Block() as block:
            @block.vector
            def _(dve):
                dve.tensor_tensor(g, gain, gate, ALU.mult)
                dve.tensor_tensor(src, src, bcast(rstd.unsqueeze(1), [P, KT, SEQ]), ALU.mult).then_inc(s, 1)
                dve.wait_ge(s, 1)
                for k in range(KT):
                    dve.scalar_tensor_tensor(self.xT[:, k, :], src[:, k, :], g[:, k:k + 1], self.xT[:, k, :], ALU.mult, ALU.add)

    def route2(self):
        nc, d, ps = self.nc, self.d, self.ps
        self.h2 = self.hT[:, :, 0:SEQ]
        A = Arena(self.arena_t, self.work, self.A.end)
        E2, n = N_EXP2, N_EXP2 * CAP
        self.xe = A.take(KT, n)
        self.selT = A.take(E2, SEQ)
        self.moe_area = A.at
        wr, iota, rows = A.take(KT, E2), A.take(SEQ), A.take(E2 * P)
        self.norm_modulate("ffn_pre", self.xT, self.h2, self.P_("ffn_pre"), self.mod2[:, 32:40, 0], self.mod2[:, 24:32, 0], A)
        lg, aff, top = A.take(2, E2), A.take(2, E2), A.take(2)
        affT = A.take(SEQ)
        affB = A.take(E2, SEQ)
        G = A.take(E2, SEQ)
        T = A.take(E2, P)
        rank = A.take(2, E2)
        sel = A.take(2, n)
        h_tok = A.take(2, D)
        S = lambda n_: self.sem("route2_" + n_)
        loaded, lmade, st, sa = S("loaded"), S("logits_made"), S("logits_shifted"), S("exped")
        amade, aturned, akept, bmade, bkept = S("affinities"), S("affinities_turned"), S("rows_kept"), S("rows_spread"), S("spread_kept")
        hturned, hkept = S("h_turned"), S("h_kept")
        vs = self.vs
        do = lambda dve, ins: vs.do(dve, ins)
        with nc.Block() as block:
            @block.sync
            def _(sp):
                sp.dma_start(wr, d["w_router_2"].rearrange("(k p) n -> p k n", p=P)).then_inc(loaded, 16)
                sp.dma_start(iota, d["k_iota"]).then_inc(loaded, 16)
                sp.dma_start(rows[0:E2], d["k_rows32"][0:E2, 0:E2 * P]).then_inc(loaded, 16)
                sp.wait_ge(loaded, 48)

            @block.tensor
            def _(pe):
                pe.wait_ge(loaded, 48)
                for c in range(2):
                    for k in range(KT):
                        ins = pe.matmul(ps[:, c, 0:E2], self.h2[:, k, c * P:(c + 1) * P], wr[:, k, :], start=k == 0, stop=k == KT - 1)
                ins.then_inc(lmade, 1)
                for k in range(KT):
                    if k >= 4:
                        pe.wait_ge(hkept, k - 3)
                    for c in range(2):
                        ins = pe.transpose(ps[:, 4 + k % 4, c * P:(c + 1) * P], self.h2[:, k, c * P:(c + 1) * P], self.ident)
                    ins.then_inc(hturned, 1)
                pe.wait_ge(amade, 1)
                for c in range(2):
                    ins = pe.transpose(ps[0:E2, 2, c * P:(c + 1) * P], aff[:, c, :], self.ident)
                ins.then_inc(aturned, 1)
                pe.wait_ge(akept, 1)
                pe.wait_ge(hkept, 8)
                for i in range(E2 // 2):
                    if i >= 4:
                        pe.wait_ge(bkept, i - 3)
                    for j in range(2):
                        e = 2 * i + j
                        ins = pe.matmul(ps[:, 4 + i % 4, j * SEQ:(j + 1) * SEQ], rows[0:E2, e * P:(e + 1) * P], affT[0:E2, :],
                                        start=True, stop=True)
                    ins.then_inc(bmade, 1)

            @block.scalar
            def _(act):
                for k in range(KT):
                    act.wait_ge(hturned, k + 1)
                    act.activation(h_tok[:, :, k * P:(k + 1) * P], ps[:, 4 + k % 4, 0:SEQ].rearrange("p (c f) -> p c f", c=2),
                                   ACT.Copy).then_inc(hkept, 1)
                act.wait_ge(st, 1)
                act.activation(aff, lg, ACT.Exp).then_inc(sa, 1)
                for i in range(E2 // 2):
                    act.wait_ge(bmade, i + 1)
                    act.activation(affB[:, 2 * i:2 * i + 2, :], ps[:, 4 + i % 4, :].rearrange("p (a t) -> p a t", a=2),
                                   ACT.Copy).then_inc(bkept, 1)

            @block.vector
            def _(dve):
                bc = lambda a: bcast(a.unsqueeze(2), [P, 2, E2])
                dve.wait_ge(lmade, 1)
                do(dve, dve.reduce_max(top, ps[:, 0:2, 0:E2], axis=AX.X))
                dve.tensor_tensor(lg, ps[:, 0:2, 0:E2], bc(top), ALU.subtract).then_inc(st, 1)
                dve.wait_ge(sa, 1)
                do(dve, dve.reduce_sum(top, aff, axis=AX.X))
                do(dve, dve.reciprocal(top, top))
                dve.tensor_tensor(aff, aff, bc(top), ALU.mult).then_inc(amade, 1)
                dve.wait_ge(aturned, 1)
                dve.tensor_copy(affT[0:E2, :], ps[0:E2, 2, 0:SEQ]).then_inc(akept, 1)
                dve.wait_ge(amade, 1)
                dve.wait_ge(bkept, E2 // 2)
                later = self.k_sel[:, (LEVELS + 1) * P:(LEVELS + 2) * P]
                for c in range(2):
                    own = bcast(aff[:, c, :].unsqueeze(2), [P, E2, P])
                    o = 1 - c
                    dve.tensor_tensor(G[:, :, o * P:(o + 1) * P], affB[:, :, o * P:(o + 1) * P], own, ALU.is_ge if o < c else ALU.is_gt)
                    dve.tensor_tensor(G[:, :, c * P:(c + 1) * P], affB[:, :, c * P:(c + 1) * P], own, ALU.is_gt)
                    do(dve, dve.tensor_tensor(T, affB[:, :, c * P:(c + 1) * P], own, ALU.is_equal))
                    do(dve, dve.tensor_tensor(T, T, bcast(later.unsqueeze(1), [P, E2, P]), ALU.mult))
                    do(dve, dve.tensor_tensor(G[:, :, c * P:(c + 1) * P], G[:, :, c * P:(c + 1) * P], T, ALU.add))
                    do(dve, dve.reduce_sum(rank[:, c, :], G, axis=AX.X))
                for c in range(2):
                    do(dve, dve.tensor_tensor(sel[:, c, :].rearrange("p (e s) -> p e s", s=CAP),
                                              bcast(iota[:, 0:CAP].unsqueeze(1), [P, E2, CAP]),
                                              bcast(rank[:, c, :].unsqueeze(2), [P, E2, CAP]), ALU.is_equal))
        selw = G.rearrange("p e t -> p (e t)").rearrange("p (c e r s) -> p c e r s", c=2, e=E2, r=4)
        wset, xmade, xkept, tmade, tkept = S("selection_weighted"), S("xe_made"), S("xe_kept"), S("sel_turned"), S("sel_kept")
        with nc.Block() as block:
            @block.vector
            def _(dve):
                for c in range(2):
                    for r in range(4):
                        ins = dve.tensor_tensor(selw[:, c, :, r, :], sel[:, c, :].rearrange("p (e s) -> p e s", s=CAP),
                                                bcast(aff[:, c, :].unsqueeze(2), [P, E2, CAP]), ALU.mult)
                ins.then_inc(wset, 1)
                for i in range(E2 // 2):
                    dve.wait_ge(tmade, i + 1)
                    dve.tensor_copy(self.selT[:, 2 * i:2 * i + 2, :], ps[:, 4 + i % 4, :].rearrange("p (a t) -> p a t", a=2)).then_inc(tkept, 1)

            @block.scalar
            def _(act):
                for k in range(KT):
                    act.wait_ge(xmade, k + 1)
                    act.activation(self.xe[:, k, :], ps[:, k % 4, :], ACT.Copy).then_inc(xkept, 1)

            @block.tensor
            def _(pe):
                for k in range(KT):
                    if k >= 4:
                        pe.wait_ge(xkept, k - 3)
                    for c in range(2):
                        ins = pe.matmul(ps[:, k % 4, :], h_tok[:, c, k * P:(k + 1) * P], sel[:, c, :], start=c == 0, stop=c == 1)
                    ins.then_inc(xmade, 1)
                pe.wait_ge(wset, 1)
                for i in range(E2 // 2):
                    if i >= 4:
                        pe.wait_ge(tkept, i - 3)
                    for j in range(2):
                        for c in range(2):
                            ins = pe.transpose(ps[:, 4 + i % 4, j * SEQ + c * P:j * SEQ + (c + 1) * P],
                                               selw[:, c, 2 * i + j, :, :].rearrange("p r s -> p (r s)"), self.ident)
                    ins.then_inc(tmade, 1)

    def moe2(self):
        nc, d, ps = self.nc, self.d, self.ps
        A = Arena(self.arena_t, self.moe_area, self.A.end)
        slots = self.ring.slots + [A.take(4096) for _ in range(3)]
        mat = [s.rearrange("p (k c) -> p k c", c=512) for s in slots]
        F_G0, F_U0, F_D0, F_G1, F_U1, F_D1 = range(6)
        xs = [A.take(KT, CAP) for _ in range(2)]
        stack = A.take(CAP)
        gq, uq, yq = A.take(512), A.take(512), A.take(2, 512)
        gs = A.take(4 * CAP)
        aT = A.take(2, 4, CAP)
        zero = A.take(512)
        S = lambda n: self.sem("moe2_" + n)
        loaded, used = [S(f"loaded{i}") for i in range(6)], [S(f"used{i}") for i in range(6)]
        xset, stacked, qmade, gkept, ukept = S("x_set"), S("stack_set"), S("quarters_made"), S("gate_kept"), S("up_kept")
        tmade, silud, aready, dmade, dkept, zeroed = (S("turned"), S("silu_made"), S("hidden_ready"), S("down_made"),
                                                      S("down_kept"), S("zeroed"))
        scat = S("scattered")
        src = [d[f"w_e_{w}_2"].rearrange("e (k p) f -> e p k f", p=P)[:, :, :, 512 * h:512 * h + 512]
               for h in range(2) for w in ("gate", "up", "down")]
        acc = lambda o: ps[:, 4 + o // 2, o % 2 * SEQ:(o % 2 + 1) * SEQ]
        last = N_EXP2 - 1
        with nc.Block() as block:
            @block.sync
            def _(sp):
                for i in range(6):
                    sp.dma_start(mat[i], src[i][0]).then_inc(loaded[i], 16)
                with sp.Fori(1, N_EXP2) as e:
                    for i in range(6):
                        sp.wait_ge(used[i], e)
                        sp.dma_start(mat[i], src[i][bass.ds(e, 1)].rearrange("o p k f -> p (o k) f")).then_inc(loaded[i], 16)

            @block.gpsimd
            def _(pool):
                with pool.Fori(0, N_EXP2 // 2) as it:
                    for j in range(2):
                        pool.wait_ge(scat, it * 2 + (j + 1))
                        pool.tensor_copy(xs[j], self.xe[:, :, bass.ds(it * (2 * CAP) + j * CAP, CAP)]).then_inc(xset, 1)

            def quarters(pe, out, lhsT, w):
                for i in range(2):
                    for q in range(4):
                        k = 2 * q + i
                        ins = pe.matmul(ps[q * CAP:(q + 1) * CAP, out, :], lhsT(k), w[:, k, :], start=i == 0, stop=i == 1,
                                        skip_group_check=True)
                return ins

            @block.tensor
            def _(pe):
                pe.wait_ge(zeroed, 1)
                pe.wait_ge(stacked, 1)
                for b in range(4):
                    pe.matmul(ps[:, 4 + b, :], zero[:, 0:P], zero, start=True, stop=False, skip_group_check=True)

                def gate_up(e, par, h):
                    if h == 0:
                        pe.wait_ge(xset, e + 1)
                    pe.wait_ge(gkept, 2 * e + h + 1)
                    pe.wait_ge(ukept, 2 * e + h + 1)
                    for b, slot in ((0, (F_G0, F_G1)[h]), (1, (F_U0, F_U1)[h])):
                        pe.wait_ge(loaded[slot], 16 * e + 16)
                        quarters(pe, b, lambda k: xs[par][:, k, :], mat[slot]).then_inc(qmade, 1)
                        pe.drain().then_inc(used[slot], 1)

                def turn(e, h):
                    pe.wait_ge(gkept, 2 * e + h + 2)
                    pe.wait_ge(aready, 2 * e + h + 1)
                    for f in range(4):
                        pe.matmul(ps[:, 2, f * CAP:(f + 1) * CAP], gq[:, f * P:(f + 1) * P], stack, start=True, stop=True)
                    pe.wait_ge(ukept, 2 * e + h + 2)
                    for f in range(4):
                        ins = pe.matmul(ps[:, 2, (4 + f) * CAP:(5 + f) * CAP], uq[:, f * P:(f + 1) * P], stack, start=True, stop=True)
                    ins.then_inc(tmade, 1)

                def down(e, h):
                    slot = (F_D0, F_D1)[h]
                    if h == 0:
                        pe.wait_ge(aready, 2 * e + 3)
                    pe.wait_ge(loaded[slot], 16 * e + 16)
                    pe.wait_ge(dkept, 2 * e + h + 1)
                    quarters(pe, 3, lambda k: aT[:, k // 4, k % 4, :], mat[slot]).then_inc(dmade, 1)
                    pe.drain().then_inc(used[slot], 1)

                def scatter(e, sel):
                    pe.wait_ge(dkept, 2 * e + 3)
                    for o in range(KT):
                        ins = pe.matmul(acc(o), yq[:, o // 4, o % 4 * P:(o % 4 + 1) * P], sel, start=False, stop=False,
                                        skip_group_check=True)
                    ins.then_inc(scat, 1)
                selT = lambda e: self.selT[:, bass.ds(e, 1), :].rearrange("p o t -> p (o t)")
                for h in range(2):
                    gate_up(0, 0, h)
                    turn(0, h)
                with pe.Fori(0, last // 2) as it:
                    for j in range(2):
                        e = it * 2 + j
                        gate_up(it * 2 + (j + 1), (j + 1) % 2, 0)
                        down(e, 0)
                        down(e, 1)
                        turn(it * 2 + (j + 1), 0)
                        gate_up(it * 2 + (j + 1), (j + 1) % 2, 1)
                        scatter(e, selT(e))
                        turn(it * 2 + (j + 1), 1)
                gate_up(last, 1, 0)
                down(last - 1, 0)
                down(last - 1, 1)
                turn(last, 0)
                gate_up(last, 1, 1)
                scatter(last - 1, self.selT[:, last - 1, :])
                turn(last, 1)
                down(last, 0)
                down(last, 1)
                scatter(last, self.selT[:, last, :])
                for b in range(4):
                    pe.matmul(ps[:, 4 + b, :], zero[:, 0:P], zero, start=False, stop=True, skip_group_check=True)

            @block.scalar
            def _(act):
                act.sem_inc(gkept, 1)
                act.sem_inc(dkept, 1)
                def gates(e, h):
                    act.wait_ge(qmade, 4 * e + 2 * h + 1)
                    act.activation(gq, ps[:, 0, :], ACT.Copy).then_inc(gkept, 1)
                    act.wait_ge(tmade, 2 * e + h + 1)
                    act.activation(gs, ps[:, 2, 0:4 * CAP], ACT.Silu).then_inc(silud, 1)

                def keep_down(e):
                    for h in range(2):
                        act.wait_ge(dmade, 2 * e + h + 1)
                        act.activation(yq[:, h, :], ps[:, 3, :], ACT.Copy).then_inc(dkept, 1)
                gates(0, 0)
                gates(0, 1)
                with act.Fori(1, N_EXP2) as e:
                    act.wait_ge(qmade, 4 * e + 1)
                    act.activation(gq, ps[:, 0, :], ACT.Copy).then_inc(gkept, 1)
                    act.wait_ge(scat, e + 1)
                    keep_down(e - 1)
                    act.wait_ge(tmade, 2 * e + 1)
                    act.activation(gs, ps[:, 2, 0:4 * CAP], ACT.Silu).then_inc(silud, 1)
                    gates(e, 1)
                act.wait_ge(scat, last + 2)
                keep_down(last)

            @block.vector
            def _(dve):
                dve.memset(zero, 0.0).then_inc(zeroed, 1)
                for q in range(4):
                    ins = dve.tensor_copy(stack[q * CAP:(q + 1) * CAP, :], self.ident[q * CAP:(q + 1) * CAP, q * CAP:(q + 1) * CAP])
                ins.then_inc(stacked, 1)
                dve.sem_inc(scat, 2)
                dve.sem_inc(ukept, 1)
                dve.sem_inc(aready, 1)
                with dve.Fori(0, N_EXP2) as e:
                    for h in range(2):
                        dve.wait_ge(qmade, 4 * e + (2 * h + 2))
                        dve.tensor_copy(uq, ps[:, 1, :]).then_inc(ukept, 1)
                        dve.wait_ge(silud, 2 * e + (h + 1))
                        dve.tensor_tensor(aT[:, h].rearrange("p f s -> p (f s)"), gs, ps[:, 2, 4 * CAP:8 * CAP], ALU.mult).then_inc(aready, 1)
        A = Arena(self.arena_t, self.moe_area, self.A.end)
        ffn = A.take(KT, SEQ)
        with nc.Block() as block:
            @block.vector
            def _(dve):
                for b in range(4):
                    dve.tensor_copy(ffn[:, 2 * b:2 * b + 2, :], ps[:, 4 + b, :].rearrange("p (a t) -> p a t", a=2))
        self.ffn = ffn
        self.add_normed("ffn_post", ffn, self.P_("ffn_post"), self.mod2[:, 40:48, 0], A)

    def finish(self):
        nc, ps = self.nc, self.ps
        A = Arena(self.arena_t, self.work, self.A.end)
        res = A.take(2, D)
        S = lambda n: self.sem("finish_" + n)
        turned, kept, stored = S("turned"), S("kept"), S("stored")
        with nc.Block() as block:
            @block.tensor
            def _(pe):
                for c in range(2):
                    for k in range(KT):
                        ins = pe.transpose(ps[:, c * 2 + k // 4, k % 4 * P:(k % 4 + 1) * P], self.xT[:, k, c * P:(c + 1) * P], self.ident)
                    ins.then_inc(turned, 1)

            @block.vector
            def _(dve):
                for c in range(2):
                    dve.wait_ge(turned, c + 1)
                    dve.tensor_copy(res[:, c, :], ps[:, 2 * c:2 * c + 2, :].rearrange("p b n -> p (b n)")).then_inc(kept, 1)

            @block.sync
            def _(sp):
                for c in range(2):
                    sp.wait_ge(kept, c + 1)
                    sp.dma_start(self.out[0, c * P:(c + 1) * P, :], res[:, c, :]).then_inc(stored, 16)
                sp.wait_ge(stored, 32)


def build_program(nc, tensors, out):
    Net(nc, shaped(tensors), out).build()


def kernel(**inputs):
    import concourse.bacc as bacc
    from concourse.bass_utils import run_bass_kernel_spmd

    nc = bacc.Bacc("TRN2", target_bir_lowering=False, num_devices=1)
    arrays, tensors = {}, {}
    for name, a in list(inputs.items()) + list(constants().items()):
        a = np.ascontiguousarray(a)
        arrays["in_" + name] = a
        tensors[name] = nc.dram_tensor("in_" + name, a.shape, mybir.dt.from_np(a.dtype), kind="ExternalInput").ap()
    out = nc.dram_tensor("out_0", (1, SEQ, D), F32, kind="ExternalOutput").ap()
    build_program(nc, tensors, out)
    r = run_bass_kernel_spmd(nc, [arrays], core_ids=[0])
    return r.results[0]["out_0"]
```

```python
import numpy as np
import concourse.bass as bass
from concourse import mybir
from concourse.alu_op_type import AluOpType as ALU
from contextlib import ExitStack

F32 = mybir.dt.float32
ACT = mybir.ActivationFunctionType
AX = mybir.AxisListType

P = 128
D = 1024
KT = D // P
SEQ = 256
CTX = 256
TOK = CTX + SEQ
NC = TOK // P
LAT = CTX // P
GRID = 64
ROWS = SEQ // GRID
EPS = 1e-6
HG_H = 8
ML_H, ML_DV = 4, 256
LEVELS = 7
N_EXP, D_EXP = 32, 512
N_GRP, PER_GRP = 4, 8
D_SSD, SSD_H, HP, SSD_G = 1536, 24, 64, 4
CONV2 = D_SSD + 2 * SSD_G * P
N_EXP2, CAP = 16, 32
BIG = 1e30
FIRST_STAGE_SEM = 150
NBANK = 6

O_HQ, O_HFF, O_HFB, O_HI, O_GA, O_MQ, O_MK, O_MV = 0, 1024, 2048, 3072, 4096, 5120, 5632, 6144
O_MI, O_GB, O_G1, O_G2 = 7168, 7184, 8208, 9232
O_UF, O_Z, O_XBC, O_DT, O_GL = 0, 512, 2048, 4608, 4656
ORDER = ((0, 1, 2, 3), (1, 0, 3, 2))

PARAMS = [
    ("b_ada", "b_ada", 0, 48), ("b_mod", "b_mod_2", 0, 48),
    ("b_hq", "b_in", O_HQ, 8), ("b_hff", "b_in", O_HFF, 8), ("b_hfb", "b_in", O_HFB, 8),
    ("norm1", "norm1_g", 0, 8),
    ("b_ga", "b_in", O_GA, 8), ("b_mq", "b_in", O_MQ, 4), ("b_mk", "b_in", O_MK, 4),
    ("b_gb", "b_in", O_GB, 8), ("b_g1", "b_in", O_G1, 8), ("b_g2", "b_in", O_G2, 8),
    ("norm2", "norm2_g", 0, 8), ("final", "final_norm_g", 0, 8),
    ("lb", "hg_lb_logits", 0, 32), ("hg_g", "hg_norm_g", 0, 8), ("ml_g", "ml_norm_g", 0, 8),
    ("cb1", "ml_conv_b", 0, 8),
    ("cw1", "ml_conv_w", 0, 40), ("cw2", "conv_w_2", 0, 60), ("cb2", "conv_b_2", 0, 20),
    ("mix_pre", "norm_mix_pre_2", 0, 8),
    ("mix_post", "norm_mix_post_2", 0, 8), ("ffn_pre", "norm_ffn_pre_2", 0, 8),
    ("ffn_post", "norm_ffn_post_2", 0, 8), ("ssd_g", "ssd_norm_2", 0, 12), ("b_gate", "b_gate_2", 0, 16),
    ("c", "c", 0, 8), ("c_ctx", "c_ctx", 0, 8), ("c2", "c_2", 0, 8), ("c_ctx2", "c_ctx_2", 0, 8),
]
N_PAR = sum(n for *_, n in PARAMS)
PAR_TILES = -(-N_PAR // P)


def param_columns():
    at, out = 0, {}
    for name, _, _, n in PARAMS:
        out[name] = (at, n)
        at += n
    return out


def constants():
    t = np.arange(P)
    sel, masks = [], []
    for flip in (False, True):
        cols, ms = [], []
        for lev in range(LEVELS):
            m = P >> (lev + 1)
            mid = (t // (2 * m)) * 2 * m + m
            second = t % (2 * m) >= m
            s, tt = t[:, None], t[None, :]
            c = np.where(second[None, :], (s >= mid[None, :]) & (s <= tt), (s > tt) & (s < mid[None, :]))
            cols.append(c)
            same = (t[:, None] // (2 * m)) == (t[None, :] // (2 * m))
            ms.append(same & ~second[:, None] & second[None, :])
        cols.append(t[:, None] <= t[None, :])
        cols.append(t[:, None] > t[None, :])
        ms.append(np.eye(P, dtype=bool))
        if flip:
            cols = [c[::-1, ::-1] for c in cols]
            ms = [c[::-1, ::-1] for c in ms]
        sel.append(np.concatenate(cols, 1))
        masks.append(np.concatenate(ms, 1))
    w = np.arange(P)[:, None] * np.arange(P)[None, :] % P * (2 * np.pi / P)
    l = np.arange(SEQ)[:, None] * np.arange(SEQ)[None, :] % SEQ * (2 * np.pi / SEQ)
    scale = 1.0 / np.sqrt(SEQ * P)
    f = np.float32
    rows = np.zeros((N_GRP, N_GRP * P))
    for h in range(N_GRP):
        rows[h, h * P:(h + 1) * P] = 1
    rows32 = np.zeros((N_EXP, N_EXP * P))
    for h in range(N_EXP):
        rows32[h, h * P:(h + 1) * P] = 1
    return {
        "k_sel": np.concatenate(sel, 1).astype(f), "k_mask": np.concatenate(masks, 1).astype(f),
        "k_dftw": np.concatenate([np.cos(w), np.sin(w)], 1).astype(f),
        "k_dftl": np.concatenate([np.cos(l) * scale, -np.sin(l) * scale], 1).astype(f),
        "k_ident": np.eye(P).astype(f), "k_rows4": rows.astype(f), "k_rows32": rows32.astype(f),
        "k_iota": np.tile(np.arange(SEQ), (P, 1)).astype(f),
    }


def bcast(ap, shape):
    return ap.broadcast_to(shape)


class Arena:

    def __init__(self, tensor, at, end):
        self.tensor, self.at, self.end = tensor, at, end

    def take(self, *dims, parts=P):
        n = 1
        for d in dims:
            n *= d
        assert self.at + n <= self.end, (self.at, n, self.end)
        v = self.tensor[0:parts, self.at:self.at + n]
        self.at += n
        if len(dims) == 2:
            v = v.rearrange("p (a b) -> p a b", b=dims[1])
        if len(dims) == 3:
            v = v.rearrange("p (a b c) -> p a b c", b=dims[1], c=dims[2])
        return v


class Steps:

    def __init__(self, sem):
        self.sem, self.n = sem, 0

    def do(self, eng, ins):
        ins.then_inc(self.sem, 1)
        self.n += 1
        eng.wait_ge(self.sem, self.n)


class Ring:

    def __init__(self, slots, loaded, used):
        self.slots, self.loaded, self.used = slots, loaded, used
        self.queue, self.sent, self.taken = [], 0, 0

    def plan(self, blocks):
        self.queue += blocks
        return len(self.queue)

    def send(self, sp, until):
        n = len(self.slots)
        while self.sent < min(until, len(self.queue)):
            src, i = self.queue[self.sent], self.sent
            if i >= n:
                sp.wait_ge(self.used[i % n], i // n)
            dst = self.slots[i % n][:, 0:src.shape[1] * src.shape[2]].rearrange("p (k c) -> p k c", c=src.shape[2])
            sp.dma_start(dst, src).then_inc(self.loaded[i % n], 16)
            self.sent += 1

    def take(self, pe):
        n, i = len(self.slots), self.taken
        pe.wait_ge(self.loaded[i % n], 16 * (i // n + 1))
        src = self.queue[i]
        self.taken += 1
        return (self.slots[i % n][:, 0:src.shape[1] * src.shape[2]].rearrange("p (k c) -> p k c", c=src.shape[2]),
                self.used[i % n])


def col_blocks(w, first, n, kt=KT, width=512):
    v = w.rearrange("(k p) n -> p k n", p=P)
    return [v[:, :, c:min(c + width, first + n)] for c in range(first, first + n, width)]


def row_blocks(w, kt=4):
    v = w.rearrange("(k p) n -> p k n", p=P)
    return [v[:, k:k + kt, :] for k in range(0, w.shape[0] // P, kt)]


def shaped(d):
    out = {}
    for name, ap in d.items():
        if name.startswith("k_"):
            out[name] = ap
        elif len(ap.shape) >= 3 and ap.shape[0] == 1 and name not in ("x", "ctx", "ctx_2"):
            out[name] = ap[0]
        else:
            out[name] = ap
    return out


class Net:

    def __init__(self, nc, d, out, last=99):
        self.nc, self.d, self.out, self.last = nc, d, out, last

    def sem(self, name):
        self.stage_sems += 1
        return self.stage.enter_context(self.nc.semaphore(name, num=FIRST_STAGE_SEM + self.stage_sems - 1))

    def lasting_sem(self, name):
        return self.ctx.enter_context(self.nc.semaphore(name))

    def build(self):
        with ExitStack() as self.ctx:
            nc, d = self.nc, self.d
            words = 53000
            self.arena_t = self.ctx.enter_context(nc.sbuf_tensor("arena", [P, words], F32))
            self.ps = self.ctx.enter_context(nc.psum_tensor("ps", [P, 8, 512], F32))
            A = self.A = Arena(self.arena_t, 0, words)
            self.ident = A.take(P)
            self.ones = A.take(P)
            self.par = A.take(PAR_TILES * P)
            self.cp = param_columns()
            self.k_sel = A.take(2 * (LEVELS + 2) * P)
            self.xT = A.take(KT, SEQ)
            self.hT = A.take(KT, TOK)
            self.mod1 = A.take(48, 2)
            self.mod2 = A.take(48, 2)
            self.lbs = A.take(2, 16)
            self.silu_c = A.take(2, 8, CAP)
            self.stack = A.take(CAP)
            self.gain1 = A.take(8, 2)
            self.gain2 = A.take(8, 2)
            slots = [A.take(4096) for _ in range(3)]
            self.ring = Ring(slots, [self.lasting_sem(f"ring_loaded{i}") for i in range(3)],
                             [self.lasting_sem(f"ring_used{i}") for i in range(3)])
            self.vs = Steps(self.lasting_sem("vector_step"))
            self.ss = Steps(self.lasting_sem("scalar_step"))
            self.gs = Steps(self.lasting_sem("pool_step"))
            self.work = A.at
            R = self.ring
            w1, w2 = d["w_in"], d["w_in_2"]
            self.ends = {}
            mods = col_blocks(d["w_ada"], 0, 6 * D) + col_blocks(d["w_mod_2"], 0, 6 * D)
            self.mod_next = 0

            def mixed(blocks):
                out = []
                for b in blocks:
                    out += [b] + mods[:1]
                    del mods[:1]
                return out
            self.ends["mod"] = R.plan(mods[:4])
            del mods[:4]
            for half in range(2):
                c = 512 * half
                self.ends[f"hgrn{half}"] = R.plan(mixed([b for o in (O_HFF, O_HFB, O_HI, O_HQ)
                                                         for b in col_blocks(w1, o + c, 512)]))
            self.ends["mlstm"] = R.plan(mixed(col_blocks(w1, O_MQ, 2048)))
            self.ends["gates1"] = R.plan(mixed(col_blocks(w1, O_GA, 1024) + col_blocks(w1, O_GB, 3072)))
            self.ends["merge1"] = R.plan(col_blocks(d["w_branch_a"], 0, D) + col_blocks(d["w_branch_b"], 0, D)
                                         + col_blocks(d["w_out"], 0, D))
            self.ends["xbc"] = R.plan(col_blocks(w2, O_XBC, CONV2))
            self.ends["rest2"] = R.plan(col_blocks(w2, O_UF, 512) + col_blocks(w2, O_Z, D_SSD) + col_blocks(w2, O_GL, 2 * D))
            self.ends["merge2"] = R.plan(row_blocks(d["w_fourier_2"]) + col_blocks(d["w_ssd_out_2"], 0, D, width=256)
                                         + col_blocks(d["w_out_2"], 0, D))
            self.stages()

    def P_(self, name):
        a, n = self.cp[name]
        return self.par[:, a:a + n]

    def stages(self):
        todo = [lambda: self.setup(), lambda: self.modulation(), lambda: self.gla(0), lambda: self.gla(1),
                lambda: self.mlstm_in(), lambda: self.mlstm(), lambda: self.merge1(), lambda: self.router1(),
                lambda: self.moe1(), lambda: self.ssd_in(), lambda: self.ssd(), lambda: self.ssd_out(),
                lambda: self.merge2(), lambda: self.route2(), lambda: self.moe2(), lambda: self.finish()]
        for stage in todo[:self.last + 1]:
            self.stage_sems = 0
            with ExitStack() as self.stage:
                stage()
                self.nc.all_engine_barrier(sems_to_clear=range(FIRST_STAGE_SEM, FIRST_STAGE_SEM + self.stage_sems))
        with self.nc.Block() as block:
            @block.sync
            def _(sp):
                for i in range(3):
                    n = -(-(self.ring.sent - i) // 3)
                    if n > 0:
                        sp.wait_ge(self.ring.loaded[i], 16 * n)

    def setup(self):
        nc, d, ring, ps = self.nc, self.d, self.ring, self.ps
        A = Arena(self.arena_t, self.work, self.A.end)
        rows = A.take(PAR_TILES, P)
        xin = A.take(4, D)
        raw = A.take(KT, TOK)
        sq = A.take(TOK)
        rstd = A.take(TOK)
        self.rawctx = raw
        sig = A.take(2, 8, 2)
        consts, pars, xl = self.sem("consts_loaded"), self.sem("params_loaded"), self.sem("x_loaded")
        zeroed, par_t, par_c = self.sem("zeroed"), self.sem("params_turned"), self.sem("params_kept")
        x_t, x_c = self.sem("x_turned"), self.sem("x_kept")
        vs, ss = self.vs, self.ss
        n_par_dma = [0]
        pieces = []
        at = 0
        spans = []
        for _, src, first, n in PARAMS:
            if spans and spans[-1][0] == src and spans[-1][1] + spans[-1][2] * P == first:
                spans[-1][2] += n
            else:
                spans.append([src, first, n])
        for src, first, n in spans:
            flat = d[src].rearrange(" ".join("abcdef"[:len(d[src].shape)]) + " -> (" + " ".join("abcdef"[:len(d[src].shape)]) + ")")
            v = flat[first:first + n * P].rearrange("(r c) -> r c", c=P)
            done = 0
            while done < n:
                tile, row = divmod(at, P)
                m = min(n - done, P - row)
                pieces.append((tile, row, m, v[done:done + m, :]))
                at += m
                done += m
        last_rows = at - (PAR_TILES - 1) * P

        with nc.Block() as block:
            @block.sync
            def _(sp):
                sp.dma_start(self.ident, d["k_ident"]).then_inc(consts, 16)
                sp.dma_start(self.k_sel, d["k_sel"]).then_inc(consts, 16)
                for i in range(2):
                    sp.dma_start(xin[:, i, :], d["ctx"][0, i * P:(i + 1) * P, :]).then_inc(xl, 16)
                for i in range(2):
                    sp.dma_start(xin[:, 2 + i, :], d["x"][0, i * P:(i + 1) * P, :]).then_inc(xl, 16)
                for tile, row, m, v in pieces[1::2]:
                    sp.dma_start(rows[row:row + m, tile, :], v).then_inc(pars, 16)
                ring.send(sp, 3)

            @block.scalar
            def _(act):
                for tile, row, m, v in pieces[0::2]:
                    act.dma_start(rows[row:row + m, tile, :], v).then_inc(pars, 16)

            @block.vector
            def _(dve):
                dve.memset(self.ones, 1.0).then_inc(zeroed, 1)
                for i in range(PAR_TILES):
                    dve.wait_ge(par_t, i + 1)
                    m = P if i < PAR_TILES - 1 else last_rows
                    dve.tensor_copy(self.par[:, i * P:i * P + m], ps[:, i % 2, 0:m]).then_inc(par_c, 1)
                for k in range(KT):
                    dve.wait_ge(x_t, k + 1)
                    dve.tensor_copy(raw[:, k, :], ps[:, 2 + k % 4, :]).then_inc(x_c, 1)

            @block.tensor
            def _(pe):
                pe.wait_ge(consts, 32)
                pe.wait_ge(pars, 16 * len(pieces))
                for i in range(PAR_TILES):
                    if i >= 2:
                        pe.wait_ge(par_c, i - 1)
                    m = P if i < PAR_TILES - 1 else last_rows
                    pe.transpose(ps[:, i % 2, 0:m], rows[0:m, i, :], self.ident[0:m, 0:m]).then_inc(par_t, 1)
                pe.wait_ge(xl, 64)
                for k in range(KT):
                    if k >= 4:
                        pe.wait_ge(x_c, k - 3)
                    for i in range(4):
                        ins = pe.transpose(ps[:, 2 + k % 4, i * P:(i + 1) * P], xin[:, i, k * P:(k + 1) * P], self.ident)
                    ins.then_inc(x_t, 1)
        self.raw = raw
        names = [("c", "c_ctx"), ("c2", "c_ctx2")]
        logits = self.P_("lb").rearrange("p (d l h) -> p d l h", d=2, l=2)
        lb, one_lb = self.lbs[:, 0, :], self.lbs[:, 1, :]
        inputs_set, sigmoids = self.sem("silu_inputs"), self.sem("silu_sigmoids")
        with nc.Block() as block:
            @block.vector
            def _(dve):
                dve.memset(self.silu_c, 0.0).then_inc(inputs_set, 1)
                for q in range(4):
                    dve.tensor_copy(self.stack[q * CAP:(q + 1) * CAP, :], self.ident[q * CAP:(q + 1) * CAP, q * CAP:(q + 1) * CAP])
                dve.wait_ge(inputs_set, 1)
                for b in range(2):
                    for v in range(2):
                        dve.tensor_copy(self.silu_c[:, b, :, v], self.P_(names[b][v])).then_inc(inputs_set, 1)
                dve.tensor_tensor(one_lb.rearrange("p (d h) -> p d h", d=2), logits[:, :, 0, :], logits[:, :, 1, :],
                                  ALU.subtract).then_inc(inputs_set, 1)
                dve.wait_ge(sigmoids, 2)
                dve.tensor_tensor(self.silu_c[:, :, :, 0:2], self.silu_c[:, :, :, 0:2], sig, ALU.mult)
                dve.tensor_scalar(one_lb, lb, -1.0, 1.0, ALU.mult, ALU.add)
                dve.tensor_copy(self.xT, raw[:, :, CTX:TOK])

            @block.scalar
            def _(act):
                act.wait_ge(inputs_set, 6)
                act.activation(lb, one_lb, ACT.Sigmoid).then_inc(sigmoids, 1)
                act.activation(sig, self.silu_c[:, :, :, 0:2], ACT.Sigmoid).then_inc(sigmoids, 1)
        self.rms("norm1", raw, KT, TOK, rstd, self.hT)
        with nc.Block() as block:
            @block.vector
            def _(dve):
                dve.tensor_tensor(self.hT, raw, bcast(rstd.unsqueeze(1), [P, KT, TOK]), ALU.mult)

    def rms(self, name, src, kt, n, out, square):
        ps = self.ps
        squared, summed = self.sem(f"{name}_squared"), self.sem(f"{name}_summed")
        meaned, rooted = self.sem(f"{name}_meaned"), self.sem(f"{name}_rooted")
        with self.nc.Block() as block:
            @block.scalar
            def _(act):
                act.activation(square, src, ACT.Square).then_inc(squared, 1)
                act.wait_ge(meaned, 1)
                act.activation(out, out, ACT.Sqrt).then_inc(rooted, 1)

            @block.tensor
            def _(pe):
                pe.wait_ge(squared, 1)
                for k in range(kt):
                    ins = pe.matmul(ps[:, 0, 0:n], self.ones, square[:, k, :], start=k == 0, stop=k == kt - 1)
                ins.then_inc(summed, 1)

            @block.vector
            def _(dve):
                dve.wait_ge(summed, 1)
                dve.tensor_scalar(out, ps[:, 0, 0:n], 1.0 / (kt * P), EPS, ALU.mult, ALU.add).then_inc(meaned, 1)
                dve.wait_ge(rooted, 1)
                dve.reciprocal(out, out)

    def mod_open(self, S, A, n):
        self.mod_rows = A.take(2, 512)
        self.mod_n, self.mod_first, self.mod_done, self.mod_turned_n = n, self.mod_next, 0, 0
        self.mod_next += n
        self.mod_made, self.mod_kept, self.mod_turned = S("mod_rows_made"), S("mod_rows_kept"), S("mod_turned")

    def mod_rows_step(self, pe):
        m = self.mod_done
        w, used = self.ring.take(pe)
        if m >= 1:
            pe.wait_ge(self.mod_kept, m)
        b = (self.mod_first + m) // 12
        for i in range(2):
            for q in range(4):
                k = 2 * q + i
                ins = pe.matmul(self.ps[q * CAP:(q + 1) * CAP, 6, :], self.silu_c[:, b, k, :], w[:, k, :], start=i == 0, stop=i == 1,
                                skip_group_check=True)
        ins.then_inc(self.mod_made, 1)
        pe.drain().then_inc(used, 1)
        self.mod_done += 1

    def mod_turn_step(self, pe):
        m = self.mod_turned_n
        pe.wait_ge(self.mod_kept, m + 1)
        for j in range(4):
            c = 2 * (4 * m + j)
            ins = pe.matmul(self.ps[:, 7, c:c + 2], self.mod_rows[:, m % 2, j * P:(j + 1) * P], self.stack[:, 0:2],
                            start=True, stop=True)
        ins.then_inc(self.mod_turned, 1)
        self.mod_turned_n += 1

    def mod_keep_step(self, act, m):
        act.wait_ge(self.mod_made, m + 1)
        if m >= 2:
            act.wait_ge(self.mod_turned, m - 1)
        act.activation(self.mod_rows[:, m % 2, :], self.ps[:, 6, :], ACT.Copy).then_inc(self.mod_kept, 1)

    def mod_add(self, dve):
        dve.wait_ge(self.mod_turned, self.mod_n)
        b, t = divmod(4 * self.mod_first, 48)
        mod, bias = (self.mod1, self.mod2)[b], self.P_(("b_ada", "b_mod")[b])
        n = 4 * self.mod_n
        return dve.tensor_tensor(mod[:, t:t + n, :], self.ps[:, 7, 0:2 * n].rearrange("p (t v) -> p t v", v=2),
                                 bcast(bias[:, t:t + n].unsqueeze(2), [P, n, 2]), ALU.add)

    def modulation(self):
        A = Arena(self.arena_t, self.work, self.A.end)
        S = lambda n: self.sem("mod_" + n)
        self.mod_open(S, A, 4)
        kept = S("kept")
        with self.nc.Block() as block:
            @block.sync
            def _(sp):
                self.ring.send(sp, self.ends["mod"] + 3)

            @block.tensor
            def _(pe):
                for m in range(4):
                    self.mod_rows_step(pe)
                    if m >= 1:
                        self.mod_turn_step(pe)
                self.mod_turn_step(pe)

            @block.scalar
            def _(act):
                for m in range(4):
                    self.mod_keep_step(act, m)

            @block.vector
            def _(dve):
                self.mod_add(dve).then_inc(kept, 1)
                dve.wait_ge(kept, 1)
                self.gain(dve, self.gain1, self.mod1, "norm1").then_inc(kept, 1)
                dve.wait_ge(kept, 2)
                self.modulate(dve, self.hT, self.gain1, self.mod1)

    def gain(self, dve, gain, mod, g):
        return dve.scalar_tensor_tensor(gain, mod[:, 8:16, :], 1.0, bcast(self.P_(g).unsqueeze(2), [P, 8, 2]),
                                        ALU.add, ALU.mult)

    def modulate(self, dve, h, gain, mod):
        for k in range(KT):
            for v, (a, b) in enumerate(((CTX, TOK), (0, CTX))):
                dve.tensor_scalar(h[:, k, a:b], h[:, k, a:b], gain[:, k, v:v + 1], mod[:, k, v:v + 1],
                                  ALU.mult, ALU.add)

    def products(self, pe, blocks, made, freed, first=0, mods=0):
        n = first
        for i, tiles in enumerate(blocks):
            w, used = self.ring.take(pe)
            for lhsT, rhs, cols, kt in tiles:
                if n >= NBANK:
                    pe.wait_ge(freed, n - NBANK + 1)
                for k in range(kt):
                    ins = pe.matmul(self.ps[:, n % NBANK, 0:cols], lhsT(w, k), rhs(w, k), start=k == 0, stop=k == kt - 1)
                ins.then_inc(made, 1)
                n += 1
            pe.drain().then_inc(used, 1)
            if i < mods:
                if self.mod_done >= 1:
                    self.mod_turn_step(pe)
                self.mod_rows_step(pe)
        if mods and self.mod_done == self.mod_n:
            self.mod_turn_step(pe)
        return n

    def feature_tiles(self, h, a, b, n=4):
        return [(lambda w, k, j=j: w[:, k, j * P:(j + 1) * P], lambda w, k: h[:, k, a:b], b - a, KT) for j in range(n)]

    def token_tiles(self, token_columns, width=512):
        return [(lambda w, k, t=t: t(k), lambda w, k: w[:, k, 0:width], width, KT) for t in token_columns]

    def gla(self, half):
        nc, d, ring, ps, hT = self.nc, self.d, self.ring, self.ps, self.hT
        A = Arena(self.arena_t, self.work, self.A.end)
        self.o_all = A.take(2, D)
        kk = A.take(8, TOK)
        zz = A.take(8, TOK)
        LT = A.take(8, NC, P)
        q = A.take(4, SEQ)
        v = A.take(NC, 512)
        st = A.take(8, 2, P)
        dec = A.take(8)
        mask = A.take(2, (LEVELS + 1) * P)
        G = [A.take(LEVELS + 1, P) for _ in range(2)]
        X = [A.take(LEVELS, P) for _ in range(2)]
        AA = [A.take(LEVELS + 1, P) for _ in range(4)]
        mod_area = Arena(self.arena_t, A.at - (LEVELS + 1) * P, A.at)
        QD = [A.take(P) for _ in range(4)]
        Es = [a.rearrange("p a b -> p (a b)")[:, 0:512] for a in AA[0:2]]
        brow = AA[2].rearrange("p a b -> p (a b)")[:, 0:512]
        KP = zz
        n = f"hgrn{half}_"
        S = lambda name: self.sem(n + name)
        lb = self.lbs.rearrange("p two (d h) -> p two d h", d=2)[:, :, :, 4 * half:4 * half + 4]

        self.mod_open(S, mod_area, 4)
        made, freed, rows_in = S("made"), S("freed"), S("rows_loaded")
        with nc.Block() as block:
            @block.sync
            def _(sp):
                sp.dma_start(brow, d["b_in"][0:1, O_HI + 512 * half:O_HI + 512 * half + 512]
                             .partition_broadcast(P)).then_inc(rows_in, 16)
                sp.dma_start(mask, d["k_mask"].rearrange("p (d n) -> p d n", d=2)).then_inc(rows_in, 16)
                ring.send(sp, self.ends[f"hgrn{half}"] + 3)

            @block.tensor
            def _(pe):
                self.products(pe, [self.feature_tiles(hT, 0, TOK), self.feature_tiles(hT, 0, TOK),
                                   self.token_tiles([lambda k, c=c: hT[:, k, c * P:(c + 1) * P] for c in range(NC)]),
                                   self.feature_tiles(hT, CTX, TOK)], made, freed, mods=4)

            @block.scalar
            def _(act):
                for m in range(4):
                    self.mod_keep_step(act, m)

            @block.vector
            def _(dve):
                dve.wait_ge(rows_in, 32)
                for t in range(16):
                    dve.wait_ge(made, t + 1)
                    bank = ps[:, t % NBANK, :]
                    if t < 8:
                        b = self.P_("b_hff" if t < 4 else "b_hfb")[:, 4 * half + t % 4:4 * half + t % 4 + 1]
                        ins = dve.tensor_scalar(zz[:, t, :], bank, b, None, ALU.add)
                    elif t < 12:
                        ins = dve.tensor_tensor(v[:, t - 8, :], bank, brow, ALU.add)
                    else:
                        b = self.P_("b_hq")[:, 4 * half + t - 12:4 * half + t - 11]
                        ins = dve.tensor_scalar(q[:, t - 12, :], bank[:, 0:SEQ], b, None, ALU.add)
                    ins.then_inc(freed, 1)
                self.mod_add(dve)

        sig, f_made, ksig = S("sigmoids"), S("forget_made"), S("k_sigmoid")
        lbu = [lb[:, i, :, :] for i in range(2)]
        fourd = lambda a: a.rearrange("p (d h) t -> p d h t", d=2)
        with nc.Block() as block:
            @block.scalar
            def _(act):
                for dr in range(2):
                    u = slice(4 * dr, 4 * dr + 4)
                    act.activation(kk[:, u, :], zz[:, u, :], ACT.Sigmoid, scale=-1.0).then_inc(ksig, 1)
                    act.wait_ge(ksig, dr + 1)
                    act.activation(zz[:, u, :], zz[:, u, :], ACT.Sigmoid).then_inc(sig, 1)
                act.activation(q, q, ACT.Silu)
                for dr in range(2):
                    u = slice(4 * dr, 4 * dr + 4)
                    act.wait_ge(f_made, 4 * dr + 4)
                    act.activation(zz[:, u, :], zz[:, u, :], ACT.Ln)

            @block.vector
            def _(dve):
                for dr in range(2):
                    dve.wait_ge(sig, dr + 1)
                    for h in range(4):
                        dve.tensor_scalar(zz[:, 4 * dr + h, :], zz[:, 4 * dr + h, :], lbu[1][:, dr, h:h + 1],
                                          lbu[0][:, dr, h:h + 1], ALU.mult, ALU.add).then_inc(f_made, 1)
                for dr in range(2):
                    for h in range(4):
                        dve.tensor_scalar(kk[:, 4 * dr + h, :], kk[:, 4 * dr + h, :], lbu[1][:, dr, h:h + 1], None,
                                          ALU.mult)

        turned, kept = S("logf_turned"), S("logf_kept")
        with nc.Block() as block:
            @block.tensor
            def _(pe):
                for u in range(8):
                    for c in range(NC):
                        ins = pe.transpose(ps[:, u, c * P:(c + 1) * P], zz[:, u, c * P:(c + 1) * P], self.ident)
                    ins.then_inc(turned, 1)

            @block.vector
            def _(dve):
                for u in range(8):
                    dve.wait_ge(turned, u + 1)
                    dve.tensor_copy(LT[:, u, :, :].rearrange("p c f -> p (c f)"), ps[:, u, :])

        sums, exped, weighted = S("decay_sums"), S("decay_exp"), S("keys_weighted")
        kturned, kback, kmade, kdone = S("keys_turned"), S("keys_back"), S("states_made"), S("states_kept")
        sel = self.k_sel.rearrange("p (d n) -> p d n", d=2)
        rest = [sel[:, dr, (LEVELS + 1) * P:(LEVELS + 2) * P] for dr in range(2)]
        with nc.Block() as block:
            @block.tensor
            def _(pe):
                def decays(u):
                    dr, (o0, o1, o2, _) = u // 4, ORDER[u // 4]
                    if u >= 2:
                        pe.wait_ge(exped, u - 1)
                    bank = ps[:, u % 2, :]
                    pe.matmul(bank[:, o0 * P:(o0 + 1) * P], LT[:, u, o0, :], rest[dr], start=True, stop=False)
                    pe.matmul(bank[:, o0 * P:(o0 + 1) * P], LT[:, u, o1, :], self.ones, start=False, stop=True)
                    pe.matmul(bank[:, o1 * P:(o1 + 1) * P], LT[:, u, o1, :], rest[dr], start=True, stop=True)
                    pe.matmul(bank[:, 256:384], LT[:, u, o2, :], rest[dr], start=True, stop=True)
                    pe.matmul(bank[:, 384:512], LT[:, u, o2, :], self.ones, start=True, stop=True).then_inc(sums, 1)

                def turn(u):
                    pe.wait_ge(weighted, 2 * u + 2)
                    if u >= 2:
                        pe.wait_ge(kback, u - 1)
                    for c in range(3):
                        ins = pe.transpose(ps[:, 2 + u % 2, c * P:(c + 1) * P], KP[:, u, c * P:(c + 1) * P], self.ident)
                    ins.then_inc(kturned, 1)

                def state(u):
                    h, o2 = u % 4, ORDER[u // 4][2]
                    pe.wait_ge(kback, u + 1)
                    if u >= 2:
                        pe.wait_ge(kdone, 2 * u - 2)
                    bank, hv = ps[:, 4 + u % 2, :], slice(h * P, (h + 1) * P)
                    pe.matmul(bank[:, 0:P], KP[:, u, 0:P], v[:, 0, hv], start=True, stop=False)
                    pe.matmul(bank[:, 0:P], KP[:, u, P:2 * P], v[:, 1, hv], start=False, stop=True)
                    pe.matmul(bank[:, P:2 * P], KP[:, u, 2 * P:3 * P], v[:, o2, hv], start=True, stop=True).then_inc(kmade, 1)

                for step in range(10):
                    if step < 8:
                        decays(step)
                    if 1 <= step < 9:
                        turn(step - 1)
                    if step >= 2:
                        state(step - 2)

            @block.scalar
            def _(act):
                def back(u):
                    act.wait_ge(kturned, u + 1)
                    act.activation(KP[:, u, 0:384], ps[:, 2 + u % 2, 0:384], ACT.Copy).then_inc(kback, 1)
                for u in range(8):
                    act.wait_ge(sums, u + 1)
                    if u >= 2:
                        act.wait_ge(weighted, 2 * u - 2)
                    act.activation(Es[u % 2], ps[:, u % 2, :], ACT.Exp).then_inc(exped, 1)
                    if u >= 1:
                        back(u - 1)
                back(7)

            @block.vector
            def _(dve):
                def keep(u):
                    dve.wait_ge(kmade, u + 1)
                    bank = ps[:, 4 + u % 2, :]
                    dve.tensor_copy(st[:, u, 0, :], bank[:, 0:P]).then_inc(kdone, 1)
                    dve.wait_ge(kdone, 2 * u + 1)
                    dve.scalar_tensor_tensor(st[:, u, 1, :], st[:, u, 0, :], dec[:, u:u + 1], bank[:, P:2 * P],
                                             ALU.mult, ALU.add).then_inc(kdone, 1)
                for u in range(8):
                    o2 = ORDER[u // 4][2]
                    dve.wait_ge(exped, u + 1)
                    dve.tensor_copy(dec[:, u:u + 1], Es[u % 2][:, 384:385])
                    dve.tensor_tensor(KP[:, u, 0:256], Es[u % 2][:, 0:256], kk[:, u, 0:256], ALU.mult).then_inc(weighted, 1)
                    dve.tensor_tensor(KP[:, u, 256:384], Es[u % 2][:, 256:384], kk[:, u, o2 * P:(o2 + 1) * P],
                                      ALU.mult).then_inc(weighted, 1)
                    if u >= 2:
                        keep(u - 2)
                keep(6)
                keep(7)

        works = [(h, c, dr) for h in range(4) for c in (2, 3) for dr in range(2)]
        gsum, gexp, xq, xk = S("level_sums"), S("level_exp"), S("queries_weighted"), S("level_keys_weighted")
        smade, amade, omade, okept = S("scores_made"), S("scores_masked"), S("o_made"), S("o_kept")
        with nc.Block() as block:
            @block.tensor
            def _(pe):
                def level_sums(i):
                    h, c, dr = works[i]
                    if i >= 1:
                        pe.wait_ge(gexp, i)
                    for b in range(2):
                        ins = pe.matmul(ps[:, b, :], LT[:, dr * 4 + h, c, :], sel[:, dr, b * 512:(b + 1) * 512],
                                        start=True, stop=True)
                    ins.then_inc(gsum, 1)

                def scores(i):
                    h, c, dr = works[i]
                    pe.wait_ge(xk, i + 1)
                    pe.wait_ge(xq, i + 1)
                    if i >= 1:
                        pe.wait_ge(amade, i)
                    for lev in range(LEVELS + 1):
                        out = ps[:, 2 + lev // 4, lev % 4 * P:(lev % 4 + 1) * P]
                        if lev < LEVELS:
                            ins = pe.matmul(out, X[i % 2][:, lev, :], X[i % 2][:, lev, :], start=True, stop=True)
                        else:
                            ins = pe.matmul(out, kk[:, dr * 4 + h, c * P:(c + 1) * P], q[:, h, (c - 2) * P:(c - 1) * P],
                                            start=True, stop=True)
                    ins.then_inc(smade, 1)

                def outputs(i):
                    h, c, _ = works[i]
                    pe.wait_ge(amade, i + 1)
                    m = i // 2
                    if m >= 2:
                        pe.wait_ge(okept, m - 1)
                    out = ps[:, 4 + m % 2, 0:P]
                    for j in (i - 1, i):
                        dr = works[j][2]
                        for lev in range(LEVELS + 1):
                            pe.matmul(out, AA[j % 4][:, lev, :], v[:, c, h * P:(h + 1) * P],
                                      start=j == i - 1 and lev == 0, stop=False)
                        ins = pe.matmul(out, QD[j % 4], st[:, dr * 4 + h, int(c == ORDER[dr][3]), :],
                                        start=False, stop=j == i)
                    ins.then_inc(omade, 1)

                for i in range(len(works) + 2):
                    if i < len(works):
                        level_sums(i)
                    if 1 <= i <= len(works):
                        scores(i - 1)
                    if i >= 2 and i % 2 == 1:
                        outputs(i - 2)

            @block.scalar
            def _(act):
                def keep(m):
                    h, c, _ = works[2 * m]
                    act.wait_ge(omade, m + 1)
                    col = (4 * half + h) * P
                    act.activation(self.o_all[:, c - 2, col:col + P], ps[:, 4 + m % 2, 0:P], ACT.Copy).then_inc(okept, 1)
                for i in range(len(works)):
                    act.wait_ge(gsum, i + 1)
                    if i >= 2:
                        act.wait_ge(xk, i - 1)
                        act.wait_ge(xq, i - 1)
                    act.activation(G[i % 2], ps[:, 0:2, :].rearrange("p b (l t) -> p (b l) t", l=4), ACT.Exp).then_inc(gexp, 1)
                    if i >= 4 and i % 2 == 0:
                        keep(i // 2 - 2)
                keep(6)
                keep(7)

            def halves(eng, i, keys, done):
                h, c, dr = works[i]
                src = kk[:, dr * 4 + h, c * P:(c + 1) * P] if keys else q[:, h, (c - 2) * P:(c - 1) * P]
                side = (0 if keys else 1) ^ dr
                for lev in range(LEVELS):
                    m = P >> (lev + 1)
                    w = lambda a: a.rearrange("p (n two m) -> p n two m", two=2, m=m)[:, :, side, :]
                    ins = eng.tensor_tensor(w(X[i % 2][:, lev, :]), w(G[i % 2][:, lev, :]), w(src), ALU.mult)
                if not keys:
                    ins = eng.tensor_tensor(QD[i % 4], G[i % 2][:, LEVELS, :], src, ALU.mult)
                ins.then_inc(done, 1)

            @block.gpsimd
            def _(pool):
                for i in range(len(works)):
                    pool.wait_ge(gexp, i + 1)
                    if i >= 2:
                        pool.wait_ge(smade, i - 1)
                    halves(pool, i, True, xk)

            @block.vector
            def _(dve):
                def masked(i):
                    dr = works[i][2]
                    dve.wait_ge(smade, i + 1)
                    if i >= 4:
                        dve.wait_ge(omade, (i - 4) // 2 + 1)
                    dve.tensor_tensor(AA[i % 4].rearrange("p l t -> p (l t)"),
                                      ps[:, 2:4, :].rearrange("p b t -> p (b t)"), mask[:, dr, :], ALU.mult).then_inc(amade, 1)
                for i in range(len(works)):
                    dve.wait_ge(gexp, i + 1)
                    if i >= 2:
                        dve.wait_ge(smade, i - 1)
                    if i >= 4:
                        dve.wait_ge(omade, (i - 4) // 2 + 1)
                    halves(dve, i, False, xq)
                    if i >= 1:
                        masked(i - 1)
                masked(len(works) - 1)

    def mlstm_in(self):
        nc, d, ring, ps, hT = self.nc, self.d, self.ring, self.ps, self.hT
        A = Arena(self.arena_t, self.work + 2 * D, self.A.end)
        self.r_all = A.take(2, D)
        self.ml_v = V = A.take(NC, ML_H, ML_DV + 1)
        self.ml_qk = A.take(8, SEQ)
        self.ml_kc = A.take(4, CTX)
        self.ml_area = A.at
        raw = A.take(8, SEQ + 4)
        rawc = A.take(4, CTX + 4)
        wif = A.take(KT, 16)
        brow = A.take(1024)
        bif = A.take(1)
        mif = A.take(TOK)
        hp = A.take(KT, SEQ)
        S = lambda name: self.sem("mlstm_" + name)
        self.mod_open(S, A, 4)
        made, freed, small, permuted = S("made"), S("freed"), S("small_loaded"), S("permuted")
        imade = S("gate_rows_made")
        grid = lambda a: a.rearrange("p (r c) -> p c r", c=GRID)
        cols = lambda a: a.rearrange("p (c r) -> p c r", r=ROWS)
        token_cols = [lambda k, c=c: hT[:, k, c * P:(c + 1) * P] for c in range(2)] + \
                     [lambda k, c=c: hp[:, k, c * P:(c + 1) * P] for c in range(2)]
        with nc.Block() as block:
            @block.sync
            def _(sp):
                sp.dma_start(brow, d["b_in"][0:1, O_MV:O_MV + D].partition_broadcast(P)).then_inc(small, 16)
                sp.dma_start(wif, d["w_in"].rearrange("(k p) n -> p k n", p=P)[:, :, O_MI:O_MI + 16]).then_inc(small, 16)
                sp.dma_start(bif[0:16, :], d["b_in"][0:1, O_MI:O_MI + 16].rearrange("a b -> b a")).then_inc(small, 16)
                ring.send(sp, self.ends["mlstm"] + 3)

            @block.scalar
            def _(act):
                for m in range(4):
                    self.mod_keep_step(act, m)

            @block.gpsimd
            def _(pool):
                pool.memset(raw, 0.0)
                pool.memset(rawc, 0.0)
                pool.memset(V[:, :, :, ML_DV:ML_DV + 1], 1.0).then_inc(permuted, 1)
                for k in range(KT):
                    pool.tensor_copy(cols(hp[:, k, :]), grid(hT[:, k, CTX:TOK])).then_inc(permuted, 1)

            @block.tensor
            def _(pe):
                def first():
                    pe.wait_ge(permuted, 1 + KT)
                self.products(pe, [self.feature_tiles(hT, CTX, TOK), self.feature_tiles(hT, 0, TOK)], made, freed, mods=2)
                first()
                self.products(pe, [self.token_tiles(token_cols), self.token_tiles(token_cols)], made, freed, first=8, mods=2)
                pe.wait_ge(small, 48)
                pe.wait_ge(freed, 13)
                for k in range(KT):
                    ins = pe.matmul(ps[0:16, 0, :], wif[:, k, :], hT[:, k, :], start=k == 0, stop=k == KT - 1)
                ins.then_inc(imade, 1)

            @block.vector
            def _(dve):
                dve.wait_ge(permuted, 1 + KT)
                dve.wait_ge(small, 48)
                for t in range(16):
                    dve.wait_ge(made, t + 1)
                    bank = ps[:, t % NBANK, :]
                    if t < 4:
                        ins = dve.tensor_scalar(cols(raw[:, t, 2:2 + SEQ]), grid(bank[:, 0:SEQ]),
                                                self.P_("b_mq")[:, t:t + 1], None, ALU.add)
                    elif t < 8:
                        b = self.P_("b_mk")[:, t - 4:t - 3]
                        dve.tensor_scalar(rawc[:, t - 4, 2:2 + CTX], bank[:, 0:CTX], b, None, ALU.add)
                        ins = dve.tensor_scalar(cols(raw[:, t, 2:2 + SEQ]), grid(bank[:, CTX:TOK]), b, None, ALU.add)
                    else:
                        blk, c = divmod(t - 8, 4)
                        ins = dve.tensor_tensor(V[:, c, 2 * blk:2 * blk + 2, 0:ML_DV],
                                                bank.rearrange("p (h v) -> p h v", v=ML_DV),
                                                brow[:, 512 * blk:512 * blk + 512].rearrange("p (h v) -> p h v", v=ML_DV), ALU.add)
                    ins.then_inc(freed, 1)
                self.mod_add(dve)
                dve.wait_ge(imade, 1)
                dve.tensor_scalar(mif[0:16, 0:CTX], ps[0:16, 0, 0:CTX], bif[0:16, :], None, ALU.add)
                dve.tensor_scalar(cols(mif[0:16, CTX:TOK]), grid(ps[0:16, 0, CTX:TOK]), bif[0:16, :], None, ALU.add)

        conv = [S(f"conv{i}") for i in range(3)]
        row_made, rows = S("rows_split"), S("rows")
        self.ml_rows = [A.take(2, TOK) for _ in range(6)]
        self.ml_rows_end = A.at
        with nc.Block() as block:
            @block.tensor
            def _(pe):
                for g in range(4):
                    ins = pe.matmul(ps[0:4, g, :], self.ident[0:16, 4 * g:4 * g + 4], mif[0:16, :], start=True, stop=True)
                ins.then_inc(row_made, 1)

            @block.vector
            def _(dve):
                dve.wait_ge(row_made, 1)
                for which, g in ((0, 0), (1, 2)):
                    dst = self.ml_rows[which]
                    dve.tensor_copy(dst[0:4, 0, :], ps[0:4, g, :])
                    for a in (0, CTX):
                        dve.tensor_copy(dst[0:4, 1, a:a + SEQ], ps[0:4, g + 1, a:a + SEQ][:, ::-1])
                w, b = self.P_("cw1"), self.P_("cb1")
                todo = [(self.ml_qk[:, t, :], raw[:, t, :], t) for t in range(8)] + \
                       [(self.ml_kc[:, t, :], rawc[:, t, :], t + 4) for t in range(4)]
                for tap in range(5):
                    for dst, src, t in todo:
                        if tap == 0:
                            ins = dve.tensor_scalar(dst, src[:, 0:SEQ], w[:, t:t + 1], b[:, t:t + 1], ALU.mult, ALU.add)
                        else:
                            ins = dve.scalar_tensor_tensor(dst, src[:, tap:tap + SEQ], w[:, 8 * tap + t:8 * tap + t + 1], dst,
                                                           ALU.mult, ALU.add)
                    ins.then_inc(conv[0], 1)
                    dve.wait_ge(conv[0], tap + 1)
                dve.wait_ge(conv[1], 1)
                dve.tensor_scalar(self.ml_qk[:, 0:4, :], self.ml_qk[:, 0:4, :], float(P) ** -0.5, None, ALU.mult)

            @block.scalar
            def _(act):
                act.wait_ge(conv[0], 5)
                act.activation(self.ml_qk, self.ml_qk, ACT.Silu).then_inc(conv[1], 1)
                act.activation(self.ml_kc, self.ml_kc, ACT.Silu)

    def mlstm(self):
        nc, d, ps = self.nc, self.d, self.ps
        I, F, B, M, T1, T2 = [r[0:4] for r in self.ml_rows]
        A = Arena(self.arena_t, self.ml_area, self.A.end)
        arg = [A.take(4, SEQ) for _ in range(2)]
        Pm = [A.take(4, SEQ) for _ in range(2)]
        A.at = max(A.at, self.ml_rows_end)
        cols = A.take(48)
        rows4 = A.take(ML_H, P)
        nat = A.take(2, TOK)
        natmu = A.take(2, SEQ)
        natem = A.take(2, SEQ)
        mask = A.take(2, 2, SEQ)
        small = A.take(4)
        S = lambda name: self.sem("ml_" + name)
        sv, sa = S("vector_rows"), S("scalar_rows")
        rowsin, turned, mset = S("rows4_loaded"), S("turned"), S("masks_set")
        incl = [self.k_sel[:, dr * (LEVELS + 2) * P + LEVELS * P:dr * (LEVELS + 2) * P + (LEVELS + 1) * P] for dr in range(2)]
        with nc.Block() as block:
            @block.sync
            def _(sp):
                sp.dma_start(rows4[0:4], d["k_rows4"].rearrange("p (a b) -> p a b", b=P)).then_inc(rowsin, 16)
                sp.wait_ge(rowsin, 16)

            @block.gpsimd
            def _(pool):
                pool.memset(mask[:, 0, 0, P:SEQ], 1.0)
                pool.memset(mask[:, 0, 1, 0:P], 0.0)
                pool.memset(mask[:, 1, 0, P:SEQ], 0.0)
                pool.memset(mask[:, 1, 1, 0:P], 1.0)
                for dr in range(2):
                    for c in range(2):
                        pool.tensor_copy(mask[:, dr, c, c * P:(c + 1) * P], incl[dr])

            @block.scalar
            def _(act):
                act.wait_ge(sv, 1)
                act.activation(T1, T1, ACT.Exp, scale=-1.0).then_inc(sa, 1)
                act.wait_ge(sa, 1)
                act.activation(T1, T1, ACT.Ln, bias=1.0).then_inc(sa, 1)
                act.wait_ge(sv, 6)
                act.activation(T2, T2, ACT.Exp, scale=-1.0).then_inc(sa, 1)

            @block.vector
            def _(dve):
                n = [0]
                def step(ins):
                    n[0] += 1
                    ins.then_inc(sv, 1)
                    dve.wait_ge(sv, n[0])
                step(dve.scalar_tensor_tensor(T1, F, -1.0, F, ALU.mult, ALU.max))
                dve.wait_ge(sa, 2)
                step(dve.scalar_tensor_tensor(F, F, 0.0, T1, ALU.min, ALU.subtract))
                dve.memset(T2, 1.0)
                dve.drain()
                for dr in range(2):
                    ins = dve.tensor_tensor_scan(B[:, dr, :], T2[:, dr, :], F[:, dr, :], 0.0, ALU.mult, ALU.add)
                step(ins)
                step(dve.tensor_tensor(I, I, B, ALU.subtract))
                for dr in range(2):
                    ins = dve.tensor_tensor_scan(M[:, dr, :], T2[:, dr, :], I[:, dr, :], 0.0, ALU.mult, ALU.max)
                step(ins)
                step(dve.tensor_tensor(T2, B, M, ALU.add))
                dve.tensor_copy(nat[0:4, 0, :], I[:, 0, :])
                for a in (0, CTX):
                    dve.tensor_copy(nat[0:4, 1, a:a + SEQ], I[:, 1, a:a + SEQ][:, ::-1])
                dve.tensor_scalar(natmu[0:4, 0, :], M[:, 0, CTX:TOK], -1.0, None, ALU.mult)
                dve.tensor_scalar(natmu[0:4, 1, :], M[:, 1, CTX:TOK][:, ::-1], -1.0, None, ALU.mult)
                dve.wait_ge(sa, 3)
                dve.tensor_copy(natem[0:4, 0, :], T2[:, 0, CTX:TOK])
                dve.tensor_copy(natem[0:4, 1, :], T2[:, 1, CTX:TOK][:, ::-1])
        with nc.Block() as block:
            @block.tensor
            def _(pe):
                for dr in range(2):
                    for c in range(NC):
                        i = dr * NC + c
                        pe.transpose(ps[:, 0, 4 * i:4 * i + 4], nat[0:4, dr, c * P:(c + 1) * P], self.ident[0:4, 0:4])
                    for c in range(2):
                        i = 8 + dr * 2 + c
                        ins = pe.transpose(ps[:, 0, 4 * i:4 * i + 4], natem[0:4, dr, c * P:(c + 1) * P], self.ident[0:4, 0:4])
                ins.then_inc(turned, 1)

            @block.vector
            def _(dve):
                dve.wait_ge(turned, 1)
                dve.tensor_copy(cols, ps[:, 0, 0:48])

        q, k, kc, V = self.ml_qk[:, 0:4, :], self.ml_qk[:, 4:8, :], self.ml_kc, self.ml_v
        units = [(h, dr) for h in range(ML_H) for dr in range(2)]
        bmade, smade, argd, exped = S("mu_rows_made"), S("scores_made"), S("arguments"), S("exped")
        pmade, pmask, nmade, nkept = S("weights_made"), S("weights_masked"), S("numerators_made"), S("outputs_kept")
        vd = S("denominators")
        tiles = {(0, 0): (0, 1, 2), (0, 1): (0, 1, 2, 3), (1, 0): (0, 1, 2, 3), (1, 1): (0, 1, 3)}
        with nc.Block() as block:
            @block.tensor
            def _(pe):
                def arguments(u):
                    h, dr = units[u]
                    if u >= 2:
                        pe.wait_ge(argd, u - 1)
                    pe.matmul(ps[:, u % 2, 0:SEQ], rows4[0:4, h, :], natmu[0:4, dr, :], start=True, stop=True).then_inc(bmade, 1)
                    if dr == 0:
                        if h >= 2:
                            pe.wait_ge(pmade, 2 * h - 2)
                        for c in range(NC):
                            lhsT = kc[:, h, c * P:(c + 1) * P] if c < LAT else k[:, h, (c - 2) * P:(c - 1) * P]
                            ins = pe.matmul(ps[:, 2 + 2 * (h % 2) + c // 2, c % 2 * SEQ:(c % 2 + 1) * SEQ], lhsT,
                                            q[:, h, :], start=True, stop=True)
                        ins.then_inc(smade, 1)

                def numerators(u):
                    h, dr = units[u]
                    pe.wait_ge(pmask, u + 1)
                    for c in range(2):
                        if u >= 1:
                            pe.wait_ge(nkept, 2 * u - 1 + c)
                        use = tiles[dr, c]
                        for i in use:
                            ins = pe.matmul(ps[:, 6 + c, 0:ML_DV + 1], Pm[u % 2][:, i, c * P:(c + 1) * P], V[:, i, h, :],
                                            start=i == use[0], stop=i == use[-1])
                        ins.then_inc(nmade, 1)
                for u in range(9):
                    if u < 8:
                        arguments(u)
                    if u >= 1:
                        numerators(u - 1)

            @block.scalar
            def _(act):
                for u in range(8):
                    act.wait_ge(argd, u + 1)
                    act.activation(arg[u % 2], arg[u % 2], ACT.Exp).then_inc(exped, 1)

            @block.gpsimd
            def _(pool):
                for u in range(8):
                    pool.wait_ge(pmade, u + 1)
                    pool.tensor_tensor(Pm[u % 2][:, 2:4, :], Pm[u % 2][:, 2:4, :], mask[:, units[u][1]], ALU.mult).then_inc(pmask, 1)

            @block.vector
            def _(dve):
                def outputs(u):
                    h, dr = units[u]
                    for c in range(2):
                        dve.wait_ge(nmade, 2 * u + c + 1)
                        num, n = ps[:, 6 + c, :], 3 * (2 * u + c)
                        em = cols[:, 32 + (dr * 2 + c) * 4 + h:33 + (dr * 2 + c) * 4 + h]
                        den, s = num[:, ML_DV:ML_DV + 1], small[:, c:c + 1]
                        dve.scalar_tensor_tensor(s, den, -1.0, em, ALU.mult, ALU.max).then_inc(vd, 1)
                        dve.wait_ge(vd, n + 1)
                        dve.tensor_tensor(s, s, den, ALU.max).then_inc(vd, 1)
                        dve.wait_ge(vd, n + 2)
                        dve.reciprocal(s, s).then_inc(vd, 1)
                        dve.wait_ge(vd, n + 3)
                        r = self.r_all[:, c, h * ML_DV:(h + 1) * ML_DV]
                        if dr == 0:
                            ins = dve.tensor_scalar(r, num[:, 0:ML_DV], small[:, c:c + 1], None, ALU.mult)
                        else:
                            ins = dve.scalar_tensor_tensor(r, num[:, 0:ML_DV], small[:, c:c + 1], r, ALU.mult, ALU.add)
                        ins.then_inc(nkept, 1)
                for u in range(8):
                    h, dr = units[u]
                    dve.wait_ge(bmade, u + 1)
                    if u >= 2:
                        dve.wait_ge(pmade, u - 1)
                    for c in range(NC):
                        i = (dr * NC + c) * 4 + h
                        ins = dve.tensor_scalar(arg[u % 2][:, c, :], ps[:, u % 2, 0:SEQ], cols[:, i:i + 1], 0.0, ALU.add, ALU.min)
                    ins.then_inc(argd, 1)
                    dve.wait_ge(exped, u + 1)
                    dve.wait_ge(smade, h + 1)
                    if u >= 2:
                        dve.wait_ge(nmade, 2 * (u - 2) + 2)
                    dve.tensor_tensor(Pm[u % 2].rearrange("p a t -> p (a t)"), arg[u % 2].rearrange("p a t -> p (a t)"),
                                      ps[:, 2 + 2 * (h % 2):4 + 2 * (h % 2), :].rearrange("p b t -> p (b t)"), ALU.mult).then_inc(pmade, 1)
                    if u >= 1:
                        outputs(u - 1)
                outputs(7)

    def merge1(self):
        nc, d, ring, ps, hT = self.nc, self.d, self.ring, self.ps, self.hT
        A = Arena(self.arena_t, self.work + 4 * D, self.A.end)
        o, r = self.o_all, self.r_all
        gates = [A.take(KT, SEQ) for _ in range(4)]
        sq = A.take(2, D)
        ss = [A.take(2, HG_H), A.take(2, ML_H)]
        S = lambda name: self.sem("merge1_" + name)
        made, freed = S("gates_made"), S("gates_kept")
        squared, summed, rooted, meaned, normed = S("squared"), S("summed"), S("rooted"), S("meaned"), S("normed")
        srcs = [(o, HG_H), (r, ML_H)]
        self.mod_open(S, A, 8)
        with nc.Block() as block:
            @block.sync
            def _(sp):
                ring.send(sp, self.ends["gates1"] + 3)

            @block.tensor
            def _(pe):
                self.products(pe, [self.feature_tiles(hT, CTX, TOK)] * 8, made, freed, mods=8)

            @block.scalar
            def _(act):
                for i, (src, _) in enumerate(srcs):
                    if i == 1:
                        act.wait_ge(summed, 1)
                    act.activation(sq, src, ACT.Square).then_inc(squared, 1)
                for i in range(2):
                    act.wait_ge(meaned, i + 1)
                    act.activation(ss[i], ss[i], ACT.Sqrt).then_inc(rooted, 1)
                for t in range(32):
                    act.wait_ge(made, t + 1)
                    g, k = divmod(t, 8)
                    bias = self.P_(("b_ga", "b_gb", "b_g1", "b_g2")[g])[:, k:k + 1]
                    act.activation(gates[g][:, k, :], ps[:, t % NBANK, 0:SEQ], ACT.Silu if g == 0 else ACT.Sigmoid,
                                   bias=bias).then_inc(freed, 1)
                    if t % 4 == 3:
                        self.mod_keep_step(act, t // 4)

            @block.vector
            def _(dve):
                for i, (src, h) in enumerate(srcs):
                    dve.wait_ge(squared, i + 1)
                    dve.reduce_sum(ss[i], sq.rearrange("p c (h v) -> p c h v", h=h), axis=AX.X).then_inc(summed, 1)
                    dve.wait_ge(summed, i + 1)
                    dve.tensor_scalar(ss[i], ss[i], float(h) / D, EPS, ALU.mult, ALU.add).then_inc(meaned, 1)
                for i, (src, h) in enumerate(srcs):
                    dve.wait_ge(rooted, i + 1)
                    dve.reciprocal(ss[i], ss[i]).then_inc(normed, 1)
                    dve.wait_ge(normed, i + 1)
                    for c in range(2):
                        v = src[:, c, :].rearrange("p (h v) -> p h v", h=h)
                        dve.tensor_tensor(v, v, bcast(ss[i][:, c, :].unsqueeze(2), [P, h, D // h]), ALU.mult)
                self.mod_add(dve)
        yT = [A.take(KT, SEQ) for _ in range(2)]
        turned, kept = S("turned"), S("turned_kept")
        grid = lambda a: a.rearrange("p (r c) -> p c r", c=GRID)
        cols = lambda a: a.rearrange("p (c r) -> p c r", r=ROWS)
        with nc.Block() as block:
            @block.tensor
            def _(pe):
                for t in range(16):
                    if t >= 8:
                        pe.wait_ge(kept, t - 7)
                    src, k = srcs[t // 8][0], t % 8
                    for c in range(2):
                        ins = pe.transpose(ps[:, t % 8, c * P:(c + 1) * P], src[:, c, k * P:(k + 1) * P], self.ident)
                    ins.then_inc(turned, 1)

            @block.vector
            def _(dve):
                for t in range(16):
                    dve.wait_ge(turned, t + 1)
                    b, k = divmod(t, 8)
                    if b == 0:
                        ins = dve.scalar_tensor_tensor(yT[0][:, k, :], ps[:, t % 8, 0:SEQ], self.P_("hg_g")[:, k:k + 1],
                                                       gates[0][:, k, :], ALU.mult, ALU.mult)
                    else:
                        ins = dve.scalar_tensor_tensor(grid(yT[1][:, k, :]), cols(ps[:, t % 8, 0:SEQ]),
                                                       self.P_("ml_g")[:, k:k + 1], grid(gates[1][:, k, :]), ALU.mult, ALU.mult)
                    ins.then_inc(kept, 1)
        y = A.take(KT, SEQ)
        t2 = [A.take(SEQ) for _ in range(2)]
        tiles = [(lambda w, k, j=j: w[:, k, j * P:(j + 1) * P], lambda w, k, b=b: yT[b][:, k, :], SEQ, KT) for b in range(2) for j in range(4)]
        self.merge_out("merge1b", [tiles[0:4]] * 2 + [tiles[4:8]] * 2, gates[2:4], y, t2, self.ends["merge1"],
                       gain=self.mod1[:, 16:24, 0])

    def merge_out(self, name, branch_tiles, gates, y, t2, end, gain=None, store=None):
        nc, ring, ps = self.nc, self.ring, self.ps
        S = lambda n: self.sem(name + "_" + n)
        made, freed, ydone, part = S("made"), S("kept"), S("y_done"), S("gated")
        with nc.Block() as block:
            @block.sync
            def _(sp):
                ring.send(sp, end)

            @block.tensor
            def _(pe):
                tiles = lambda src: [(lambda w, k, j=j: w[:, k, j * P:(j + 1) * P], lambda w, k: src[:, k, :], SEQ, KT)
                                     for j in range(4)]
                n = self.products(pe, branch_tiles, made, freed)
                pe.wait_ge(ydone, KT)
                self.products(pe, [tiles(y)] * 2, made, freed, first=n)

            @block.vector
            def _(dve):
                for t in range(24):
                    dve.wait_ge(made, t + 1)
                    b, k = divmod(t, 8)
                    bank = ps[:, t % NBANK, 0:SEQ]
                    if b == 0:
                        ins = dve.tensor_tensor(y[:, k, :], bank, gates[0][:, k, :], ALU.mult)
                    elif b == 1:
                        ins = dve.tensor_tensor(t2[k % 2], bank, gates[1][:, k, :], ALU.mult)
                    elif store is None:
                        ins = dve.scalar_tensor_tensor(self.xT[:, k, :], bank, gain[:, k:k + 1], self.xT[:, k, :], ALU.mult, ALU.add)
                    else:
                        ins = dve.tensor_copy(store[:, k, :], bank)
                    ins.then_inc(freed, 1)
                    if b == 1:
                        dve.wait_ge(freed, t + 1)
                        dve.tensor_tensor(y[:, k, :], y[:, k, :], t2[k % 2], ALU.add).then_inc(ydone, 1)

    def norm_modulate(self, name, src, dst, gain_col, scale, shift, A):
        rstd, sq, g = A.take(SEQ), A.take(KT, SEQ), A.take(KT)
        self.rms(name, src, KT, SEQ, rstd, sq)
        s = self.sem(name + "_scaled")
        with self.nc.Block() as block:
            @block.vector
            def _(dve):
                if scale is not None:
                    dve.scalar_tensor_tensor(g, scale, 1.0, gain_col, ALU.add, ALU.mult)
                else:
                    dve.tensor_copy(g, gain_col)
                dve.tensor_tensor(dst, src, bcast(rstd.unsqueeze(1), [P, KT, SEQ]), ALU.mult).then_inc(s, 1)
                dve.wait_ge(s, 1)
                for k in range(KT):
                    dve.tensor_scalar(dst[:, k, :], dst[:, k, :], g[:, k:k + 1], shift[:, k:k + 1] if shift is not None else None,
                                      ALU.mult, ALU.add if shift is not None else ALU.bypass)

    def router1(self):
        nc, d, ps = self.nc, self.d, self.ps
        A = Arena(self.arena_t, self.work, self.A.end)
        self.h2 = self.hT[:, :, 0:SEQ]
        self.wgt = A.take(2, N_EXP)
        self.rank = A.take(2, N_EXP)
        self.rounds = A.take(1).bitcast(mybir.dt.int32)
        self.moe_area = A.at
        wr = A.take(KT, N_GRP + N_EXP)
        br = A.take(N_GRP + N_EXP)
        iota = A.take(SEQ)
        self.norm_modulate("norm2", self.xT, self.h2, self.P_("norm2"), self.mod1[:, 32:40, 0], self.mod1[:, 24:32, 0], A)
        S = lambda n: self.sem("router1_" + n)
        loaded, made, st, sa = S("loaded"), S("logits_made"), S("step"), S("exped")
        n = N_GRP + N_EXP
        lg, e, e2, pri = A.take(2, n), A.take(2, N_EXP), A.take(2, N_EXP), A.take(2, N_EXP)
        oh1, oh2, comb = A.take(2, N_EXP), A.take(2, N_EXP), self.wgt
        gh, gex = A.take(2, N_GRP), A.take(2, N_GRP)
        desc = A.take(N_EXP)
        v = A.take(8, 2)
        chosen, chosen2 = A.take(2, N_EXP), A.take(2, N_EXP)
        with nc.Block() as block:
            @block.sync
            def _(sp):
                sp.dma_start(wr[:, :, 0:N_GRP], d["w_group"].rearrange("(k p) n -> p k n", p=P)).then_inc(loaded, 16)
                sp.dma_start(wr[:, :, N_GRP:n], d["w_router"].rearrange("(k p) n -> p k n", p=P)).then_inc(loaded, 16)
                sp.dma_start(br[:, 0:N_GRP], d["b_group"].partition_broadcast(P)).then_inc(loaded, 16)
                sp.dma_start(br[:, N_GRP:n], d["b_router"].partition_broadcast(P)).then_inc(loaded, 16)
                sp.dma_start(iota, d["k_iota"]).then_inc(loaded, 16)
                sp.wait_ge(loaded, 80)

            @block.tensor
            def _(pe):
                pe.wait_ge(loaded, 80)
                for c in range(2):
                    for k in range(KT):
                        ins = pe.matmul(ps[:, c, 0:n], self.h2[:, k, c * P:(c + 1) * P], wr[:, k, :], start=k == 0, stop=k == KT - 1)
                ins.then_inc(made, 1)

            @block.scalar
            def _(act):
                act.wait_ge(st, 3)
                act.activation(gex, gex, ACT.Exp).then_inc(sa, 1)
                act.wait_ge(st, 4)
                act.activation(v[:, 4, :], v[:, 4, :], ACT.Exp).then_inc(sa, 1)

            @block.vector
            def _(dve):
                vs = self.vs
                do = lambda ins: vs.do(dve, ins)
                bc = lambda a, m: bcast(a.unsqueeze(2), [P, 2, m])
                dve.wait_ge(made, 1)
                dve.wait_ge(loaded, 80)
                do(dve.tensor_tensor(lg, ps[:, 0:2, 0:n], bcast(br.unsqueeze(1), [P, 2, n]), ALU.add))
                do(dve.tensor_scalar(desc, iota[:, 0:N_EXP], -1.0, float(N_EXP), ALU.mult, ALU.add))

                def first_max(src, m, top, hot, tmp):
                    do(dve.reduce_max(top, src, axis=AX.X))
                    do(dve.tensor_tensor(tmp, src, bc(top, m), ALU.is_equal))
                    do(dve.tensor_tensor(tmp, tmp, bcast(desc[:, 0:m].unsqueeze(1), [P, 2, m]), ALU.mult))
                    do(dve.reduce_max(v[:, 7, :], tmp, axis=AX.X))
                    do(dve.tensor_tensor(hot, tmp, bc(v[:, 7, :], m), ALU.is_equal))
                g = lg[:, :, 0:N_GRP]
                first_max(g, N_GRP, v[:, 0, :], gh, pri[:, :, 0:N_GRP])
                dve.tensor_tensor(gex, g, bc(v[:, 0, :], N_GRP), ALU.subtract).then_inc(st, 3)
                do(dve.tensor_scalar(gh, gh, BIG, -BIG, ALU.mult, ALU.add))
                do(dve.tensor_tensor(e.rearrange("p c (g e) -> p c g e", g=N_GRP),
                                     lg[:, :, N_GRP:n].rearrange("p c (g e) -> p c g e", g=N_GRP),
                                     bcast(gh.unsqueeze(3), [P, 2, N_GRP, PER_GRP]), ALU.add))
                first_max(e, N_EXP, v[:, 1, :], oh1, pri)
                do(dve.scalar_tensor_tensor(e2, oh1, -3 * BIG, e, ALU.mult, ALU.add))
                first_max(e2, N_EXP, v[:, 2, :], oh2, pri)
                dve.tensor_tensor(v[:, 4, :], v[:, 2, :], v[:, 1, :], ALU.subtract).then_inc(st, 1)
                dve.wait_ge(sa, 2)
                do(dve.reduce_sum(v[:, 3, :], gex, axis=AX.X))
                do(dve.tensor_scalar(v[:, 5, :], v[:, 4, :], 1.0, None, ALU.add))
                do(dve.tensor_tensor(v[:, 5, :], v[:, 5, :], v[:, 3, :], ALU.mult))
                do(dve.reciprocal(v[:, 5, :], v[:, 5, :]))
                do(dve.tensor_tensor(v[:, 6, :], v[:, 5, :], v[:, 4, :], ALU.mult))
                do(dve.tensor_tensor(chosen, oh1, oh2, ALU.add))
                do(dve.tensor_tensor(oh1, oh1, bc(v[:, 5, :], N_EXP), ALU.mult))
                do(dve.tensor_tensor(oh2, oh2, bc(v[:, 6, :], N_EXP), ALU.mult))
                do(dve.tensor_tensor(comb, oh1, oh2, ALU.add))
        counted, rk = S("counted"), S("rank_steps")
        before = self.k_sel[:, (2 * LEVELS + 3) * P:(2 * LEVELS + 4) * P]
        most = A.take(1)
        with nc.Block() as block:
            @block.tensor
            def _(pe):
                pe.matmul(ps[:, 0, 0:N_EXP], before, chosen[:, 0, :], start=True, stop=True)
                pe.matmul(ps[:, 1, 0:N_EXP], before, chosen[:, 1, :], start=True, stop=False)
                pe.matmul(ps[:, 1, 0:N_EXP], self.ones, chosen[:, 0, :], start=False, stop=True)
                for c in range(2):
                    ins = pe.matmul(ps[:, 2, 0:N_EXP], self.ones, chosen[:, c, :], start=c == 0, stop=c == 1)
                ins.then_inc(counted, 1)

            @block.vector
            def _(dve):
                dve.tensor_scalar(chosen2, chosen, -1e4, 1e4, ALU.mult, ALU.add).then_inc(rk, 1)
                dve.wait_ge(rk, 1)
                dve.wait_ge(counted, 1)
                dve.tensor_tensor(self.rank, ps[:, 0:2, 0:N_EXP], chosen2, ALU.add)
                dve.reduce_max(most, ps[:, 2, 0:N_EXP], axis=AX.X).then_inc(rk, 1)
                dve.wait_ge(rk, 2)
                dve.tensor_scalar(self.rounds, most, 1.0 / CAP, (CAP - 1.0) / CAP - 0.5 + 0.5 / CAP, ALU.mult, ALU.add)

    def gather(self, n_exp, rank, wgt, xe, selT, iota, A, S):
        nc, ps = self.nc, self.ps
        n = n_exp * CAP
        sel, selw, h_tok = A.take(2, n), A.take(2 * 4 * n).rearrange("p (c e r s) -> p c e r s", c=2, e=n_exp, r=4), A.take(2, D)
        sset, wset, hturned, hkept = S("selected"), S("selection_weighted"), S("h_turned"), S("h_kept")
        xmade, xkept, tmade, tkept = S("xe_made"), S("xe_kept"), S("selection_turned"), S("selection_kept")
        by_slot = lambda c: sel[:, c, :].rearrange("p (e s) -> p e s", s=CAP)
        wide = n // 512
        with nc.Block() as block:
            @block.vector
            def _(dve):
                for c in range(2):
                    dve.tensor_tensor(by_slot(c), bcast(iota[:, 0:CAP].unsqueeze(1), [P, n_exp, CAP]),
                                      bcast(rank[:, c, :].unsqueeze(2), [P, n_exp, CAP]), ALU.is_equal).then_inc(sset, 1)
                dve.wait_ge(sset, 2)
                for c in range(2):
                    for r in range(4):
                        ins = dve.tensor_tensor(selw[:, c, :, r, :], by_slot(c), bcast(wgt[:, c, :].unsqueeze(2), [P, n_exp, CAP]), ALU.mult)
                ins.then_inc(wset, 1)
                for i in range(n_exp // 2):
                    dve.wait_ge(tmade, i + 1)
                    dve.tensor_copy(selT[:, 2 * i:2 * i + 2, :], ps[:, 4 + i % 4, :].rearrange("p (a t) -> p a t", a=2)).then_inc(tkept, 1)

            @block.scalar
            def _(act):
                for k in range(KT):
                    act.wait_ge(hturned, k + 1)
                    act.activation(h_tok[:, :, k * P:(k + 1) * P], ps[:, 4 + k % 4, 0:SEQ].rearrange("p (c f) -> p c f", c=2),
                                   ACT.Copy).then_inc(hkept, 1)
                for i in range(KT * wide):
                    act.wait_ge(xmade, i + 1)
                    act.activation(xe[:, i // wide, i % wide * 512:(i % wide + 1) * 512], ps[:, i % 4, :], ACT.Copy).then_inc(xkept, 1)

            @block.tensor
            def _(pe):
                for k in range(KT):
                    if k >= 4:
                        pe.wait_ge(hkept, k - 3)
                    for c in range(2):
                        ins = pe.transpose(ps[:, 4 + k % 4, c * P:(c + 1) * P], self.h2[:, k, c * P:(c + 1) * P], self.ident)
                    ins.then_inc(hturned, 1)
                pe.wait_ge(hkept, KT)
                pe.wait_ge(sset, 2)
                for i in range(KT * wide):
                    k, w = divmod(i, wide)
                    if i >= 4:
                        pe.wait_ge(xkept, i - 3)
                    for c in range(2):
                        ins = pe.matmul(ps[:, i % 4, :], h_tok[:, c, k * P:(k + 1) * P], sel[:, c, w * 512:(w + 1) * 512],
                                        start=c == 0, stop=c == 1)
                    ins.then_inc(xmade, 1)
                pe.wait_ge(wset, 1)
                for i in range(n_exp // 2):
                    if i >= 4:
                        pe.wait_ge(tkept, i - 3)
                    for j in range(2):
                        for c in range(2):
                            ins = pe.transpose(ps[:, 4 + i % 4, j * SEQ + c * P:j * SEQ + (c + 1) * P],
                                               selw[:, c, 2 * i + j, :, :].rearrange("p r s -> p (r s)"), self.ident)
                    ins.then_inc(tmade, 1)

    def moe1(self):
        nc, d, ps = self.nc, self.d, self.ps
        A = Arena(self.arena_t, self.moe_area, self.A.end)
        xe = A.take(KT, N_EXP * CAP)
        selT = A.take(N_EXP, SEQ)
        xs = [self.hT[:, :, CTX + CAP * j:CTX + CAP * (j + 1)] for j in range(2)]
        stack, gs, aT = self.stack, A.take(4 * CAP), A.take(4, CAP)
        gq, uq, iota = A.take(512), A.take(512), A.take(CAP)
        yq = self.hT[:, :, CTX + P:TOK]
        zero = gq
        slot_area = A.at
        slots = self.ring.slots + [A.take(4096) for _ in range(3)]
        rounds = nc.values_load(self.rounds[0:1, 0:1], min_val=1, max_val=SEQ // CAP)
        src = [d["w_gate"].rearrange("e (k p) f -> e p k f", p=P), d["w_up"].rearrange("e (k p) f -> e p k f", p=P),
               d["w_down"].rearrange("e (k p) n -> e p k n", p=P)]
        mat = [s.rearrange("p (k c) -> p k c", c=D if i % 3 == 2 else 512) for i, s in enumerate(slots)]
        acc = lambda o: ps[:, 4 + o // 2, o % 2 * SEQ:(o % 2 + 1) * SEQ]
        first_sem = self.stage_sems
        last = N_EXP - 1
        S = lambda n: self.sem("moe1_" + n)
        with nc.Fori(0, rounds):
            loaded, used = [S(f"loaded{i}") for i in range(6)], [S(f"used{i}") for i in range(6)]
            tabled = S("iota_loaded")
            with nc.Block() as block:
                @block.sync
                def _(sp):
                    for i in range(3):
                        sp.dma_start(mat[i], src[i][0]).then_inc(loaded[i], 16)
                    sp.dma_start(iota, d["k_iota"][:, 0:CAP]).then_inc(tabled, 16)
                    sp.wait_ge(tabled, 16)
            self.gather(N_EXP, self.rank, self.wgt, xe, selT, iota, Arena(self.arena_t, slot_area, self.A.end), S)
            xset, qmade, gkept, ukept = S("x_set"), S("quarters_made"), S("gate_kept"), S("up_kept")
            tmade, silud, aready, dmade, dkept, zeroed = (S("turned"), S("silu_made"), S("hidden_ready"), S("down_made"),
                                                          S("down_kept"), S("zeroed"))
            scat = S("scattered")
            with nc.Block() as block:
                @block.sync
                def _(sp):
                    for i in range(3, 6):
                        sp.dma_start(mat[i], src[i % 3][1]).then_inc(loaded[i], 16)
                    with sp.Fori(1, N_EXP // 2) as it:
                        for i in range(6):
                            sp.wait_ge(used[i], it)
                            sp.dma_start(mat[i], src[i % 3][bass.ds(it * 2 + i // 3, 1)].rearrange("o p k f -> p (o k) f")
                                         ).then_inc(loaded[i], 16)

                @block.gpsimd
                def _(pool):
                    with pool.Fori(0, N_EXP // 2) as it:
                        for j in range(2):
                            pool.wait_ge(scat, it * 2 + (j + 1))
                            pool.tensor_copy(xs[j], xe[:, :, bass.ds(it * (2 * CAP) + j * CAP, CAP)]).then_inc(xset, 1)

                @block.tensor
                def _(pe):
                    pe.wait_ge(zeroed, 1)
                    for b in range(4):
                        ins = pe.matmul(ps[:, 4 + b, :], zero[:, 0:P], zero, start=True, stop=False, skip_group_check=True)
                    ins.then_inc(gkept, 1)

                    def gate_up(e, j, it):
                        pe.wait_ge(xset, e + 1)
                        pe.wait_ge(gkept, e + 1)
                        pe.wait_ge(ukept, e + 1)
                        for b in range(2):
                            pe.wait_ge(loaded[3 * j + b], it * 16 + 16)
                            for i in range(2):
                                for q in range(4):
                                    ins = pe.matmul(ps[q * CAP:(q + 1) * CAP, b, :], xs[j][:, 2 * q + i, :], mat[3 * j + b][:, 2 * q + i, :],
                                                    start=i == 0, stop=i == 1, skip_group_check=True)
                            ins.then_inc(qmade, 1)
                            pe.drain().then_inc(used[3 * j + b], 1)

                    def turn(e):
                        pe.wait_ge(gkept, e + 2)
                        pe.wait_ge(aready, e + 1)
                        for f in range(4):
                            pe.matmul(ps[:, 2, f * CAP:(f + 1) * CAP], gq[:, f * P:(f + 1) * P], stack, start=True, stop=True)
                        pe.wait_ge(ukept, e + 2)
                        for f in range(4):
                            ins = pe.matmul(ps[:, 2, (4 + f) * CAP:(5 + f) * CAP], uq[:, f * P:(f + 1) * P], stack, start=True, stop=True)
                        ins.then_inc(tmade, 1)

                    def down(e, j, it, h):
                        slot = 3 * j + 2
                        if h == 0:
                            pe.wait_ge(aready, e + 2)
                            pe.wait_ge(loaded[slot], it * 16 + 16)
                        pe.wait_ge(dkept, 2 * e + h + 1)
                        for q in range(4):
                            ins = pe.matmul(ps[q * CAP:(q + 1) * CAP, 3, :], aT[:, q, :], mat[slot][:, q, h * 512:(h + 1) * 512],
                                            start=True, stop=True, skip_group_check=True)
                        ins.then_inc(dmade, 1)
                        if h == 1:
                            pe.drain().then_inc(used[slot], 1)

                    def scatter(e, sel):
                        pe.wait_ge(dkept, 2 * e + 3)
                        for o in range(KT):
                            ins = pe.matmul(acc(o), yq[:, o, :], sel, start=False, stop=False,
                                            skip_group_check=True)
                        ins.then_inc(scat, 1)

                    def expert_step(it, j, it_next):
                        e, jn = it * 2 + j, 1 - j
                        gate_up(it * 2 + (j + 1), jn, it_next)
                        down(e, j, it, 0)
                        down(e, j, it, 1)
                        turn(it * 2 + (j + 1))
                        scatter(e, selT[:, e, :] if isinstance(e, int) else selT[:, bass.ds(e, 1), :].rearrange("p o t -> p (o t)"))
                    gate_up(0, 0, 0)
                    turn(0)
                    with pe.Fori(0, last // 2) as it:
                        expert_step(it, 0, it)
                        expert_step(it, 1, it + 1)
                    expert_step(last // 2, 0, last // 2)
                    down(last, 1, last // 2, 0)
                    down(last, 1, last // 2, 1)
                    scatter(last, selT[:, last, :])
                    pe.wait_ge(zeroed, 2)
                    for b in range(4):
                        pe.matmul(ps[:, 4 + b, :], zero[:, 0:P], zero, start=False, stop=True, skip_group_check=True)

                @block.scalar
                def _(act):
                    act.sem_inc(dkept, 1)
                    act.wait_ge(gkept, 1)
                    act.wait_ge(qmade, 1)
                    act.activation(gq, ps[:, 0, :], ACT.Copy).then_inc(gkept, 1)
                    act.wait_ge(tmade, 1)
                    act.activation(gs, ps[:, 2, 0:4 * CAP], ACT.Silu).then_inc(silud, 1)

                    def keep_down(e):
                        act.wait_ge(scat, e + 1)
                        for h in range(2):
                            act.wait_ge(dmade, 2 * e + (h - 1))
                            act.activation(yq[:, 4 * h:4 * h + 4, :], ps[:, 3, :].rearrange("p (o c) -> p o c", c=P), ACT.Copy).then_inc(dkept, 1)
                    with act.Fori(1, N_EXP) as e:
                        act.wait_ge(qmade, 2 * e + 1)
                        act.activation(gq, ps[:, 0, :], ACT.Copy).then_inc(gkept, 1)
                        keep_down(e)
                        act.wait_ge(tmade, e + 1)
                        act.activation(gs, ps[:, 2, 0:4 * CAP], ACT.Silu).then_inc(silud, 1)
                    keep_down(N_EXP)

                @block.vector
                def _(dve):
                    dve.memset(zero, 0.0).then_inc(zeroed, 1)
                    dve.sem_inc(scat, 2)
                    dve.sem_inc(ukept, 1)
                    dve.sem_inc(aready, 1)
                    with dve.Fori(0, N_EXP) as e:
                        dve.wait_ge(qmade, 2 * e + 2)
                        dve.tensor_copy(uq, ps[:, 1, :]).then_inc(ukept, 1)
                        dve.wait_ge(silud, e + 1)
                        dve.tensor_tensor(aT.rearrange("p f s -> p (f s)"), gs, ps[:, 2, 4 * CAP:8 * CAP], ALU.mult).then_inc(aready, 1)
                    dve.wait_ge(tmade, N_EXP)
                    dve.memset(zero, 0.0).then_inc(zeroed, 1)
            with nc.Block() as block:
                @block.vector
                def _(dve):
                    for o in range(KT):
                        dve.scalar_tensor_tensor(self.xT[:, o, :], acc(o), self.mod1[:, 40 + o, 0:1], self.xT[:, o, :], ALU.mult, ALU.add)
                    dve.tensor_scalar(self.rank, self.rank, -float(CAP), None, ALU.add)
            nc.all_engine_barrier(sems_to_clear=range(FIRST_STAGE_SEM + first_sem, FIRST_STAGE_SEM + self.stage_sems))
        with nc.Block() as block:
            @block.sync
            def _(sp):
                self.ring.send(sp, self.ends["merge1"] + 3)
        A = Arena(self.arena_t, self.work, self.A.end)
        self.norm_modulate("final", self.xT, self.xT, self.P_("final"), None, None, A)

    def ssd_in(self):
        nc, d, ring, ps, hT = self.nc, self.d, self.ring, self.ps, self.hT
        A = Arena(self.arena_t, self.work, self.A.end)
        xin, raw, rstd, sq = A.take(2, D), A.take(KT, TOK), A.take(TOK), A.take(KT, TOK)
        S = lambda n: self.sem("ssd_in_" + n)
        xl, turned, kept, scaled = S("ctx_loaded"), S("ctx_turned"), S("ctx_kept"), S("scaled")
        with nc.Block() as block:
            @block.sync
            def _(sp):
                for i in range(2):
                    sp.dma_start(xin[:, i, :], d["ctx_2"][0, i * P:(i + 1) * P, :]).then_inc(xl, 16)

            @block.tensor
            def _(pe):
                pe.wait_ge(xl, 32)
                for k in range(KT):
                    for i in range(2):
                        ins = pe.transpose(ps[:, k, i * P:(i + 1) * P], xin[:, i, k * P:(k + 1) * P], self.ident)
                    ins.then_inc(turned, 1)

            @block.vector
            def _(dve):
                dve.tensor_copy(raw[:, :, CTX:TOK], self.xT)
                self.gain(dve, self.gain2, self.mod2, "mix_pre")
                for k in range(KT):
                    dve.wait_ge(turned, k + 1)
                    dve.tensor_copy(raw[:, k, 0:CTX], ps[:, k, 0:CTX])
        self.rms("mix_pre", raw, KT, TOK, rstd, sq)
        with nc.Block() as block:
            @block.vector
            def _(dve):
                dve.tensor_tensor(hT, raw, bcast(rstd.unsqueeze(1), [P, KT, TOK]), ALU.mult).then_inc(scaled, 1)
                dve.wait_ge(scaled, 1)
                self.modulate(dve, hT, self.gain2, self.mod2)

        A = Arena(self.arena_t, self.work, self.A.end)
        self.s_lat = lat = A.take(20, SEQ)
        self.s_y = A.take(2, D_SSD)
        at = A.at
        rawc, rawl = A.take(16, CTX + 2), A.take(20, ROWS, GRID + 2)
        end = A.at
        A.at = at
        self.s_x, self.s_B = A.take(NC, D_SSD), A.take(NC, SSD_G * P)
        A.at = end
        self.s_ctx = ctx = A.take(16, CTX)
        self.s_H = A.take(2, 2, D_SSD)
        self.s_dt, self.s_dtA = A.take(NC, 2 * SSD_H), A.take(NC, 2 * SSD_H)
        self.s_area = A.at
        wdt, bdt, al, tmp = A.take(KT, 48), A.take(48), A.take(48), A.take(NC, 48)
        made, freed, small, zeroed, dmade = S("made"), S("freed"), S("small_loaded"), S("zeroed"), S("dt_made")
        rows = lambda a: a.rearrange("p (r c) -> p r c", c=GRID)
        with nc.Block() as block:
            @block.sync
            def _(sp):
                sp.dma_start(wdt, d["w_in_2"].rearrange("(k p) n -> p k n", p=P)[:, :, O_DT:O_DT + 48]).then_inc(small, 16)
                sp.dma_start(bdt, d["dt_bias_2"].rearrange("a b -> (a b)").partition_broadcast(P)).then_inc(small, 16)
                sp.dma_start(al, d["a_log_2"].rearrange("a b -> (a b)").partition_broadcast(P)).then_inc(small, 16)
                ring.send(sp, self.ends["xbc"] + 3)

            @block.gpsimd
            def _(pool):
                pool.memset(rawc, 0.0)
                pool.memset(rawl, 0.0).then_inc(zeroed, 1)

            @block.tensor
            def _(pe):
                self.products(pe, [self.feature_tiles(hT, 0, TOK)] * 4 + [self.feature_tiles(hT, CTX, TOK)], made, freed)
                pe.wait_ge(small, 48)
                pe.wait_ge(freed, 17)
                for c in range(NC):
                    for k in range(KT):
                        ins = pe.matmul(ps[:, 4, c * 48:(c + 1) * 48], hT[:, k, c * P:(c + 1) * P], wdt[:, k, :],
                                        start=k == 0, stop=k == KT - 1)
                ins.then_inc(dmade, 1)

            @block.vector
            def _(dve):
                dve.wait_ge(zeroed, 1)
                for t in range(20):
                    dve.wait_ge(made, t + 1)
                    bank = ps[:, t % NBANK, :]
                    if t < 16:
                        dve.tensor_copy(rawc[:, t, 1:1 + CTX], bank[:, 0:CTX])
                    ins = dve.tensor_copy(rawl[:, t, :, 1:1 + GRID], rows(bank[:, CTX:TOK] if t < 16 else bank[:, 0:SEQ]))
                    ins.then_inc(freed, 1)
                dve.wait_ge(dmade, 1)
                dve.tensor_tensor(self.s_dt, ps[:, 4, 0:NC * 48].rearrange("p (c n) -> p c n", n=48),
                                  bcast(bdt.unsqueeze(1), [P, NC, 48]), ALU.add)
        tap_done, silud, sv, sa = S("tap_done"), S("silu_done"), S("dt_steps"), S("dt_functions")
        with nc.Block() as block:
            @block.vector
            def _(dve):
                dt, dtA = self.s_dt, self.s_dtA
                dve.scalar_tensor_tensor(tmp, dt, -1.0, dt, ALU.mult, ALU.max).then_inc(sv, 1)
                w, b = self.P_("cw2"), self.P_("cb2")
                todo = [(rows(lat[:, t, :]), lambda tap, t=t: rawl[:, t, :, tap:tap + GRID], t) for t in range(20)] + \
                       [(ctx[:, t, :], lambda tap, t=t: rawc[:, t, tap:tap + CTX], t) for t in range(16)]
                for tap in range(3):
                    for dst, src, t in todo:
                        if tap == 0:
                            ins = dve.tensor_scalar(dst, src(tap), w[:, t:t + 1], b[:, t:t + 1], ALU.mult, ALU.add)
                        else:
                            ins = dve.scalar_tensor_tensor(dst, src(tap), w[:, 20 * tap + t:20 * tap + t + 1], dst, ALU.mult, ALU.add)
                    ins.then_inc(tap_done, 1)
                    dve.wait_ge(tap_done, tap + 1)
                dve.wait_ge(sa, 3)
                dve.scalar_tensor_tensor(dt, dt, 0.0, tmp, ALU.max, ALU.add).then_inc(sv, 1)
                dve.wait_ge(sv, 2)
                dve.scalar_tensor_tensor(dtA, dt, -1.0, bcast(al.unsqueeze(1), [P, NC, 48]), ALU.mult, ALU.mult)

            @block.scalar
            def _(act):
                act.activation(al, al, ACT.Exp).then_inc(sa, 1)
                act.wait_ge(sv, 1)
                act.activation(tmp, tmp, ACT.Exp, scale=-1.0).then_inc(sa, 1)
                act.wait_ge(sa, 2)
                act.activation(tmp, tmp, ACT.Ln, bias=1.0).then_inc(sa, 1)
                act.wait_ge(tap_done, 3)
                act.activation(lat, lat, ACT.Silu)
                act.activation(ctx, ctx, ACT.Silu)
        t2, k2 = S("x_turned"), S("x_kept")
        with nc.Block() as block:
            @block.tensor
            def _(pe):
                for t in range(16):
                    if t >= 8:
                        pe.wait_ge(k2, t - 7)
                    for c in range(NC):
                        src = ctx[:, t, c * P:(c + 1) * P] if c < 2 else lat[:, t, (c - 2) * P:(c - 1) * P]
                        ins = pe.transpose(ps[:, t % 8, c * P:(c + 1) * P], src, self.ident)
                    ins.then_inc(t2, 1)

            @block.vector
            def _(dve):
                for t in range(16):
                    dve.wait_ge(t2, t + 1)
                    dst = self.s_x[:, :, t * P:(t + 1) * P] if t < 12 else self.s_B[:, :, (t - 12) * P:(t - 11) * P]
                    dve.tensor_copy(dst, ps[:, t % 8, :].rearrange("p (c f) -> p c f", c=NC)).then_inc(k2, 1)

    def ssd(self):
        nc, ps = self.nc, self.ps
        lat, y, x, Bt, H, dt, dtA = self.s_lat, self.s_y, self.s_x, self.s_B, self.s_H, self.s_dt, self.s_dtA
        free = self.s_ctx.rearrange("p t c -> p (t c)")
        xw = [free[:, i * D_SSD:(i + 1) * D_SSD] for i in range(2)]
        xdt = xw
        CB = free[:, 2 * D_SSD:2 * D_SSD + 1024].rearrange("p (d g t) -> p d g t", d=2, g=4)
        A = Arena(self.arena_t, self.s_area, self.A.end)
        ex, wt = A.take(2, 6, SSD_H), A.take(2, 3, SSD_H)
        old = self.silu_c.rearrange("p b k v -> p (b k v)")[:, 0:3 * P].rearrange("p (h t) -> p h t", h=3)
        R = [old, A.take(3, P)]
        E = [A.take(3, P) for _ in range(2)]
        Pm = [A.take(3, P) for _ in range(2)]
        S = lambda n: self.sem("ssd_" + n)
        sel = self.k_sel.rearrange("p (d n) -> p d n", d=2)
        rest = [sel[:, dr, (LEVELS + 1) * P:(LEVELS + 2) * P] for dr in range(2)]
        incl = [sel[:, dr, LEVELS * P:(LEVELS + 1) * P] for dr in range(2)]
        hd = lambda a, h: a.rearrange("p (h v) -> p h v", h=h)
        dsum, dexp, wts = S("decay_sums"), S("decays"), S("weights")
        with nc.Block() as block:
            @block.tensor
            def _(pe):
                for dr in range(2):
                    o0, o1, o2, o3 = ORDER[dr]
                    da = lambda c: dtA[:, c, dr * SSD_H:(dr + 1) * SSD_H]
                    out = lambda i: ps[:, 0, (dr * 6 + i) * SSD_H:(dr * 6 + i + 1) * SSD_H]
                    pe.matmul(out(0), rest[dr], da(o0), start=True, stop=False)
                    pe.matmul(out(0), self.ones, da(o1), start=False, stop=True)
                    pe.matmul(out(1), rest[dr], da(o1), start=True, stop=True)
                    pe.matmul(out(2), rest[dr], da(o2), start=True, stop=True)
                    pe.matmul(out(3), self.ones, da(o2), start=True, stop=True)
                    for c in range(2):
                        ins = pe.matmul(out(4 + c), incl[dr], da(2 + c), start=True, stop=True)
                ins.then_inc(dsum, 1)

            @block.scalar
            def _(act):
                act.wait_ge(dsum, 1)
                act.activation(ex.rearrange("p a b c -> p (a b c)"),
                               ps[:, 0, 0:12 * SSD_H], ACT.Exp).then_inc(dexp, 1)

            @block.vector
            def _(dve):
                dve.wait_ge(dexp, 1)
                for dr in range(2):
                    for i in range(3):
                        dve.tensor_tensor(wt[:, dr, i, :], ex[:, dr, i, :], dt[:, ORDER[dr][i], dr * SSD_H:(dr + 1) * SSD_H], ALU.mult)
        xmade, smade, skept = S("x_weighted"), S("states_made"), S("states_kept")
        jobs = [(dr, i) for dr in range(2) for i in range(3)]
        with nc.Block() as block:
            @block.tensor
            def _(pe):
                for n, (dr, i) in enumerate(jobs):
                    c = ORDER[dr][i]
                    pe.wait_ge(xmade, n + 1)
                    if dr == 1 and i == 0:
                        pe.wait_ge(skept, 1)
                    if dr == 1 and i == 2:
                        pe.wait_ge(skept, 2)
                    for g in range(SSD_G):
                        ins = pe.matmul(ps[:, (4 if i == 2 else 0) + g, 0:384], Bt[:, c, g * P:(g + 1) * P],
                                        xw[n % 2][:, g * 384:(g + 1) * 384], start=i != 1, stop=i != 0)
                    ins.then_inc(smade, 1)

            @block.vector
            def _(dve):
                def weigh(n):
                    dr, i = jobs[n]
                    if n >= 2:
                        dve.wait_ge(smade, n - 1)
                    dve.tensor_tensor(hd(xw[n % 2], SSD_H), hd(x[:, ORDER[dr][i], :], SSD_H),
                                      bcast(wt[:, dr, i, :].unsqueeze(2), [P, SSD_H, HP]), ALU.mult).then_inc(xmade, 1)

                def keep(dr):
                    four = lambda a: a.rearrange("p (g n) -> p g n", g=4)
                    dve.wait_ge(smade, 3 * dr + 2)
                    dve.tensor_copy(four(H[:, dr, 0, :]), ps[:, 0:4, 0:384]).then_inc(skept, 1)
                    dve.wait_ge(skept, 2 * dr + 1)
                    dve.tensor_tensor(hd(H[:, dr, 1, :], SSD_H), hd(H[:, dr, 0, :], SSD_H),
                                      bcast(ex[:, dr, 3, :].unsqueeze(2), [P, SSD_H, HP]), ALU.mult).then_inc(wts, 1)
                    dve.wait_ge(wts, dr + 1)
                    dve.wait_ge(smade, 3 * dr + 3)
                    dve.tensor_tensor(four(H[:, dr, 1, :]), four(H[:, dr, 1, :]), ps[:, 4:8, 0:384], ALU.add).then_inc(skept, 1)
                for n in range(6):
                    weigh(n)
                    if n == 3:
                        keep(0)
                keep(1)

        cbm, cbk, xd = S("cb_made"), S("cb_kept"), S("x_scaled")
        rmade, dmade, emade, pmade, ymade = S("selectors"), S("exponents"), S("exped"), S("weighted"), S("diagonal_made")
        omade, okept, oscaled, yk = S("offsets_made"), S("offsets_kept"), S("offsets_scaled"), S("y_kept")
        tmp = [self.hT[:, 0:6, HP * i:HP * (i + 1)] for i in range(2)]
        units = [(c, hb, dr) for c in range(2) for hb in range(8) for dr in range(2)]
        with nc.Block() as block:
            @block.tensor
            def _(pe):
                def exponents(i):
                    pe.wait_ge(rmade, i + 1)
                    if i >= 2:
                        pe.wait_ge(emade, i - 1)
                    pe.matmul(ps[:, 3 + i % 2, 0:384], rest[units[i][2]], R[i % 2].rearrange("p h t -> p (h t)"),
                              start=True, stop=True).then_inc(dmade, 1)

                def diagonal(i):
                    c, hb, _ = units[i]
                    pe.wait_ge(pmade, i + 1)
                    for h in range(3):
                        for dr in range(2):
                            col = (hb * 3 + h) * HP
                            ins = pe.matmul(ps[:, col // 512, col % 512:col % 512 + HP], Pm[dr][:, h, :],
                                            xdt[dr][:, col:col + HP], start=dr == 0, stop=dr == 1)
                    ins.then_inc(ymade, 1)
                for c in range(2):
                    for dr in range(2):
                        n = 2 * c + dr
                        if n >= 1:
                            pe.wait_ge(cbk, n)
                        for g in range(4):
                            ins = pe.matmul(ps[:, 5, g * P:(g + 1) * P], lat[:, 12 + g, c * P:(c + 1) * P],
                                            lat[:, 16 + g, c * P:(c + 1) * P], start=True, stop=True)
                        ins.then_inc(cbm, 1)
                    for n in range(8):
                        dr, g = divmod(n, 4)
                        m = 8 * c + n
                        if m >= 2:
                            pe.wait_ge(oscaled, m - 1)
                        which = int(2 + c == ORDER[dr][3])
                        pe.matmul(ps[:, 6 + m % 2, 0:384], lat[:, 16 + g, c * P:(c + 1) * P],
                                  H[:, dr, which, g * 384:(g + 1) * 384], start=True, stop=True).then_inc(omade, 1)
                    if c == 1:
                        pe.wait_ge(yk, 1)
                    for i in range(16 * c, 16 * c + 17):
                        if i < 16 * c + 16:
                            exponents(i)
                        if i > 16 * c and (i - 1) % 2 == 1:
                            diagonal(i - 1)

            @block.gpsimd
            def _(pool):
                for i, (c, hb, dr) in enumerate(units):
                    if i >= 2:
                        pool.wait_ge(dmade, i - 1)
                    h = dr * SSD_H + hb * 3
                    pool.tensor_tensor(R[i % 2], bcast(incl[dr].unsqueeze(1), [P, 3, P]),
                                       bcast(dtA[:, 2 + c, h:h + 3].unsqueeze(2), [P, 3, P]), ALU.mult).then_inc(rmade, 1)

            @block.scalar
            def _(act):
                for i in range(len(units)):
                    act.wait_ge(dmade, i + 1)
                    if i >= 2:
                        act.wait_ge(pmade, i - 1)
                    act.activation(E[i % 2].rearrange("p h t -> p (h t)"), ps[:, 3 + i % 2, 0:384], ACT.Exp).then_inc(emade, 1)

            @block.vector
            def _(dve):
                for c in range(2):
                    for dr in range(2):
                        dve.wait_ge(cbm, 2 * c + dr + 1)
                        if c == 1:
                            dve.wait_ge(ymade, 8)
                        dve.tensor_tensor(CB[:, dr], ps[:, 5, :].rearrange("p (g t) -> p g t", g=4),
                                          bcast(incl[dr].unsqueeze(1), [P, 4, P]), ALU.mult).then_inc(cbk, 1)
                        dve.tensor_tensor(hd(xdt[dr], SSD_H), hd(x[:, 2 + c, :], SSD_H),
                                          bcast(dt[:, 2 + c, dr * SSD_H:(dr + 1) * SSD_H].unsqueeze(2), [P, SSD_H, HP]), ALU.mult)
                    for n in range(8):
                        dr, g = divmod(n, 4)
                        m = 8 * c + n
                        dve.wait_ge(omade, m + 1)
                        ysl = y[:, c, g * 384:(g + 1) * 384]
                        dst = hd(ysl, 6) if dr == 0 else tmp[m % 2]
                        dve.tensor_tensor(dst, hd(ps[:, 6 + m % 2, 0:384], 6),
                                          bcast(ex[:, dr, 4 + c, g * 6:(g + 1) * 6].unsqueeze(2), [P, 6, HP]), ALU.mult).then_inc(oscaled, 1)
                        if dr == 1:
                            dve.wait_ge(oscaled, m + 1)
                            dve.tensor_tensor(hd(ysl, 6), hd(ysl, 6), tmp[m % 2], ALU.add).then_inc(okept, 1)
                    dve.wait_ge(cbk, 2 * c + 2)
                    for i in range(16 * c, 16 * c + 16):
                        _, hb, dr = units[i]
                        dve.wait_ge(emade, i + 1)
                        if i >= 2:
                            dve.wait_ge(ymade, i // 2)
                        dve.tensor_tensor(Pm[dr], E[i % 2], bcast(CB[:, dr, hb // 2, :].unsqueeze(1), [P, 3, P]), ALU.mult).then_inc(pmade, 1)
                    dve.wait_ge(ymade, 8 * c + 8)
                    dve.wait_ge(okept, 4 * c + 4)
                    dve.tensor_tensor(y[:, c, :], y[:, c, :], ps[:, 0:3, :].rearrange("p b n -> p (b n)"), ALU.add).then_inc(yk, 1)

    def ssd_out(self):
        nc, d, ring, ps, hT = self.nc, self.d, self.ring, self.ps, self.hT
        lat, y = self.s_lat, self.s_y
        A = Arena(self.arena_t, self.work + 20 * SEQ + 2 * D_SSD, self.A.end)
        self.m_f, self.m_y, self.m_g = A.take(4, SEQ), A.take(12, SEQ), A.take(16, SEQ)
        self.merge_area = A.at
        uT, zT, sq, rstd = A.take(4, SEQ), A.take(12, SEQ), A.take(12, SEQ), A.take(SEQ)
        F1 = A.take(2, 4, SEQ)
        dftw, dftl, dsk, skips = A.take(2 * P), A.take(2, 2 * SEQ), A.take(12), A.take(SSD_H)
        spread = self.sem("skips_spread")
        S = lambda n: self.sem("ssd_out_" + n)
        made, freed, small = S("made"), S("freed"), S("tables_loaded")
        turned, kept, f1, f1k, f2 = S("y_turned"), S("y_kept"), S("width_made"), S("width_kept"), S("length_made")
        with nc.Block() as block:
            @block.sync
            def _(sp):
                sp.dma_start(dftw, d["k_dftw"]).then_inc(small, 16)
                sp.dma_start(dftl, d["k_dftl"].rearrange("(c p) n -> p c n", p=P)).then_inc(small, 16)
                sp.dma_start(skips, d["d_skip_2"].partition_broadcast(P)).then_inc(small, 16)
                ring.send(sp, self.ends["rest2"] + 3)

            @block.tensor
            def _(pe):
                self.products(pe, [self.feature_tiles(hT, CTX, TOK)] * 8, made, freed)
                pe.wait_ge(freed, 32)
                for t in range(12):
                    if t >= 8:
                        pe.wait_ge(kept, t - 7)
                    for c in range(2):
                        ins = pe.transpose(ps[:, t % 8, c * P:(c + 1) * P], y[:, c, t * P:(t + 1) * P], self.ident)
                    ins.then_inc(turned, 1)

            @block.scalar
            def _(act):
                for t in range(32):
                    act.wait_ge(made, t + 1)
                    bank = ps[:, t % NBANK, 0:SEQ]
                    if t < 4:
                        ins = act.activation(uT[:, t, :], bank, ACT.Copy)
                    elif t < 16:
                        ins = act.activation(zT[:, t - 4, :], bank, ACT.Silu)
                    else:
                        ins = act.activation(self.m_g[:, t - 16, :], bank, ACT.Sigmoid, bias=self.P_("b_gate")[:, t - 16:t - 15])
                    ins.then_inc(freed, 1)

            @block.vector
            def _(dve):
                dve.wait_ge(small, 48)
                for two in range(2):
                    half = slice(two * HP, (two + 1) * HP)
                    dve.tensor_copy(dsk[half, :], skips[half, :].rearrange("p (i two) -> p i two", two=2)[:, :, two]).then_inc(spread, 1)
                dve.wait_ge(spread, 2)
                dve.wait_ge(freed, 32)
                for t in range(12):
                    dve.wait_ge(turned, t + 1)
                    dve.scalar_tensor_tensor(self.m_y[:, t, :], lat[:, t, :], dsk[:, t:t + 1], ps[:, t % 8, 0:SEQ],
                                             ALU.mult, ALU.add).then_inc(kept, 1)
                dve.wait_ge(kept, 12)
                dve.tensor_tensor(self.m_y, self.m_y, zT, ALU.mult)
        self.rms("ssd_norm", self.m_y, 12, SEQ, rstd, sq)
        scaled = S("y_scaled")
        with nc.Block() as block:
            @block.vector
            def _(dve):
                dve.tensor_tensor(self.m_y, self.m_y, bcast(rstd.unsqueeze(1), [P, 12, SEQ]), ALU.mult).then_inc(scaled, 1)
                dve.wait_ge(scaled, 1)
                for t in range(12):
                    dve.tensor_scalar(self.m_y[:, t, :], self.m_y[:, t, :], self.P_("ssd_g")[:, t:t + 1], None, ALU.mult)
                for g in range(4):
                    dve.wait_ge(f2, g + 1)
                    dve.tensor_copy(self.m_f[:, g, :], ps[:, 4 + g, 0:SEQ])

            @block.tensor
            def _(pe):
                for c in range(2):
                    for g in range(4):
                        ins = pe.matmul(ps[:, c * 2 + g // 2, g % 2 * SEQ:(g % 2 + 1) * SEQ], uT[:, g, c * P:(c + 1) * P], dftw,
                                        start=True, stop=True)
                    ins.then_inc(f1, 1)
                pe.wait_ge(f1k, 2)
                for g in range(4):
                    for n in range(4):
                        c, part = divmod(n, 2)
                        ins = pe.matmul(ps[:, 4 + g, 0:SEQ], F1[:, c, g, part * P:(part + 1) * P], dftl[:, c, part * SEQ:(part + 1) * SEQ],
                                        start=n == 0, stop=n == 3)
                    ins.then_inc(f2, 1)

            @block.scalar
            def _(act):
                for c in range(2):
                    act.wait_ge(f1, c + 1)
                    act.activation(F1[:, c].rearrange("p g n -> p (g n)"), ps[:, 2 * c:2 * c + 2, :].rearrange("p b n -> p (b n)"),
                                   ACT.Copy).then_inc(f1k, 1)

    def merge2(self):
        A = Arena(self.arena_t, self.merge_area, self.A.end)
        y, mix, t2 = A.take(KT, SEQ), A.take(KT, SEQ), [A.take(SEQ) for _ in range(2)]
        first = [(lambda w, k, j=j: w[:, k, j * P:(j + 1) * P], lambda w, k: self.m_f[:, k, :], SEQ, 4) for j in range(8)]
        second = [(lambda w, k, j=j: w[:, k, j * P:(j + 1) * P], lambda w, k: self.m_y[:, k, :], SEQ, 12) for j in range(2)]
        self.merge_out("merge2", [first] + [second] * 4, [self.m_g[:, 0:8, :], self.m_g[:, 8:16, :]], y, t2,
                       self.ends["merge2"], store=mix)
        self.add_normed("mix_post", mix, self.P_("mix_post"), self.mod2[:, 16:24, 0], A)

    def add_normed(self, name, src, gain, gate, A):
        rstd, sq, g = A.take(SEQ), A.take(KT, SEQ), A.take(KT)
        self.rms(name, src, KT, SEQ, rstd, sq)
        s = self.sem(name + "_scaled")
        with self.nc.Block() as block:
            @block.vector
            def _(dve):
                dve.tensor_tensor(g, gain, gate, ALU.mult)
                dve.tensor_tensor(src, src, bcast(rstd.unsqueeze(1), [P, KT, SEQ]), ALU.mult).then_inc(s, 1)
                dve.wait_ge(s, 1)
                for k in range(KT):
                    dve.scalar_tensor_tensor(self.xT[:, k, :], src[:, k, :], g[:, k:k + 1], self.xT[:, k, :], ALU.mult, ALU.add)

    def route2(self):
        nc, d, ps = self.nc, self.d, self.ps
        self.h2 = self.hT[:, :, 0:SEQ]
        A = Arena(self.arena_t, self.work, self.A.end)
        E2, n = N_EXP2, N_EXP2 * CAP
        self.xe = A.take(KT, n)
        self.selT = A.take(E2, SEQ)
        self.moe_area = A.at
        wr, iota, rows = A.take(KT, E2), A.take(SEQ), A.take(E2 * P)
        self.norm_modulate("ffn_pre", self.xT, self.h2, self.P_("ffn_pre"), self.mod2[:, 32:40, 0], self.mod2[:, 24:32, 0], A)
        lg, aff, top = A.take(2, E2), A.take(2, E2), A.take(2)
        affT = A.take(SEQ)
        affB = A.take(E2, SEQ)
        G = A.take(E2, SEQ)
        T = A.take(E2, P)
        rank = A.take(2, E2)
        sel = A.take(2, n)
        h_tok = A.take(2, D)
        S = lambda n_: self.sem("route2_" + n_)
        loaded, lmade, st, sa = S("loaded"), S("logits_made"), S("logits_shifted"), S("exped")
        amade, aturned, akept, bmade, bkept = S("affinities"), S("affinities_turned"), S("rows_kept"), S("rows_spread"), S("spread_kept")
        hturned, hkept = S("h_turned"), S("h_kept")
        vs = self.vs
        do = lambda dve, ins: vs.do(dve, ins)
        with nc.Block() as block:
            @block.sync
            def _(sp):
                sp.dma_start(wr, d["w_router_2"].rearrange("(k p) n -> p k n", p=P)).then_inc(loaded, 16)
                sp.dma_start(iota, d["k_iota"]).then_inc(loaded, 16)
                sp.dma_start(rows[0:E2], d["k_rows32"][0:E2, 0:E2 * P]).then_inc(loaded, 16)
                sp.wait_ge(loaded, 48)

            @block.tensor
            def _(pe):
                pe.wait_ge(loaded, 48)
                for c in range(2):
                    for k in range(KT):
                        ins = pe.matmul(ps[:, c, 0:E2], self.h2[:, k, c * P:(c + 1) * P], wr[:, k, :], start=k == 0, stop=k == KT - 1)
                ins.then_inc(lmade, 1)
                for k in range(KT):
                    if k >= 4:
                        pe.wait_ge(hkept, k - 3)
                    for c in range(2):
                        ins = pe.transpose(ps[:, 4 + k % 4, c * P:(c + 1) * P], self.h2[:, k, c * P:(c + 1) * P], self.ident)
                    ins.then_inc(hturned, 1)
                pe.wait_ge(amade, 1)
                for c in range(2):
                    ins = pe.transpose(ps[0:E2, 2, c * P:(c + 1) * P], aff[:, c, :], self.ident)
                ins.then_inc(aturned, 1)
                pe.wait_ge(akept, 1)
                pe.wait_ge(hkept, 8)
                for i in range(E2 // 2):
                    if i >= 4:
                        pe.wait_ge(bkept, i - 3)
                    for j in range(2):
                        e = 2 * i + j
                        ins = pe.matmul(ps[:, 4 + i % 4, j * SEQ:(j + 1) * SEQ], rows[0:E2, e * P:(e + 1) * P], affT[0:E2, :],
                                        start=True, stop=True)
                    ins.then_inc(bmade, 1)

            @block.scalar
            def _(act):
                for k in range(KT):
                    act.wait_ge(hturned, k + 1)
                    act.activation(h_tok[:, :, k * P:(k + 1) * P], ps[:, 4 + k % 4, 0:SEQ].rearrange("p (c f) -> p c f", c=2),
                                   ACT.Copy).then_inc(hkept, 1)
                act.wait_ge(st, 1)
                act.activation(aff, lg, ACT.Exp).then_inc(sa, 1)
                for i in range(E2 // 2):
                    act.wait_ge(bmade, i + 1)
                    act.activation(affB[:, 2 * i:2 * i + 2, :], ps[:, 4 + i % 4, :].rearrange("p (a t) -> p a t", a=2),
                                   ACT.Copy).then_inc(bkept, 1)

            @block.vector
            def _(dve):
                bc = lambda a: bcast(a.unsqueeze(2), [P, 2, E2])
                dve.wait_ge(lmade, 1)
                do(dve, dve.reduce_max(top, ps[:, 0:2, 0:E2], axis=AX.X))
                dve.tensor_tensor(lg, ps[:, 0:2, 0:E2], bc(top), ALU.subtract).then_inc(st, 1)
                dve.wait_ge(sa, 1)
                do(dve, dve.reduce_sum(top, aff, axis=AX.X))
                do(dve, dve.reciprocal(top, top))
                dve.tensor_tensor(aff, aff, bc(top), ALU.mult).then_inc(amade, 1)
                dve.wait_ge(aturned, 1)
                dve.tensor_copy(affT[0:E2, :], ps[0:E2, 2, 0:SEQ]).then_inc(akept, 1)
                dve.wait_ge(amade, 1)
                dve.wait_ge(bkept, E2 // 2)
                later = self.k_sel[:, (LEVELS + 1) * P:(LEVELS + 2) * P]
                for c in range(2):
                    own = bcast(aff[:, c, :].unsqueeze(2), [P, E2, P])
                    o = 1 - c
                    dve.tensor_tensor(G[:, :, o * P:(o + 1) * P], affB[:, :, o * P:(o + 1) * P], own, ALU.is_ge if o < c else ALU.is_gt)
                    dve.tensor_tensor(G[:, :, c * P:(c + 1) * P], affB[:, :, c * P:(c + 1) * P], own, ALU.is_gt)
                    do(dve, dve.tensor_tensor(T, affB[:, :, c * P:(c + 1) * P], own, ALU.is_equal))
                    do(dve, dve.tensor_tensor(T, T, bcast(later.unsqueeze(1), [P, E2, P]), ALU.mult))
                    do(dve, dve.tensor_tensor(G[:, :, c * P:(c + 1) * P], G[:, :, c * P:(c + 1) * P], T, ALU.add))
                    do(dve, dve.reduce_sum(rank[:, c, :], G, axis=AX.X))
                for c in range(2):
                    do(dve, dve.tensor_tensor(sel[:, c, :].rearrange("p (e s) -> p e s", s=CAP),
                                              bcast(iota[:, 0:CAP].unsqueeze(1), [P, E2, CAP]),
                                              bcast(rank[:, c, :].unsqueeze(2), [P, E2, CAP]), ALU.is_equal))
        selw = G.rearrange("p e t -> p (e t)").rearrange("p (c e r s) -> p c e r s", c=2, e=E2, r=4)
        wset, xmade, xkept, tmade, tkept = S("selection_weighted"), S("xe_made"), S("xe_kept"), S("sel_turned"), S("sel_kept")
        with nc.Block() as block:
            @block.vector
            def _(dve):
                for c in range(2):
                    for r in range(4):
                        ins = dve.tensor_tensor(selw[:, c, :, r, :], sel[:, c, :].rearrange("p (e s) -> p e s", s=CAP),
                                                bcast(aff[:, c, :].unsqueeze(2), [P, E2, CAP]), ALU.mult)
                ins.then_inc(wset, 1)
                for i in range(E2 // 2):
                    dve.wait_ge(tmade, i + 1)
                    dve.tensor_copy(self.selT[:, 2 * i:2 * i + 2, :], ps[:, 4 + i % 4, :].rearrange("p (a t) -> p a t", a=2)).then_inc(tkept, 1)

            @block.scalar
            def _(act):
                for k in range(KT):
                    act.wait_ge(xmade, k + 1)
                    act.activation(self.xe[:, k, :], ps[:, k % 4, :], ACT.Copy).then_inc(xkept, 1)

            @block.tensor
            def _(pe):
                for k in range(KT):
                    if k >= 4:
                        pe.wait_ge(xkept, k - 3)
                    for c in range(2):
                        ins = pe.matmul(ps[:, k % 4, :], h_tok[:, c, k * P:(k + 1) * P], sel[:, c, :], start=c == 0, stop=c == 1)
                    ins.then_inc(xmade, 1)
                pe.wait_ge(wset, 1)
                for i in range(E2 // 2):
                    if i >= 4:
                        pe.wait_ge(tkept, i - 3)
                    for j in range(2):
                        for c in range(2):
                            ins = pe.transpose(ps[:, 4 + i % 4, j * SEQ + c * P:j * SEQ + (c + 1) * P],
                                               selw[:, c, 2 * i + j, :, :].rearrange("p r s -> p (r s)"), self.ident)
                    ins.then_inc(tmade, 1)

    def moe2(self):
        nc, d, ps = self.nc, self.d, self.ps
        A = Arena(self.arena_t, self.moe_area, self.A.end)
        slots = self.ring.slots + [A.take(4096) for _ in range(3)]
        mat = [s.rearrange("p (k c) -> p k c", c=512) for s in slots]
        F_G0, F_U0, F_D0, F_G1, F_U1, F_D1 = range(6)
        xs = [A.take(KT, CAP) for _ in range(2)]
        stack = self.stack
        gq, uq, yq = A.take(512), A.take(512), A.take(2, 512)
        gs = A.take(4 * CAP)
        aT = A.take(2, 4, CAP)
        zero = A.take(512)
        S = lambda n: self.sem("moe2_" + n)
        loaded, used = [S(f"loaded{i}") for i in range(6)], [S(f"used{i}") for i in range(6)]
        xset, qmade, gkept, ukept = S("x_set"), S("quarters_made"), S("gate_kept"), S("up_kept")
        tmade, silud, aready, dmade, dkept, zeroed = (S("turned"), S("silu_made"), S("hidden_ready"), S("down_made"),
                                                      S("down_kept"), S("zeroed"))
        scat = S("scattered")
        src = [d[f"w_e_{w}_2"].rearrange("e (k p) f -> e p k f", p=P)[:, :, :, 512 * h:512 * h + 512]
               for h in range(2) for w in ("gate", "up", "down")]
        acc = lambda o: ps[:, 4 + o // 2, o % 2 * SEQ:(o % 2 + 1) * SEQ]
        last = N_EXP2 - 1
        with nc.Block() as block:
            @block.sync
            def _(sp):
                for i in range(6):
                    sp.dma_start(mat[i], src[i][0]).then_inc(loaded[i], 16)
                with sp.Fori(1, N_EXP2) as e:
                    for i in range(6):
                        sp.wait_ge(used[i], e)
                        sp.dma_start(mat[i], src[i][bass.ds(e, 1)].rearrange("o p k f -> p (o k) f")).then_inc(loaded[i], 16)

            @block.gpsimd
            def _(pool):
                with pool.Fori(0, N_EXP2 // 2) as it:
                    for j in range(2):
                        pool.wait_ge(scat, it * 2 + (j + 1))
                        pool.tensor_copy(xs[j], self.xe[:, :, bass.ds(it * (2 * CAP) + j * CAP, CAP)]).then_inc(xset, 1)

            def quarters(pe, out, lhsT, w):
                for i in range(2):
                    for q in range(4):
                        k = 2 * q + i
                        ins = pe.matmul(ps[q * CAP:(q + 1) * CAP, out, :], lhsT(k), w[:, k, :], start=i == 0, stop=i == 1,
                                        skip_group_check=True)
                return ins

            @block.tensor
            def _(pe):
                pe.wait_ge(zeroed, 1)
                for b in range(4):
                    pe.matmul(ps[:, 4 + b, :], zero[:, 0:P], zero, start=True, stop=False, skip_group_check=True)

                def gate_up(e, par, h):
                    if h == 0:
                        pe.wait_ge(xset, e + 1)
                    pe.wait_ge(gkept, 2 * e + h + 1)
                    pe.wait_ge(ukept, 2 * e + h + 1)
                    for b, slot in ((0, (F_G0, F_G1)[h]), (1, (F_U0, F_U1)[h])):
                        pe.wait_ge(loaded[slot], 16 * e + 16)
                        quarters(pe, b, lambda k: xs[par][:, k, :], mat[slot]).then_inc(qmade, 1)
                        pe.drain().then_inc(used[slot], 1)

                def turn(e, h):
                    pe.wait_ge(gkept, 2 * e + h + 2)
                    pe.wait_ge(aready, 2 * e + h + 1)
                    for f in range(4):
                        pe.matmul(ps[:, 2, f * CAP:(f + 1) * CAP], gq[:, f * P:(f + 1) * P], stack, start=True, stop=True)
                    pe.wait_ge(ukept, 2 * e + h + 2)
                    for f in range(4):
                        ins = pe.matmul(ps[:, 2, (4 + f) * CAP:(5 + f) * CAP], uq[:, f * P:(f + 1) * P], stack, start=True, stop=True)
                    ins.then_inc(tmade, 1)

                def down(e, h):
                    slot = (F_D0, F_D1)[h]
                    if h == 0:
                        pe.wait_ge(aready, 2 * e + 3)
                    pe.wait_ge(loaded[slot], 16 * e + 16)
                    pe.wait_ge(dkept, 2 * e + h + 1)
                    quarters(pe, 3, lambda k: aT[:, k // 4, k % 4, :], mat[slot]).then_inc(dmade, 1)
                    pe.drain().then_inc(used[slot], 1)

                def scatter(e, sel):
                    pe.wait_ge(dkept, 2 * e + 3)
                    for o in range(KT):
                        ins = pe.matmul(acc(o), yq[:, o // 4, o % 4 * P:(o % 4 + 1) * P], sel, start=False, stop=False,
                                        skip_group_check=True)
                    ins.then_inc(scat, 1)
                selT = lambda e: self.selT[:, bass.ds(e, 1), :].rearrange("p o t -> p (o t)")
                for h in range(2):
                    gate_up(0, 0, h)
                    turn(0, h)
                with pe.Fori(0, last // 2) as it:
                    for j in range(2):
                        e = it * 2 + j
                        gate_up(it * 2 + (j + 1), (j + 1) % 2, 0)
                        down(e, 0)
                        down(e, 1)
                        turn(it * 2 + (j + 1), 0)
                        gate_up(it * 2 + (j + 1), (j + 1) % 2, 1)
                        scatter(e, selT(e))
                        turn(it * 2 + (j + 1), 1)
                gate_up(last, 1, 0)
                down(last - 1, 0)
                down(last - 1, 1)
                turn(last, 0)
                gate_up(last, 1, 1)
                scatter(last - 1, self.selT[:, last - 1, :])
                turn(last, 1)
                down(last, 0)
                down(last, 1)
                scatter(last, self.selT[:, last, :])
                for b in range(4):
                    pe.matmul(ps[:, 4 + b, :], zero[:, 0:P], zero, start=False, stop=True, skip_group_check=True)

            @block.scalar
            def _(act):
                act.sem_inc(gkept, 1)
                act.sem_inc(dkept, 1)
                def gates(e, h):
                    act.wait_ge(qmade, 4 * e + 2 * h + 1)
                    act.activation(gq, ps[:, 0, :], ACT.Copy).then_inc(gkept, 1)
                    act.wait_ge(tmade, 2 * e + h + 1)
                    act.activation(gs, ps[:, 2, 0:4 * CAP], ACT.Silu).then_inc(silud, 1)

                def keep_down(e):
                    for h in range(2):
                        act.wait_ge(dmade, 2 * e + h + 1)
                        act.activation(yq[:, h, :], ps[:, 3, :], ACT.Copy).then_inc(dkept, 1)
                gates(0, 0)
                gates(0, 1)
                with act.Fori(1, N_EXP2) as e:
                    act.wait_ge(qmade, 4 * e + 1)
                    act.activation(gq, ps[:, 0, :], ACT.Copy).then_inc(gkept, 1)
                    act.wait_ge(scat, e + 1)
                    keep_down(e - 1)
                    act.wait_ge(tmade, 2 * e + 1)
                    act.activation(gs, ps[:, 2, 0:4 * CAP], ACT.Silu).then_inc(silud, 1)
                    gates(e, 1)
                act.wait_ge(scat, last + 2)
                keep_down(last)

            @block.vector
            def _(dve):
                dve.memset(zero, 0.0).then_inc(zeroed, 1)
                dve.sem_inc(scat, 2)
                dve.sem_inc(ukept, 1)
                dve.sem_inc(aready, 1)
                with dve.Fori(0, N_EXP2) as e:
                    for h in range(2):
                        dve.wait_ge(qmade, 4 * e + (2 * h + 2))
                        dve.tensor_copy(uq, ps[:, 1, :]).then_inc(ukept, 1)
                        dve.wait_ge(silud, 2 * e + (h + 1))
                        dve.tensor_tensor(aT[:, h].rearrange("p f s -> p (f s)"), gs, ps[:, 2, 4 * CAP:8 * CAP], ALU.mult).then_inc(aready, 1)
        A = Arena(self.arena_t, self.moe_area, self.A.end)
        ffn = A.take(KT, SEQ)
        with nc.Block() as block:
            @block.vector
            def _(dve):
                for b in range(4):
                    dve.tensor_copy(ffn[:, 2 * b:2 * b + 2, :], ps[:, 4 + b, :].rearrange("p (a t) -> p a t", a=2))
        self.ffn = ffn
        self.add_normed("ffn_post", ffn, self.P_("ffn_post"), self.mod2[:, 40:48, 0], A)

    def finish(self):
        nc, ps = self.nc, self.ps
        A = Arena(self.arena_t, self.work, self.A.end)
        res = A.take(2, D)
        S = lambda n: self.sem("finish_" + n)
        turned, kept, stored = S("turned"), S("kept"), S("stored")
        with nc.Block() as block:
            @block.tensor
            def _(pe):
                for c in range(2):
                    for k in range(KT):
                        ins = pe.transpose(ps[:, c * 2 + k // 4, k % 4 * P:(k % 4 + 1) * P], self.xT[:, k, c * P:(c + 1) * P], self.ident)
                    ins.then_inc(turned, 1)

            @block.vector
            def _(dve):
                for c in range(2):
                    dve.wait_ge(turned, c + 1)
                    dve.tensor_copy(res[:, c, :], ps[:, 2 * c:2 * c + 2, :].rearrange("p b n -> p (b n)")).then_inc(kept, 1)

            @block.sync
            def _(sp):
                for c in range(2):
                    sp.wait_ge(kept, c + 1)
                    sp.dma_start(self.out[0, c * P:(c + 1) * P, :], res[:, c, :]).then_inc(stored, 16)
                sp.wait_ge(stored, 32)


def build_program(nc, tensors, out):
    Net(nc, shaped(tensors), out).build()


def kernel(**inputs):
    import concourse.bacc as bacc
    from concourse.bass_utils import run_bass_kernel_spmd

    nc = bacc.Bacc("TRN2", target_bir_lowering=False, num_devices=1)
    arrays, tensors = {}, {}
    for name, a in list(inputs.items()) + list(constants().items()):
        a = np.ascontiguousarray(a)
        arrays["in_" + name] = a
        tensors[name] = nc.dram_tensor("in_" + name, a.shape, mybir.dt.from_np(a.dtype), kind="ExternalInput").ap()
    out = nc.dram_tensor("out_0", (1, SEQ, D), F32, kind="ExternalOutput").ap()
    build_program(nc, tensors, out)
    r = run_bass_kernel_spmd(nc, [arrays], core_ids=[0])
    return r.results[0]["out_0"]
```

```python
import numpy as np
import concourse.bass as bass
from concourse import mybir
from concourse.alu_op_type import AluOpType as ALU
from contextlib import ExitStack

F32 = mybir.dt.float32
F32R = mybir.dt.float32r
ACT = mybir.ActivationFunctionType
AX = mybir.AxisListType

P = 128
D = 1024
KT = D // P
SEQ = 256
CTX = 256
TOK = CTX + SEQ
NC = TOK // P
LAT = CTX // P
GRID = 64
ROWS = SEQ // GRID
EPS = 1e-6
HG_H = 8
ML_H, ML_DV = 4, 256
LEVELS = 7
N_EXP, D_EXP = 32, 512
N_GRP, PER_GRP = 4, 8
D_SSD, SSD_H, HP, SSD_G = 1536, 24, 64, 4
CONV2 = D_SSD + 2 * SSD_G * P
N_EXP2, CAP = 16, 32
BIG = 1e30
FIRST_STAGE_SEM = 150
NBANK = 6

O_HQ, O_HFF, O_HFB, O_HI, O_GA, O_MQ, O_MK, O_MV = 0, 1024, 2048, 3072, 4096, 5120, 5632, 6144
O_MI, O_GB, O_G1, O_G2 = 7168, 7184, 8208, 9232
O_UF, O_Z, O_XBC, O_DT, O_GL = 0, 512, 2048, 4608, 4656
ORDER = ((0, 1, 2, 3), (1, 0, 3, 2))

PARAMS = [
    ("b_ada", "b_ada", 0, 48), ("b_mod", "b_mod_2", 0, 48),
    ("b_hq", "b_in", O_HQ, 8), ("b_hff", "b_in", O_HFF, 8), ("b_hfb", "b_in", O_HFB, 8),
    ("norm1", "norm1_g", 0, 8),
    ("b_ga", "b_in", O_GA, 8), ("b_mq", "b_in", O_MQ, 4), ("b_mk", "b_in", O_MK, 4),
    ("b_gb", "b_in", O_GB, 8), ("b_g1", "b_in", O_G1, 8), ("b_g2", "b_in", O_G2, 8),
    ("norm2", "norm2_g", 0, 8), ("final", "final_norm_g", 0, 8),
    ("lb", "hg_lb_logits", 0, 32), ("hg_g", "hg_norm_g", 0, 8), ("ml_g", "ml_norm_g", 0, 8),
    ("cb1", "ml_conv_b", 0, 8),
    ("cw1", "ml_conv_w", 0, 40), ("cw2", "conv_w_2", 0, 60), ("cb2", "conv_b_2", 0, 20),
    ("mix_pre", "norm_mix_pre_2", 0, 8),
    ("mix_post", "norm_mix_post_2", 0, 8), ("ffn_pre", "norm_ffn_pre_2", 0, 8),
    ("ffn_post", "norm_ffn_post_2", 0, 8), ("ssd_g", "ssd_norm_2", 0, 12), ("b_gate", "b_gate_2", 0, 16),
    ("c", "c", 0, 8), ("c_ctx", "c_ctx", 0, 8), ("c2", "c_2", 0, 8), ("c_ctx2", "c_ctx_2", 0, 8),
]
N_PAR = sum(n for *_, n in PARAMS)
PAR_TILES = -(-N_PAR // P)


def param_columns():
    at, out = 0, {}
    for name, _, _, n in PARAMS:
        out[name] = (at, n)
        at += n
    return out


def constants():
    t = np.arange(P)
    sel, masks = [], []
    for flip in (False, True):
        cols, ms = [], []
        for lev in range(LEVELS):
            m = P >> (lev + 1)
            mid = (t // (2 * m)) * 2 * m + m
            second = t % (2 * m) >= m
            s, tt = t[:, None], t[None, :]
            c = np.where(second[None, :], (s >= mid[None, :]) & (s <= tt), (s > tt) & (s < mid[None, :]))
            cols.append(c)
            same = (t[:, None] // (2 * m)) == (t[None, :] // (2 * m))
            ms.append(same & ~second[:, None] & second[None, :])
        cols.append(t[:, None] <= t[None, :])
        cols.append(t[:, None] > t[None, :])
        ms.append(np.eye(P, dtype=bool))
        if flip:
            cols = [c[::-1, ::-1] for c in cols]
            ms = [c[::-1, ::-1] for c in ms]
        sel.append(np.concatenate(cols, 1))
        masks.append(np.concatenate(ms, 1))
    w = np.arange(P)[:, None] * np.arange(P)[None, :] % P * (2 * np.pi / P)
    l = np.arange(SEQ)[:, None] * np.arange(SEQ)[None, :] % SEQ * (2 * np.pi / SEQ)
    scale = 1.0 / np.sqrt(SEQ * P)
    f = np.float32
    rows = np.zeros((N_GRP, N_GRP * P))
    for h in range(N_GRP):
        rows[h, h * P:(h + 1) * P] = 1
    rows16 = np.zeros((N_EXP2, N_EXP2 * P))
    for h in range(N_EXP2):
        rows16[h, h * P:(h + 1) * P] = 1
    return {
        "k_sel": np.concatenate(sel, 1).astype(f), "k_mask": np.concatenate(masks, 1).astype(f),
        "k_dftw": np.concatenate([np.cos(w), np.sin(w)], 1).astype(f),
        "k_dftl": np.concatenate([np.cos(l) * scale, -np.sin(l) * scale], 1).astype(f),
        "k_ident": np.eye(P).astype(f), "k_rows4": rows.astype(f), "k_rows16": rows16.astype(f),
        "k_iota": np.tile(np.arange(SEQ), (P, 1)).astype(f),
    }


def bcast(ap, shape):
    return ap.broadcast_to(shape)


class Arena:

    def __init__(self, tensor, at, end):
        self.tensor, self.at, self.end = tensor, at, end

    def take(self, *dims, parts=P):
        n = 1
        for d in dims:
            n *= d
        assert self.at + n <= self.end, (self.at, n, self.end)
        v = self.tensor[0:parts, self.at:self.at + n]
        self.at += n
        if len(dims) == 2:
            v = v.rearrange("p (a b) -> p a b", b=dims[1])
        if len(dims) == 3:
            v = v.rearrange("p (a b c) -> p a b c", b=dims[1], c=dims[2])
        return v


class Steps:

    def __init__(self, sem):
        self.sem, self.n = sem, 0

    def do(self, eng, ins):
        ins.then_inc(self.sem, 1)
        self.n += 1
        eng.wait_ge(self.sem, self.n)


class Ring:

    def __init__(self, slots, loaded, used):
        self.slots, self.loaded, self.used = slots, loaded, used
        self.queue, self.sent, self.taken = [], 0, 0

    def plan(self, blocks):
        self.queue += blocks
        return len(self.queue)

    def send(self, sp, until):
        n = len(self.slots)
        while self.sent < min(until, len(self.queue)):
            src, i = self.queue[self.sent], self.sent
            if i >= n:
                sp.wait_ge(self.used[i % n], i // n)
            dst = self.slots[i % n][:, 0:src.shape[1] * src.shape[2]].rearrange("p (k c) -> p k c", c=src.shape[2])
            sp.dma_start(dst, src).then_inc(self.loaded[i % n], 16)
            self.sent += 1

    def take(self, pe):
        n, i = len(self.slots), self.taken
        pe.wait_ge(self.loaded[i % n], 16 * (i // n + 1))
        src = self.queue[i]
        self.taken += 1
        return (self.slots[i % n][:, 0:src.shape[1] * src.shape[2]].rearrange("p (k c) -> p k c", c=src.shape[2]),
                self.used[i % n])

    def hand_over(self, sp):
        slots = []
        for _ in self.slots:
            slots.append(self.slots[self.taken % len(self.slots)])
            _, used = self.take(sp)
            sp.sem_inc(used, 1)
        return slots


def col_blocks(w, first, n, kt=KT, width=512):
    v = w.rearrange("(k p) n -> p k n", p=P)
    return [v[:, :, c:min(c + width, first + n)] for c in range(first, first + n, width)]


def row_blocks(w, kt=4):
    v = w.rearrange("(k p) n -> p k n", p=P)
    return [v[:, k:k + kt, :] for k in range(0, w.shape[0] // P, kt)]


def shaped(d):
    out = {}
    for name, ap in d.items():
        if name.startswith("k_"):
            out[name] = ap
        elif len(ap.shape) >= 3 and ap.shape[0] == 1 and name not in ("x", "ctx", "ctx_2"):
            out[name] = ap[0]
        else:
            out[name] = ap
    return out


class Net:

    def __init__(self, nc, d, out, last=99):
        self.nc, self.d, self.out, self.last = nc, d, out, last

    def sem(self, name):
        self.stage_sems += 1
        return self.stage.enter_context(self.nc.semaphore(name, num=FIRST_STAGE_SEM + self.stage_sems - 1))

    def lasting_sem(self, name):
        return self.ctx.enter_context(self.nc.semaphore(name))

    def build(self):
        with ExitStack() as self.ctx:
            nc, d = self.nc, self.d
            words = 50350
            self.arena_t = self.ctx.enter_context(nc.sbuf_tensor("arena", [P, words], F32))
            sel_words = 2 * (LEVELS + 2) * P
            self.short_t = self.ctx.enter_context(nc.sbuf_tensor("short_numbers", [P, sel_words + 4 * P], F32R))
            self.k_sel12 = self.short_t[:, 0:sel_words]
            self.k_sel = self.k_sel12.bitcast(F32)
            self.short = [self.short_t[:, sel_words + i * P:sel_words + (i + 1) * P] for i in range(4)]
            self.ps = self.ctx.enter_context(nc.psum_tensor("ps", [P, 8, 512], F32))
            A = self.A = Arena(self.arena_t, 0, words)
            self.ident = A.take(P)
            self.ones = A.take(P)
            self.par = A.take(PAR_TILES * P)
            self.cp = param_columns()
            self.xT = A.take(KT, SEQ)
            self.hT = A.take(KT, TOK)
            self.mod1 = A.take(48, 2)
            self.mod2 = A.take(48, 2)
            self.lbs = A.take(2, 16)
            self.silu_c = A.take(2, 8, CAP)
            self.stack = A.take(CAP)
            self.gain1 = A.take(8, 2)
            self.gain2 = A.take(8, 2)
            slots = [A.take(4096) for _ in range(3)]
            self.ring = Ring(slots, [self.lasting_sem(f"ring_loaded{i}") for i in range(3)],
                             [self.lasting_sem(f"ring_used{i}") for i in range(3)])
            self.vs = Steps(self.lasting_sem("vector_step"))
            self.ss = Steps(self.lasting_sem("scalar_step"))
            self.gs = Steps(self.lasting_sem("pool_step"))
            self.work = A.at
            R = self.ring
            w1, w2 = d["w_in"], d["w_in_2"]
            self.ends = {}
            mods = col_blocks(d["w_ada"], 0, 6 * D) + col_blocks(d["w_mod_2"], 0, 6 * D)
            self.mod_next = 0

            def mixed(blocks):
                out = []
                for b in blocks:
                    out += [b] + mods[:1]
                    del mods[:1]
                return out
            self.ends["mod"] = R.plan(mods[:4])
            del mods[:4]
            for half in range(2):
                c = 512 * half
                self.ends[f"hgrn{half}"] = R.plan(mixed([b for o in (O_HFF, O_HFB, O_HI, O_HQ)
                                                         for b in col_blocks(w1, o + c, 512)]))
            self.ends["mlstm"] = R.plan(mixed(col_blocks(w1, O_MQ, 2048)))
            self.ends["gates1"] = R.plan(mixed(col_blocks(w1, O_GA, 1024) + col_blocks(w1, O_GB, 3072)))
            self.ends["merge1"] = R.plan(col_blocks(d["w_branch_a"], 0, D) + col_blocks(d["w_branch_b"], 0, D)
                                         + col_blocks(d["w_out"], 0, D))
            self.ends["experts1"] = R.plan(col_blocks(d["w_gate"][0], 0, 512) + col_blocks(d["w_up"][0], 0, 512)
                                           + col_blocks(d["w_gate"][1], 0, 512))
            self.ends["xbc"] = R.plan(col_blocks(w2, O_XBC, CONV2))
            self.ends["rest2"] = R.plan(col_blocks(w2, O_UF, 512) + col_blocks(w2, O_Z, D_SSD) + col_blocks(w2, O_GL, 2 * D))
            self.ends["merge2"] = R.plan(row_blocks(d["w_fourier_2"]) + col_blocks(d["w_ssd_out_2"], 0, D, width=256)
                                         + col_blocks(d["w_out_2"], 0, D))
            self.ends["experts2"] = R.plan([b for w, c in (("gate", 0), ("up", 0), ("gate", 512))
                                            for b in col_blocks(d[f"w_e_{w}_2"][0], c, 512)])
            self.stages()

    def P_(self, name):
        a, n = self.cp[name]
        return self.par[:, a:a + n]

    def stages(self):
        todo = [lambda: self.setup(), lambda: self.gla(0), lambda: self.gla(1),
                lambda: self.mlstm_in(), lambda: self.mlstm(), lambda: self.merge1(), lambda: self.router1(),
                lambda: self.moe1(), lambda: self.ssd_in(), lambda: self.ssd(), lambda: self.ssd_out(),
                lambda: self.merge2(), lambda: self.route2(), lambda: self.moe2(), lambda: self.finish()]
        for stage in todo[:self.last + 1]:
            self.stage_sems = 0
            with ExitStack() as self.stage:
                stage()
                self.nc.all_engine_barrier(sems_to_clear=range(FIRST_STAGE_SEM, FIRST_STAGE_SEM + self.stage_sems))
        with self.nc.Block() as block:
            @block.sync
            def _(sp):
                for i in range(3):
                    n = -(-(self.ring.sent - i) // 3)
                    if n > 0:
                        sp.wait_ge(self.ring.loaded[i], 16 * n)

    def setup(self):
        nc, d, ring, ps = self.nc, self.d, self.ring, self.ps
        A = Arena(self.arena_t, self.work, self.A.end)
        rows = A.take(PAR_TILES, P)
        xin = A.take(4, D)
        raw, sq = A.take(KT, TOK), A.take(KT, TOK)
        rstd = A.take(TOK)
        sig = A.take(2, 8, 2)
        sel_in = A.take(2 * (LEVELS + 2) * P)
        S = lambda n: self.sem("setup_" + n)
        ident_in, tables, pars, xl = S("ident_loaded"), S("tables_loaded"), S("params_loaded"), S("x_loaded")
        par_t, par_c, x_t, x_c = S("params_turned"), S("params_kept"), S("x_turned"), S("x_kept")
        ones_set, inputs_set, sigmoids, silud = S("ones_set"), S("silu_inputs"), S("silu_sigmoids"), S("silu_made")
        squared, summed, meaned, rooted, steps = S("squared"), S("summed"), S("meaned"), S("rooted"), S("h_steps")
        self.mod_open(S, A, 4)
        pieces = []
        at = 0
        spans = []
        for _, src, first, n in PARAMS:
            if spans and spans[-1][0] == src and spans[-1][1] + spans[-1][2] * P == first:
                spans[-1][2] += n
            else:
                spans.append([src, first, n])
        for src, first, n in spans:
            flat = d[src].rearrange(" ".join("abcdef"[:len(d[src].shape)]) + " -> (" + " ".join("abcdef"[:len(d[src].shape)]) + ")")
            v = flat[first:first + n * P].rearrange("(r c) -> r c", c=P)
            done = 0
            while done < n:
                tile, row = divmod(at, P)
                m = min(n - done, P - row)
                pieces.append((tile, row, m, v[done:done + m, :]))
                at += m
                done += m
        last_rows = at - (PAR_TILES - 1) * P

        names = [("c", "c_ctx"), ("c2", "c_ctx2")]
        logits = self.P_("lb").rearrange("p (d l h) -> p d l h", d=2, l=2)
        lb, one_lb = self.lbs[:, 0, :], self.lbs[:, 1, :]
        with nc.Block() as block:
            @block.sync
            def _(sp):
                sp.dma_start(self.ident, d["k_ident"]).then_inc(ident_in, 16)
                for i in range(4):
                    src = d[("ctx", "x")[i // 2]][0, i % 2 * P:(i % 2 + 1) * P, :]
                    sp.dma_start(xin[:, i, :], src).then_inc(xl, 16)
                for tile, row, m, v in pieces[1::2]:
                    sp.dma_start(rows[row:row + m, tile, :], v).then_inc(pars, 16)
                ring.send(sp, self.ends["mod"])
                sp.dma_start(sel_in, d["k_sel"]).then_inc(tables, 16)
                ring.send(sp, self.ends["mod"] + 3)

            @block.gpsimd
            def _(pool):
                pool.wait_ge(tables, 16)
                pool.tensor_copy(self.k_sel12, sel_in)

            @block.tensor
            def _(pe):
                pe.wait_ge(ident_in, 16)
                pe.wait_ge(pars, 16 * len(pieces))
                for i in range(PAR_TILES):
                    if i >= 2:
                        pe.wait_ge(par_c, i - 1)
                    m = P if i < PAR_TILES - 1 else last_rows
                    pe.transpose(ps[:, i % 2, 0:m], rows[0:m, i, :], self.ident[0:m, 0:m]).then_inc(par_t, 1)
                pe.wait_ge(xl, 64)
                for k in range(KT):
                    if k >= 4:
                        pe.wait_ge(x_c, k - 3)
                    for i in range(4):
                        ins = pe.transpose(ps[:, 2 + k % 4, i * P:(i + 1) * P], xin[:, i, k * P:(k + 1) * P], self.ident)
                    ins.then_inc(x_t, 1)
                pe.wait_ge(silud, 1)
                self.mod_rows_step(pe)
                pe.wait_ge(par_c, PAR_TILES)
                pe.wait_ge(ones_set, 1)
                for k in range(KT):
                    pe.wait_ge(squared, k + 1)
                    ins = pe.matmul(ps[:, 0, :], self.ones, sq[:, k, :], start=k == 0, stop=k == KT - 1)
                ins.then_inc(summed, 1)
                for m in range(3):
                    self.mod_rows_step(pe)
                    self.mod_turn_step(pe)
                self.mod_turn_step(pe)

            @block.scalar
            def _(act):
                for tile, row, m, v in pieces[0::2]:
                    act.dma_start(rows[row:row + m, tile, :], v).then_inc(pars, 16)
                act.wait_ge(inputs_set, 6)
                act.activation(lb, one_lb, ACT.Sigmoid).then_inc(sigmoids, 1)
                act.activation(sig, self.silu_c[:, :, :, 0:2], ACT.Sigmoid).then_inc(sigmoids, 1)
                for k in range(KT):
                    act.wait_ge(x_c, k + 1)
                    act.activation(sq[:, k, :], raw[:, k, :], ACT.Square).then_inc(squared, 1)
                self.mod_keep_step(act, 0)
                act.wait_ge(meaned, 1)
                act.activation(rstd, rstd, ACT.Sqrt).then_inc(rooted, 1)
                for m in range(1, 4):
                    self.mod_keep_step(act, m)

            @block.vector
            def _(dve):
                dve.memset(self.ones, 1.0).then_inc(ones_set, 1)
                dve.memset(self.silu_c, 0.0).then_inc(inputs_set, 1)
                for i in range(PAR_TILES):
                    dve.wait_ge(par_t, i + 1)
                    m = P if i < PAR_TILES - 1 else last_rows
                    dve.tensor_copy(self.par[:, i * P:i * P + m], ps[:, i % 2, 0:m]).then_inc(par_c, 1)
                dve.wait_ge(par_c, PAR_TILES)
                dve.wait_ge(inputs_set, 1)
                for b in range(2):
                    for v in range(2):
                        dve.tensor_copy(self.silu_c[:, b, :, v], self.P_(names[b][v])).then_inc(inputs_set, 1)
                dve.tensor_tensor(one_lb.rearrange("p (d h) -> p d h", d=2), logits[:, :, 0, :], logits[:, :, 1, :],
                                  ALU.subtract).then_inc(inputs_set, 1)
                dve.wait_ge(ident_in, 16)
                for q in range(4):
                    dve.tensor_copy(self.stack[q * CAP:(q + 1) * CAP, :],
                                    self.ident[q * CAP:(q + 1) * CAP, q * CAP:(q + 1) * CAP]).then_inc(ones_set, 1)
                dve.wait_ge(sigmoids, 2)
                dve.tensor_tensor(self.silu_c[:, :, :, 0:2], self.silu_c[:, :, :, 0:2], sig, ALU.mult).then_inc(silud, 1)
                dve.tensor_scalar(one_lb, lb, -1.0, 1.0, ALU.mult, ALU.add)
                for k in range(KT):
                    dve.wait_ge(x_t, k + 1)
                    dve.tensor_copy(raw[:, k, :], ps[:, 2 + k % 4, :]).then_inc(x_c, 1)
                dve.wait_ge(summed, 1)
                dve.tensor_scalar(rstd, ps[:, 0, :], 1.0 / D, EPS, ALU.mult, ALU.add).then_inc(meaned, 1)
                dve.wait_ge(x_c, KT)
                dve.tensor_copy(self.xT, raw[:, :, CTX:TOK])
                dve.wait_ge(rooted, 1)
                dve.reciprocal(rstd, rstd).then_inc(steps, 1)
                dve.wait_ge(steps, 1)
                dve.tensor_tensor(self.hT, raw, bcast(rstd.unsqueeze(1), [P, KT, TOK]), ALU.mult).then_inc(steps, 1)
                self.mod_add(dve).then_inc(steps, 1)
                dve.wait_ge(steps, 3)
                self.gain(dve, self.gain1, self.mod1, "norm1").then_inc(steps, 1)
                dve.wait_ge(steps, 4)
                self.modulate(dve, self.hT, self.gain1, self.mod1)

    def rms(self, name, src, kt, n, out, square, before=None, after=None, act_after=None, pe_after=None):
        ps = self.ps
        squared, summed = self.sem(f"{name}_squared"), self.sem(f"{name}_summed")
        meaned, rooted, inverted = self.sem(f"{name}_meaned"), self.sem(f"{name}_rooted"), self.sem(f"{name}_inverted")
        with self.nc.Block() as block:
            @block.scalar
            def _(act):
                for k in range(kt):
                    act.activation(square[:, k, :], src[:, k, :], ACT.Square).then_inc(squared, 1)
                act.wait_ge(meaned, 1)
                act.activation(out, out, ACT.Sqrt).then_inc(rooted, 1)
                if act_after:
                    act_after(act)

            @block.tensor
            def _(pe):
                for k in range(kt):
                    pe.wait_ge(squared, k + 1)
                    ins = pe.matmul(ps[:, 0, 0:n], self.ones, square[:, k, :], start=k == 0, stop=k == kt - 1)
                ins.then_inc(summed, 1)
                if pe_after:
                    pe_after(pe)

            @block.vector
            def _(dve):
                if before:
                    before(dve)
                dve.wait_ge(summed, 1)
                dve.tensor_scalar(out, ps[:, 0, 0:n], 1.0 / (kt * P), EPS, ALU.mult, ALU.add).then_inc(meaned, 1)
                dve.wait_ge(rooted, 1)
                dve.reciprocal(out, out).then_inc(inverted, 1)
                dve.wait_ge(inverted, 1)
                if after:
                    after(dve)

    def mod_open(self, S, A, n):
        self.mod_rows = A.take(2, 512)
        self.mod_n, self.mod_first, self.mod_done, self.mod_turned_n = n, self.mod_next, 0, 0
        self.mod_next += n
        self.mod_made, self.mod_kept, self.mod_turned = S("mod_rows_made"), S("mod_rows_kept"), S("mod_turned")

    def mod_rows_step(self, pe):
        m = self.mod_done
        w, used = self.ring.take(pe)
        if m >= 1:
            pe.wait_ge(self.mod_kept, m)
        b = (self.mod_first + m) // 12
        for i in range(2):
            for q in range(4):
                k = 2 * q + i
                ins = pe.matmul(self.ps[q * CAP:(q + 1) * CAP, 6, :], self.silu_c[:, b, k, :], w[:, k, :], start=i == 0, stop=i == 1,
                                skip_group_check=True)
        ins.then_inc(self.mod_made, 1)
        pe.drain().then_inc(used, 1)
        self.mod_done += 1

    def mod_turn_step(self, pe):
        m = self.mod_turned_n
        pe.wait_ge(self.mod_kept, m + 1)
        for j in range(4):
            c = 2 * (4 * m + j)
            ins = pe.matmul(self.ps[:, 7, c:c + 2], self.mod_rows[:, m % 2, j * P:(j + 1) * P], self.stack[:, 0:2],
                            start=True, stop=True)
        ins.then_inc(self.mod_turned, 1)
        self.mod_turned_n += 1

    def mod_keep_step(self, act, m):
        act.wait_ge(self.mod_made, m + 1)
        if m >= 2:
            act.wait_ge(self.mod_turned, m - 1)
        act.activation(self.mod_rows[:, m % 2, :], self.ps[:, 6, :], ACT.Copy).then_inc(self.mod_kept, 1)

    def mod_add(self, dve):
        dve.wait_ge(self.mod_turned, self.mod_n)
        b, t = divmod(4 * self.mod_first, 48)
        mod, bias = (self.mod1, self.mod2)[b], self.P_(("b_ada", "b_mod")[b])
        n = 4 * self.mod_n
        return dve.tensor_tensor(mod[:, t:t + n, :], self.ps[:, 7, 0:2 * n].rearrange("p (t v) -> p t v", v=2),
                                 bcast(bias[:, t:t + n].unsqueeze(2), [P, n, 2]), ALU.add)

    def gain(self, dve, gain, mod, g):
        return dve.scalar_tensor_tensor(gain, mod[:, 8:16, :], 1.0, bcast(self.P_(g).unsqueeze(2), [P, 8, 2]),
                                        ALU.add, ALU.mult)

    def modulate(self, dve, h, gain, mod):
        for k in range(KT):
            for v, (a, b) in enumerate(((CTX, TOK), (0, CTX))):
                dve.tensor_scalar(h[:, k, a:b], h[:, k, a:b], gain[:, k, v:v + 1], mod[:, k, v:v + 1],
                                  ALU.mult, ALU.add)

    def products(self, pe, blocks, made, freed, first=0, mods=0):
        n = first
        for i, tiles in enumerate(blocks):
            w, used = self.ring.take(pe)
            for lhsT, rhs, cols, kt in tiles:
                if n >= NBANK:
                    pe.wait_ge(freed, n - NBANK + 1)
                for k in range(kt):
                    ins = pe.matmul(self.ps[:, n % NBANK, 0:cols], lhsT(w, k), rhs(w, k), start=k == 0, stop=k == kt - 1)
                ins.then_inc(made, 1)
                n += 1
            pe.drain().then_inc(used, 1)
            if i < mods:
                if self.mod_done >= 1:
                    self.mod_turn_step(pe)
                self.mod_rows_step(pe)
        if mods and self.mod_done == self.mod_n:
            self.mod_turn_step(pe)
        return n

    def feature_tiles(self, h, a, b, n=4):
        return [(lambda w, k, j=j: w[:, k, j * P:(j + 1) * P], lambda w, k: h[:, k, a:b], b - a, KT) for j in range(n)]

    def token_tiles(self, token_columns, width=512):
        return [(lambda w, k, t=t: t(k), lambda w, k: w[:, k, 0:width], width, KT) for t in token_columns]

    def gla(self, half):
        nc, d, ring, ps, hT = self.nc, self.d, self.ring, self.ps, self.hT
        A = Arena(self.arena_t, self.work, self.A.end)
        self.o_all = A.take(2, D)
        kk = A.take(8, TOK)
        zz = A.take(8, TOK)
        LT = A.take(8, NC, P)
        q = A.take(4, SEQ)
        v = A.take(NC, 512)
        st = A.take(8, 2, P)
        dec = A.take(8)
        mask = A.take(2, (LEVELS + 1) * P)
        G = [A.take(LEVELS + 1, P) for _ in range(2)]
        X = [A.take(LEVELS, P) for _ in range(2)]
        AA = [A.take(LEVELS + 1, P) for _ in range(4)]
        mod_area = Arena(self.arena_t, A.at - (LEVELS + 1) * P, A.at)
        QD = [A.take(P) for _ in range(4)]
        Es = [a.rearrange("p a b -> p (a b)")[:, 0:512] for a in AA[0:2]]
        brow = AA[2].rearrange("p a b -> p (a b)")[:, 0:512]
        KP = zz
        n = f"hgrn{half}_"
        S = lambda name: self.sem(n + name)
        lb = self.lbs.rearrange("p two (d h) -> p two d h", d=2)[:, :, :, 4 * half:4 * half + 4]

        self.mod_open(S, mod_area, 4)
        made, freed, rows_in = S("made"), S("freed"), S("rows_loaded")
        sig, f_made, ksig, logf = S("sigmoids"), S("forget_made"), S("k_sigmoid"), S("logf_made")
        turned, kept = S("logf_turned"), S("logf_kept")
        lbu = [lb[:, i, :, :] for i in range(2)]
        with nc.Block() as block:
            @block.sync
            def _(sp):
                sp.dma_start(brow, d["b_in"][0:1, O_HI + 512 * half:O_HI + 512 * half + 512]
                             .partition_broadcast(P)).then_inc(rows_in, 16)
                sp.dma_start(mask, d["k_mask"].rearrange("p (d n) -> p d n", d=2)).then_inc(rows_in, 16)
                ring.send(sp, self.ends[f"hgrn{half}"] + 3)

            @block.tensor
            def _(pe):
                self.products(pe, [self.feature_tiles(hT, 0, TOK), self.feature_tiles(hT, 0, TOK),
                                   self.token_tiles([lambda k, c=c: hT[:, k, c * P:(c + 1) * P] for c in range(NC)]),
                                   self.feature_tiles(hT, CTX, TOK)], made, freed, mods=4)
                pe.wait_ge(freed, 16)
                for u in range(8):
                    pe.wait_ge(logf, u // 4 + 1)
                    if u >= NBANK:
                        pe.wait_ge(kept, u - NBANK + 1)
                    for c in range(NC):
                        ins = pe.transpose(ps[:, u % NBANK, c * P:(c + 1) * P], zz[:, u, c * P:(c + 1) * P], self.ident)
                    ins.then_inc(turned, 1)

            @block.scalar
            def _(act):
                self.mod_keep_step(act, 0)
                self.mod_keep_step(act, 1)
                act.wait_ge(freed, 8)
                for dr in range(2):
                    u = slice(4 * dr, 4 * dr + 4)
                    act.activation(kk[:, u, :], zz[:, u, :], ACT.Sigmoid, scale=-1.0).then_inc(ksig, 1)
                    act.wait_ge(ksig, dr + 1)
                    act.activation(zz[:, u, :], zz[:, u, :], ACT.Sigmoid).then_inc(sig, 1)
                for dr in range(2):
                    u = slice(4 * dr, 4 * dr + 4)
                    act.wait_ge(f_made, 4 * dr + 4)
                    act.activation(zz[:, u, :], zz[:, u, :], ACT.Ln).then_inc(logf, 1)
                self.mod_keep_step(act, 2)
                self.mod_keep_step(act, 3)
                act.wait_ge(freed, 16)
                act.activation(q, q, ACT.Silu)

            @block.vector
            def _(dve):
                def forget(dr):
                    dve.wait_ge(sig, dr + 1)
                    for h in range(4):
                        dve.tensor_scalar(zz[:, 4 * dr + h, :], zz[:, 4 * dr + h, :], lbu[1][:, dr, h:h + 1],
                                          lbu[0][:, dr, h:h + 1], ALU.mult, ALU.add).then_inc(f_made, 1)

                def keys(dr):
                    for h in range(4):
                        dve.tensor_scalar(kk[:, 4 * dr + h, :], kk[:, 4 * dr + h, :], lbu[1][:, dr, h:h + 1], None,
                                          ALU.mult)
                dve.wait_ge(rows_in, 32)
                for t in range(16):
                    dve.wait_ge(made, t + 1)
                    bank = ps[:, t % NBANK, :]
                    if t < 8:
                        b = self.P_("b_hff" if t < 4 else "b_hfb")[:, 4 * half + t % 4:4 * half + t % 4 + 1]
                        ins = dve.tensor_scalar(zz[:, t, :], bank, b, None, ALU.add)
                    elif t < 12:
                        ins = dve.tensor_tensor(v[:, t - 8, :], bank, brow, ALU.add)
                    else:
                        b = self.P_("b_hq")[:, 4 * half + t - 12:4 * half + t - 11]
                        ins = dve.tensor_scalar(q[:, t - 12, :], bank[:, 0:SEQ], b, None, ALU.add)
                    ins.then_inc(freed, 1)
                    if 9 <= t < 13:
                        (forget if t < 11 else keys)((t - 9) % 2)
                self.mod_add(dve)
                for u in range(8):
                    dve.wait_ge(turned, u + 1)
                    dve.tensor_copy(LT[:, u, :, :].rearrange("p c f -> p (c f)"), ps[:, u % NBANK, :]).then_inc(kept, 1)

        sums, exped, weighted = S("decay_sums"), S("decay_exp"), S("keys_weighted")
        kturned, kback, kmade, kdone = S("keys_turned"), S("keys_back"), S("states_made"), S("states_kept")
        sel = self.k_sel.rearrange("p (d n) -> p d n", d=2)
        rest = [sel[:, dr, (LEVELS + 1) * P:(LEVELS + 2) * P] for dr in range(2)]
        with nc.Block() as block:
            @block.tensor
            def _(pe):
                def decays(u):
                    dr, (o0, o1, o2, _) = u // 4, ORDER[u // 4]
                    if u >= 2:
                        pe.wait_ge(exped, u - 1)
                    bank = ps[:, u % 2, :]
                    pe.matmul(bank[:, o0 * P:(o0 + 1) * P], LT[:, u, o0, :], rest[dr], start=True, stop=False)
                    pe.matmul(bank[:, o0 * P:(o0 + 1) * P], LT[:, u, o1, :], self.ones, start=False, stop=True)
                    pe.matmul(bank[:, o1 * P:(o1 + 1) * P], LT[:, u, o1, :], rest[dr], start=True, stop=True)
                    pe.matmul(bank[:, 256:384], LT[:, u, o2, :], rest[dr], start=True, stop=True)
                    pe.matmul(bank[:, 384:512], LT[:, u, o2, :], self.ones, start=True, stop=True).then_inc(sums, 1)

                def turn(u):
                    pe.wait_ge(weighted, 2 * u + 2)
                    if u >= 2:
                        pe.wait_ge(kback, u - 1)
                    for c in range(3):
                        ins = pe.transpose(ps[:, 2 + u % 2, c * P:(c + 1) * P], KP[:, u, c * P:(c + 1) * P], self.ident)
                    ins.then_inc(kturned, 1)

                def state(u):
                    h, o2 = u % 4, ORDER[u // 4][2]
                    pe.wait_ge(kback, u + 1)
                    if u >= 2:
                        pe.wait_ge(kdone, 2 * u - 2)
                    bank, hv = ps[:, 4 + u % 2, :], slice(h * P, (h + 1) * P)
                    pe.matmul(bank[:, 0:P], KP[:, u, 0:P], v[:, 0, hv], start=True, stop=False)
                    pe.matmul(bank[:, 0:P], KP[:, u, P:2 * P], v[:, 1, hv], start=False, stop=True)
                    pe.matmul(bank[:, P:2 * P], KP[:, u, 2 * P:3 * P], v[:, o2, hv], start=True, stop=True).then_inc(kmade, 1)

                for step in range(10):
                    if step < 8:
                        decays(step)
                    if 1 <= step < 9:
                        turn(step - 1)
                    if step >= 2:
                        state(step - 2)

            @block.scalar
            def _(act):
                def back(u):
                    act.wait_ge(kturned, u + 1)
                    act.activation(KP[:, u, 0:384], ps[:, 2 + u % 2, 0:384], ACT.Copy).then_inc(kback, 1)
                for u in range(8):
                    act.wait_ge(sums, u + 1)
                    if u >= 2:
                        act.wait_ge(weighted, 2 * u - 2)
                    act.activation(Es[u % 2], ps[:, u % 2, :], ACT.Exp).then_inc(exped, 1)
                    if u >= 1:
                        back(u - 1)
                back(7)

            @block.vector
            def _(dve):
                def keep(u):
                    dve.wait_ge(kmade, u + 1)
                    bank = ps[:, 4 + u % 2, :]
                    dve.tensor_copy(st[:, u, 0, :], bank[:, 0:P]).then_inc(kdone, 1)
                    dve.wait_ge(kdone, 2 * u + 1)
                    dve.scalar_tensor_tensor(st[:, u, 1, :], st[:, u, 0, :], dec[:, u:u + 1], bank[:, P:2 * P],
                                             ALU.mult, ALU.add).then_inc(kdone, 1)
                for u in range(8):
                    o2 = ORDER[u // 4][2]
                    dve.wait_ge(exped, u + 1)
                    dve.tensor_copy(dec[:, u:u + 1], Es[u % 2][:, 384:385])
                    dve.tensor_tensor(KP[:, u, 0:256], Es[u % 2][:, 0:256], kk[:, u, 0:256], ALU.mult).then_inc(weighted, 1)
                    dve.tensor_tensor(KP[:, u, 256:384], Es[u % 2][:, 256:384], kk[:, u, o2 * P:(o2 + 1) * P],
                                      ALU.mult).then_inc(weighted, 1)
                    if u >= 2:
                        keep(u - 2)
                keep(6)
                keep(7)

        works = [(h, c, dr) for h in range(4) for c in (2, 3) for dr in range(2)]
        gsum, gexp, xq, xk = S("level_sums"), S("level_exp"), S("queries_weighted"), S("level_keys_weighted")
        split, short = S("logf_split"), (self.short[0:2], self.short[2:4])
        sel12 = self.k_sel12.rearrange("p (d n) -> p d n", d=2)
        smade, amade, omade, okept = S("scores_made"), S("scores_masked"), S("o_made"), S("o_kept")
        with nc.Block() as block:
            @block.tensor
            def _(pe):
                def level_sums(i):
                    h, c, dr = works[i]
                    if i >= 1:
                        pe.wait_ge(gexp, i)
                    pe.wait_ge(split, 2 * i + 2)
                    for b in range(2):
                        for part in range(2):
                            ins = pe.matmul(ps[:, b, :], short[i % 2][part], sel12[:, dr, b * 512:(b + 1) * 512],
                                            start=part == 0, stop=part == 1)
                    ins.then_inc(gsum, 1)

                def scores(i):
                    h, c, dr = works[i]
                    pe.wait_ge(xk, i + 1)
                    pe.wait_ge(xq, i + 1)
                    if i >= 1:
                        pe.wait_ge(amade, i)
                    for lev in range(LEVELS + 1):
                        out = ps[:, 2 + lev // 4, lev % 4 * P:(lev % 4 + 1) * P]
                        if lev < LEVELS:
                            ins = pe.matmul(out, X[i % 2][:, lev, :], X[i % 2][:, lev, :], start=True, stop=True)
                        else:
                            ins = pe.matmul(out, kk[:, dr * 4 + h, c * P:(c + 1) * P], q[:, h, (c - 2) * P:(c - 1) * P],
                                            start=True, stop=True)
                    ins.then_inc(smade, 1)

                def outputs(i):
                    h, c, dr = works[i]
                    pe.wait_ge(amade, i + 1)
                    m = i // 2
                    if m >= 2 and dr == 0:
                        pe.wait_ge(okept, m - 1)
                    out = ps[:, 4 + m % 2, 0:P]
                    for lev in range(LEVELS + 1):
                        pe.matmul(out, AA[i % 4][:, lev, :], v[:, c, h * P:(h + 1) * P],
                                  start=dr == 0 and lev == 0, stop=False)
                    ins = pe.matmul(out, QD[i % 4], st[:, dr * 4 + h, int(c == ORDER[dr][3]), :], start=False, stop=dr == 1)
                    if dr == 1:
                        ins.then_inc(omade, 1)

                for i in range(len(works) + 2):
                    if i < len(works):
                        level_sums(i)
                    if 1 <= i <= len(works):
                        scores(i - 1)
                    if i >= 2:
                        outputs(i - 2)

            @block.scalar
            def _(act):
                def keep(m):
                    h, c, _ = works[2 * m]
                    act.wait_ge(omade, m + 1)
                    col = (4 * half + h) * P
                    act.activation(self.o_all[:, c - 2, col:col + P], ps[:, 4 + m % 2, 0:P], ACT.Copy).then_inc(okept, 1)
                for i in range(len(works)):
                    act.wait_ge(gsum, i + 1)
                    if i >= 2:
                        act.wait_ge(xk, i - 1)
                        act.wait_ge(xq, i - 1)
                    act.activation(G[i % 2], ps[:, 0:2, :].rearrange("p b (l t) -> p (b l) t", l=4), ACT.Exp).then_inc(gexp, 1)
                    if i >= 4 and i % 2 == 0:
                        keep(i // 2 - 2)
                keep(6)
                keep(7)

            def halves(eng, i, keys, done):
                h, c, dr = works[i]
                src = kk[:, dr * 4 + h, c * P:(c + 1) * P] if keys else q[:, h, (c - 2) * P:(c - 1) * P]
                side = (0 if keys else 1) ^ dr
                for lev in range(LEVELS):
                    m = P >> (lev + 1)
                    w = lambda a: a.rearrange("p (n two m) -> p n two m", two=2, m=m)[:, :, side, :]
                    ins = eng.tensor_tensor(w(X[i % 2][:, lev, :]), w(G[i % 2][:, lev, :]), w(src), ALU.mult)
                if not keys:
                    ins = eng.tensor_tensor(QD[i % 4], G[i % 2][:, LEVELS, :], src, ALU.mult)
                ins.then_inc(done, 1)

            @block.gpsimd
            def _(pool):
                for i in range(len(works)):
                    pool.wait_ge(gexp, i + 1)
                    if i >= 2:
                        pool.wait_ge(smade, i - 1)
                    halves(pool, i, True, xk)

            @block.vector
            def _(dve):
                def masked(i):
                    dr = works[i][2]
                    dve.wait_ge(smade, i + 1)
                    if i >= 4:
                        dve.wait_ge(omade, (i - 4) // 2 + 1)
                    dve.tensor_tensor(AA[i % 4].rearrange("p l t -> p (l t)"),
                                      ps[:, 2:4, :].rearrange("p b t -> p (b t)"), mask[:, dr, :], ALU.mult).then_inc(amade, 1)
                def parts(i):
                    h, c, dr = works[i]
                    if i >= 2:
                        dve.wait_ge(gsum, i - 1)
                    high, low = short[i % 2]
                    dve.tensor_copy(high, LT[:, dr * 4 + h, c, :]).then_inc(split, 1)
                    dve.wait_ge(split, 2 * i + 1)
                    dve.tensor_tensor(low, LT[:, dr * 4 + h, c, :], high.bitcast(F32), ALU.subtract).then_inc(split, 1)
                parts(0)
                parts(1)
                for i in range(len(works)):
                    dve.wait_ge(gexp, i + 1)
                    if i >= 2:
                        dve.wait_ge(smade, i - 1)
                    if i >= 4:
                        dve.wait_ge(omade, (i - 4) // 2 + 1)
                    halves(dve, i, False, xq)
                    if i + 2 < len(works):
                        parts(i + 2)
                    if i >= 1:
                        masked(i - 1)
                masked(len(works) - 1)

    def mlstm_in(self):
        nc, d, ring, ps, hT = self.nc, self.d, self.ring, self.ps, self.hT
        A = Arena(self.arena_t, self.work + 2 * D, self.A.end)
        self.r_all = A.take(2, D)
        self.ml_v = V = A.take(NC, ML_H, ML_DV + 1)
        self.ml_qk = A.take(8, SEQ)
        self.ml_kc = A.take(4, CTX)
        self.ml_area = A.at
        raw = A.take(8, SEQ + 4)
        rawc = A.take(4, CTX + 4)
        wif = A.take(KT, 16)
        brow = A.take(1024)
        bif = A.take(1)
        mif = A.take(TOK)
        hp = A.take(KT, SEQ)
        S = lambda name: self.sem("mlstm_" + name)
        self.mod_open(S, A, 4)
        made, freed, small, permuted = S("made"), S("freed"), S("small_loaded"), S("permuted")
        imade, tap_done, silud = S("gate_rows_made"), S("tap_done"), S("silu_made")
        grid = lambda a: a.rearrange("p (r c) -> p c r", c=GRID)
        cols = lambda a: a.rearrange("p (c r) -> p c r", r=ROWS)
        token_cols = [lambda k, c=c: hT[:, k, c * P:(c + 1) * P] for c in range(2)] + \
                     [lambda k, c=c: hp[:, k, c * P:(c + 1) * P] for c in range(2)]
        with nc.Block() as block:
            @block.sync
            def _(sp):
                sp.dma_start(brow, d["b_in"][0:1, O_MV:O_MV + D].partition_broadcast(P)).then_inc(small, 16)
                sp.dma_start(wif, d["w_in"].rearrange("(k p) n -> p k n", p=P)[:, :, O_MI:O_MI + 16]).then_inc(small, 16)
                sp.dma_start(bif[0:16, :], d["b_in"][0:1, O_MI:O_MI + 16].rearrange("a b -> b a")).then_inc(small, 16)
                ring.send(sp, self.ends["mlstm"] + 3)

            @block.scalar
            def _(act):
                for m in range(3):
                    self.mod_keep_step(act, m)
                act.wait_ge(tap_done, 5)
                act.activation(self.ml_qk, self.ml_qk, ACT.Silu).then_inc(silud, 1)
                act.activation(self.ml_kc, self.ml_kc, ACT.Silu)
                self.mod_keep_step(act, 3)

            @block.gpsimd
            def _(pool):
                pool.memset(raw, 0.0)
                pool.memset(rawc, 0.0)
                pool.memset(V[:, :, :, ML_DV:ML_DV + 1], 1.0).then_inc(permuted, 1)
                for k in range(KT):
                    pool.tensor_copy(cols(hp[:, k, :]), grid(hT[:, k, CTX:TOK])).then_inc(permuted, 1)

            @block.tensor
            def _(pe):
                def first():
                    pe.wait_ge(permuted, 1 + KT)
                self.products(pe, [self.feature_tiles(hT, CTX, TOK), self.feature_tiles(hT, 0, TOK)], made, freed, mods=2)
                first()
                self.products(pe, [self.token_tiles(token_cols), self.token_tiles(token_cols)], made, freed, first=8, mods=2)
                pe.wait_ge(small, 48)
                pe.wait_ge(freed, 13)
                for k in range(KT):
                    ins = pe.matmul(ps[0:16, 0, :], wif[:, k, :], hT[:, k, :], start=k == 0, stop=k == KT - 1)
                ins.then_inc(imade, 1)

            @block.vector
            def _(dve):
                w, b5 = self.P_("cw1"), self.P_("cb1")

                def convolve(tap):
                    if tap == 0:
                        dve.wait_ge(freed, 8)
                    else:
                        dve.wait_ge(tap_done, tap)
                    todo = [(self.ml_qk[:, t, :], raw[:, t, :], t) for t in range(8)] + \
                           [(self.ml_kc[:, t, :], rawc[:, t, :], t + 4) for t in range(4)]
                    for dst, src, t in todo:
                        if tap == 0:
                            ins = dve.tensor_scalar(dst, src[:, 0:SEQ], w[:, t:t + 1], b5[:, t:t + 1], ALU.mult, ALU.add)
                        else:
                            ins = dve.scalar_tensor_tensor(dst, src[:, tap:tap + SEQ], w[:, 8 * tap + t:8 * tap + t + 1], dst,
                                                           ALU.mult, ALU.add)
                    ins.then_inc(tap_done, 1)
                dve.wait_ge(permuted, 1 + KT)
                dve.wait_ge(small, 48)
                for t in range(16):
                    dve.wait_ge(made, t + 1)
                    bank = ps[:, t % NBANK, :]
                    if t < 4:
                        ins = dve.tensor_scalar(cols(raw[:, t, 2:2 + SEQ]), grid(bank[:, 0:SEQ]),
                                                self.P_("b_mq")[:, t:t + 1], None, ALU.add)
                    elif t < 8:
                        b = self.P_("b_mk")[:, t - 4:t - 3]
                        dve.tensor_scalar(rawc[:, t - 4, 2:2 + CTX], bank[:, 0:CTX], b, None, ALU.add)
                        ins = dve.tensor_scalar(cols(raw[:, t, 2:2 + SEQ]), grid(bank[:, CTX:TOK]), b, None, ALU.add)
                    else:
                        blk, c = divmod(t - 8, 4)
                        ins = dve.tensor_tensor(V[:, c, 2 * blk:2 * blk + 2, 0:ML_DV],
                                                bank.rearrange("p (h v) -> p h v", v=ML_DV),
                                                brow[:, 512 * blk:512 * blk + 512].rearrange("p (h v) -> p h v", v=ML_DV), ALU.add)
                    ins.then_inc(freed, 1)
                    if 8 <= t < 13:
                        convolve(t - 8)
                dve.wait_ge(silud, 1)
                dve.tensor_scalar(self.ml_qk[:, 0:4, :], self.ml_qk[:, 0:4, :], float(P) ** -0.5, None, ALU.mult)
                self.mod_add(dve)
                dve.wait_ge(imade, 1)
                dve.tensor_scalar(mif[0:16, 0:CTX], ps[0:16, 0, 0:CTX], bif[0:16, :], None, ALU.add)
                dve.tensor_scalar(cols(mif[0:16, CTX:TOK]), grid(ps[0:16, 0, CTX:TOK]), bif[0:16, :], None, ALU.add)

        row_made, rows = S("rows_split"), S("rows")
        self.ml_rows = [A.take(2, TOK) for _ in range(6)]
        self.ml_rows_end = A.at
        with nc.Block() as block:
            @block.tensor
            def _(pe):
                for g in range(4):
                    ins = pe.matmul(ps[0:4, g, :], self.ident[0:16, 4 * g:4 * g + 4], mif[0:16, :], start=True, stop=True)
                ins.then_inc(row_made, 1)

            @block.vector
            def _(dve):
                dve.wait_ge(row_made, 1)
                for which, g in ((0, 0), (1, 2)):
                    dst = self.ml_rows[which]
                    dve.tensor_copy(dst[0:4, 0, :], ps[0:4, g, :])
                    for a in (0, CTX):
                        dve.tensor_copy(dst[0:4, 1, a:a + SEQ], ps[0:4, g + 1, a:a + SEQ][:, ::-1])

    def mlstm(self):
        nc, d, ps = self.nc, self.d, self.ps
        I, F, B, M, T1, T2 = [r[0:4] for r in self.ml_rows]
        A = Arena(self.arena_t, self.ml_area, self.A.end)
        arg = [A.take(4, SEQ) for _ in range(2)]
        Pm = [A.take(4, SEQ) for _ in range(2)]
        A.at = max(A.at, self.ml_rows_end)
        cols = A.take(48)
        rows4 = A.take(ML_H, P)
        nat = A.take(2, TOK)
        natmu = A.take(2, SEQ)
        natem = A.take(2, SEQ)
        mask = A.take(2, 2, SEQ)
        small = A.take(4)
        S = lambda name: self.sem("ml_" + name)
        sv, sa = S("vector_rows"), S("scalar_rows")
        rowsin, turned, mset = S("rows4_loaded"), S("turned"), S("masks_set")
        incl = [self.k_sel[:, dr * (LEVELS + 2) * P + LEVELS * P:dr * (LEVELS + 2) * P + (LEVELS + 1) * P] for dr in range(2)]
        with nc.Block() as block:
            @block.sync
            def _(sp):
                sp.dma_start(rows4[0:4], d["k_rows4"].rearrange("p (a b) -> p a b", b=P)).then_inc(rowsin, 16)
                sp.wait_ge(rowsin, 16)

            @block.gpsimd
            def _(pool):
                pool.memset(mask[:, 0, 0, P:SEQ], 1.0)
                pool.memset(mask[:, 0, 1, 0:P], 0.0)
                pool.memset(mask[:, 1, 0, P:SEQ], 0.0)
                pool.memset(mask[:, 1, 1, 0:P], 1.0)
                for dr in range(2):
                    for c in range(2):
                        pool.tensor_copy(mask[:, dr, c, c * P:(c + 1) * P], incl[dr])

            @block.scalar
            def _(act):
                act.wait_ge(sv, 1)
                act.activation(T1, T1, ACT.Exp, scale=-1.0).then_inc(sa, 1)
                act.wait_ge(sa, 1)
                act.activation(T1, T1, ACT.Ln, bias=1.0).then_inc(sa, 1)
                act.wait_ge(sv, 6)
                act.activation(T2, T2, ACT.Exp, scale=-1.0).then_inc(sa, 1)

            @block.vector
            def _(dve):
                n = [0]
                def step(ins):
                    n[0] += 1
                    ins.then_inc(sv, 1)
                    dve.wait_ge(sv, n[0])
                step(dve.scalar_tensor_tensor(T1, F, -1.0, F, ALU.mult, ALU.max))
                dve.wait_ge(sa, 2)
                step(dve.scalar_tensor_tensor(F, F, 0.0, T1, ALU.min, ALU.subtract))
                dve.memset(T2, 1.0)
                dve.drain()
                for dr in range(2):
                    ins = dve.tensor_tensor_scan(B[:, dr, :], T2[:, dr, :], F[:, dr, :], 0.0, ALU.mult, ALU.add)
                step(ins)
                step(dve.tensor_tensor(I, I, B, ALU.subtract))
                for dr in range(2):
                    ins = dve.tensor_tensor_scan(M[:, dr, :], T2[:, dr, :], I[:, dr, :], 0.0, ALU.mult, ALU.max)
                step(ins)
                step(dve.tensor_tensor(T2, B, M, ALU.add))
                dve.tensor_copy(nat[0:4, 0, :], I[:, 0, :])
                for a in (0, CTX):
                    dve.tensor_copy(nat[0:4, 1, a:a + SEQ], I[:, 1, a:a + SEQ][:, ::-1])
                dve.tensor_scalar(natmu[0:4, 0, :], M[:, 0, CTX:TOK], -1.0, None, ALU.mult)
                dve.tensor_scalar(natmu[0:4, 1, :], M[:, 1, CTX:TOK][:, ::-1], -1.0, None, ALU.mult)
                dve.wait_ge(sa, 3)
                dve.tensor_copy(natem[0:4, 0, :], T2[:, 0, CTX:TOK])
                dve.tensor_copy(natem[0:4, 1, :], T2[:, 1, CTX:TOK][:, ::-1])
        with nc.Block() as block:
            @block.tensor
            def _(pe):
                for dr in range(2):
                    for c in range(NC):
                        i = dr * NC + c
                        pe.transpose(ps[:, 0, 4 * i:4 * i + 4], nat[0:4, dr, c * P:(c + 1) * P], self.ident[0:4, 0:4])
                    for c in range(2):
                        i = 8 + dr * 2 + c
                        ins = pe.transpose(ps[:, 0, 4 * i:4 * i + 4], natem[0:4, dr, c * P:(c + 1) * P], self.ident[0:4, 0:4])
                ins.then_inc(turned, 1)

            @block.vector
            def _(dve):
                dve.wait_ge(turned, 1)
                dve.tensor_copy(cols, ps[:, 0, 0:48])

        q, k, kc, V = self.ml_qk[:, 0:4, :], self.ml_qk[:, 4:8, :], self.ml_kc, self.ml_v
        units = [(h, dr) for h in range(ML_H) for dr in range(2)]
        bmade, smade, argd, exped = S("mu_rows_made"), S("scores_made"), S("arguments"), S("exped")
        pmade, pmask, nmade, nkept = S("weights_made"), S("weights_masked"), S("numerators_made"), S("outputs_kept")
        vd = S("denominators")
        tiles = {(0, 0): (0, 1, 2), (0, 1): (0, 1, 2, 3), (1, 0): (0, 1, 2, 3), (1, 1): (0, 1, 3)}
        with nc.Block() as block:
            @block.tensor
            def _(pe):
                def arguments(u):
                    h, dr = units[u]
                    if u >= 2:
                        pe.wait_ge(argd, u - 1)
                    pe.matmul(ps[:, u % 2, 0:SEQ], rows4[0:4, h, :], natmu[0:4, dr, :], start=True, stop=True).then_inc(bmade, 1)
                    if dr == 0:
                        if h >= 2:
                            pe.wait_ge(pmade, 2 * h - 2)
                        for c in range(NC):
                            lhsT = kc[:, h, c * P:(c + 1) * P] if c < LAT else k[:, h, (c - 2) * P:(c - 1) * P]
                            ins = pe.matmul(ps[:, 2 + 2 * (h % 2) + c // 2, c % 2 * SEQ:(c % 2 + 1) * SEQ], lhsT,
                                            q[:, h, :], start=True, stop=True)
                        ins.then_inc(smade, 1)

                def numerators(u):
                    h, dr = units[u]
                    pe.wait_ge(pmask, u + 1)
                    for c in range(2):
                        if u >= 1:
                            pe.wait_ge(nkept, 2 * u - 1 + c)
                        use = tiles[dr, c]
                        for i in use:
                            ins = pe.matmul(ps[:, 6 + c, 0:ML_DV + 1], Pm[u % 2][:, i, c * P:(c + 1) * P], V[:, i, h, :],
                                            start=i == use[0], stop=i == use[-1])
                        ins.then_inc(nmade, 1)
                for u in range(9):
                    if u < 8:
                        arguments(u)
                    if u >= 1:
                        numerators(u - 1)

            @block.scalar
            def _(act):
                for u in range(8):
                    act.wait_ge(argd, u + 1)
                    act.activation(arg[u % 2], arg[u % 2], ACT.Exp).then_inc(exped, 1)

            @block.gpsimd
            def _(pool):
                for u in range(8):
                    pool.wait_ge(pmade, u + 1)
                    pool.tensor_tensor(Pm[u % 2][:, 2:4, :], Pm[u % 2][:, 2:4, :], mask[:, units[u][1]], ALU.mult).then_inc(pmask, 1)

            @block.vector
            def _(dve):
                def outputs(u):
                    h, dr = units[u]
                    for c in range(2):
                        dve.wait_ge(nmade, 2 * u + c + 1)
                        num, n = ps[:, 6 + c, :], 3 * (2 * u + c)
                        em = cols[:, 32 + (dr * 2 + c) * 4 + h:33 + (dr * 2 + c) * 4 + h]
                        den, s = num[:, ML_DV:ML_DV + 1], small[:, c:c + 1]
                        dve.scalar_tensor_tensor(s, den, -1.0, em, ALU.mult, ALU.max).then_inc(vd, 1)
                        dve.wait_ge(vd, n + 1)
                        dve.tensor_tensor(s, s, den, ALU.max).then_inc(vd, 1)
                        dve.wait_ge(vd, n + 2)
                        dve.reciprocal(s, s).then_inc(vd, 1)
                        dve.wait_ge(vd, n + 3)
                        r = self.r_all[:, c, h * ML_DV:(h + 1) * ML_DV]
                        if dr == 0:
                            ins = dve.tensor_scalar(r, num[:, 0:ML_DV], small[:, c:c + 1], None, ALU.mult)
                        else:
                            ins = dve.scalar_tensor_tensor(r, num[:, 0:ML_DV], small[:, c:c + 1], r, ALU.mult, ALU.add)
                        ins.then_inc(nkept, 1)
                for u in range(8):
                    h, dr = units[u]
                    dve.wait_ge(bmade, u + 1)
                    if u >= 2:
                        dve.wait_ge(pmade, u - 1)
                    for c in range(NC):
                        i = (dr * NC + c) * 4 + h
                        ins = dve.tensor_scalar(arg[u % 2][:, c, :], ps[:, u % 2, 0:SEQ], cols[:, i:i + 1], 0.0, ALU.add, ALU.min)
                    ins.then_inc(argd, 1)
                    dve.wait_ge(exped, u + 1)
                    dve.wait_ge(smade, h + 1)
                    if u >= 2:
                        dve.wait_ge(nmade, 2 * (u - 2) + 2)
                    dve.tensor_tensor(Pm[u % 2].rearrange("p a t -> p (a t)"), arg[u % 2].rearrange("p a t -> p (a t)"),
                                      ps[:, 2 + 2 * (h % 2):4 + 2 * (h % 2), :].rearrange("p b t -> p (b t)"), ALU.mult).then_inc(pmade, 1)
                    if u >= 1:
                        outputs(u - 1)
                outputs(7)

    def merge1(self):
        nc, d, ring, ps, hT = self.nc, self.d, self.ring, self.ps, self.hT
        A = Arena(self.arena_t, self.work + 4 * D, self.A.end)
        o, r = self.o_all, self.r_all
        gates = [A.take(KT, SEQ) for _ in range(4)]
        sq = A.take(2, D)
        ss = [A.take(2, HG_H), A.take(2, ML_H)]
        S = lambda name: self.sem("merge1_" + name)
        made, freed = S("gates_made"), S("gates_kept")
        squared, summed, rooted, meaned, normed = S("squared"), S("summed"), S("rooted"), S("meaned"), S("normed")
        srcs = [(o, HG_H), (r, ML_H)]
        self.mod_open(S, A, 8)
        with nc.Block() as block:
            @block.sync
            def _(sp):
                ring.send(sp, self.ends["gates1"] + 3)

            @block.tensor
            def _(pe):
                self.products(pe, [self.feature_tiles(hT, CTX, TOK)] * 8, made, freed, mods=8)

            @block.scalar
            def _(act):
                for i, (src, _) in enumerate(srcs):
                    if i == 1:
                        act.wait_ge(summed, 1)
                    act.activation(sq, src, ACT.Square).then_inc(squared, 1)
                for i in range(2):
                    act.wait_ge(meaned, i + 1)
                    act.activation(ss[i], ss[i], ACT.Sqrt).then_inc(rooted, 1)
                for t in range(32):
                    act.wait_ge(made, t + 1)
                    g, k = divmod(t, 8)
                    bias = self.P_(("b_ga", "b_gb", "b_g1", "b_g2")[g])[:, k:k + 1]
                    act.activation(gates[g][:, k, :], ps[:, t % NBANK, 0:SEQ], ACT.Silu if g == 0 else ACT.Sigmoid,
                                   bias=bias).then_inc(freed, 1)
                    if t % 4 == 3:
                        self.mod_keep_step(act, t // 4)

            @block.vector
            def _(dve):
                for i, (src, h) in enumerate(srcs):
                    dve.wait_ge(squared, i + 1)
                    dve.reduce_sum(ss[i], sq.rearrange("p c (h v) -> p c h v", h=h), axis=AX.X).then_inc(summed, 1)
                    dve.wait_ge(summed, i + 1)
                    dve.tensor_scalar(ss[i], ss[i], float(h) / D, EPS, ALU.mult, ALU.add).then_inc(meaned, 1)
                for i, (src, h) in enumerate(srcs):
                    dve.wait_ge(rooted, i + 1)
                    dve.reciprocal(ss[i], ss[i]).then_inc(normed, 1)
                    dve.wait_ge(normed, i + 1)
                    for c in range(2):
                        v = src[:, c, :].rearrange("p (h v) -> p h v", h=h)
                        dve.tensor_tensor(v, v, bcast(ss[i][:, c, :].unsqueeze(2), [P, h, D // h]), ALU.mult)
                self.mod_add(dve)
        yT = [A.take(KT, SEQ) for _ in range(2)]
        turned, kept = S("turned"), S("turned_kept")
        grid = lambda a: a.rearrange("p (r c) -> p c r", c=GRID)
        cols = lambda a: a.rearrange("p (c r) -> p c r", r=ROWS)
        with nc.Block() as block:
            @block.tensor
            def _(pe):
                for t in range(16):
                    if t >= 8:
                        pe.wait_ge(kept, t - 7)
                    src, k = srcs[t // 8][0], t % 8
                    for c in range(2):
                        ins = pe.transpose(ps[:, t % 8, c * P:(c + 1) * P], src[:, c, k * P:(k + 1) * P], self.ident)
                    ins.then_inc(turned, 1)

            @block.vector
            def _(dve):
                for t in range(16):
                    dve.wait_ge(turned, t + 1)
                    b, k = divmod(t, 8)
                    if b == 0:
                        ins = dve.scalar_tensor_tensor(yT[0][:, k, :], ps[:, t % 8, 0:SEQ], self.P_("hg_g")[:, k:k + 1],
                                                       gates[0][:, k, :], ALU.mult, ALU.mult)
                    else:
                        ins = dve.scalar_tensor_tensor(grid(yT[1][:, k, :]), cols(ps[:, t % 8, 0:SEQ]),
                                                       self.P_("ml_g")[:, k:k + 1], grid(gates[1][:, k, :]), ALU.mult, ALU.mult)
                    ins.then_inc(kept, 1)
        y = A.take(KT, SEQ)
        t2 = [A.take(SEQ) for _ in range(2)]
        tiles = [(lambda w, k, j=j: w[:, k, j * P:(j + 1) * P], lambda w, k, b=b: yT[b][:, k, :], SEQ, KT) for b in range(2) for j in range(4)]
        self.merge_out("merge1b", [tiles[0:4]] * 2 + [tiles[4:8]] * 2, gates[2:4], y, t2, self.ends["experts1"],
                       gain=self.mod1[:, 16:24, 0])

    def merge_out(self, name, branch_tiles, gates, y, t2, end, gain=None, store=None):
        nc, ring, ps = self.nc, self.ring, self.ps
        S = lambda n: self.sem(name + "_" + n)
        made, freed, ydone, part = S("made"), S("kept"), S("y_done"), S("gated")
        with nc.Block() as block:
            @block.sync
            def _(sp):
                ring.send(sp, end)

            @block.tensor
            def _(pe):
                tiles = lambda src: [(lambda w, k, j=j: w[:, k, j * P:(j + 1) * P], lambda w, k: src[:, k, :], SEQ, KT)
                                     for j in range(4)]
                n = self.products(pe, branch_tiles, made, freed)
                pe.wait_ge(ydone, KT)
                self.products(pe, [tiles(y)] * 2, made, freed, first=n)

            @block.vector
            def _(dve):
                for t in range(24):
                    dve.wait_ge(made, t + 1)
                    b, k = divmod(t, 8)
                    bank = ps[:, t % NBANK, 0:SEQ]
                    if b == 0:
                        ins = dve.tensor_tensor(y[:, k, :], bank, gates[0][:, k, :], ALU.mult)
                    elif b == 1:
                        ins = dve.tensor_tensor(t2[k % 2], bank, gates[1][:, k, :], ALU.mult)
                    elif store is None:
                        ins = dve.scalar_tensor_tensor(self.xT[:, k, :], bank, gain[:, k:k + 1], self.xT[:, k, :], ALU.mult, ALU.add)
                    else:
                        ins = dve.tensor_copy(store[:, k, :], bank)
                    ins.then_inc(freed, 1)
                    if b == 1:
                        dve.wait_ge(freed, t + 1)
                        dve.tensor_tensor(y[:, k, :], y[:, k, :], t2[k % 2], ALU.add).then_inc(ydone, 1)

    def norm_modulate(self, name, src, dst, gain_col, scale, shift, A, pe_after=None, dve_after=None, act_each=None):
        rstd, sq, g = A.take(SEQ), A.take(KT, SEQ), A.take(KT)
        gained, scaled = self.sem(name + "_gain"), self.sem(name + "_scaled")

        def gains(dve):
            if scale is not None:
                dve.scalar_tensor_tensor(g, scale, 1.0, gain_col, ALU.add, ALU.mult).then_inc(gained, 1)
            else:
                dve.tensor_copy(g, gain_col).then_inc(gained, 1)

        def scaling(dve):
            dve.wait_ge(gained, 1)
            for k in range(KT):
                dve.scalar_tensor_tensor(dst[:, k, :], src[:, k, :], g[:, k:k + 1], rstd, ALU.mult, ALU.mult).then_inc(scaled, 1)
            if dve_after:
                dve_after(dve)

        def shifting(act):
            for k in range(KT):
                act.wait_ge(scaled, k + 1)
                if act_each:
                    act_each(act, k)
                else:
                    act.activation(dst[:, k, :], dst[:, k, :], ACT.Identity, bias=shift[:, k:k + 1])
        self.rms(name, src, KT, SEQ, rstd, sq, before=gains, after=scaling, act_after=shifting if shift is not None or act_each else None,
                 pe_after=pe_after)

    def router1(self):
        nc, d, ps = self.nc, self.d, self.ps
        A = Arena(self.arena_t, self.work, self.A.end)
        self.h2 = self.hT[:, :, 0:SEQ]
        self.wgt = A.take(2, N_EXP)
        self.rank = A.take(2, N_EXP)
        self.rounds = A.take(1).bitcast(mybir.dt.int32)
        self.moe_area = A.at
        wr = A.take(KT, N_GRP + N_EXP)
        br = A.take(N_GRP + N_EXP)
        iota = A.take(SEQ)
        self.norm_modulate("norm2", self.xT, self.h2, self.P_("norm2"), self.mod1[:, 32:40, 0], self.mod1[:, 24:32, 0], A)
        S = lambda n: self.sem("router1_" + n)
        loaded, made, st, sa = S("loaded"), S("logits_made"), S("step"), S("exped")
        n = N_GRP + N_EXP
        lg, e, e2, pri = A.take(2, n), A.take(2, N_EXP), A.take(2, N_EXP), A.take(2, N_EXP)
        oh1, oh2, comb = A.take(2, N_EXP), A.take(2, N_EXP), self.wgt
        gh, gex = A.take(2, N_GRP), A.take(2, N_GRP)
        desc = A.take(N_EXP)
        v = A.take(8, 2)
        chosen, chosen2 = A.take(2, N_EXP), A.take(2, N_EXP)
        with nc.Block() as block:
            @block.sync
            def _(sp):
                sp.dma_start(wr[:, :, 0:N_GRP], d["w_group"].rearrange("(k p) n -> p k n", p=P)).then_inc(loaded, 16)
                sp.dma_start(wr[:, :, N_GRP:n], d["w_router"].rearrange("(k p) n -> p k n", p=P)).then_inc(loaded, 16)
                sp.dma_start(br[:, 0:N_GRP], d["b_group"].partition_broadcast(P)).then_inc(loaded, 16)
                sp.dma_start(br[:, N_GRP:n], d["b_router"].partition_broadcast(P)).then_inc(loaded, 16)
                sp.dma_start(iota, d["k_iota"]).then_inc(loaded, 16)
                sp.wait_ge(loaded, 80)

            @block.tensor
            def _(pe):
                pe.wait_ge(loaded, 80)
                for c in range(2):
                    for k in range(KT):
                        ins = pe.matmul(ps[:, c, 0:n], self.h2[:, k, c * P:(c + 1) * P], wr[:, k, :], start=k == 0, stop=k == KT - 1)
                ins.then_inc(made, 1)

            @block.scalar
            def _(act):
                act.wait_ge(st, 3)
                act.activation(gex, gex, ACT.Exp).then_inc(sa, 1)
                act.wait_ge(st, 4)
                act.activation(v[:, 4, :], v[:, 4, :], ACT.Exp).then_inc(sa, 1)

            @block.vector
            def _(dve):
                vs = self.vs
                do = lambda ins: vs.do(dve, ins)
                bc = lambda a, m: bcast(a.unsqueeze(2), [P, 2, m])
                dve.wait_ge(made, 1)
                dve.wait_ge(loaded, 80)
                do(dve.tensor_tensor(lg, ps[:, 0:2, 0:n], bcast(br.unsqueeze(1), [P, 2, n]), ALU.add))
                do(dve.tensor_scalar(desc, iota[:, 0:N_EXP], -1.0, float(N_EXP), ALU.mult, ALU.add))

                def first_max(src, m, top, hot, tmp):
                    do(dve.reduce_max(top, src, axis=AX.X))
                    do(dve.tensor_tensor(tmp, src, bc(top, m), ALU.is_equal))
                    do(dve.tensor_tensor(tmp, tmp, bcast(desc[:, 0:m].unsqueeze(1), [P, 2, m]), ALU.mult))
                    do(dve.reduce_max(v[:, 7, :], tmp, axis=AX.X))
                    do(dve.tensor_tensor(hot, tmp, bc(v[:, 7, :], m), ALU.is_equal))
                g = lg[:, :, 0:N_GRP]
                first_max(g, N_GRP, v[:, 0, :], gh, pri[:, :, 0:N_GRP])
                dve.tensor_tensor(gex, g, bc(v[:, 0, :], N_GRP), ALU.subtract).then_inc(st, 3)
                do(dve.tensor_scalar(gh, gh, BIG, -BIG, ALU.mult, ALU.add))
                do(dve.tensor_tensor(e.rearrange("p c (g e) -> p c g e", g=N_GRP),
                                     lg[:, :, N_GRP:n].rearrange("p c (g e) -> p c g e", g=N_GRP),
                                     bcast(gh.unsqueeze(3), [P, 2, N_GRP, PER_GRP]), ALU.add))
                first_max(e, N_EXP, v[:, 1, :], oh1, pri)
                do(dve.scalar_tensor_tensor(e2, oh1, -3 * BIG, e, ALU.mult, ALU.add))
                first_max(e2, N_EXP, v[:, 2, :], oh2, pri)
                dve.tensor_tensor(v[:, 4, :], v[:, 2, :], v[:, 1, :], ALU.subtract).then_inc(st, 1)
                dve.wait_ge(sa, 2)
                do(dve.reduce_sum(v[:, 3, :], gex, axis=AX.X))
                do(dve.tensor_scalar(v[:, 5, :], v[:, 4, :], 1.0, None, ALU.add))
                do(dve.tensor_tensor(v[:, 5, :], v[:, 5, :], v[:, 3, :], ALU.mult))
                do(dve.reciprocal(v[:, 5, :], v[:, 5, :]))
                do(dve.tensor_tensor(v[:, 6, :], v[:, 5, :], v[:, 4, :], ALU.mult))
                do(dve.tensor_tensor(chosen, oh1, oh2, ALU.add))
                do(dve.tensor_tensor(oh1, oh1, bc(v[:, 5, :], N_EXP), ALU.mult))
                do(dve.tensor_tensor(oh2, oh2, bc(v[:, 6, :], N_EXP), ALU.mult))
                do(dve.tensor_tensor(comb, oh1, oh2, ALU.add))
        counted, rk = S("counted"), S("rank_steps")
        before = self.k_sel[:, (2 * LEVELS + 3) * P:(2 * LEVELS + 4) * P]
        most = A.take(1)
        with nc.Block() as block:
            @block.tensor
            def _(pe):
                pe.matmul(ps[:, 0, 0:N_EXP], before, chosen[:, 0, :], start=True, stop=True)
                pe.matmul(ps[:, 1, 0:N_EXP], before, chosen[:, 1, :], start=True, stop=False)
                pe.matmul(ps[:, 1, 0:N_EXP], self.ones, chosen[:, 0, :], start=False, stop=True)
                for c in range(2):
                    ins = pe.matmul(ps[:, 2, 0:N_EXP], self.ones, chosen[:, c, :], start=c == 0, stop=c == 1)
                ins.then_inc(counted, 1)

            @block.vector
            def _(dve):
                dve.tensor_scalar(chosen2, chosen, -1e4, 1e4, ALU.mult, ALU.add).then_inc(rk, 1)
                dve.wait_ge(rk, 1)
                dve.wait_ge(counted, 1)
                dve.tensor_tensor(self.rank, ps[:, 0:2, 0:N_EXP], chosen2, ALU.add)
                dve.reduce_max(most, ps[:, 2, 0:N_EXP], axis=AX.X).then_inc(rk, 1)
                dve.wait_ge(rk, 2)
                dve.tensor_scalar(self.rounds, most, 1.0 / CAP, (CAP - 1.0) / CAP - 0.5 + 0.5 / CAP, ALU.mult, ALU.add)

    def gather(self, n_exp, rank, wgt, xe, selT, iota, A, S):
        nc, ps = self.nc, self.ps
        n = n_exp * CAP
        sel = A.take(2, n)
        selw = [A.take(2 * 2 * P).rearrange("p (e c r s) -> p e c r s", e=2, c=2, r=4) for _ in range(4)]
        h_tok = lambda c, k: self.hT[:, k, CTX + c * P:CTX + (c + 1) * P]
        sset, wset, hturned, hkept = S("selected"), S("selection_weighted"), S("h_turned"), S("h_kept")
        xmade, xkept, tmade, tkept = S("xe_made"), S("xe_kept"), S("selection_turned"), S("selection_kept")
        by_slot = lambda c: sel[:, c, :].rearrange("p (e s) -> p e s", s=CAP)
        wide = n // 512
        with nc.Block() as block:
            @block.vector
            def _(dve):
                for c in range(2):
                    dve.tensor_tensor(by_slot(c), bcast(iota[:, 0:CAP].unsqueeze(1), [P, n_exp, CAP]),
                                      bcast(rank[:, c, :].unsqueeze(2), [P, n_exp, CAP]), ALU.is_equal).then_inc(sset, 1)
                dve.wait_ge(sset, 2)

                def keep(i):
                    dve.wait_ge(tmade, i + 1)
                    dve.tensor_copy(selT[:, 2 * i:2 * i + 2, :], ps[:, 4 + i % 4, :].rearrange("p (a t) -> p a t", a=2)).then_inc(tkept, 1)
                for i in range(n_exp // 2):
                    if i >= 4:
                        dve.wait_ge(tmade, i - 3)
                    for e in (2 * i, 2 * i + 1):
                        for c in range(2):
                            ins = dve.tensor_tensor(selw[i % 4][:, e % 2, c], bcast(sel[:, c, e * CAP:(e + 1) * CAP].unsqueeze(1), [P, 4, CAP]),
                                                    bcast(wgt[:, c, e:e + 1].unsqueeze(2), [P, 4, CAP]), ALU.mult)
                    ins.then_inc(wset, 1)
                    if i >= 3:
                        keep(i - 3)
                for i in range(n_exp // 2 - 3, n_exp // 2):
                    keep(i)

            @block.scalar
            def _(act):
                for k in range(KT):
                    act.wait_ge(hturned, k + 1)
                    act.activation(self.hT[:, k, CTX:TOK], ps[:, 4 + k % 4, 0:SEQ], ACT.Copy).then_inc(hkept, 1)
                for i in range(KT * wide):
                    act.wait_ge(xmade, i + 1)
                    act.activation(xe[:, i // wide, i % wide * 512:(i % wide + 1) * 512], ps[:, i % 4, :], ACT.Copy).then_inc(xkept, 1)

            @block.tensor
            def _(pe):
                for k in range(KT):
                    if k >= 4:
                        pe.wait_ge(hkept, k - 3)
                    for c in range(2):
                        ins = pe.transpose(ps[:, 4 + k % 4, c * P:(c + 1) * P], self.h2[:, k, c * P:(c + 1) * P], self.ident)
                    ins.then_inc(hturned, 1)
                pe.wait_ge(hkept, KT)
                pe.wait_ge(sset, 2)
                for i in range(KT * wide):
                    k, w = divmod(i, wide)
                    if i >= 4:
                        pe.wait_ge(xkept, i - 3)
                    for c in range(2):
                        ins = pe.matmul(ps[:, i % 4, :], h_tok(c, k), sel[:, c, w * 512:(w + 1) * 512],
                                        start=c == 0, stop=c == 1)
                    ins.then_inc(xmade, 1)
                for i in range(n_exp // 2):
                    pe.wait_ge(wset, i + 1)
                    if i >= 4:
                        pe.wait_ge(tkept, i - 3)
                    for j in range(2):
                        for c in range(2):
                            ins = pe.transpose(ps[:, 4 + i % 4, j * SEQ + c * P:j * SEQ + (c + 1) * P],
                                               selw[i % 4][:, j, c].rearrange("p r s -> p (r s)"), self.ident)
                    ins.then_inc(tmade, 1)

    def moe1(self):
        nc, d, ps = self.nc, self.d, self.ps
        A = Arena(self.arena_t, self.moe_area, self.A.end)
        xe = A.take(KT, N_EXP * CAP)
        selT = A.take(N_EXP, SEQ)
        xs = [self.hT[:, :, CTX + CAP * j:CTX + CAP * (j + 1)] for j in range(2)]
        stack, gs, aT = self.stack, A.take(4 * CAP), A.take(4, CAP)
        gq, uq, iota = A.take(512), A.take(512), A.take(CAP)
        yq = self.hT[:, :, CTX + P:TOK]
        zero = gq
        slot_area = A.at
        held = []
        with nc.Block() as block:
            @block.sync
            def _(sp):
                held.extend(self.ring.hand_over(sp))
        slots = held + [A.take(4096) for _ in range(3)]
        rounds = nc.values_load(self.rounds[0:1, 0:1], min_val=1, max_val=SEQ // CAP)
        src = [d["w_gate"].rearrange("e (k p) f -> e p k f", p=P), d["w_up"].rearrange("e (k p) f -> e p k f", p=P),
               d["w_down"].rearrange("e (k p) n -> e p k n", p=P)]
        mat = [s.rearrange("p (k c) -> p k c", c=512 if i < 4 else D) for i, s in enumerate(slots)]
        block_of = lambda i, it: src[(0, 1, 0, 1, 2, 2)[i]][bass.ds(it * 2 + (0, 0, 1, 1, 0, 1)[i], 1)].rearrange("o p k f -> p (o k) f")
        acc = lambda o: ps[:, 4 + o // 2, o % 2 * SEQ:(o % 2 + 1) * SEQ]
        first_sem = self.stage_sems
        last = N_EXP - 1
        S = lambda n: self.sem("moe1_" + n)
        with nc.Fori(0, rounds):
            loaded, used = [S(f"loaded{i}") for i in range(6)], [S(f"used{i}") for i in range(6)]
            next_round = S("next_round_loaded")
            tabled = S("iota_loaded")
            with nc.Block() as block:
                @block.sync
                def _(sp):
                    for i in range(3):
                        sp.sem_inc(loaded[i], 16)
                    sp.dma_start(iota, d["k_iota"][:, 0:CAP]).then_inc(tabled, 16)
                    sp.dma_start(mat[3], src[1][1]).then_inc(loaded[3], 16)
                    sp.dma_start(mat[4], src[2][0]).then_inc(loaded[4], 16)
                    sp.wait_ge(tabled, 16)
            self.gather(N_EXP, self.rank, self.wgt, xe, selT, iota, Arena(self.arena_t, slot_area + 2 * 4096, self.A.end), S)
            xset, qmade, gkept, ukept = S("x_set"), S("quarters_made"), S("gate_kept"), S("up_kept")
            tmade, silud, aready, dmade, dkept, zeroed = (S("turned"), S("silu_made"), S("hidden_ready"), S("down_made"),
                                                          S("down_kept"), S("zeroed"))
            scat = S("scattered")
            with nc.Block() as block:
                @block.sync
                def _(sp):
                    sp.sem_inc(used[5], 1)
                    with sp.Fori(1, N_EXP // 2) as it:
                        for i in (0, 1, 5, 2, 3, 4):
                            j = it - 1 if i == 5 else it
                            sp.wait_ge(used[i], it)
                            sp.dma_start(mat[i], block_of(i, j)).then_inc(loaded[i], 16)
                    sp.wait_ge(used[5], N_EXP // 2)
                    sp.dma_start(mat[5], src[2][N_EXP - 1]).then_inc(loaded[5], 16)
                    for i in range(3):
                        sp.wait_ge(used[i], N_EXP // 2)
                        sp.dma_start(mat[i], src[i % 2][i // 2]).then_inc(next_round, 16)
                    sp.wait_ge(next_round, 48)

                @block.gpsimd
                def _(pool):
                    with pool.Fori(0, N_EXP // 2) as it:
                        for j in range(2):
                            pool.wait_ge(scat, it * 2 + (j + 1))
                            pool.tensor_copy(xs[j], xe[:, :, bass.ds(it * (2 * CAP) + j * CAP, CAP)]).then_inc(xset, 1)

                @block.tensor
                def _(pe):
                    pe.wait_ge(zeroed, 1)
                    for b in range(4):
                        ins = pe.matmul(ps[:, 4 + b, :], zero[:, 0:P], zero, start=True, stop=False, skip_group_check=True)
                    ins.then_inc(gkept, 1)

                    def gate_up(e, j, it):
                        pe.wait_ge(xset, e + 1)
                        pe.wait_ge(gkept, e + 1)
                        pe.wait_ge(ukept, e + 1)
                        for b in range(2):
                            pe.wait_ge(loaded[2 * j + b], it * 16 + 16)
                            for i in range(2):
                                for q in range(4):
                                    ins = pe.matmul(ps[q * CAP:(q + 1) * CAP, b, :], xs[j][:, 2 * q + i, :], mat[2 * j + b][:, 2 * q + i, :],
                                                    start=i == 0, stop=i == 1, skip_group_check=True)
                            ins.then_inc(qmade, 1)
                            pe.drain().then_inc(used[2 * j + b], 1)

                    def turn(e):
                        pe.wait_ge(gkept, e + 2)
                        pe.wait_ge(aready, e + 1)
                        for f in range(4):
                            pe.matmul(ps[:, 2, f * CAP:(f + 1) * CAP], gq[:, f * P:(f + 1) * P], stack, start=True, stop=True)
                        pe.wait_ge(ukept, e + 2)
                        for f in range(4):
                            ins = pe.matmul(ps[:, 2, (4 + f) * CAP:(5 + f) * CAP], uq[:, f * P:(f + 1) * P], stack, start=True, stop=True)
                        ins.then_inc(tmade, 1)

                    def down(e, j, it, h):
                        slot = 4 + j
                        if h == 0:
                            pe.wait_ge(aready, e + 2)
                            pe.wait_ge(loaded[slot], it * 16 + 16)
                        pe.wait_ge(dkept, 2 * e + h + 1)
                        for q in range(4):
                            ins = pe.matmul(ps[q * CAP:(q + 1) * CAP, 3, :], aT[:, q, :], mat[slot][:, q, h * 512:(h + 1) * 512],
                                            start=True, stop=True, skip_group_check=True)
                        ins.then_inc(dmade, 1)
                        if h == 1:
                            pe.drain().then_inc(used[slot], 1)

                    def scatter(e, sel):
                        pe.wait_ge(dkept, 2 * e + 3)
                        for o in range(KT):
                            ins = pe.matmul(acc(o), yq[:, o, :], sel, start=False, stop=False,
                                            skip_group_check=True)
                        ins.then_inc(scat, 1)

                    def expert_step(it, j, it_next):
                        e, jn = it * 2 + j, 1 - j
                        gate_up(it * 2 + (j + 1), jn, it_next)
                        down(e, j, it, 0)
                        down(e, j, it, 1)
                        turn(it * 2 + (j + 1))
                        scatter(e, selT[:, e, :] if isinstance(e, int) else selT[:, bass.ds(e, 1), :].rearrange("p o t -> p (o t)"))
                    gate_up(0, 0, 0)
                    turn(0)
                    with pe.Fori(0, last // 2) as it:
                        expert_step(it, 0, it)
                        expert_step(it, 1, it + 1)
                    expert_step(last // 2, 0, last // 2)
                    down(last, 1, last // 2, 0)
                    down(last, 1, last // 2, 1)
                    scatter(last, selT[:, last, :])
                    pe.wait_ge(zeroed, 2)
                    for b in range(4):
                        pe.matmul(ps[:, 4 + b, :], zero[:, 0:P], zero, start=False, stop=True, skip_group_check=True)

                @block.scalar
                def _(act):
                    act.sem_inc(dkept, 1)
                    act.wait_ge(gkept, 1)
                    act.wait_ge(qmade, 1)
                    act.activation(gq, ps[:, 0, :], ACT.Copy).then_inc(gkept, 1)
                    act.wait_ge(tmade, 1)
                    act.activation(gs, ps[:, 2, 0:4 * CAP], ACT.Silu).then_inc(silud, 1)

                    def keep_down(e):
                        act.wait_ge(scat, e + 1)
                        for h in range(2):
                            act.wait_ge(dmade, 2 * e + (h - 1))
                            act.activation(yq[:, 4 * h:4 * h + 4, :], ps[:, 3, :].rearrange("p (o c) -> p o c", c=P), ACT.Copy).then_inc(dkept, 1)
                    with act.Fori(1, N_EXP) as e:
                        act.wait_ge(qmade, 2 * e + 1)
                        act.activation(gq, ps[:, 0, :], ACT.Copy).then_inc(gkept, 1)
                        keep_down(e)
                        act.wait_ge(tmade, e + 1)
                        act.activation(gs, ps[:, 2, 0:4 * CAP], ACT.Silu).then_inc(silud, 1)
                    keep_down(N_EXP)

                @block.vector
                def _(dve):
                    dve.memset(zero, 0.0).then_inc(zeroed, 1)
                    dve.sem_inc(scat, 2)
                    dve.sem_inc(ukept, 1)
                    dve.sem_inc(aready, 1)
                    with dve.Fori(0, N_EXP) as e:
                        dve.wait_ge(qmade, 2 * e + 2)
                        dve.tensor_copy(uq, ps[:, 1, :]).then_inc(ukept, 1)
                        dve.wait_ge(silud, e + 1)
                        dve.tensor_tensor(aT.rearrange("p f s -> p (f s)"), gs, ps[:, 2, 4 * CAP:8 * CAP], ALU.mult).then_inc(aready, 1)
                    dve.wait_ge(tmade, N_EXP)
                    dve.memset(zero, 0.0).then_inc(zeroed, 1)
            with nc.Block() as block:
                @block.vector
                def _(dve):
                    for o in range(KT):
                        dve.scalar_tensor_tensor(self.xT[:, o, :], acc(o), self.mod1[:, 40 + o, 0:1], self.xT[:, o, :], ALU.mult, ALU.add)
                    dve.tensor_scalar(self.rank, self.rank, -float(CAP), None, ALU.add)
            nc.all_engine_barrier(sems_to_clear=range(FIRST_STAGE_SEM + first_sem, FIRST_STAGE_SEM + self.stage_sems))
        A = Arena(self.arena_t, self.work, self.A.end)
        xin, raw = A.take(2, D), A.take(KT, TOK)
        self.raw2 = raw
        S = lambda n: self.sem("context2_" + n)
        xl, turned = S("loaded"), S("turned")
        with nc.Block() as block:
            @block.sync
            def _(sp):
                for i in range(2):
                    sp.dma_start(xin[:, i, :], d["ctx_2"][0, i * P:(i + 1) * P, :]).then_inc(xl, 16)
                self.ring.send(sp, self.ends["experts1"] + 3)

        def turn_context(pe):
            pe.wait_ge(xl, 32)
            for k in range(KT):
                for i in range(2):
                    ins = pe.transpose(ps[:, 4 + k // 2, k % 2 * CTX + i * P:k % 2 * CTX + (i + 1) * P], xin[:, i, k * P:(k + 1) * P], self.ident)
                ins.then_inc(turned, 1)

        def keep_context(dve):
            self.gain(dve, self.gain2, self.mod2, "mix_pre")
            for b in range(4):
                dve.wait_ge(turned, 2 * b + 2)
                dve.tensor_copy(raw[:, 2 * b:2 * b + 2, 0:CTX], ps[:, 4 + b, :].rearrange("p (k t) -> p k t", k=2))

        def copy_latent(act, k):
            act.activation(raw[:, k, CTX:TOK], self.xT[:, k, :], ACT.Copy)
        self.norm_modulate("final", self.xT, self.xT, self.P_("final"), None, None, A,
                           pe_after=turn_context, dve_after=keep_context, act_each=copy_latent)
    def ssd_in(self):
        nc, d, ring, ps, hT = self.nc, self.d, self.ring, self.ps, self.hT
        A = Arena(self.arena_t, self.work, self.A.end)
        A.take(2, D)
        raw, rstd, sq = A.take(KT, TOK), A.take(TOK), A.take(KT, TOK)
        S = lambda n: self.sem("ssd_in_" + n)
        scaled = S("scaled")

        def scaling(dve):
            for k in range(KT):
                for v, (a, b) in enumerate(((CTX, TOK), (0, CTX))):
                    dve.scalar_tensor_tensor(hT[:, k, a:b], raw[:, k, a:b], self.gain2[:, k, v:v + 1], rstd[:, a:b],
                                             ALU.mult, ALU.mult).then_inc(scaled, 1)

        def shifting(act):
            for k in range(KT):
                for v, (a, b) in enumerate(((CTX, TOK), (0, CTX))):
                    act.wait_ge(scaled, 2 * k + v + 1)
                    act.activation(hT[:, k, a:b], hT[:, k, a:b], ACT.Identity, bias=self.mod2[:, k, v:v + 1])
        self.rms("mix_pre", raw, KT, TOK, rstd, sq, after=scaling, act_after=shifting)

        A = Arena(self.arena_t, self.work, self.A.end)
        self.s_lat = lat = A.take(20, SEQ)
        self.s_y = A.take(2, D_SSD)
        at = A.at
        rawc, rawl = A.take(16, CTX + 2), A.take(20, ROWS, GRID + 2)
        end = A.at
        A.at = at
        self.s_x, self.s_B = A.take(NC, D_SSD), A.take(NC, SSD_G * P)
        A.at = end
        self.s_ctx = ctx = A.take(16, CTX)
        self.s_H = A.take(2, 2, D_SSD)
        self.s_dt, self.s_dtA = A.take(NC, 2 * SSD_H), A.take(NC, 2 * SSD_H)
        self.s_area = A.at
        wdt, bdt, al, tmp = A.take(KT, 48), A.take(48), A.take(48), A.take(NC, 48)
        tap_done, sv, sa = S("tap_done"), S("dt_steps"), S("dt_functions")
        made, freed, small, zeroed, dmade = S("made"), S("freed"), S("small_loaded"), S("zeroed"), S("dt_made")
        rows = lambda a: a.rearrange("p (r c) -> p r c", c=GRID)
        with nc.Block() as block:
            @block.sync
            def _(sp):
                sp.dma_start(wdt, d["w_in_2"].rearrange("(k p) n -> p k n", p=P)[:, :, O_DT:O_DT + 48]).then_inc(small, 16)
                sp.dma_start(bdt, d["dt_bias_2"].rearrange("a b -> (a b)").partition_broadcast(P)).then_inc(small, 16)
                sp.dma_start(al, d["a_log_2"].rearrange("a b -> (a b)").partition_broadcast(P)).then_inc(small, 16)
                ring.send(sp, self.ends["xbc"] + 3)

            @block.gpsimd
            def _(pool):
                pool.memset(rawc, 0.0)
                pool.memset(rawl, 0.0).then_inc(zeroed, 1)

            @block.tensor
            def _(pe):
                n = self.products(pe, [self.feature_tiles(hT, 0, TOK)], made, freed)
                pe.wait_ge(small, 48)
                for c in range(NC):
                    for k in range(KT):
                        ins = pe.matmul(ps[:, 7, c * 48:(c + 1) * 48], hT[:, k, c * P:(c + 1) * P], wdt[:, k, :],
                                        start=k == 0, stop=k == KT - 1)
                ins.then_inc(dmade, 1)
                self.products(pe, [self.feature_tiles(hT, 0, TOK)] * 3 + [self.feature_tiles(hT, CTX, TOK)], made, freed, first=n)

            @block.scalar
            def _(act):
                act.wait_ge(small, 48)
                act.activation(al, al, ACT.Exp).then_inc(sa, 1)
                act.wait_ge(sv, 2)
                act.activation(tmp, tmp, ACT.Exp, scale=-1.0).then_inc(sa, 1)
                act.wait_ge(sa, 2)
                act.activation(tmp, tmp, ACT.Ln, bias=1.0).then_inc(sa, 1)
                for b in range(5):
                    act.wait_ge(tap_done, 3 * b + 3)
                    act.activation(lat[:, 4 * b:4 * b + 4, :], lat[:, 4 * b:4 * b + 4, :], ACT.Silu)
                    if b < 4:
                        act.activation(ctx[:, 4 * b:4 * b + 4, :], ctx[:, 4 * b:4 * b + 4, :], ACT.Silu)

            @block.vector
            def _(dve):
                w, bias = self.P_("cw2"), self.P_("cb2")

                def convolve(b):
                    dve.wait_ge(freed, 4 * b + 4)
                    todo = [(rows(lat[:, t, :]), lambda tap, t=t: rawl[:, t, :, tap:tap + GRID], t) for t in range(4 * b, 4 * b + 4)]
                    if b < 4:
                        todo += [(ctx[:, t, :], lambda tap, t=t: rawc[:, t, tap:tap + CTX], t) for t in range(4 * b, 4 * b + 4)]
                    for tap in range(3):
                        for dst, src, t in todo:
                            if tap == 0:
                                ins = dve.tensor_scalar(dst, src(tap), w[:, t:t + 1], bias[:, t:t + 1], ALU.mult, ALU.add)
                            else:
                                ins = dve.scalar_tensor_tensor(dst, src(tap), w[:, 20 * tap + t:20 * tap + t + 1], dst, ALU.mult, ALU.add)
                        ins.then_inc(tap_done, 1)
                        dve.wait_ge(tap_done, 3 * b + tap + 1)

                def time_steps():
                    dt = self.s_dt
                    dve.wait_ge(small, 48)
                    dve.wait_ge(dmade, 1)
                    dve.tensor_tensor(dt, ps[:, 7, 0:NC * 48].rearrange("p (c n) -> p c n", n=48),
                                      bcast(bdt.unsqueeze(1), [P, NC, 48]), ALU.add).then_inc(sv, 1)
                    dve.wait_ge(sv, 1)
                    dve.scalar_tensor_tensor(tmp, dt, -1.0, dt, ALU.mult, ALU.max).then_inc(sv, 1)
                    dve.wait_ge(sa, 3)
                    dve.scalar_tensor_tensor(dt, dt, 0.0, tmp, ALU.max, ALU.add).then_inc(sv, 1)
                    dve.wait_ge(sv, 3)
                    dve.scalar_tensor_tensor(self.s_dtA, dt, -1.0, bcast(al.unsqueeze(1), [P, NC, 48]), ALU.mult, ALU.mult)
                dve.wait_ge(zeroed, 1)
                for t in range(20):
                    dve.wait_ge(made, t + 1)
                    bank = ps[:, t % NBANK, :]
                    if t < 16:
                        dve.tensor_copy(rawc[:, t, 1:1 + CTX], bank[:, 0:CTX])
                    ins = dve.tensor_copy(rawl[:, t, :, 1:1 + GRID], rows(bank[:, CTX:TOK] if t < 16 else bank[:, 0:SEQ]))
                    ins.then_inc(freed, 1)
                    if t == 5:
                        time_steps()
                    if t % 4 == 1 and t > 4:
                        convolve(t // 4 - 1)
                convolve(4)
        t2, k2 = S("x_turned"), S("x_kept")
        with nc.Block() as block:
            @block.tensor
            def _(pe):
                for t in range(16):
                    if t >= 8:
                        pe.wait_ge(k2, t - 7)
                    for c in range(NC):
                        src = ctx[:, t, c * P:(c + 1) * P] if c < 2 else lat[:, t, (c - 2) * P:(c - 1) * P]
                        ins = pe.transpose(ps[:, t % 8, c * P:(c + 1) * P], src, self.ident)
                    ins.then_inc(t2, 1)

            @block.vector
            def _(dve):
                for t in range(16):
                    dve.wait_ge(t2, t + 1)
                    dst = self.s_x[:, :, t * P:(t + 1) * P] if t < 12 else self.s_B[:, :, (t - 12) * P:(t - 11) * P]
                    dve.tensor_copy(dst, ps[:, t % 8, :].rearrange("p (c f) -> p c f", c=NC)).then_inc(k2, 1)

    def ssd(self):
        nc, ps = self.nc, self.ps
        lat, y, x, Bt, H, dt, dtA = self.s_lat, self.s_y, self.s_x, self.s_B, self.s_H, self.s_dt, self.s_dtA
        free = self.s_ctx.rearrange("p t c -> p (t c)")
        xw = [free[:, i * D_SSD:(i + 1) * D_SSD] for i in range(2)]
        xdt = xw
        CB = free[:, 2 * D_SSD:2 * D_SSD + 1024].rearrange("p (d g t) -> p d g t", d=2, g=4)
        A = Arena(self.arena_t, self.s_area, self.A.end)
        ex, wt = A.take(2, 6, SSD_H), A.take(2, 3, SSD_H)
        old = self.silu_c.rearrange("p b k v -> p (b k v)")[:, 0:3 * P].rearrange("p (h t) -> p h t", h=3)
        R = [old, A.take(3, P)]
        E = [A.take(3, P) for _ in range(2)]
        Pm = [A.take(3, P), self.hT[:, 0:3, P:2 * P]]
        S = lambda n: self.sem("ssd_" + n)
        sel = self.k_sel.rearrange("p (d n) -> p d n", d=2)
        rest = [sel[:, dr, (LEVELS + 1) * P:(LEVELS + 2) * P] for dr in range(2)]
        incl = [sel[:, dr, LEVELS * P:(LEVELS + 1) * P] for dr in range(2)]
        hd = lambda a, h: a.rearrange("p (h v) -> p h v", h=h)
        dsum, dexp, wts = S("decay_sums"), S("decays"), S("weights")
        with nc.Block() as block:
            @block.tensor
            def _(pe):
                for dr in range(2):
                    o0, o1, o2, o3 = ORDER[dr]
                    da = lambda c: dtA[:, c, dr * SSD_H:(dr + 1) * SSD_H]
                    out = lambda i: ps[:, 0, (dr * 6 + i) * SSD_H:(dr * 6 + i + 1) * SSD_H]
                    pe.matmul(out(0), rest[dr], da(o0), start=True, stop=False)
                    pe.matmul(out(0), self.ones, da(o1), start=False, stop=True)
                    pe.matmul(out(1), rest[dr], da(o1), start=True, stop=True)
                    pe.matmul(out(2), rest[dr], da(o2), start=True, stop=True)
                    pe.matmul(out(3), self.ones, da(o2), start=True, stop=True)
                    for c in range(2):
                        ins = pe.matmul(out(4 + c), incl[dr], da(2 + c), start=True, stop=True)
                ins.then_inc(dsum, 1)

            @block.scalar
            def _(act):
                act.wait_ge(dsum, 1)
                act.activation(ex.rearrange("p a b c -> p (a b c)"),
                               ps[:, 0, 0:12 * SSD_H], ACT.Exp).then_inc(dexp, 1)

            @block.vector
            def _(dve):
                dve.wait_ge(dexp, 1)
                for dr in range(2):
                    for i in range(3):
                        dve.tensor_tensor(wt[:, dr, i, :], ex[:, dr, i, :], dt[:, ORDER[dr][i], dr * SSD_H:(dr + 1) * SSD_H], ALU.mult)
        xmade, smade, skept = S("x_weighted"), S("states_made"), S("states_kept")
        jobs = [(dr, i) for dr in range(2) for i in range(3)]
        with nc.Block() as block:
            @block.tensor
            def _(pe):
                for n, (dr, i) in enumerate(jobs):
                    c = ORDER[dr][i]
                    pe.wait_ge(xmade, n + 1)
                    if dr == 1 and i == 0:
                        pe.wait_ge(skept, 1)
                    if dr == 1 and i == 2:
                        pe.wait_ge(skept, 2)
                    for g in range(SSD_G):
                        ins = pe.matmul(ps[:, (4 if i == 2 else 0) + g, 0:384], Bt[:, c, g * P:(g + 1) * P],
                                        xw[n % 2][:, g * 384:(g + 1) * 384], start=i != 1, stop=i != 0)
                    ins.then_inc(smade, 1)

            @block.vector
            def _(dve):
                def weigh(n):
                    dr, i = jobs[n]
                    if n >= 2:
                        dve.wait_ge(smade, n - 1)
                    dve.tensor_tensor(hd(xw[n % 2], SSD_H), hd(x[:, ORDER[dr][i], :], SSD_H),
                                      bcast(wt[:, dr, i, :].unsqueeze(2), [P, SSD_H, HP]), ALU.mult).then_inc(xmade, 1)

                def keep(dr):
                    four = lambda a: a.rearrange("p (g n) -> p g n", g=4)
                    dve.wait_ge(smade, 3 * dr + 2)
                    dve.tensor_copy(four(H[:, dr, 0, :]), ps[:, 0:4, 0:384]).then_inc(skept, 1)
                    dve.wait_ge(skept, 2 * dr + 1)
                    dve.tensor_tensor(hd(H[:, dr, 1, :], SSD_H), hd(H[:, dr, 0, :], SSD_H),
                                      bcast(ex[:, dr, 3, :].unsqueeze(2), [P, SSD_H, HP]), ALU.mult).then_inc(wts, 1)
                    dve.wait_ge(wts, dr + 1)
                    dve.wait_ge(smade, 3 * dr + 3)
                    dve.tensor_tensor(four(H[:, dr, 1, :]), four(H[:, dr, 1, :]), ps[:, 4:8, 0:384], ALU.add).then_inc(skept, 1)
                for n in range(6):
                    weigh(n)
                    if n == 3:
                        keep(0)
                keep(1)

        cbm, cbk, xd = S("cb_made"), S("cb_kept"), S("x_scaled")
        rmade, dmade, emade, pmade, ymade = S("selectors"), S("exponents"), S("exped"), S("weighted"), S("diagonal_made")
        omade, okept, oscaled, yk = S("offsets_made"), S("offsets_kept"), S("offsets_scaled"), S("y_kept")
        tmp = [self.hT[:, 0:6, HP * i:HP * (i + 1)] for i in range(2)]
        units = [(c, hb, dr) for c in range(2) for hb in range(8) for dr in range(2)]
        with nc.Block() as block:
            @block.tensor
            def _(pe):
                def exponents(i):
                    pe.wait_ge(rmade, i + 1)
                    if i >= 2:
                        pe.wait_ge(emade, i - 1)
                    pe.matmul(ps[:, 3 + i % 2, 0:384], rest[units[i][2]], R[i % 2].rearrange("p h t -> p (h t)"),
                              start=True, stop=True).then_inc(dmade, 1)

                def diagonal(i):
                    c, hb, _ = units[i]
                    pe.wait_ge(pmade, i + 1)
                    for h in range(3):
                        for dr in range(2):
                            col = (hb * 3 + h) * HP
                            ins = pe.matmul(ps[:, col // 512, col % 512:col % 512 + HP], Pm[dr][:, h, :],
                                            xdt[dr][:, col:col + HP], start=dr == 0, stop=dr == 1)
                    ins.then_inc(ymade, 1)
                for c in range(2):
                    for dr in range(2):
                        n = 2 * c + dr
                        if n >= 1:
                            pe.wait_ge(cbk, n)
                        for g in range(4):
                            ins = pe.matmul(ps[:, 5, g * P:(g + 1) * P], lat[:, 12 + g, c * P:(c + 1) * P],
                                            lat[:, 16 + g, c * P:(c + 1) * P], start=True, stop=True)
                        ins.then_inc(cbm, 1)
                    for n in range(8):
                        dr, g = divmod(n, 4)
                        m = 8 * c + n
                        if m >= 2:
                            pe.wait_ge(oscaled, m - 1)
                        which = int(2 + c == ORDER[dr][3])
                        pe.matmul(ps[:, 6 + m % 2, 0:384], lat[:, 16 + g, c * P:(c + 1) * P],
                                  H[:, dr, which, g * 384:(g + 1) * 384], start=True, stop=True).then_inc(omade, 1)
                    if c == 1:
                        pe.wait_ge(yk, 1)
                    for i in range(16 * c, 16 * c + 17):
                        if i < 16 * c + 16:
                            exponents(i)
                        if i > 16 * c and (i - 1) % 2 == 1:
                            diagonal(i - 1)

            @block.gpsimd
            def _(pool):
                for i, (c, hb, dr) in enumerate(units):
                    if i >= 2:
                        pool.wait_ge(dmade, i - 1)
                    h = dr * SSD_H + hb * 3
                    pool.tensor_tensor(R[i % 2], bcast(incl[dr].unsqueeze(1), [P, 3, P]),
                                       bcast(dtA[:, 2 + c, h:h + 3].unsqueeze(2), [P, 3, P]), ALU.mult).then_inc(rmade, 1)

            @block.scalar
            def _(act):
                for i in range(len(units)):
                    act.wait_ge(dmade, i + 1)
                    if i >= 2:
                        act.wait_ge(pmade, i - 1)
                    act.activation(E[i % 2].rearrange("p h t -> p (h t)"), ps[:, 3 + i % 2, 0:384], ACT.Exp).then_inc(emade, 1)

            @block.vector
            def _(dve):
                for c in range(2):
                    for dr in range(2):
                        dve.wait_ge(cbm, 2 * c + dr + 1)
                        if c == 1:
                            dve.wait_ge(ymade, 8)
                        dve.tensor_tensor(CB[:, dr], ps[:, 5, :].rearrange("p (g t) -> p g t", g=4),
                                          bcast(incl[dr].unsqueeze(1), [P, 4, P]), ALU.mult).then_inc(cbk, 1)
                        dve.tensor_tensor(hd(xdt[dr], SSD_H), hd(x[:, 2 + c, :], SSD_H),
                                          bcast(dt[:, 2 + c, dr * SSD_H:(dr + 1) * SSD_H].unsqueeze(2), [P, SSD_H, HP]), ALU.mult)
                    for n in range(8):
                        dr, g = divmod(n, 4)
                        m = 8 * c + n
                        dve.wait_ge(omade, m + 1)
                        ysl = y[:, c, g * 384:(g + 1) * 384]
                        dst = hd(ysl, 6) if dr == 0 else tmp[m % 2]
                        dve.tensor_tensor(dst, hd(ps[:, 6 + m % 2, 0:384], 6),
                                          bcast(ex[:, dr, 4 + c, g * 6:(g + 1) * 6].unsqueeze(2), [P, 6, HP]), ALU.mult).then_inc(oscaled, 1)
                        if dr == 1:
                            dve.wait_ge(oscaled, m + 1)
                            dve.tensor_tensor(hd(ysl, 6), hd(ysl, 6), tmp[m % 2], ALU.add).then_inc(okept, 1)
                    dve.wait_ge(cbk, 2 * c + 2)
                    for i in range(16 * c, 16 * c + 16):
                        _, hb, dr = units[i]
                        dve.wait_ge(emade, i + 1)
                        if i >= 2:
                            dve.wait_ge(ymade, i // 2)
                        dve.tensor_tensor(Pm[dr], E[i % 2], bcast(CB[:, dr, hb // 2, :].unsqueeze(1), [P, 3, P]), ALU.mult).then_inc(pmade, 1)
                    dve.wait_ge(ymade, 8 * c + 8)
                    dve.wait_ge(okept, 4 * c + 4)
                    dve.tensor_tensor(y[:, c, :], y[:, c, :], ps[:, 0:3, :].rearrange("p b n -> p (b n)"), ALU.add).then_inc(yk, 1)

    def ssd_out(self):
        nc, d, ring, ps, hT = self.nc, self.d, self.ring, self.ps, self.hT
        lat, y = self.s_lat, self.s_y
        A = Arena(self.arena_t, self.work + 20 * SEQ + 2 * D_SSD, self.A.end)
        self.m_f, self.m_y, self.m_g = A.take(4, SEQ), A.take(12, SEQ), A.take(16, SEQ)
        self.merge_area = A.at
        uT, zT, sq, rstd = A.take(4, SEQ), A.take(12, SEQ), A.take(12, SEQ), A.take(SEQ)
        F1 = A.take(2, 4, SEQ)
        dftw, dftl, dsk, skips = A.take(2 * P), A.take(2, 2 * SEQ), A.take(12), A.take(SSD_H)
        spread = self.sem("skips_spread")
        S = lambda n: self.sem("ssd_out_" + n)
        made, freed, small = S("made"), S("freed"), S("tables_loaded")
        turned, kept, f1, f1k, f2 = S("y_turned"), S("y_kept"), S("width_made"), S("width_kept"), S("length_made")
        with nc.Block() as block:
            @block.sync
            def _(sp):
                sp.dma_start(dftw, d["k_dftw"]).then_inc(small, 16)
                sp.dma_start(dftl, d["k_dftl"].rearrange("(c p) n -> p c n", p=P)).then_inc(small, 16)
                sp.dma_start(skips, d["d_skip_2"].partition_broadcast(P)).then_inc(small, 16)
                ring.send(sp, self.ends["rest2"] + 3)

            @block.tensor
            def _(pe):
                self.products(pe, [self.feature_tiles(hT, CTX, TOK)] * 8, made, freed)
                pe.wait_ge(freed, 32)
                for t in range(12):
                    if t >= 8:
                        pe.wait_ge(kept, t - 7)
                    for c in range(2):
                        ins = pe.transpose(ps[:, t % 8, c * P:(c + 1) * P], y[:, c, t * P:(t + 1) * P], self.ident)
                    ins.then_inc(turned, 1)

            @block.scalar
            def _(act):
                for t in range(32):
                    act.wait_ge(made, t + 1)
                    bank = ps[:, t % NBANK, 0:SEQ]
                    if t < 4:
                        ins = act.activation(uT[:, t, :], bank, ACT.Copy)
                    elif t < 16:
                        ins = act.activation(zT[:, t - 4, :], bank, ACT.Silu)
                    else:
                        ins = act.activation(self.m_g[:, t - 16, :], bank, ACT.Sigmoid, bias=self.P_("b_gate")[:, t - 16:t - 15])
                    ins.then_inc(freed, 1)

            @block.vector
            def _(dve):
                dve.wait_ge(small, 48)
                for two in range(2):
                    half = slice(two * HP, (two + 1) * HP)
                    dve.tensor_copy(dsk[half, :], skips[half, :].rearrange("p (i two) -> p i two", two=2)[:, :, two]).then_inc(spread, 1)
                dve.wait_ge(spread, 2)
                dve.wait_ge(freed, 32)
                for t in range(12):
                    dve.wait_ge(turned, t + 1)
                    dve.scalar_tensor_tensor(self.m_y[:, t, :], lat[:, t, :], dsk[:, t:t + 1], ps[:, t % 8, 0:SEQ],
                                             ALU.mult, ALU.add).then_inc(kept, 1)
                dve.wait_ge(kept, 12)
                dve.tensor_tensor(self.m_y, self.m_y, zT, ALU.mult)
        self.rms("ssd_norm", self.m_y, 12, SEQ, rstd, sq)
        with nc.Block() as block:
            @block.vector
            def _(dve):
                for t in range(12):
                    dve.scalar_tensor_tensor(self.m_y[:, t, :], self.m_y[:, t, :], self.P_("ssd_g")[:, t:t + 1], rstd, ALU.mult, ALU.mult)
                for g in range(4):
                    dve.wait_ge(f2, g + 1)
                    dve.tensor_copy(self.m_f[:, g, :], ps[:, 4 + g, 0:SEQ])

            @block.tensor
            def _(pe):
                for c in range(2):
                    for g in range(4):
                        ins = pe.matmul(ps[:, c * 2 + g // 2, g % 2 * SEQ:(g % 2 + 1) * SEQ], uT[:, g, c * P:(c + 1) * P], dftw,
                                        start=True, stop=True)
                    ins.then_inc(f1, 1)
                pe.wait_ge(f1k, 2)
                for g in range(4):
                    for n in range(4):
                        c, part = divmod(n, 2)
                        ins = pe.matmul(ps[:, 4 + g, 0:SEQ], F1[:, c, g, part * P:(part + 1) * P], dftl[:, c, part * SEQ:(part + 1) * SEQ],
                                        start=n == 0, stop=n == 3)
                    ins.then_inc(f2, 1)

            @block.scalar
            def _(act):
                for c in range(2):
                    act.wait_ge(f1, c + 1)
                    act.activation(F1[:, c].rearrange("p g n -> p (g n)"), ps[:, 2 * c:2 * c + 2, :].rearrange("p b n -> p (b n)"),
                                   ACT.Copy).then_inc(f1k, 1)

    def merge2(self):
        A = Arena(self.arena_t, self.merge_area, self.A.end)
        y, mix, t2 = A.take(KT, SEQ), A.take(KT, SEQ), [A.take(SEQ) for _ in range(2)]
        first = [(lambda w, k, j=j: w[:, k, j * P:(j + 1) * P], lambda w, k: self.m_f[:, k, :], SEQ, 4) for j in range(8)]
        second = [(lambda w, k, j=j: w[:, k, j * P:(j + 1) * P], lambda w, k: self.m_y[:, k, :], SEQ, 12) for j in range(2)]
        self.merge_out("merge2", [first] + [second] * 4, [self.m_g[:, 0:8, :], self.m_g[:, 8:16, :]], y, t2,
                       self.ends["experts2"], store=mix)
        self.add_normed("mix_post", mix, self.P_("mix_post"), self.mod2[:, 16:24, 0], A)

    def add_normed(self, name, src, gain, gate, A):
        rstd, sq, g = A.take(SEQ), A.take(KT, SEQ), A.take(KT)
        gained, scaled = self.sem(name + "_gain"), self.sem(name + "_scaled")

        def adding(dve):
            dve.wait_ge(gained, 1)
            for k in range(KT):
                dve.scalar_tensor_tensor(src[:, k, :], src[:, k, :], g[:, k:k + 1], rstd, ALU.mult, ALU.mult).then_inc(scaled, 1)
            for k in range(KT):
                dve.wait_ge(scaled, k + 1)
                dve.tensor_tensor(self.xT[:, k, :], self.xT[:, k, :], src[:, k, :], ALU.add)
        self.rms(name, src, KT, SEQ, rstd, sq, before=lambda dve: dve.tensor_tensor(g, gain, gate, ALU.mult).then_inc(gained, 1),
                 after=adding)

    def route2(self):
        nc, d, ps = self.nc, self.d, self.ps
        self.h2 = self.hT[:, :, 0:SEQ]
        A = Arena(self.arena_t, self.work, self.A.end)
        E2, n = N_EXP2, N_EXP2 * CAP
        at = A.at
        self.xe = A.take(KT, n)
        self.selT = A.take(E2, SEQ)
        self.more_slots = [A.take(4096) for _ in range(3)]
        self.ahead = self.lasting_sem("expert_ahead")
        src = self.experts2()
        self.moe_area = A.at
        wr, iota, rows = A.take(KT, E2), A.take(CAP), A.take(E2 * P)
        early = Arena(self.arena_t, at, at + 8192)
        self.norm_modulate("ffn_pre", self.xT, self.h2, self.P_("ffn_pre"), self.mod2[:, 32:40, 0], self.mod2[:, 24:32, 0], early)
        early.at = at
        lg, aff, top = A.take(2, E2), A.take(2, E2), A.take(2)
        affT = A.take(SEQ)
        G = A.take(E2, SEQ)
        T, U, every, ahead = early.take(4, SEQ), early.take(4, SEQ), early.take(SEQ), early.take(2, SEQ)
        rank, ties = A.take(2, E2), A.take(2, E2)
        sel = A.take(2, n)
        h_tok = lambda c, k: self.hT[:, k, CTX + c * P:CTX + (c + 1) * P]
        S = lambda n_: self.sem("route2_" + n_)
        loaded, lmade, st, sa = S("loaded"), S("logits_made"), S("logits_shifted"), S("exped")
        amade, aturned, akept, bmade = S("affinities"), S("affinities_turned"), S("rows_kept"), S("rows_spread")
        masked, counted = S("masks_set"), S("tokens_counted")
        hturned, hkept = S("h_turned"), S("h_kept")
        vs = self.vs
        do = lambda dve, ins: vs.do(dve, ins)
        with nc.Block() as block:
            @block.sync
            def _(sp):
                sp.dma_start(wr, d["w_router_2"].rearrange("(k p) n -> p k n", p=P)).then_inc(loaded, 16)
                sp.dma_start(iota, d["k_iota"][:, 0:CAP]).then_inc(loaded, 16)
                sp.dma_start(rows[0:E2], d["k_rows16"]).then_inc(loaded, 16)
                for m, i in zip(self.more_slots, (4, 2, 5)):
                    sp.dma_start(m.rearrange("p (k c) -> p k c", c=512), src[i][0]).then_inc(self.ahead, 16)
                sp.wait_ge(loaded, 48)

            @block.tensor
            def _(pe):
                pe.wait_ge(loaded, 48)
                for c in range(2):
                    for k in range(KT):
                        ins = pe.matmul(ps[:, c, 0:E2], self.h2[:, k, c * P:(c + 1) * P], wr[:, k, :], start=k == 0, stop=k == KT - 1)
                ins.then_inc(lmade, 1)
                for k in range(KT):
                    if k >= 4:
                        pe.wait_ge(hkept, k - 3)
                    for c in range(2):
                        ins = pe.transpose(ps[:, 4 + k % 4, c * P:(c + 1) * P], self.h2[:, k, c * P:(c + 1) * P], self.ident)
                    ins.then_inc(hturned, 1)
                pe.wait_ge(amade, 1)
                for c in range(2):
                    ins = pe.transpose(ps[0:E2, 2, c * P:(c + 1) * P], aff[:, c, :], self.ident)
                ins.then_inc(aturned, 1)
                pe.wait_ge(akept, 1)
                pe.wait_ge(hkept, 8)
                for i in range(E2 // 2):
                    if i >= 4:
                        pe.wait_ge(counted, 4 * (i - 3))
                    for j in range(2):
                        e = 2 * i + j
                        ins = pe.matmul(ps[:, 4 + i % 4, j * SEQ:(j + 1) * SEQ], rows[0:E2, e * P:(e + 1) * P], affT[0:E2, :],
                                        start=True, stop=True)
                    ins.then_inc(bmade, 1)

            @block.scalar
            def _(act):
                for k in range(KT):
                    act.wait_ge(hturned, k + 1)
                    act.activation(self.hT[:, k, CTX:TOK], ps[:, 4 + k % 4, 0:SEQ], ACT.Copy).then_inc(hkept, 1)
                act.wait_ge(st, 1)
                act.activation(aff, lg, ACT.Exp).then_inc(sa, 1)

            @block.gpsimd
            def _(pool):
                later = self.k_sel[:, (LEVELS + 1) * P:(LEVELS + 2) * P]
                pool.memset(every, 1.0).then_inc(masked, 1)
                pool.memset(ahead[:, 0, P:SEQ], 0.0)
                pool.memset(ahead[:, 1, 0:P], 1.0).then_inc(masked, 1)
                for c in range(2):
                    pool.tensor_copy(ahead[:, c, c * P:(c + 1) * P], later).then_inc(masked, 1)

            @block.vector
            def _(dve):
                bc = lambda a: bcast(a.unsqueeze(2), [P, 2, E2])
                dve.wait_ge(lmade, 1)
                do(dve, dve.reduce_max(top, ps[:, 0:2, 0:E2], axis=AX.X))
                dve.tensor_tensor(lg, ps[:, 0:2, 0:E2], bc(top), ALU.subtract).then_inc(st, 1)
                dve.wait_ge(sa, 1)
                do(dve, dve.reduce_sum(top, aff, axis=AX.X))
                do(dve, dve.reciprocal(top, top))
                dve.tensor_tensor(aff, aff, bc(top), ALU.mult).then_inc(amade, 1)
                dve.wait_ge(aturned, 1)
                dve.tensor_copy(affT[0:E2, :], ps[0:E2, 2, 0:SEQ]).then_inc(akept, 1)
                dve.wait_ge(amade, 1)
                dve.wait_ge(masked, 4)
                for e in range(E2):
                    dve.wait_ge(bmade, e // 2 + 1)
                    row = ps[:, 4 + e // 2 % 4, e % 2 * SEQ:(e % 2 + 1) * SEQ]
                    for c in range(2):
                        own, junk = aff[:, c, e:e + 1], T[:, 2 * (e % 2) + c, :]
                        if e >= 2:
                            dve.wait_ge(counted, 2 * e + c - 3)
                        dve.scalar_tensor_tensor(junk, row, own, every, ALU.is_gt, ALU.mult, accum_out=rank[:, c, e:e + 1])
                        ins = dve.scalar_tensor_tensor(U[:, 2 * (e % 2) + c, :], row, own, ahead[:, c, :], ALU.is_equal, ALU.mult,
                                                       accum_out=ties[:, c, e:e + 1])
                        ins.then_inc(counted, 1)
                dve.wait_ge(counted, 2 * E2)
                do(dve, dve.tensor_tensor(rank, rank, ties, ALU.add))
                for c in range(2):
                    do(dve, dve.tensor_tensor(sel[:, c, :].rearrange("p (e s) -> p e s", s=CAP),
                                              bcast(iota[:, 0:CAP].unsqueeze(1), [P, E2, CAP]),
                                              bcast(rank[:, c, :].unsqueeze(2), [P, E2, CAP]), ALU.is_equal))
        selw = G.rearrange("p e t -> p (e t)").rearrange("p (c e r s) -> p c e r s", c=2, e=E2, r=4)
        wset, xmade, xkept, tmade, tkept = S("selection_weighted"), S("xe_made"), S("xe_kept"), S("sel_turned"), S("sel_kept")
        with nc.Block() as block:
            @block.vector
            def _(dve):
                for c in range(2):
                    for r in range(4):
                        ins = dve.tensor_tensor(selw[:, c, :, r, :], sel[:, c, :].rearrange("p (e s) -> p e s", s=CAP),
                                                bcast(aff[:, c, :].unsqueeze(2), [P, E2, CAP]), ALU.mult)
                ins.then_inc(wset, 1)
                for i in range(E2 // 2):
                    dve.wait_ge(tmade, i + 1)
                    dve.tensor_copy(self.selT[:, 2 * i:2 * i + 2, :], ps[:, 4 + i % 4, :].rearrange("p (a t) -> p a t", a=2)).then_inc(tkept, 1)

            @block.scalar
            def _(act):
                for k in range(KT):
                    act.wait_ge(xmade, k + 1)
                    act.activation(self.xe[:, k, :], ps[:, k % 4, :], ACT.Copy).then_inc(xkept, 1)

            @block.tensor
            def _(pe):
                for k in range(KT):
                    if k >= 4:
                        pe.wait_ge(xkept, k - 3)
                    for c in range(2):
                        ins = pe.matmul(ps[:, k % 4, :], h_tok(c, k), sel[:, c, :], start=c == 0, stop=c == 1)
                    ins.then_inc(xmade, 1)
                pe.wait_ge(wset, 1)
                for i in range(E2 // 2):
                    if i >= 4:
                        pe.wait_ge(tkept, i - 3)
                    for j in range(2):
                        for c in range(2):
                            ins = pe.transpose(ps[:, 4 + i % 4, j * SEQ + c * P:j * SEQ + (c + 1) * P],
                                               selw[:, c, 2 * i + j, :, :].rearrange("p r s -> p (r s)"), self.ident)
                    ins.then_inc(tmade, 1)

    def experts2(self):
        return [self.d[f"w_e_{w}_2"].rearrange("e (k p) f -> e p k f", p=P)[:, :, :, 512 * h:512 * h + 512]
                for h in range(2) for w in ("gate", "up", "down")]

    def moe2(self):
        nc, d, ps = self.nc, self.d, self.ps
        A = Arena(self.arena_t, self.moe_area, self.A.end)
        F_G0, F_U0, F_D0, F_G1, F_U1, F_D1 = range(6)
        xs = [A.take(KT, CAP) for _ in range(2)]
        stack = self.stack
        gq, uq, yq = A.take(512), A.take(512), A.take(2, 512)
        gs = A.take(4 * CAP)
        aT = A.take(2, 4, CAP)
        zero = A.take(512)
        S = lambda n: self.sem("moe2_" + n)
        loaded, used = [S(f"loaded{i}") for i in range(6)], [S(f"used{i}") for i in range(6)]
        xset, qmade, gkept, ukept = S("x_set"), S("quarters_made"), S("gate_kept"), S("up_kept")
        tmade, silud, aready, dmade, dkept, zeroed = (S("turned"), S("silu_made"), S("hidden_ready"), S("down_made"),
                                                      S("down_kept"), S("zeroed"))
        scat = S("scattered")
        src = self.experts2()
        mat = [None] * 6
        acc = lambda o: ps[:, 4 + o // 2, o % 2 * SEQ:(o % 2 + 1) * SEQ]
        last = N_EXP2 - 1
        with nc.Block() as block:
            @block.sync
            def _(sp):
                def load(i, e):
                    sp.wait_ge(used[i], e)
                    sp.dma_start(mat[i], src[i][bass.ds(e, 1)].rearrange("o p k f -> p (o k) f")).then_inc(loaded[i], 16)
                mat[F_G0], mat[F_U0], mat[F_G1] = [s.rearrange("p (k c) -> p k c", c=512) for s in self.ring.hand_over(sp)]
                mat[F_U1], mat[F_D0], mat[F_D1] = [s.rearrange("p (k c) -> p k c", c=512) for s in self.more_slots]
                sp.wait_ge(self.ahead, 48)
                for i in range(6):
                    sp.sem_inc(loaded[i], 16)
                for i in (F_G0, F_U0, F_G1, F_U1):
                    load(i, 1)
                with sp.Fori(2, N_EXP2) as e:
                    for i in (F_G0, F_U0, F_D0, F_D1, F_G1, F_U1):
                        load(i, e - 1 if i in (F_D0, F_D1) else e)
                for i in (F_D0, F_D1):
                    load(i, last)

            @block.gpsimd
            def _(pool):
                with pool.Fori(0, N_EXP2 // 2) as it:
                    for j in range(2):
                        pool.wait_ge(scat, it * 2 + (j + 1))
                        pool.tensor_copy(xs[j], self.xe[:, :, bass.ds(it * (2 * CAP) + j * CAP, CAP)]).then_inc(xset, 1)

            def quarters(pe, out, lhsT, w):
                for i in range(2):
                    for q in range(4):
                        k = 2 * q + i
                        ins = pe.matmul(ps[q * CAP:(q + 1) * CAP, out, :], lhsT(k), w[:, k, :], start=i == 0, stop=i == 1,
                                        skip_group_check=True)
                return ins

            @block.tensor
            def _(pe):
                pe.wait_ge(zeroed, 1)
                for b in range(4):
                    pe.matmul(ps[:, 4 + b, :], zero[:, 0:P], zero, start=True, stop=False, skip_group_check=True)

                def gate_up(e, par, h):
                    if h == 0:
                        pe.wait_ge(xset, e + 1)
                    pe.wait_ge(gkept, 2 * e + h + 1)
                    pe.wait_ge(ukept, 2 * e + h + 1)
                    for b, slot in ((0, (F_G0, F_G1)[h]), (1, (F_U0, F_U1)[h])):
                        pe.wait_ge(loaded[slot], 16 * e + 16)
                        quarters(pe, b, lambda k: xs[par][:, k, :], mat[slot]).then_inc(qmade, 1)
                        pe.drain().then_inc(used[slot], 1)

                def turn(e, h):
                    pe.wait_ge(gkept, 2 * e + h + 2)
                    pe.wait_ge(aready, 2 * e + h + 1)
                    for f in range(4):
                        pe.matmul(ps[:, 2, f * CAP:(f + 1) * CAP], gq[:, f * P:(f + 1) * P], stack, start=True, stop=True)
                    pe.wait_ge(ukept, 2 * e + h + 2)
                    for f in range(4):
                        ins = pe.matmul(ps[:, 2, (4 + f) * CAP:(5 + f) * CAP], uq[:, f * P:(f + 1) * P], stack, start=True, stop=True)
                    ins.then_inc(tmade, 1)

                def down(e, h):
                    slot = (F_D0, F_D1)[h]
                    if h == 0:
                        pe.wait_ge(aready, 2 * e + 3)
                    pe.wait_ge(loaded[slot], 16 * e + 16)
                    pe.wait_ge(dkept, 2 * e + h + 1)
                    quarters(pe, 3, lambda k: aT[:, k // 4, k % 4, :], mat[slot]).then_inc(dmade, 1)
                    pe.drain().then_inc(used[slot], 1)

                def scatter(e, sel):
                    pe.wait_ge(dkept, 2 * e + 3)
                    for o in range(KT):
                        ins = pe.matmul(acc(o), yq[:, o // 4, o % 4 * P:(o % 4 + 1) * P], sel, start=False, stop=False,
                                        skip_group_check=True)
                    ins.then_inc(scat, 1)
                selT = lambda e: self.selT[:, bass.ds(e, 1), :].rearrange("p o t -> p (o t)")
                for h in range(2):
                    gate_up(0, 0, h)
                    turn(0, h)
                with pe.Fori(0, last // 2) as it:
                    for j in range(2):
                        e = it * 2 + j
                        gate_up(it * 2 + (j + 1), (j + 1) % 2, 0)
                        down(e, 0)
                        down(e, 1)
                        turn(it * 2 + (j + 1), 0)
                        gate_up(it * 2 + (j + 1), (j + 1) % 2, 1)
                        scatter(e, selT(e))
                        turn(it * 2 + (j + 1), 1)
                gate_up(last, 1, 0)
                down(last - 1, 0)
                down(last - 1, 1)
                turn(last, 0)
                gate_up(last, 1, 1)
                scatter(last - 1, self.selT[:, last - 1, :])
                turn(last, 1)
                down(last, 0)
                down(last, 1)
                scatter(last, self.selT[:, last, :])
                for b in range(4):
                    pe.matmul(ps[:, 4 + b, :], zero[:, 0:P], zero, start=False, stop=True, skip_group_check=True)

            @block.scalar
            def _(act):
                act.sem_inc(gkept, 1)
                act.sem_inc(dkept, 1)
                def gates(e, h):
                    act.wait_ge(qmade, 4 * e + 2 * h + 1)
                    act.activation(gq, ps[:, 0, :], ACT.Copy).then_inc(gkept, 1)
                    act.wait_ge(tmade, 2 * e + h + 1)
                    act.activation(gs, ps[:, 2, 0:4 * CAP], ACT.Silu).then_inc(silud, 1)

                def keep_down(e):
                    for h in range(2):
                        act.wait_ge(dmade, 2 * e + h + 1)
                        act.activation(yq[:, h, :], ps[:, 3, :], ACT.Copy).then_inc(dkept, 1)
                gates(0, 0)
                gates(0, 1)
                with act.Fori(1, N_EXP2) as e:
                    act.wait_ge(qmade, 4 * e + 1)
                    act.activation(gq, ps[:, 0, :], ACT.Copy).then_inc(gkept, 1)
                    act.wait_ge(scat, e + 1)
                    keep_down(e - 1)
                    act.wait_ge(tmade, 2 * e + 1)
                    act.activation(gs, ps[:, 2, 0:4 * CAP], ACT.Silu).then_inc(silud, 1)
                    gates(e, 1)
                act.wait_ge(scat, last + 2)
                keep_down(last)

            @block.vector
            def _(dve):
                dve.memset(zero, 0.0).then_inc(zeroed, 1)
                dve.sem_inc(scat, 2)
                dve.sem_inc(ukept, 1)
                dve.sem_inc(aready, 1)
                with dve.Fori(0, N_EXP2) as e:
                    for h in range(2):
                        dve.wait_ge(qmade, 4 * e + (2 * h + 2))
                        dve.tensor_copy(uq, ps[:, 1, :]).then_inc(ukept, 1)
                        dve.wait_ge(silud, 2 * e + (h + 1))
                        dve.tensor_tensor(aT[:, h].rearrange("p f s -> p (f s)"), gs, ps[:, 2, 4 * CAP:8 * CAP], ALU.mult).then_inc(aready, 1)
        A = Arena(self.arena_t, self.moe_area, self.A.end)
        ffn = A.take(KT, SEQ)
        with nc.Block() as block:
            @block.vector
            def _(dve):
                for b in range(4):
                    dve.tensor_copy(ffn[:, 2 * b:2 * b + 2, :], ps[:, 4 + b, :].rearrange("p (a t) -> p a t", a=2))
        self.ffn = ffn
        self.add_normed("ffn_post", ffn, self.P_("ffn_post"), self.mod2[:, 40:48, 0], A)

    def finish(self):
        nc, ps = self.nc, self.ps
        A = Arena(self.arena_t, self.work, self.A.end)
        res = A.take(2, D)
        S = lambda n: self.sem("finish_" + n)
        turned, kept, stored = S("turned"), S("kept"), S("stored")
        with nc.Block() as block:
            @block.tensor
            def _(pe):
                for c in range(2):
                    for k in range(KT):
                        ins = pe.transpose(ps[:, c * 2 + k // 4, k % 4 * P:(k % 4 + 1) * P], self.xT[:, k, c * P:(c + 1) * P], self.ident)
                    ins.then_inc(turned, 1)

            @block.vector
            def _(dve):
                for c in range(2):
                    dve.wait_ge(turned, c + 1)
                    dve.tensor_copy(res[:, c, :], ps[:, 2 * c:2 * c + 2, :].rearrange("p b n -> p (b n)")).then_inc(kept, 1)

            @block.sync
            def _(sp):
                for c in range(2):
                    sp.wait_ge(kept, c + 1)
                    sp.dma_start(self.out[0, c * P:(c + 1) * P, :], res[:, c, :]).then_inc(stored, 16)
                sp.wait_ge(stored, 32)




def build_program(nc, tensors, out):
    Net(nc, shaped(tensors), out).build()


def kernel(**inputs):
    import concourse.bacc as bacc
    from concourse.bass_utils import run_bass_kernel_spmd

    nc = bacc.Bacc("TRN2", target_bir_lowering=False, num_devices=1)
    arrays, tensors = {}, {}
    for name, a in list(inputs.items()) + list(constants().items()):
        a = np.ascontiguousarray(a)
        arrays["in_" + name] = a
        tensors[name] = nc.dram_tensor("in_" + name, a.shape, mybir.dt.from_np(a.dtype), kind="ExternalInput").ap()
    out = nc.dram_tensor("out_0", (1, SEQ, D), F32, kind="ExternalOutput").ap()
    build_program(nc, tensors, out)
    r = run_bass_kernel_spmd(nc, [arrays], core_ids=[0])
    return r.results[0]["out_0"]
```
